# Optimizing a Trainium2 kernel written in Bass

```python
import math
import jax, jax.numpy as jnp
from jax import lax
import numpy as np

D_MODEL = 1024
BATCH = 1
SEQ = 512
DEPTH = 2

N_MEM = 256
N_A_LAYERS = DEPTH // 2
N_B_LAYERS = DEPTH - N_A_LAYERS
QBLOCK = 128

TOK_HEADS = 12
HEAD_DIM = 64
MEM_HEADS = 4
MEM_HEAD_DIM = 64
TOK_WIDTH = TOK_HEADS * HEAD_DIM
MEM_WIDTH = MEM_HEADS * MEM_HEAD_DIM
MIX_WIDTH = TOK_WIDTH + MEM_WIDTH

MLA_Q_RANK = 256
MLA_KV_RANK = 128
MLA_NOPE = 64
MLA_ROPE = 32
MLA_V = HEAD_DIM
ROPE_THETA = 10000.0
MLA_IN = MLA_Q_RANK + MLA_KV_RANK + MLA_ROPE + MEM_WIDTH

NSA_GROUPS = 2
NSA_HPG = TOK_HEADS // NSA_GROUPS
NSA_BRANCHES = 3
CMP_LEN = 32
CMP_STRIDE = 16
CMP_HIDDEN = 256
SEL_LEN = 64
SEL_TOPK = 16
WINDOW = 512
NSA_IN = TOK_WIDTH + TOK_HEADS * NSA_BRANCHES + MEM_WIDTH
NSA_KV = NSA_BRANCHES * 2 * NSA_GROUPS * HEAD_DIM

D_FF = 2816

DN_ALPHA = (2 * DEPTH) ** 0.25
DN_BETA = (8 * DEPTH) ** -0.25

LN_EPS = 1e-5
RMS_EPS = 1e-6
NEG = -1e30
FORCE_BONUS = 1e4


def layer_norm(x, g, b):
    xf = x.astype(jnp.float32)
    mu = jnp.mean(xf, -1, keepdims=True)
    var = jnp.mean(jnp.square(xf - mu), -1, keepdims=True)
    return ((xf - mu) * lax.rsqrt(var + LN_EPS) * g + b).astype(x.dtype)

def rms_norm(x, g):
    xf = x.astype(jnp.float32)
    return (xf * lax.rsqrt(jnp.mean(xf * xf, -1, keepdims=True) + RMS_EPS) * g).astype(x.dtype)

def masked_softmax(s, mask, axis=-1):
    s = jnp.where(mask, s.astype(jnp.float32), NEG)
    m = jnp.max(s, axis=axis, keepdims=True)
    e = jnp.exp(s - m) * mask
    return e / jnp.maximum(jnp.sum(e, axis=axis, keepdims=True), 1e-30)

def swiglu(x, w_gu, w_down):
    g, u = jnp.split(x @ w_gu, 2, axis=-1)
    return (jax.nn.silu(g) * u) @ w_down

def rope(x, pos):
    half = x.shape[-1] // 2
    freq = ROPE_THETA ** (-jnp.arange(half, dtype=jnp.float32) / half)
    ang = pos.astype(jnp.float32)[:, None] * freq[None, :]
    cos, sin = jnp.cos(ang), jnp.sin(ang)
    x1, x2 = x[..., :half], x[..., half:]
    return jnp.concatenate([x1 * cos - x2 * sin, x2 * cos + x1 * sin], -1).astype(x.dtype)

def alibi_slopes(n):
    def pow2(k):
        start = 2.0 ** (-8.0 / k)
        return [start ** (i + 1) for i in range(k)]
    if math.log2(n).is_integer():
        s = pow2(n)
    else:
        c = 2 ** math.floor(math.log2(n))
        s = pow2(c) + pow2(2 * c)[0::2][: n - c]
    return np.asarray(s, np.float32)

def memory_attention(q_mem, mem, w_mem_kv):
    B, T, _ = q_mem.shape
    M = mem.shape[1]
    k, v = jnp.split(mem @ w_mem_kv, 2, axis=-1)
    q = q_mem.reshape(B, T, MEM_HEADS, MEM_HEAD_DIM)
    k = k.reshape(B, M, MEM_HEADS, MEM_HEAD_DIM)
    v = v.reshape(B, M, MEM_HEADS, MEM_HEAD_DIM)
    s = jnp.einsum('bthd,bmhd->bhtm', q, k).astype(jnp.float32) * (MEM_HEAD_DIM ** -0.5)
    p = jax.nn.softmax(s, axis=-1).astype(v.dtype)
    return jnp.einsum('bhtm,bmhd->bthd', p, v).reshape(B, T, MEM_WIDTH)

def mla_mix(x, w_in, q_norm_g, kv_norm_g, w_uq, w_ukv, pos):
    B, T, _ = x.shape
    H = TOK_HEADS
    c_q, c_kv, k_r, q_mem = jnp.split(
        x @ w_in, [MLA_Q_RANK, MLA_Q_RANK + MLA_KV_RANK, MLA_Q_RANK + MLA_KV_RANK + MLA_ROPE], axis=-1)
    q = (rms_norm(c_q, q_norm_g) @ w_uq).reshape(B, T, H, MLA_NOPE + MLA_ROPE).transpose(0, 2, 1, 3)
    q = jnp.concatenate([q[..., :MLA_NOPE], rope(q[..., MLA_NOPE:], pos)], -1)
    kv = (rms_norm(c_kv, kv_norm_g) @ w_ukv).reshape(B, T, H, MLA_NOPE + MLA_V).transpose(0, 2, 1, 3)
    k_nope, v = kv[..., :MLA_NOPE], kv[..., MLA_NOPE:]
    k_r = rope(k_r, pos)
    k = jnp.concatenate([k_nope, jnp.broadcast_to(k_r[:, None], (B, H, T, MLA_ROPE))], -1)
    scale = (MLA_NOPE + MLA_ROPE) ** -0.5
    key_pos = jnp.arange(T)

    def block(c):
        t0 = c * QBLOCK
        tq = t0 + jnp.arange(QBLOCK)
        qb = lax.dynamic_slice_in_dim(q, t0, QBLOCK, axis=2)
        s = jnp.einsum('bhqd,bhkd->bhqk', qb, k) * scale
        p = masked_softmax(s, key_pos[None, :] <= tq[:, None]).astype(v.dtype)
        return jnp.einsum('bhqk,bhkd->bqhd', p, v)

    o = lax.map(block, jnp.arange(T // QBLOCK))
    o = o.transpose(1, 0, 2, 3, 4).reshape(B, T, TOK_WIDTH)
    return o, q_mem

def nsa_shared_kv(h, w_kv, cmp_pos, cmp_w1, cmp_b1, cmp_w2):
    B, T, _ = h.shape
    G = NSA_GROUPS
    kv = (h @ w_kv).reshape(B, T, NSA_BRANCHES, 2, G, HEAD_DIM).transpose(2, 3, 0, 4, 1, 5)
    n_cmp = (T - CMP_LEN) // CMP_STRIDE + 1
    idx = np.arange(n_cmp)[:, None] * CMP_STRIDE + np.arange(CMP_LEN)[None, :]

    def compress(z, j):
        blocks = z[:, :, idx] + cmp_pos[j]
        flat = blocks.reshape(B, G, n_cmp, CMP_LEN * HEAD_DIM)
        return jax.nn.gelu(flat @ cmp_w1[j] + cmp_b1[j]) @ cmp_w2[j]

    kc = compress(kv[0, 0], 0)
    vc = compress(kv[0, 1], 1)
    n_sel = T // SEL_LEN
    ks = kv[1, 0].reshape(B, G, n_sel, SEL_LEN, HEAD_DIM)
    vs = kv[1, 1].reshape(B, G, n_sel, SEL_LEN, HEAD_DIM)
    pad = ((0, 0), (0, 0), (WINDOW, 0), (0, 0))
    kw_pad = jnp.pad(kv[2, 0], pad)
    vw_pad = jnp.pad(kv[2, 1], pad)
    return kc, vc, ks, vs, kw_pad, vw_pad

def nsa_mix(x, w_in, kc, vc, ks, vs, kw_pad, vw_pad, slopes):
    B, T, _ = x.shape
    G, HPG = NSA_GROUPS, NSA_HPG
    q, gates, q_mem = jnp.split(x @ w_in, [TOK_WIDTH, TOK_WIDTH + TOK_HEADS * NSA_BRANCHES], axis=-1)
    q = q.reshape(B, T, G, HPG, HEAD_DIM).transpose(0, 2, 3, 1, 4)
    gates = jax.nn.sigmoid(gates.reshape(B, T, G, HPG, NSA_BRANCHES).transpose(0, 2, 3, 1, 4))
    m = slopes.reshape(G, HPG)[None, :, :, None, None]
    n_cmp = kc.shape[2]
    n_sel = ks.shape[2]
    topk = min(SEL_TOPK, n_sel)
    cmp_start = np.arange(n_cmp) * CMP_STRIDE
    cmp_end = jnp.asarray(cmp_start + CMP_LEN - 1)
    cmp_center = jnp.asarray(cmp_start + (CMP_LEN - 1) * 0.5, dtype=jnp.float32)
    sel_start = np.arange(n_sel) * SEL_LEN
    overlap = np.clip(np.minimum(cmp_start[:, None] + CMP_LEN, sel_start[None, :] + SEL_LEN)
                      - np.maximum(cmp_start[:, None], sel_start[None, :]), 0, None)
    agg = jnp.asarray(overlap / CMP_LEN, dtype=jnp.float32)
    blk = jnp.arange(n_sel)
    scale = HEAD_DIM ** -0.5
    gather = jax.vmap(jax.vmap(lambda blocks, i: blocks[i]))

    def block(c):
        t0 = c * QBLOCK
        tq = t0 + jnp.arange(QBLOCK)
        qb = lax.dynamic_slice_in_dim(q, t0, QBLOCK, axis=3)
        gb = lax.dynamic_slice_in_dim(gates, t0, QBLOCK, axis=3)
        dist_c = tq[:, None].astype(jnp.float32) - cmp_center[None, :]
        s_c = jnp.einsum('bghqd,bgnd->bghqn', qb, kc) * scale - m * dist_c
        p_c = masked_softmax(s_c, cmp_end[None, :] <= tq[:, None])
        o_c = jnp.einsum('bghqn,bgnd->bghqd', p_c.astype(vc.dtype), vc)
        imp = jnp.einsum('bghqn,nj->bgqj', p_c, agg)
        cur = tq // SEL_LEN
        forced = (blk[None] == 0) | (blk[None] == cur[:, None]) | (blk[None] == cur[:, None] - 1)
        imp = jnp.where(forced, imp + FORCE_BONUS, imp)
        imp = jnp.where(blk[None] * SEL_LEN <= tq[:, None], imp, NEG)
        _, sel = lax.top_k(imp, topk)
        k_sel = gather(ks, sel)
        v_sel = gather(vs, sel)
        pos_s = sel[..., None] * SEL_LEN + jnp.arange(SEL_LEN)
        dist_s = (tq[None, None, :, None, None] - pos_s)[:, :, None]
        s_s = jnp.einsum('bghqd,bgqkld->bghqkl', qb, k_sel) * scale - m[..., None] * dist_s
        p_s = masked_softmax(s_s, dist_s >= 0, axis=(-2, -1))
        o_s = jnp.einsum('bghqkl,bgqkld->bghqd', p_s.astype(v_sel.dtype), v_sel)
        kw = lax.dynamic_slice_in_dim(kw_pad, t0, WINDOW + QBLOCK, axis=2)
        vw = lax.dynamic_slice_in_dim(vw_pad, t0, WINDOW + QBLOCK, axis=2)
        pos_w = t0 - WINDOW + jnp.arange(WINDOW + QBLOCK)
        dist_w = tq[:, None] - pos_w[None, :]
        mask_w = (dist_w >= 0) & (dist_w < WINDOW) & (pos_w[None, :] >= 0)
        s_w = jnp.einsum('bghqd,bgkd->bghqk', qb, kw) * scale - m * dist_w
        p_w = masked_softmax(s_w, mask_w)
        o_w = jnp.einsum('bghqk,bgkd->bghqd', p_w.astype(vw.dtype), vw)
        o = gb[..., 0:1] * o_c + gb[..., 1:2] * o_s + gb[..., 2:3] * o_w
        return o.transpose(0, 3, 1, 2, 4).reshape(B, QBLOCK, TOK_WIDTH)

    o = lax.map(block, jnp.arange(T // QBLOCK))
    o = o.transpose(1, 0, 2, 3).reshape(B, T, TOK_WIDTH)
    return o, q_mem

def first_inputs(seed: int = 0) -> dict:
    key = jax.random.key(seed)
    ks = jax.random.split(key, 20)

    def nrm(k, shape, fan_in, gain=1.0):
        return jax.random.normal(k, shape, jnp.float32) * (gain * fan_in ** -0.5)

    def gain(k, shape):
        return 1.0 + 0.02 * jax.random.normal(k, shape, jnp.float32)

    return {
        "x": jax.random.normal(ks[0], (BATCH, SEQ, D_MODEL), jnp.float32),
        "mem": jax.random.normal(ks[1], (BATCH, N_MEM, D_MODEL), jnp.float32),
        "ln_g": gain(ks[2], (DEPTH, 3, D_MODEL)),
        "ln_b": 0.02 * jax.random.normal(ks[3], (DEPTH, 3, D_MODEL), jnp.float32),
        "ffn_w_gu": nrm(ks[4], (DEPTH, 2, D_MODEL, 2 * D_FF), D_MODEL),
        "ffn_w_down": nrm(ks[5], (DEPTH, 2, D_FF, D_MODEL), D_FF, DN_BETA),
        "w_mem_kv": nrm(ks[6], (DEPTH, D_MODEL, 2 * MEM_WIDTH), D_MODEL),
        "w_out": nrm(ks[7], (DEPTH, MIX_WIDTH, D_MODEL), MIX_WIDTH, DN_BETA),
        "mla_w_in": nrm(ks[8], (N_A_LAYERS, D_MODEL, MLA_IN), D_MODEL),
        "mla_q_norm_g": gain(ks[9], (N_A_LAYERS, MLA_Q_RANK)),
        "mla_kv_norm_g": gain(ks[10], (N_A_LAYERS, MLA_KV_RANK)),
        "mla_w_uq": nrm(ks[11], (N_A_LAYERS, MLA_Q_RANK, TOK_HEADS * (MLA_NOPE + MLA_ROPE)), MLA_Q_RANK),
        "mla_w_ukv": nrm(ks[12], (N_A_LAYERS, MLA_KV_RANK, TOK_HEADS * (MLA_NOPE + MLA_V)), MLA_KV_RANK),
        "nsa_w_in": nrm(ks[13], (N_B_LAYERS, D_MODEL, NSA_IN), D_MODEL),
        "nsa_w_kv": nrm(ks[14], (D_MODEL, NSA_KV), D_MODEL),
        "cmp_pos": 0.1 * jax.random.normal(ks[15], (2, CMP_LEN, HEAD_DIM), jnp.float32),
        "cmp_w1": nrm(ks[16], (2, CMP_LEN * HEAD_DIM, CMP_HIDDEN), CMP_LEN * HEAD_DIM),
        "cmp_b1": 0.02 * jax.random.normal(ks[17], (2, CMP_HIDDEN), jnp.float32),
        "cmp_w2": nrm(ks[18], (2, CMP_HIDDEN, HEAD_DIM), CMP_HIDDEN),
    }

def first_block(x, mem, ln_g, ln_b, ffn_w_gu, ffn_w_down, w_mem_kv, w_out,
              mla_w_in, mla_q_norm_g, mla_kv_norm_g, mla_w_uq, mla_w_ukv,
              nsa_w_in, nsa_w_kv, cmp_pos, cmp_w1, cmp_b1, cmp_w2):
    T = x.shape[1]
    pos = jnp.arange(T)
    slopes = jnp.asarray(alibi_slopes(TOK_HEADS))
    shared = None
    for layer in range(DEPTH):
        x = layer_norm(DN_ALPHA * x + 0.5 * swiglu(x, ffn_w_gu[layer, 0], ffn_w_down[layer, 0]),
                       ln_g[layer, 0], ln_b[layer, 0])
        if layer < N_A_LAYERS:
            o_tok, q_mem = mla_mix(x, mla_w_in[layer], mla_q_norm_g[layer], mla_kv_norm_g[layer],
                                   mla_w_uq[layer], mla_w_ukv[layer], pos)
        else:
            b = layer - N_A_LAYERS
            kc, vc, ks_, vs_, kw_pad, vw_pad = shared
            o_tok, q_mem = nsa_mix(x, nsa_w_in[b], kc, vc, ks_, vs_, kw_pad, vw_pad, slopes)
        o_mem = memory_attention(q_mem, mem, w_mem_kv[layer])
        mix = jnp.concatenate([o_tok, o_mem], axis=-1) @ w_out[layer]
        x = layer_norm(DN_ALPHA * x + mix, ln_g[layer, 1], ln_b[layer, 1])
        x = layer_norm(DN_ALPHA * x + 0.5 * swiglu(x, ffn_w_gu[layer, 1], ffn_w_down[layer, 1]),
                       ln_g[layer, 2], ln_b[layer, 2])
        if layer == N_A_LAYERS - 1:
            shared = nsa_shared_kv(x, nsa_w_kv, cmp_pos, cmp_w1, cmp_b1, cmp_w2)
    return x


GRID_W = 64
CTX_LEN = 256
MIX_WIDTH_2 = D_MODEL
S5_WIDTH = (3 * MIX_WIDTH_2) // 4
FNET_WIDTH = MIX_WIDTH_2 - S5_WIDTH
S5_H = 16
S5_GROUPS = S5_WIDTH // S5_H
S5_P = 64
FNET_GROUPS = 4
FNET_GW = FNET_WIDTH // FNET_GROUPS
POOL_WIDTH = MIX_WIDTH_2 // 2
CONV_WIDTH = MIX_WIDTH_2 - POOL_WIDTH
POOL_WINDOWS = (2, 4, 8, 16)
POOL_GROUPS = len(POOL_WINDOWS)
POOL_GW = POOL_WIDTH // POOL_GROUPS
CONV_K = 3
N_EVEN = (DEPTH + 1) // 2
N_ODD = DEPTH // 2
EVEN_IN = S5_WIDTH + FNET_WIDTH + MIX_WIDTH_2
ODD_IN = POOL_WIDTH + 3 * CONV_WIDTH + MIX_WIDTH_2
STEP_MIN = 1e-3
STEP_MAX = 1e-1
EPS = 1e-6
POS_BASE = 10000.0


def rmsnorm(x, g):
    xf = x.astype(jnp.float32)
    y = xf * lax.rsqrt(jnp.mean(xf * xf, axis=-1, keepdims=True) + EPS)
    return (y * g.astype(jnp.float32)).astype(x.dtype)

def ada_params(cond, w, b):
    m = jax.nn.silu(cond) @ w + b
    return jnp.split(m, 3, axis=-1)

def sincos_2d(n_tok, dim):
    rows = n_tok // GRID_W
    r = jnp.arange(rows, dtype=jnp.float32)
    col = jnp.arange(GRID_W, dtype=jnp.float32)
    rr, cc = jnp.meshgrid(r, col, indexing='ij')
    rr = rr.reshape(-1, 1)
    cc = cc.reshape(-1, 1)
    quarter = dim // 4
    omega = POS_BASE ** (-jnp.arange(quarter, dtype=jnp.float32) / quarter)
    return jnp.concatenate([jnp.sin(rr * omega), jnp.cos(rr * omega),
                            jnp.sin(cc * omega), jnp.cos(cc * omega)], axis=-1)

def _linear_recurrence(e1, e2):
    a1, b1 = e1
    a2, b2 = e2
    return a2 * a1, a2 * b1 + b2

def s5_direction(u, lam_re, lam_im, log_step, b_re, b_im, c_re, c_im):
    f32 = jnp.float32
    lam = lax.complex(lam_re.astype(f32), lam_im.astype(f32))
    step = jnp.exp(log_step.astype(f32))[:, None]
    lam_bar = jnp.exp(lam * step)
    b_bar = ((lam_bar - 1.0) / lam)[..., None] * lax.complex(b_re.astype(f32), b_im.astype(f32))
    bu = lax.complex(jnp.einsum('btgh,gph->btgp', u, b_bar.real),
                     jnp.einsum('btgh,gph->btgp', u, b_bar.imag))
    a = jnp.broadcast_to(lam_bar, bu.shape)
    _, s = lax.associative_scan(_linear_recurrence, (a, bu), axis=1)
    return (jnp.einsum('btgp,ghp->btgh', s.real, c_re.astype(f32))
            - jnp.einsum('btgp,ghp->btgh', s.imag, c_im.astype(f32)))

def s5_bidir(u_lat, u_ctx, need_ctx, lam_re, lam_im, log_step, b_re, b_im, c_re, c_im, d_skip):
    bsz, t_lat, _ = u_lat.shape
    t_ctx = u_ctx.shape[1]
    ul = u_lat.astype(jnp.float32).reshape(bsz, t_lat, S5_GROUPS, S5_H)
    uc = u_ctx.astype(jnp.float32).reshape(bsz, t_ctx, S5_GROUPS, S5_H)
    yf = s5_direction(jnp.concatenate([uc, ul], axis=1),
                      lam_re[0], lam_im[0], log_step[0], b_re[0], b_im[0], c_re[0], c_im[0])
    yb = s5_direction(jnp.concatenate([jnp.flip(uc, 1), jnp.flip(ul, 1)], axis=1),
                      lam_re[1], lam_im[1], log_step[1], b_re[1], b_im[1], c_re[1], c_im[1])
    d = d_skip.astype(jnp.float32)
    y_lat = yf[:, t_ctx:] + jnp.flip(yb[:, t_ctx:], 1) + d * ul
    y_lat = y_lat.reshape(bsz, t_lat, S5_WIDTH)
    if not need_ctx:
        return y_lat, None
    y_ctx = yf[:, :t_ctx] + jnp.flip(yb[:, :t_ctx], 1) + d * uc
    return y_lat, y_ctx.reshape(bsz, t_ctx, S5_WIDTH)

def fnet_mix(u, f_w):
    bsz, t, _ = u.shape
    g = u.astype(jnp.float32).reshape(bsz, t, FNET_GROUPS, FNET_GW).transpose(0, 2, 1, 3)
    f = jnp.fft.fft2(g, axes=(-2, -1), norm='ortho').real
    y = jnp.einsum('bgtc,gcd->btgd', f, f_w.astype(jnp.float32))
    return y.reshape(bsz, t, FNET_WIDTH)

def even_branch_out(ya, ub, z, glu_w, glu_b, f_w, w_out):
    ya = jax.nn.gelu(ya)
    ya = ya * jax.nn.sigmoid(ya @ glu_w.astype(jnp.float32) + glu_b.astype(jnp.float32))
    yb = fnet_mix(ub, f_w)
    y = jnp.concatenate([ya, yb], axis=-1).astype(z.dtype) * jax.nn.silu(z)
    return y @ w_out

def even_mixer(hl, hc, need_ctx, w_in, w_out, lam_re, lam_im, log_step, b_re, b_im,
               c_re, c_im, d_skip, glu_w, glu_b, f_w):
    pl = hl @ w_in
    pc = hc @ w_in if need_ctx else hc @ w_in[:, :S5_WIDTH]
    ya_l, ya_c = s5_bidir(pl[..., :S5_WIDTH], pc[..., :S5_WIDTH], need_ctx,
                          lam_re, lam_im, log_step, b_re, b_im, c_re, c_im, d_skip)
    out_l = even_branch_out(ya_l, pl[..., S5_WIDTH:MIX_WIDTH_2], pl[..., MIX_WIDTH_2:],
                            glu_w, glu_b, f_w, w_out)
    if not need_ctx:
        return out_l, None
    out_c = even_branch_out(ya_c, pc[..., S5_WIDTH:MIX_WIDTH_2], pc[..., MIX_WIDTH_2:],
                            glu_w, glu_b, f_w, w_out)
    return out_l, out_c

def centered_mean(v, window):
    bsz, t, ch = v.shape
    s = jnp.concatenate([jnp.zeros((bsz, 1, ch), v.dtype), jnp.cumsum(v, axis=1)], axis=1)
    pos = jnp.arange(t)
    lo = jnp.clip(pos - window // 2, 0, t)
    hi = jnp.clip(pos + window // 2, 0, t)
    total = jnp.take(s, hi, axis=1) - jnp.take(s, lo, axis=1)
    return total / (hi - lo).astype(v.dtype)[None, :, None]

def pool_mix(u, p_w, p_scale):
    bsz, t, _ = u.shape
    g = u.astype(jnp.float32).reshape(bsz, t, POOL_GROUPS, POOL_GW)
    pooled = jnp.stack([centered_mean(g[:, :, i], POOL_WINDOWS[i]) - g[:, :, i]
                        for i in range(POOL_GROUPS)], axis=2)
    y = jnp.einsum('btgc,gcd->btgd', pooled, p_w.astype(jnp.float32)).reshape(bsz, t, POOL_WIDTH)
    return (y * p_scale.astype(jnp.float32)).astype(u.dtype)

def short_conv(v, w):
    return lax.conv_general_dilated(v, w[:, None, :].astype(v.dtype), window_strides=(1,),
                                    padding=[(CONV_K // 2, CONV_K // 2)],
                                    dimension_numbers=('NWC', 'WIO', 'NWC'),
                                    feature_group_count=v.shape[-1])

def odd_mixer(h, w_in, w_out, p_w, p_scale, conv_w):
    p = h @ w_in
    o1 = POOL_WIDTH
    o2 = o1 + CONV_WIDTH
    o3 = o2 + CONV_WIDTH
    o4 = o3 + CONV_WIDTH
    y_c = pool_mix(p[..., :o1], p_w, p_scale)
    c_gate, x_path, b_gate, z = p[..., o1:o2], p[..., o2:o3], p[..., o3:o4], p[..., o4:]
    y_d = b_gate * short_conv(c_gate * x_path, conv_w)
    y = jnp.concatenate([y_c, y_d], axis=-1) * jax.nn.silu(z)
    return y @ w_out

def second_inputs(seed: int = 0) -> dict:
    key = jax.random.key(seed)
    ks = jax.random.split(key, 26)
    f32 = jnp.float32
    D = D_MODEL

    def nrm(k, shape, s):
        return jax.random.normal(k, shape, f32) * s

    s5_state_shape = (N_EVEN, 2, S5_GROUPS, S5_P)
    return {
        'x': nrm(ks[0], (BATCH, SEQ, D), 1.0),
        'c': nrm(ks[1], (BATCH, D), 1.0),
        'ctx': nrm(ks[2], (BATCH, CTX_LEN, D), 1.0),
        'c_ctx': nrm(ks[3], (D,), 1.0),
        'norm_g': 1.0 + nrm(ks[4], (DEPTH, D), 0.02),
        'ada_w': nrm(ks[5], (DEPTH, D, 3 * D), 0.5 * D ** -0.5),
        'ada_b': nrm(ks[6], (DEPTH, 3 * D), 0.02),
        'even_w_in': nrm(ks[7], (N_EVEN, D, EVEN_IN), D ** -0.5),
        'even_w_out': nrm(ks[8], (N_EVEN, MIX_WIDTH_2, D), MIX_WIDTH_2 ** -0.5),
        's5_lam_re': -0.5 + nrm(ks[9], s5_state_shape, 0.01),
        's5_lam_im': jnp.pi * jnp.arange(S5_P, dtype=f32) + nrm(ks[10], s5_state_shape, 0.01),
        's5_log_step': jax.random.uniform(ks[11], (N_EVEN, 2, S5_GROUPS), f32,
                                          math.log(STEP_MIN), math.log(STEP_MAX)),
        's5_b_re': nrm(ks[12], (N_EVEN, 2, S5_GROUPS, S5_P, S5_H), (2 * S5_H) ** -0.5),
        's5_b_im': nrm(ks[13], (N_EVEN, 2, S5_GROUPS, S5_P, S5_H), (2 * S5_H) ** -0.5),
        's5_c_re': nrm(ks[14], (N_EVEN, 2, S5_GROUPS, S5_H, S5_P), S5_P ** -0.5),
        's5_c_im': nrm(ks[15], (N_EVEN, 2, S5_GROUPS, S5_H, S5_P), S5_P ** -0.5),
        's5_d': 1.0 + nrm(ks[16], (N_EVEN, S5_GROUPS, S5_H), 0.1),
        's5_glu_w': nrm(ks[17], (N_EVEN, S5_WIDTH, S5_WIDTH), S5_WIDTH ** -0.5),
        's5_glu_b': nrm(ks[18], (N_EVEN, S5_WIDTH), 0.02),
        'fnet_w': nrm(ks[19], (N_EVEN, FNET_GROUPS, FNET_GW, FNET_GW), FNET_GW ** -0.5),
        'odd_w_in': nrm(ks[20], (N_ODD, D, ODD_IN), D ** -0.5),
        'odd_w_out': nrm(ks[21], (N_ODD, MIX_WIDTH_2, D), MIX_WIDTH_2 ** -0.5),
        'pool_w': nrm(ks[22], (N_ODD, POOL_GROUPS, POOL_GW, POOL_GW), POOL_GW ** -0.5),
        'pool_scale': 1.0 + nrm(ks[23], (N_ODD, POOL_WIDTH), 0.1),
        'conv_w': nrm(ks[24], (N_ODD, CONV_K, CONV_WIDTH), CONV_K ** -0.5),
        'final_g': 1.0 + nrm(ks[25], (D,), 0.02),
    }

def second_block(x, c, ctx, c_ctx, norm_g, ada_w, ada_b, even_w_in, even_w_out,
              s5_lam_re, s5_lam_im, s5_log_step, s5_b_re, s5_b_im, s5_c_re, s5_c_im,
              s5_d, s5_glu_w, s5_glu_b, fnet_w, odd_w_in, odd_w_out, pool_w,
              pool_scale, conv_w, final_g):
    n_tok = x.shape[1]
    xl = x + sincos_2d(n_tok, x.shape[-1]).astype(x.dtype)[None]
    xc = ctx
    need_ctx = [any(j % 2 == 0 for j in range(l + 1, DEPTH)) for l in range(DEPTH)]
    for l in range(DEPTH):
        i = l // 2
        shift, scale, gate = ada_params(c, ada_w[l], ada_b[l])
        hl = rmsnorm(xl, norm_g[l]) * (1.0 + scale[:, None]) + shift[:, None]
        use_ctx_in = (l % 2 == 0) or need_ctx[l]
        if use_ctx_in:
            shift_c, scale_c, gate_c = ada_params(c_ctx, ada_w[l], ada_b[l])
            hc = rmsnorm(xc, norm_g[l]) * (1.0 + scale_c) + shift_c
        if l % 2 == 0:
            out_l, out_c = even_mixer(hl, hc, need_ctx[l], even_w_in[i], even_w_out[i],
                                      s5_lam_re[i], s5_lam_im[i], s5_log_step[i],
                                      s5_b_re[i], s5_b_im[i], s5_c_re[i], s5_c_im[i],
                                      s5_d[i], s5_glu_w[i], s5_glu_b[i], fnet_w[i])
        else:
            out_l = odd_mixer(hl, odd_w_in[i], odd_w_out[i], pool_w[i], pool_scale[i], conv_w[i])
            out_c = (odd_mixer(hc, odd_w_in[i], odd_w_out[i], pool_w[i], pool_scale[i], conv_w[i])
                     if need_ctx[l] else None)
        xl = xl + gate[:, None] * out_l.astype(xl.dtype)
        if need_ctx[l]:
            xc = xc + gate_c * out_c.astype(xc.dtype)
    return rmsnorm(xl, final_g)


def setup_inputs(seed=0):
    out = dict(first_inputs(seed))
    for name, value in second_inputs(seed + 1).items():
        if name != "x":
            out[name + "_2"] = value
    return out


def reference(
    x, mem, ln_g, ln_b, ffn_w_gu, ffn_w_down, w_mem_kv, w_out, mla_w_in, mla_q_norm_g,
    mla_kv_norm_g, mla_w_uq, mla_w_ukv, nsa_w_in, nsa_w_kv, cmp_pos, cmp_w1, cmp_b1, cmp_w2,
    c_2, ctx_2, c_ctx_2, norm_g_2, ada_w_2, ada_b_2, even_w_in_2, even_w_out_2, s5_lam_re_2,
    s5_lam_im_2, s5_log_step_2, s5_b_re_2, s5_b_im_2, s5_c_re_2, s5_c_im_2, s5_d_2, s5_glu_w_2,
    s5_glu_b_2, fnet_w_2, odd_w_in_2, odd_w_out_2, pool_w_2, pool_scale_2, conv_w_2, final_g_2,
):
    x = first_block(
        x, mem, ln_g, ln_b, ffn_w_gu, ffn_w_down, w_mem_kv, w_out, mla_w_in, mla_q_norm_g,
        mla_kv_norm_g, mla_w_uq, mla_w_ukv, nsa_w_in, nsa_w_kv, cmp_pos, cmp_w1, cmp_b1, cmp_w2,
    )
    return second_block(
        x, c_2, ctx_2, c_ctx_2, norm_g_2, ada_w_2, ada_b_2, even_w_in_2, even_w_out_2,
        s5_lam_re_2, s5_lam_im_2, s5_log_step_2, s5_b_re_2, s5_b_im_2, s5_c_re_2, s5_c_im_2,
        s5_d_2, s5_glu_w_2, s5_glu_b_2, fnet_w_2, odd_w_in_2, odd_w_out_2, pool_w_2,
        pool_scale_2, conv_w_2, final_g_2,
    )


_drawn_inputs = setup_inputs


def setup_inputs(seed=0):
    import zlib

    import numpy as np

    out = dict(_drawn_inputs(seed))
    spreads = {}
    factors = {'mem': 2.69,
     'mla_q_norm_g': 8.0,
     'mla_kv_norm_g': 8.0,
     'cmp_pos': 6.988,
     'cmp_b1': 8.0,
     'ctx_2': 64.0,
     'c_ctx_2': 64.0,
     'norm_g_2': 8.0,
     'ada_b_2': 3.833,
     's5_lam_re_2': 64.0,
     's5_lam_im_2': 40.432,
     's5_log_step_2': 56.784,
     's5_b_re_2': 51.672,
     's5_b_im_2': 45.44,
     's5_c_re_2': 54.96,
     's5_c_im_2': 54.704,
     's5_d_2': 7.831,
     's5_glu_w_2': 3.008,
     's5_glu_b_2': 43.049,
     'pool_scale_2': 40.747,
     'final_g_2': 7.966}
    for name, (base, spread) in spreads.items():
        noise = np.random.default_rng([zlib.crc32(name.encode()), seed]).standard_normal(out[name].shape)
        drawn = base * np.exp(spread * noise) if base else spread * noise
        out[name] = __import__('jax').numpy.asarray(drawn.astype(out[name].dtype))
    for name, factor in factors.items():
        out[name] = (out[name] * factor).astype(out[name].dtype)
    return out
```

```python
from contextlib import ExitStack

import numpy as np

import concourse.bass as bass
from concourse import mybir

F32 = mybir.dt.float32
F32R = mybir.dt.float32r
I32 = mybir.dt.int32
ACT = mybir.ActivationFunctionType
ALU = mybir.AluOpType
AX = mybir.AxisListType

P = 128
D = 1024
T = 512
M = 256
KD = D // P
TT = T // P
MT = M // P
DFF = 2816
FT = DFF // P
HEADS, HD = 12, 64
MEM_HEADS = 4
TOKW = HEADS * HD
QR, ROPE = 256, 32
QK = HD + ROPE
GROUPS, HPG = 2, 6
CMP_LEN, CMP_STRIDE, CMP_HID = 32, 16, 256
NCMP = (T - CMP_LEN) // CMP_STRIDE + 1
NPAD = 32
SEL_SCALE = HD ** -0.5
MLA_SCALE = QK ** -0.5
ALPHA = (2 * 2) ** 0.25
NEG = -1e30
S5G, S5H, S5P = 48, 16, 64
L = 8
CTX = 256
NCL, NCC = T // L, CTX // L
NC = NCC + NCL
GT = 8
S5T = S5G // GT
STRIP = 2 * L + 1
FNW = 256
POOL_WINDOWS = (2, 4, 8, 16)

PAN = 8 * P
CHUNKS = (8, 8, 6)
STAGES = (("mem", 8), ("ffn0", 68), ("mla", 6), ("wo0", 8), ("ffn1", 68), ("kv", 6), ("ffn2", 68),
          ("nsa", 9), ("wo1", 8), ("ffn3", 68), ("even", 16), ("glu", 6), ("ewo", 8), ("odd", 24), ("owo", 8))
BASE = {}
_n = 0
for _name, _count in STAGES:
    BASE[_name] = _n
    _n += _count
PANELS = _n


def alibi(n):
    c = 2 ** int(np.floor(np.log2(n)))
    s = [(2.0 ** (-8.0 / c)) ** (i + 1) for i in range(c)]
    s2 = [(2.0 ** (-8.0 / (2 * c))) ** (i + 1) for i in range(2 * c)]
    return np.asarray(s + s2[0::2][: n - c], np.float32)


def constants():
    f = np.float32
    c = {}
    c["ident"] = np.eye(P, dtype=f)
    half = ROPE // 2
    freq = 10000.0 ** (-np.arange(half) / half)
    ang = np.arange(T)[None, :] * freq[:, None]
    cos = np.concatenate([np.cos(ang), np.cos(ang)])
    sin = np.concatenate([-np.sin(ang), np.sin(ang)])
    c["rope"] = np.concatenate([cos, sin, cos, sin]).astype(f)
    perm = np.zeros((ROPE, ROPE), f)
    perm[(np.arange(ROPE) + half) % ROPE, np.arange(ROPE)] = 1
    c["perm"] = perm
    dist = np.arange(P)[:, None] + (T - P) - np.arange(T)[None, :]
    c["causal"] = np.where(dist >= 0, 0, NEG).astype(f)
    slopes = alibi(HEADS).astype(np.float64)
    c["alibi"] = np.stack([np.where(dist >= 0, -m * dist / SEL_SCALE, NEG) for m in slopes]).astype(f)
    t = np.arange(T)
    start = np.arange(NCMP) * CMP_STRIDE
    ok = (start + CMP_LEN - 1)[None, :] <= t[:, None]
    okp = np.zeros((T, NPAD), bool)
    okp[:, :NCMP] = ok
    dc = np.zeros((T, NPAD))
    dc[:, :NCMP] = t[:, None] - (start + (CMP_LEN - 1) * 0.5)[None, :]
    cb = np.stack([np.where(okp, -m * dc / SEL_SCALE, NEG) for m in slopes])
    c["cmpbias"] = cb.reshape(GROUPS, HPG, TT, P, NPAD).transpose(1, 3, 2, 0, 4).reshape(HPG, P, TT * 2 * NPAD).astype(f)
    c["cmpmask"] = okp.reshape(TT, P, NPAD).transpose(1, 0, 2).reshape(P, TT * NPAD).astype(f)
    rows, grid = T // 64, 64
    rr, cc = np.meshgrid(np.arange(rows), np.arange(grid), indexing="ij")
    om = 10000.0 ** (-np.arange(D // 4) / (D // 4))
    rr, cc = rr.reshape(-1, 1), cc.reshape(-1, 1)
    pe = np.concatenate([np.sin(rr * om), np.cos(rr * om), np.sin(cc * om), np.cos(cc * om)], -1)
    c["sincos"] = pe.T.reshape(KD, P, T).transpose(1, 0, 2).reshape(P, KD * T).astype(f)
    k = np.arange(64)
    a = 2 * np.pi * np.outer(k, k) / 64
    bd = np.zeros((P, 2 * P))
    for b in range(2):
        s = slice(64 * b, 64 * b + 64)
        bd[s, 64 * b:64 * b + 64] = np.cos(a)
        bd[s, P + 64 * b:P + 64 * b + 64] = -np.sin(a)
    c["dftc"] = bd.astype(f)
    at = 2 * np.pi * (np.outer(t, t) % T) / T
    norm = 1 / np.sqrt(T * 64)
    dt = np.stack([np.cos(at), np.sin(at)]) * norm
    c["dftt"] = dt.reshape(2, TT, P, T).transpose(2, 0, 1, 3).reshape(P, 2 * TT * T).astype(f)
    inv = np.zeros((4, T))
    for i, w in enumerate(POOL_WINDOWS):
        inv[i] = 1.0 / (np.clip(t + w // 2, 0, T) - np.clip(t - w // 2, 0, T))
    c["poolinv"] = np.ascontiguousarray(np.broadcast_to(inv[None], (P, 4, T)).reshape(P, 4 * T)).astype(f)
    sel = np.zeros((2, P), f)
    sel[0, :64] = 1
    sel[1, 64:] = 1
    c["dirsel"] = sel
    return c

VECTORS = (("norm_g_2", "l (k p) -> (l k) p"), ("ada_b_2", "l (k p) -> (l k) p"), ("final_g_2", "(k p) -> k p"),
           ("s5_glu_b_2", "o (k p) -> (o k) p"), ("pool_scale_2", "o (k p) -> (o k) p"), ("conv_w_2", "o c (k p) -> (o c k) p"),
           ("cmp_b1", "j (k p) -> (j k) p"), ("mla_q_norm_g", "o (k p) -> (o k) p"), ("mla_kv_norm_g", "o (k p) -> (o k) p"),
           ("c_2", "o (k p) -> (o k) p"), ("c_ctx_2", "(k p) -> k p"))
COL_LOADS = 2 + len(VECTORS) + 2

STILES = ((3, 4, 0), (2, 5, 0), (0, 5, 3 * P), (1, 6, 0))
POFF = {3: 0, 2: 4 * P, 0: 7 * P, 1: 8 * P}
TBLOCKS = tuple((0, q * P, q, 0) for q in range(4)) + tuple((1, (q - 1) * P, q, 1) for q in range(1, 4)) + (
    (1, 3 * P, 3, 3),) + tuple((2, (q - 2) * P, q, 2) for q in range(2, 4))
PTOFF = {(q, kb): bank * T + col for bank, col, q, kb in TBLOCKS}

PAD = 16
S5_LOADS = 13
MAGIC = 1.5 * 2.0 ** 23
LN2 = (0.693359375, float(np.log(2.0) - 0.693359375))
TURN = (6.28125, float(np.float32(2 * np.pi - 6.28125)), float(2 * np.pi - 6.28125 - np.float32(2 * np.pi - 6.28125)))
ODD_COLS = tuple(range(0, 4 * P, P)) + tuple((4 + 4 * e + k) * P for k in range(4) for e in range(3)) + tuple(range(2 * D, 3 * D, P))
UP_PARTS = ((0, 4), (0, 2, 4), (0, 3))


def kv_count(g):
    if g < 6:
        return g + 1, g + 1
    return 6 + (g - 6) // 2 + 1, 6 + (g - 5) // 2




def program(nc, A, C, out, scratch):
    ctx = ExitStack()
    with ctx:
        def sb(name, shape, dt=F32):
            return ctx.enter_context(nc.sbuf_tensor(name, shape, dt))

        def sem(name):
            return ctx.enter_context(nc.semaphore(name))

        raw = sb("raw", [P, 4, PAN])
        wh = sb("wh", [P, 2, PAN], F32R)
        wl = sb("wl", [P, 2, PAN], F32R)
        XT = sb("XT", [P, KD, T])
        XH = sb("XH", [P, KD, T], F32R)
        XL = sb("XL", [P, KD, T], F32R)
        IDENT = sb("IDENT", [P, P])
        ONES = sb("ONES", [P, P])
        EPS = sb("EPS", [P, 3])
        COL = sb("COL", [P, 96 + 117])
        POS = sb("POS", [P, 2, CMP_LEN])
        ACC = sb("ACC", [P, T])
        NS = sb("NS", [P, 6, T])
        SQ, SD, RST = NS[:, 0:2, :], NS[:, 2:4, :], NS[:, 4:6, :]
        KM = sb("KM", [P, 2, 2, M])
        VM = sb("VM", [P, 2, MT, M])
        CS = sb("CS", [P, KD, 2])
        MOD = sb("MOD", [P, 2, 24, 2])
        AG = sb("AG", [P, 2, KD, 2])
        L8 = sb("L8", [P, 2, 2, S5G])
        CSS = sb("CSS", [P, 4])
        ps = ctx.enter_context(nc.psum_tensor("ps", [P, 8, T], F32))

        YB = KM[:].rearrange("p l j m -> p (l j m)").rearrange("p (j t) -> p j t", j=2)
        SCM = SQ[:, 0, 0:4 * S5G].rearrange("p (a r g) -> p a r g", a=2, r=2)
        SCA = SQ[:, 1, 0:2 * S5G].rearrange("p (r g) -> p r g", r=2)

        def phase():
            return ExitStack()

        with phase() as ph:
            def pb(name, shape, dt=F32):
                return ph.enter_context(nc.sbuf_tensor(name, shape, dt))
            XN = pb("XN", [P, TT, D])
            MN = pb("MN", [P, MT, D])
            MH = pb("MH", [P, KD, M], F32R)
            ML = pb("ML", [P, KD, M], F32R)
            MV = pb("MV", [P, 4, M])
            CN1 = pb("CN1", [96, P])
            CN2 = pb("CN2", [117, P])
            PN = pb("PN", [64, 2, HD])
        with phase() as ph:
            HH = pb("HH", [P, 8, T], F32R)
            HL = pb("HL", [P, 8, T], F32R)
            SG = pb("SG", [P, 2, T])
            HF = pb("HF", [P, 2, T])
            with ExitStack() as ph:
                Z = pb("Z", [S5H, GT, (STRIP - 2) * S5H])
                PS5 = pb("PS5", [P, 3, S5G])
                TS5 = pb("TS5", [P, 12, S5G])
                KI5 = pb("KI5", [P, S5G], I32)
                PC = pb("PC", [P, 2, S5G, L])
                PB = pb("PB", [P, 2, S5G, L])
                FB5 = pb("FB5", [P, 2, S5G])
                BB = pb("BB", [P, 2, S5G, S5H])
                CR = pb("CR", [P, 2, S5G, S5H])
                DT = pb("DT", [S5H, S5G])
                PW = RST.rearrange("p s t -> p (s t)")[:, 0:2 * (L + 1) * S5G].rearrange("p (r k g) -> p r k g", r=2, k=L + 1)
                T1 = SQ.rearrange("p s t -> p (s t)")
                T2 = SD.rearrange("p s t -> p (s t)")
                DD = ACC[0:S5H, 0:GT * S5H].rearrange("p (g h) -> p g h", g=GT)
                BK = pb("BK", [P, 2, GT, P])
                BT = pb("BT", [P, 2, GT, P])
                SW = pb("SW", [P, 2, GT, STRIP * S5H])
                flat = SW[:].rearrange("p a b c -> p (a b c)")
                BN = flat[:, 0:1536].rearrange("p (r g h) -> p r g h", r=2, g=S5G)
                CN = flat[:, 1536:3072].rearrange("p (r t d q) -> p r t d q", r=2, t=6, d=2)
                LAMN = flat[0:S5G, 3072:3328].rearrange("g (r c) -> g r c", r=2)
                LSN = flat[0:2, 3328:3328 + S5G]
                DN = flat[0:S5G, 3400:3400 + S5H]
                DSEL = flat[0:2, 3500:3500 + P]
        with phase() as ph:
            O = pb("O", [P, TT, D])
            PR = pb("PR", [P, 2, 1280])
            PT = pb("PT", [P, 2, 1280])
            MX = pb("MX", [P, 2, TT])
            NB = pb("NB", [P, 2, TT])
            SM = pb("SM", [P, 2, TT])
            RS = pb("RS", [P, 2, TT])
            QM = pb("QM", [P, 2, T])
            with ExitStack() as ph:
                ROT = pb("ROT", [P, T])
                PERM = pb("PERM", [ROPE, ROPE])
                CAUS = pb("CAUS", [P, T])
                CQ = pb("CQ", [P, 2, T])
                CKV = pb("CKV", [P, T])
                KR = ACC[0:ROPE, :]
                KT = pb("KT", [QK, HEADS, T])
                V = pb("V", [P, TT, TOKW])
                WUKV = pb("WUKV", [P, 2, HEADS, HD])
                WQ = pb("WQ", [P, 2, 2, P])
                QT = pb("QT", [QK, 2, T])
                RT = pb("RT", [QK, 2, T])
                KR2 = RT[0:ROPE]
            with ExitStack() as mid:
                def mb(name, shape, dt=F32):
                    return mid.enter_context(nc.sbuf_tensor(name, shape, dt))
                AW = mb("AW", [P, 2, KD, 2 * P])
                KS = mb("KS", [P, T])
                KW = mb("KW", [P, T])
                VS = mb("VS", [P, TT, P])
                VW = mb("VW", [P, TT, P])
                KCB = mb("KCB", [P, 2 * NPAD])
                VCB = mb("VCB", [2 * NPAD, P])
                with ExitStack() as ph:
                    ZC = pb("ZC", [P, 2, T])
                    VT = pb("VT", [P, 2, T])
                    W1 = (AW[:].rearrange("p s k c -> p (s k) c"), pb("W1", [P, CMP_LEN // 2, CMP_HID])[:])
                    ZB = pb("ZB", [P, 2, CMP_LEN // 2, GROUPS, NPAD])
                    H1 = pb("H1", [P, 2, 2, GROUPS, NPAD])
                    W2 = pb("W2", [P, 2, 2, HD])
                with ExitStack() as ph:
                    QP = pb("QP", [P, HPG, T])
                    QS = pb("QS", [P, 2, T])
                    BIAS = pb("BIAS", [P, 2, GROUPS, T])
                    CB = pb("CB", [P, 2, TT * GROUPS * NPAD])
                    CMASK = pb("CMASK", [P, TT * NPAD])
                    SC = pb("SC", [P, TT, GROUPS, NPAD])
                    MC = pb("MC", [P, TT, GROUPS])
                    SMC = pb("SMC", [P, TT, GROUPS])
                    GTT = pb("GTT", [HEADS * 3, T])
                    G = pb("G", [P, 3, HPG, TT, GROUPS])
                    PTC = pb("PTC", [2 * NPAD, T])
                    W4 = pb("W4", [P, 2, TT])
        with phase() as ph:
            U = pb("U", [P, S5G, NC])
            H = pb("H", [P, 2, S5G, NC])
            UT = H[:].rearrange("p r g c -> p (r g c)")[:, 0:6 * (CTX + T)].rearrange("p (j t c) -> p j t c", j=6, t=L)
            ZS = pb("ZS", [P, KD, T])
            with ExitStack() as late:
                def lb(name, shape, dt=F32):
                    return late.enter_context(nc.sbuf_tensor(name, shape, dt))
                UB = lb("UB", [P, 2, T])
                FB = UB
                with ExitStack() as ph:
                    BS = pb("BS", [P, 2, 2, GT, P])
                with ExitStack() as ph:
                    FA = pb("FA", [P, TT, 2, 2 * P])
                    DFTT = pb("DFTT", [P, 2, TT, T])
                    DFTC = pb("DFTC", [P, 2 * P])
                    FW = pb("FW", [P, 2, P])
            with ExitStack() as ph:
                MW = pb("MW", [P, 2, 3, GT, P])
                SS = pb("SS", [P, 2, 2, GT, NCL])
            YS = NS[:].rearrange("p s t -> p (s t)").rearrange("p (g c) -> p g c", g=S5G)
            with ExitStack() as ph:
                YH = pb("YH", [P, KD, T], F32R)
                YL = pb("YL", [P, KD, T], F32R)
        with phase() as ph:
            pb("feed_forward", [P, 20, T])
            CH = pb("CH", [P, KD, CTX], F32R)
            CL = pb("CL", [P, KD, CTX], F32R)
            SCT = pb("SCT", [P, KD, T])
            CXN = pb("CXN", [P, 2, D])
            CXT = pb("CXT", [P, KD, CTX])
            NT = SCT
        with phase() as ph:
            YT = pb("YT", [P, 6, L, NCL])
            YA = pb("YA", [P, 6, T])
            YF = pb("YF", [P, 2, T])
            SIG = pb("SIG", [P, 2, T])
        with phase() as ph:
            with ExitStack() as ph2:
                NO = ph2.enter_context(nc.sbuf_tensor("NO", [P, KD, T], F32))
            PU = pb("PU", [P, 4, PAD + T + PAD])
            PS = pb("PS", [P, 2, PAD + T + PAD])
            PP = pb("PP", [P, 2, T])
            YQ = pb("YQ", [P, 2, T])
            PINV = pb("PINV", [P, 4, T])
            PWT = pb("PWT", [P, 4, P])
            CG = pb("CG", [P, 2, T])
            CV = pb("CV", [P, 2, T + 2])
            CX = pb("CX", [P, 2, T])
            YO = pb("YO", [P, KD, T])
            ZO = pb("ZO", [P, 2, T])
        with phase() as ph:
            XO = pb("XO", [P, TT, D])

        raw_in = [sem(f"raw_in{s}") for s in range(4)]
        w_hi = sem("w_hi")
        w_lo = sem("w_lo")
        pe_panel = sem("pe_panel")
        taken = [sem(f"taken{s}") for s in range(4)]
        x_split = sem("x_split")
        x_hi = sem("x_hi")
        tr = sem("tr")
        tr_done = sem("tr_done")
        setup = sem("setup")
        ident_in = sem("ident_in")
        x_in = sem("x_in")
        mem_in = sem("mem_in")
        col_in = sem("col_in")
        mem_hi = sem("mem_hi")
        mem_split = sem("mem_split")
        vm_ps = sem("vm_ps")
        vm_ready = sem("vm_ready")
        h_ready = sem("h_ready")
        ln_acc = sem("ln_acc")
        ln_mu = sem("ln_mu")
        ln_c = sem("ln_c")
        sq_ready = sem("sq_ready")
        sq_used = sem("sq_used")
        sd_ready = sem("sd_ready")
        rstd_ready = sem("rstd_ready")
        ln_n = sem("ln_n")
        ln_hi = sem("ln_hi")
        ln_aff = sem("ln_aff")
        mla_in_s = sem("mla_in_s")
        cq_norm = sem("cq_norm")
        kr_ps = sem("kr_ps")
        kr_rot = sem("kr_rot")
        kr_act = sem("kr_act")
        kr_dve = sem("kr_dve")
        kv_ps = sem("kv_ps")
        kv_act = sem("kv_act")
        kv_dve = sem("kv_dve")
        wq_in = [sem(f"wq_in{s}") for s in range(2)]
        q_ps = sem("q_ps")
        q_nope = sem("q_nope")
        q_rot = sem("q_rot")
        q_rope = sem("q_rope")
        s_ps = sem("s_ps")
        s_sb = sem("s_sb")
        nb_ready = sem("nb_ready")
        p_ready = sem("p_ready")
        t_ps = sem("t_ps")
        pt_act = sem("pt_act")
        pt_dve = sem("pt_dve")
        pv_ps = sem("pv_ps")
        rs_ready = sem("rs_ready")
        o_done = sem("o_done")
        mix_ps = sem("mix_ps")
        mix_hi = sem("mix_hi")
        dve_link = sem("dve_link")
        pool_link = sem("pool_link")
        s5_in = sem("s5_in")
        s5_tr = sem("s5_tr")
        cr_out = sem("cr_out")
        s5_dve = sem("s5_dve")
        sin_in = sem("sin_in")
        sin_out = sem("sin_out")
        f_ready = sem("f_ready")
        bk_ready = sem("bk_ready")
        s5_t = sem("s5_t")
        bt_act = sem("bt_act")
        bt_dve = sem("bt_dve")
        s5_z = sem("s5_z")
        z_out = sem("z_out")
        s5_out = sem("s5_out")
        cs_ready = sem("cs_ready")
        aw_in = [sem(f"aw_in{s}") for s in range(2)]
        ada_used = sem("ada_used")
        mod_ready = sem("mod_ready")
        w1_in = sem("w1_in")
        zeros = sem("zeros")
        vt_ps = sem("vt_ps")
        vt_out = sem("vt_out")
        zb_ready = sem("zb_ready")
        hid_ps = sem("hid_ps")
        gelu_out = sem("gelu_out")
        kc_ps = sem("kc_ps")
        kc_out = sem("kc_out")
        g_ps = sem("g_ps")
        g_out = sem("g_out")
        bias_in = [sem(f"bias_in{s}") for s in range(2)]
        cmask_in = sem("cmask_in")
        qs_ready = sem("qs_ready")
        c_ps = sem("c_ps")
        c_sc = sem("c_sc")
        c_sub = sem("c_sub")
        c_exp = sem("c_exp")
        c_mask = sem("c_mask")
        c_sum = sem("c_sum")
        c_p = sem("c_p")
        c_t = sem("c_t")
        c_pt = sem("c_pt")
        c_pv = sem("c_pv")
        c_o = sem("c_o")
        w4_ready = sem("w4_ready")
        cx_in = sem("cx_in")
        sct_ready = sem("sct_ready")
        cx_sd = sem("cx_sd")
        cx_n = sem("cx_n")
        cx_ps = sem("cx_ps")
        cx_f = sem("cx_f")
        cx_hi = sem("cx_hi")
        cx_split = sem("cx_split")
        uc_out = sem("uc_out")
        shuffle_out = sem("shuffle_out")
        shuffle_in = sem("shuffle_in")
        bs_in = [sem(f"bs_in{s}") for s in range(2)]
        b_ps = sem("b_ps")
        h_act = sem("h_act")
        h_dve = sem("h_dve")
        dft_in = sem("dft_in")
        fnet_ps = sem("fnet_ps")
        fnet_out = sem("fnet_out")
        scan = sem("scan")
        mw_in = [sem(f"mw_in{s}") for s in range(2)]
        ss_act = sem("ss_act")
        ss_dve = sem("ss_dve")
        y_ps = sem("y_ps")
        y_sb = sem("y_sb")
        ya_ready = sem("ya_ready")
        ya_hi = sem("ya_hi")
        p1_ready = sem("p1_ready")
        y_full = sem("y_full")
        y_ready = sem("y_ready")
        odd_in = sem("odd_in")
        odd_zero = sem("odd_zero")
        pool_ready = sem("pool_ready")
        pw_ps = sem("pw_ps")
        yc_ready = sem("yc_ready")
        out_ps = sem("out_ps")
        out_sb = sem("out_sb")
        out_done = sem("out_done")

        LN_SQ = {"ffn0": 0, "mla": 8, "wo0": 11, "ffn1": 19, "ffn2": 27, "wo1": 35, "ffn3": 43, "even": 51, "odd": 59, "final": 67}
        LN_NO = {"ffn0": 0, "wo0": 1, "ffn1": 2, "ffn2": 3, "wo1": 4, "ffn3": 5, "even": 6, "odd": 7, "final": 8}
        HI_NO = {"ffn0": 0, "wo0": 1, "ffn1": 2, "ffn2": 3, "wo1": 4, "even": 5, "odd": 6}
        XS = {"ffn0": 0, "mla": 8, "wo0": 16, "ffn1": 24, "kv": 32, "ffn2": 32, "nsa": 40, "wo1": 48, "ffn3": 56, "even": 64,
              "glu": 72, "odd": 78}
        LN_COL = {"ffn0": 0, "wo0": 8, "ffn1": 16, "ffn2": 24, "wo1": 32, "ffn3": 40}

        def wait(eng, s, value):
            if not (isinstance(value, int) and value <= 0):
                eng.wait_ge(s, value)

        def taken_at(stage, j, i=0):
            p = BASE[stage] + j
            return taken[p % 4], p // 4 + 1 + i

        block = ctx.enter_context(nc.Block())

        def nothing(k):
            pass

        @block.sync
        def _(sp):
            def load(stage, j, i, src, nk=8):
                p = BASE[stage] + j
                if not (isinstance(i, int) and p + 4 * i < 4):
                    sp.wait_ge(w_lo, p - 3 + 4 * i)
                dst = raw[:, p % 4, 0:nk * P].rearrange("p (k c) -> p k c", k=nk)
                sp.dma_start(dst, src).then_inc(raw_in[p % 4], 16)

            def rows(w):
                return w.rearrange("(k p) n -> p k n", p=P)

            def plain(stage, w, cols, part=slice(None)):
                v = rows(w)
                for j, c in list(enumerate(cols))[part]:
                    load(stage, j, 0, v[:, :, c:c + P], v.shape[1])

            def ffn(stage, layer, half):
                gu, down = rows(A["ffn_w_gu"][layer, half]), rows(A["ffn_w_down"][layer, half])
                off, f0 = 0, 0
                for nf in CHUNKS:
                    with sp.Fori(0, nf // 2) as i:
                        for j in range(4):
                            c = (j % 2) * DFF + (f0 + j // 2) * P
                            load(stage, off + j, i, gu[:, :, bass.ds(i * (2 * P) + c, P)])
                    off += 2 * nf
                    with sp.Fori(0, KD // 4) as i:
                        for j in range(4):
                            load(stage, off + j, i, down[:, f0:f0 + nf, bass.ds(i * (4 * P) + j * P, P)], nf)
                    off += KD
                    f0 += nf

            sp.dma_start(IDENT[:], C["ident"]).then_inc(ident_in, 16)
            sp.dma_start(MN[:], A["mem"][0].rearrange("(m p) d -> p m d", p=P)).then_inc(mem_in, 16)
            sp.dma_start(XN[:], A["x"][0].rearrange("(t p) d -> p t d", p=P)).then_inc(x_in, 16)
            for layer in range(2):
                v = rows(A["w_mem_kv"][layer])
                for j in range(4):
                    load("mem", 4 * layer + j, 0, v[:, :, j * P:(j + 1) * P])
            ffn("ffn0", 0, 0)
            plain("mla", A["mla_w_in"][0], (0, P, QR, QR + P, QR + P + ROPE, QR + 2 * P + ROPE))
            plain("wo0", A["w_out"][0], range(0, D, P), slice(0, 4))
            sp.wait_ge(pe_panel, BASE["mla"])
            for e in range(2):
                sp.dma_start(WUKV[:, e], A["mla_w_ukv"][0].rearrange("p (h e c) -> p e h c", e=2, c=HD)[:, e]).then_inc(mla_in_s, 16)
            sp.dma_start(ROT[:], C["rope"]).then_inc(mla_in_s, 16)
            sp.dma_start(PERM[:], C["perm"]).then_inc(mla_in_s, 16)
            sp.dma_start(CAUS[:], C["causal"]).then_inc(mla_in_s, 16)
            wuq = A["mla_w_uq"][0].rearrange("(k p) (h c) -> p k h c", p=P, c=QK)

            def load_q(i, s):
                w = wuq[:, :, bass.ds(2 * i + s, 1), :].rearrange("p k o c -> p k (o c)")
                half = HD + ROPE // 2
                if not isinstance(i, int):
                    sp.wait_ge(q_ps, 2 * i + s - 1)
                sp.dma_start(WQ[:, s, :, 0:QK], w).then_inc(wq_in[s], 16)
                sp.dma_start(WQ[:, s, :, QK:QK + ROPE // 2], w[:, :, half:QK]).then_inc(wq_in[s], 16)
                sp.dma_start(WQ[:, s, :, QK + ROPE // 2:P], w[:, :, HD:half]).then_inc(wq_in[s], 16)
            for s in range(2):
                load_q(0, s)
            with sp.Fori(1, HEADS // 2) as i:
                for s in range(2):
                    load_q(i, s)
            plain("wo0", A["w_out"][0], range(0, D, P), slice(4, 8))
            ffn("ffn1", 0, 1)
            plain("kv", A["nsa_w_kv"], range(0, 6 * P, P))
            ffn("ffn2", 1, 0)
            nsa = A["nsa_w_in"][0]
            plain("nsa", nsa, (TOKW, TOKW + 3 * HEADS, TOKW + 3 * HEADS + P) + tuple(range(0, TOKW, P)))
            alibi_pairs = C["alibi"].rearrange("(g j) p t -> j p g t", g=GROUPS)
            sp.wait_ge(pe_panel, BASE["nsa"])
            sp.dma_start(CMASK[:], C["cmpmask"]).then_inc(cmask_in, 16)

            def load_bias(j, s):
                bias = alibi_pairs[bass.ds(j, 1)].rearrange("o p g t -> p (o g) t")
                cmp_bias = C["cmpbias"][bass.ds(j, 1)].rearrange("o p n -> p (o n)")
                if not isinstance(j, int):
                    sp.wait_ge(s_sb, 4 * j + 12)
                    sp.wait_ge(c_sc, 2 * j - 3)
                sp.dma_start(BIAS[:, s], bias).then_inc(bias_in[s], 16)
                sp.dma_start(CB[:, s], cmp_bias).then_inc(bias_in[s], 16)
            for s in range(2):
                load_bias(s, s)
            plain("wo1", A["w_out"][1], range(0, D, P), slice(0, 4))
            with sp.Fori(1, HPG // 2) as i:
                for s in range(2):
                    load_bias(2 * i + s, s)
            plain("wo1", A["w_out"][1], range(0, D, P), slice(4, 8))
            ffn("ffn3", 1, 1)
            plain("even", A["even_w_in_2"][0], range(0, 2 * D, P))
            plain("glu", A["s5_glu_w_2"][0], range(0, 6 * P, P))
            plain("ewo", A["even_w_out_2"][0], range(0, D, P))
            plain("odd", A["odd_w_in_2"][0], ODD_COLS)
            plain("owo", A["odd_w_out_2"][0], range(0, D, P))
            rows_out = out[0].rearrange("(t p) d -> p t d", p=P)
            for half in range(2):
                sp.wait_ge(out_sb, 4 * half + 4)
                sp.dma_start(rows_out[:, :, half * T:(half + 1) * T], XO[:, :, half * T:(half + 1) * T]).then_inc(out_done, 16)
            sp.wait_ge(out_done, 32)

        @block.tensor
        def _(pe):
            def panel(stage, j, i, hi, lo, nk=8, n=T, need=None):
                p = BASE[stage] + j
                pe.wait_ge(w_lo, p + 1 + 4 * i)
                if not (isinstance(i, int) and p + 4 * i < 4):
                    pe.wait_ge(taken[p % 4], p // 4 + i)
                for k in range(nk):
                    if need is not None:
                        pe.wait_ge(*need(k))
                    for a, (w, x) in enumerate(((wh, hi), (wl, hi), (wh, lo))):
                        mm = pe.matmul(ps[:, p % 4, 0:n], w[:, p % 2, k * P:(k + 1) * P], x[:, k, 0:n],
                                       start=(k == 0 and a == 0), stop=(k == nk - 1 and a == 2))
                mm.then_inc(pe_panel, 1)

            def panels(stage, count, base, nk=8):
                first = lambda k: (x_split, base + k + 1)
                if count >= 8:
                    with pe.Fori(0, count // 4) as i:
                        for j in range(4):
                            panel(stage, j, i, XH, XL, nk, need=first if j == 0 else None)
                for j in range(count // 4 * 4 if count >= 8 else 0, count):
                    panel(stage, j, 0, XH, XL, nk, need=first if j == 0 else None)

            def ffn(stage, fill):
                no = int(stage[3])
                off, f0 = 0, 22 * no
                at = 0
                for c, nf in enumerate(CHUNKS):
                    need = lambda k: (x_split, XS[stage] + k + 1)
                    for a, b in zip(UP_PARTS[c], UP_PARTS[c][1:]):
                        with pe.Fori(a, b) as i:
                            for j in range(4):
                                panel(stage, off + j, i, XH, XL, need=need if c == 0 and j == 0 else None)
                        fill(at)
                        at += 1
                    off += 2 * nf
                    need = lambda k: (h_ready, f0 + k + 3)
                    with pe.Fori(0, KD // 4) as i:
                        for j in range(4):
                            panel(stage, off + j, i, HH, HL, nf, need=need if j == 0 else None)
                    if c < 2:
                        fill(at)
                        at += 1
                    off += KD
                    f0 += nf

            def norm(stage):
                no, q0 = LN_NO[stage], LN_SQ[stage]
                pe.wait_ge(ln_acc, 8 * no + 8)
                pe.matmul(ps[:, 4, :], ONES[:], ACC[:], start=True, stop=True).then_inc(ln_mu, 1)
                squares(q0, 8, 5)

            def squares(q0, count, bank, n=T):
                for d in range(count):
                    pe.wait_ge(sq_ready, q0 + d + 1)
                    pe.matmul(ps[:, bank, 0:n], ONES[:], SQ[:, (q0 + d) % 2, 0:n], start=d == 0, stop=d == count - 1
                              ).then_inc(sq_used, 1)

            def probs_t(u, s):
                pe.wait_ge(p_ready, u + 1)
                wait(pe, pt_act, 2 * u)
                wait(pe, pt_dve, u)
                for bank, col, q, kb in TBLOCKS:
                    mm = pe.transpose(ps[:, bank, col:col + P], PR[:, s, POFF[q] + kb * P:POFF[q] + (kb + 1) * P], IDENT[:])
                mm.then_inc(t_ps, 1)

            def pv(u, s, vals):
                pe.wait_ge(pt_act, 2 * u + 2)
                pe.wait_ge(pt_dve, u + 1)
                wait(pe, o_done, u)
                for q in range(TT):
                    for kb in range(q + 1):
                        mm = pe.matmul(ps[:, 7, q * HD:(q + 1) * HD], PT[:, s, PTOFF[q, kb]:PTOFF[q, kb] + P],
                                       vals(kb), start=kb == 0, stop=kb == q)
                mm.then_inc(pv_ps, 1)

            def scores(u, q, keys):
                wait(pe, s_sb, u)
                for t, bank, col in STILES:
                    n = (t + 1) * P
                    mm = pe.matmul(ps[:, bank, col:col + n], q(t), keys(n), start=True, stop=True)
                mm.then_inc(s_ps, 1)

            def mem_scores(u, h, first):
                r = slice((h % 2) * HD, (h % 2) * HD + HD)
                pe.wait_ge(p_ready, u) if not first else wait(pe, s_sb, u)
                for t in range(TT):
                    mm = pe.matmul(ps[:, 4 + t // 2, (t % 2) * M:(t % 2 + 1) * M], QM[r, h // 2, t * P:(t + 1) * P],
                                   KM[r, mem_layer[0], h // 2, :], start=True, stop=True)
                mm.then_inc(s_ps, 1)

            def mem_probs_t(u, s):
                pe.wait_ge(p_ready, u + 1)
                wait(pe, pt_act, 2 * u)
                wait(pe, pt_dve, u)
                for m in range(MT):
                    for t in range(TT):
                        mm = pe.transpose(ps[:, m, t * P:(t + 1) * P], PR[:, s, t * M + m * P:t * M + (m + 1) * P], IDENT[:])
                mm.then_inc(t_ps, 1)

            def mem_pv(u, s, h):
                pe.wait_ge(pt_act, 2 * u + 2)
                pe.wait_ge(pt_dve, u + 1)
                wait(pe, o_done, u)
                for t in range(TT):
                    for m in range(MT):
                        mm = pe.matmul(ps[:, 7, t * HD:(t + 1) * HD], PT[:, s, m * T + t * P:m * T + (t + 1) * P],
                                       VM[:, mem_layer[0], m, h * HD:(h + 1) * HD], start=m == 0, stop=m == MT - 1)
                mm.then_inc(pv_ps, 1)

            def mix_t(base, mix0):
                for k in range(KD):
                    pe.wait_ge(x_split, base + k - 3 if k > 3 else base)
                    for t in range(TT):
                        mm = pe.transpose(ps[:, 4 + k % 4, t * P:(t + 1) * P], O[:, t, k * P:(k + 1) * P], IDENT[:])
                    mm.then_inc(mix_ps, 1)

            def s5_fill(t):
                pe.wait_ge(bk_ready, t + 1)
                wait(pe, z_out, 4 * t)
                for b in range(4):
                    for g in range(4):
                        mm = pe.transpose(ps[:, 4 + b, g * P:(g + 1) * P], BK[:, b // 2, (b % 2) * 4 + g, :], IDENT[:])
                    mm.then_inc(s5_t, 1)
                for b in range(4):
                    if b < 2:
                        pe.wait_ge(bt_act, 2 * t + b + 1)
                    else:
                        pe.wait_ge(bt_dve, 2 * t + b - 1)
                    for e in range(2):
                        g = 2 * b + e
                        for r in range(2):
                            mm = pe.matmul(ps[0:S5H, 4 + b, e * 240:(e + 1) * 240], BB[:, r, t * GT + g, :],
                                           SW[:, r, g, S5H:(STRIP - 1) * S5H], start=r == 0, stop=r == 1)
                    mm.then_inc(s5_z, 1)

            def ada_fill(layer, f):
                if layer == 0 and f == 0:
                    pe.wait_ge(cs_ready, 1)
                if layer == 1 and f == 0:
                    pe.wait_ge(mod_ready, 1)
                for n in (2 * f, 2 * f + 1):
                    pe.wait_ge(aw_in[n % 2], 16 * (6 * layer + n // 2 + 1))
                    for c in range(2):
                        m = 2 * n + c
                        for k in range(KD):
                            mm = pe.matmul(ps[:, 6, 2 * m:2 * m + 2], AW[:, n % 2, k, c * P:(c + 1) * P], CS[:, k, :],
                                           start=k == 0, stop=k == KD - 1)
                    mm.then_inc(ada_used, 1)

            def ffn2_fill(f):
                ada_fill(1, f)
                if f == 0:
                    pe.wait_ge(gelu_out, 4)
                    pe.wait_ge(vt_out, 2)
                    for m in range(2):
                        pe.matmul(ps[0:HD, 4, 0:2 * NPAD], W2[:, 0, m, :], H1[:, 0, m].rearrange("p g n -> p (g n)"), start=m == 0, stop=m == 1)
                    for m in range(2):
                        mm = pe.matmul(ps[0:2 * NPAD, 5, 0:HD], H1[:, 1, m].rearrange("p g n -> p (g n)"), W2[:, 1, m, :], start=m == 0, stop=m == 1)
                    mm.then_inc(kc_ps, 1)

            def ffn3_fill(f):
                if f == 2:
                    pe.wait_ge(cx_n, 2)
                    for k2 in range(4):
                        for e in range(2):
                            for m in range(MT):
                                k = 2 * k2 + e
                                mm = pe.transpose(ps[:, 4 + k2, e * CTX + m * P:e * CTX + (m + 1) * P], CXN[:, m, k * P:(k + 1) * P], IDENT[:])
                        mm.then_inc(cx_ps, 1)

            mem_layer = [0]

            pe.wait_ge(ident_in, 16)
            pe.wait_ge(mem_in, 16)
            for k2 in range(4):
                for e in range(2):
                    for m in range(MT):
                        k = 2 * k2 + e
                        mm = pe.transpose(ps[:, 4 + k2, e * M + m * P:e * M + (m + 1) * P], MN[:, m, k * P:(k + 1) * P], IDENT[:])
                mm.then_inc(tr, 1)
            pe.wait_ge(x_in, 16)
            for k in range(KD):
                if k < 4:
                    pe.wait_ge(mem_split, k + 1)
                else:
                    pe.wait_ge(x_split, k - 3)
                for t in range(TT):
                    mm = pe.transpose(ps[:, 4 + k % 4, t * P:(t + 1) * P], XN[:, t, k * P:(k + 1) * P], IDENT[:])
                mm.then_inc(tr, 1)
            pe.wait_ge(col_in, 16 * COL_LOADS)
            pe.wait_ge(x_split, 5)
            pe.transpose(ps[:, 4, 0:96], CN1[:], IDENT[0:96, 0:96])
            pe.transpose(ps[:, 4, 96:96 + 117], CN2[:], IDENT[0:117, 0:117])
            pe.transpose(ps[:, 4, 256:256 + 64], PN[:].rearrange("a b c -> a (b c)"), IDENT[0:64, 0:64]).then_inc(tr, 1)

            for j in range(8):
                panel("mem", j, 0, MH, ML, n=M, need=(lambda k: (mem_split, k // 2 + 1)) if j == 0 else None)
            for layer in range(2):
                for j in range(2):
                    pe.wait_ge(*taken_at("mem", 4 * layer + 2 + j))
                    if layer == 0 and j == 0:
                        pe.wait_ge(tr_done, 1)
                        pe.wait_ge(x_split, 8)
                    for m in range(MT):
                        mm = pe.transpose(ps[:, 4 + 2 * layer + j, m * P:(m + 1) * P], MV[:, 2 * layer + j, m * P:(m + 1) * P], IDENT[:])
                    mm.then_inc(vm_ps, 1)

            pe.wait_ge(setup, 2)
            pe.wait_ge(s5_in, 16 * S5_LOADS)
            pe.wait_ge(vm_ready, 4)
            for r in range(2):
                pe.transpose(ps[:, 4, r * S5G:(r + 1) * S5G], LAMN[:, r, :], IDENT[0:S5G, 0:S5G])
            pe.matmul(ps[:, 4, 2 * S5G:3 * S5G], DSEL, LSN, start=True, stop=True)
            pe.transpose(ps[0:S5H, 4, 3 * S5G:4 * S5G], DN, IDENT[0:S5G, 0:S5G]).then_inc(s5_tr, 1)
            for n in range(12):
                mm = pe.transpose(ps[:, 5 + n // 4, (n % 4) * P:(n % 4 + 1) * P], CN[:, n // 6, n % 6].rearrange("p d q -> p (d q)"), IDENT[:])
                if n % 4 == 3:
                    mm.then_inc(s5_tr, 1)
            ffn("ffn0", s5_fill)
            pe.wait_ge(z_out, 4 * S5T)
            norm("ffn0")
            for j in range(6):
                panel("mla", j, 0, XH, XL, need=(lambda k: (x_split, XS["mla"] + k + 1)) if j == 0 else None)
                if j == 2:
                    squares(LN_SQ["mla"], 2, 4)
            squares(LN_SQ["mla"] + 2, 1, 5)
            pe.wait_ge(mla_in_s, 80)
            pe.wait_ge(*taken_at("mla", 3))
            pe.wait_ge(vm_ready, 4)
            pe.matmul(ps[ROPE:2 * ROPE, 6, :], PERM[:], KR, start=True, stop=True).then_inc(kr_ps, 1)
            pe.wait_ge(cq_norm, 3)
            pe.wait_ge(kr_rot, 1)
            for g in range(14):
                if g < 6:
                    lhs, rhs, n = WUKV[:, 0, 2 * g:2 * g + 2, :].rearrange("p h c -> p (h c)"), CKV[:], T
                else:
                    t, half = (g - 6) // 2, g % 2
                    lhs, rhs, n = CKV[:, t * P:(t + 1) * P], WUKV[:, 1, 6 * half:6 * half + 6, :], 6 * HD
                if g >= 4:
                    pe.wait_ge(kv_act, kv_count(g - 4)[0])
                    pe.wait_ge(kv_dve, kv_count(g - 4)[1])
                pe.matmul(ps[:, 4 + g % 4, 0:n], lhs, rhs, start=True, stop=True).then_inc(kv_ps, 1)

            def project_q(h, s, turn):
                pe.wait_ge(wq_in[s], 48 * turn + 48)
                wait(pe, q_nope, h)
                wait(pe, q_rot, 2 * h)
                for k in range(2):
                    mm = pe.matmul(ps[:, 3, :], WQ[:, s, k, :], CQ[:, k, :], start=k == 0, stop=k == 1)
                mm.then_inc(q_ps, 1)

            def mla_scores(h, s):
                pe.wait_ge(q_nope, h + 1)
                pe.wait_ge(q_rope, h + 1)
                scores(h, lambda t: QT[:, s, t * P:(t + 1) * P],
                       lambda n: KT[:, bass.ds(h, 1), 0:n].rearrange("p o n -> p (o n)"))

            def mla_pv(h, s):
                pv(h, s, lambda kb: V[:, kb, bass.ds(h * HD, HD)])

            pe.wait_ge(kv_act, kv_count(13)[0])
            pe.wait_ge(kv_dve, kv_count(13)[1])
            pe.wait_ge(kr_act, 1)
            pe.wait_ge(kr_dve, 1)
            pe.wait_ge(*taken_at("mla", 5))
            pe.wait_ge(*taken_at("mla", 2))
            project_q(0, 0, 0)
            project_q(1, 1, 0)
            mla_scores(0, 0)

            def mla_pair(i):
                for s in range(2):
                    u = 2 * i + s
                    probs_t(u, s)
                    mla_scores(u + 1, 1 - s)
                    project_q(u + 2, s, i + 1)
                    mla_pv(u, s)

            mla_pair(0)
            with pe.Fori(1, HEADS // 2 - 1) as i:
                mla_pair(i)
            probs_t(10, 0)
            mla_scores(11, 1)
            mla_pv(10, 0)
            probs_t(11, 1)
            mem_scores(12, 0, True)
            mla_pv(11, 1)
            for h in range(MEM_HEADS):
                u = 12 + h
                mem_probs_t(u, u % 2)
                if h < 3:
                    mem_scores(u + 1, h + 1, False)
                mem_pv(u, u % 2, h)
            pe.wait_ge(o_done, 16)
            mix_t(XS["wo0"], 0)
            panels("wo0", 8, XS["wo0"])
            norm("wo0")
            ffn("ffn1", lambda f: ada_fill(0, f))
            norm("ffn1")

            for j in range(6):
                panel("kv", j, 0, XH, XL, need=(lambda k: (x_split, XS["kv"] + k + 1)) if j == 0 else None)
            for e in range(2):
                pe.wait_ge(*taken_at("kv", 3 + 2 * e))
                for t in range(TT):
                    mm = pe.transpose(ps[:, 4 + e, t * P:(t + 1) * P], VT[:, e, t * P:(t + 1) * P], IDENT[:])
                mm.then_inc(vt_ps, 1)
            pe.wait_ge(w1_in, 96)
            pe.wait_ge(mod_ready, 1)
            for j in range(2):
                pe.wait_ge(zb_ready, j + 1)
                for m in range(2):
                    for l in range(CMP_LEN // 2):
                        mm = pe.matmul(ps[:, 6 + j, m * 2 * NCMP:(m + 1) * 2 * NCMP], W1[j][:, l, m * P:(m + 1) * P], ZB[:, j, l, :, 0:NCMP],
                                       start=l == 0, stop=l == CMP_LEN // 2 - 1)
                    mm.then_inc(hid_ps, 1)

            ffn("ffn2", ffn2_fill)
            pe.wait_ge(kc_out, 2)
            norm("ffn2")
            for j in range(9):
                panel("nsa", j, 0, XH, XL, need=(lambda k: (x_split, XS["nsa"] + k + 1)) if j == 0 else None)
                if j == 2:
                    pe.wait_ge(*taken_at("nsa", 0))
                    for t in range(TT):
                        mm = pe.transpose(ps[:, 4, t * 36:(t + 1) * 36], GTT[:, t * P:(t + 1) * P], IDENT[0:36, 0:36])
                    mm.then_inc(g_ps, 1)

            def nsa_scores(u, k, q):
                r = slice((k % 2) * HD, (k % 2) * HD + HD)
                keys = (KS, KW)[k // 2]
                scores(u, lambda t: QS[r, q, t * P:(t + 1) * P], lambda n: keys[r, 0:n])

            def nsa_pv(u, k):
                vals = (VS, VW)[k // 2]
                pv(u, k % 2, lambda kb: vals[:, kb, (k % 2) * HD:(k % 2 + 1) * HD])

            def cmp_scores(j, q):
                wait(pe, c_o, j)
                for t in range(TT):
                    mm = pe.matmul(ps[:, 3, t * 2 * NPAD:(t + 1) * 2 * NPAD], QS[:, q, t * P:(t + 1) * P], KCB[:], start=True, stop=True)
                mm.then_inc(c_ps, 1)

            def cmp_t(j):
                pe.wait_ge(c_p, j + 1)
                for t in range(TT):
                    mm = pe.transpose(ps[0:2 * NPAD, 3, t * P:(t + 1) * P], SC[:, t].rearrange("p g n -> p (g n)"), IDENT[:])
                mm.then_inc(c_t, 1)

            def cmp_pv(j):
                pe.wait_ge(c_pt, j + 1)
                for t in range(TT):
                    mm = pe.matmul(ps[:, 3, t * P:(t + 1) * P], PTC[:, t * P:(t + 1) * P], VCB[:], start=True, stop=True)
                mm.then_inc(c_pv, 1)

            for j in range(5, 9):
                pe.wait_ge(*taken_at("nsa", j))
            pe.wait_ge(g_out, 1)
            pe.wait_ge(qs_ready, 1)
            nsa_scores(16, 0, 0)

            def nsa_pair(j, q, last=False):
                for k in range(4):
                    u = 16 + 4 * j + k
                    probs_t(u, k % 2)
                    if k == 0:
                        cmp_scores(j, q)
                    if k < 3:
                        nsa_scores(u + 1, k + 1, q)
                    elif not last:
                        pe.wait_ge(qs_ready, j + 2)
                        nsa_scores(u + 1, 0, 1 - q)
                    else:
                        mem_scores(u + 1, 0, True)
                    if k == 2:
                        cmp_t(j)
                    if k == 3:
                        cmp_pv(j)
                    nsa_pv(u, k)

            nsa_pair(0, 0)
            nsa_pair(1, 1)
            with pe.Fori(1, HPG // 2 - 1) as i:
                for q in range(2):
                    nsa_pair(2 * i + q, q)
            mem_layer[0] = 1
            nsa_pair(4, 0)
            nsa_pair(5, 1, last=True)
            for h in range(MEM_HEADS):
                u = 40 + h
                mem_probs_t(u, u % 2)
                if h < 3:
                    mem_scores(u + 1, h + 1, False)
                mem_pv(u, u % 2, h)
            pe.wait_ge(o_done, 44)
            pe.wait_ge(c_o, HPG)
            mix_t(XS["wo1"], 8)
            panels("wo1", 8, XS["wo1"])
            norm("wo1")
            ffn("ffn3", ffn3_fill)
            pe.wait_ge(cx_f, 8)
            norm("ffn3")

            squares(LN_SQ["even"], 8, 5)
            for j in range(6):
                p = BASE["even"] + j
                pe.wait_ge(w_lo, p + 1)
                wait(pe, uc_out, j - 1)
                pe.wait_ge(*taken_at("even", j - 4))
                for k in range(KD):
                    if j == 0:
                        pe.wait_ge(x_split, XS["even"] + k + 1)
                        pe.wait_ge(cx_split, k + 1)
                    for a, (w, x, c) in enumerate(((wh, XH, CH), (wl, XH, CH), (wh, XL, CL))):
                        lhs = w[:, p % 2, k * P:(k + 1) * P]
                        first, last = k == 0 and a == 0, k == KD - 1 and a == 2
                        pe.matmul(ps[:, 4 + j % 2, 0:CTX], lhs, c[:, k, :], start=first, stop=last)
                        mm = pe.matmul(ps[:, p % 4, :], lhs, x[:, k, :], start=first, stop=last)
                mm.then_inc(pe_panel, 1)
            for j in range(6, 10):
                panel("even", j, 0, XH, XL)
            pe.wait_ge(shuffle_in, 16 * L)
            for t in range(S5T):
                pe.wait_ge(bs_in[t % 2], 16 * (t // 2 + 1))
                for b in range(4):
                    if t == 0 and b < 2:
                        pe.wait_ge(uc_out, 6)
                    wait(pe, h_act, 4 * (t - 1) + b + 1)
                    wait(pe, h_dve, 4 * (t - 1) + b + 1)
                    for g in range(4):
                        e = (b % 2) * 4 + g
                        mm = pe.matmul(ps[:, 4 + b, g * NC:(g + 1) * NC], BS[:, t % 2, b // 2, e, :], U[:, t * GT + e, :], start=True, stop=True)
                    mm.then_inc(b_ps, 1)
            for j in range(10, 16):
                panel("even", j, 0, XH, XL)
            for j in range(2):
                pe.wait_ge(*taken_at("even", 6 + j))
            pe.wait_ge(dft_in, 16 * 6)
            for t in range(TT):
                pe.wait_ge(h_act, 4 * (S5T - 1) + t + 1)
                pe.wait_ge(h_dve, 4 * (S5T - 1) + t + 1)
                for j in range(2):
                    mm = pe.matmul(ps[:, 4 + t, j * 2 * P:(j + 1) * 2 * P], UB[:, j, t * P:(t + 1) * P], DFTC[:], start=True, stop=True)
                mm.then_inc(fnet_ps, 1)
            for j in range(2):
                pe.wait_ge(fnet_out, 4)
                for t in range(TT):
                    for e in range(2):
                        mm = pe.matmul(ps[:, 4 + j, :], FA[:, t, j, e * P:(e + 1) * P], DFTT[:, e, t, :],
                                       start=t == 0 and e == 0, stop=t == TT - 1 and e == 1)
                mm.then_inc(fnet_ps, 1)
            for j in range(2):
                pe.wait_ge(fnet_out, 5 + j)
                pe.matmul(ps[:, 6 + j, :], FW[:, j, :], FB[:, j, :], start=True, stop=True).then_inc(fnet_ps, 1)
            pe.wait_ge(fnet_out, 8)
            for t in range(S5T):
                pe.wait_ge(mw_in[t % 2], 32 * (t // 2 + 1))
                pe.wait_ge(ss_act, t + 1)
                pe.wait_ge(ss_dve, t + 1)
                wait(pe, y_sb, t - 3)
                for g in range(GT):
                    dst = ps[:, 4 + t % 4, g * NCL:(g + 1) * NCL]
                    pe.matmul(dst, MW[:, t % 2, 0, g, :], U[:, t * GT + g, NCC:], start=True, stop=False)
                    pe.matmul(dst, MW[:, t % 2, 1, g, :], SS[:, t % 2, 0, g, :], start=False, stop=False)
                    mm = pe.matmul(dst, MW[:, t % 2, 2, g, :], SS[:, t % 2, 1, g, :], start=False, stop=True)
                mm.then_inc(y_ps, 1)
            for j in range(6):
                panel("glu", j, 0, XH, XL, 6, need=(lambda k: (x_split, XS["glu"] + k + 1)) if j == 0 else None)
            for j in range(8):
                panel("ewo", j, 0, YH, YL, need=(lambda k: (y_ready, k + 3 if k < 6 else k - 5)) if j == 0 else None)
            squares(LN_SQ["odd"], 8, 5)

            for j in range(24):
                panel("odd", j, 0, XH, XL, need=(lambda k: (x_split, XS["odd"] + k + 1)) if j == 0 else None)
                if j in (7, 10, 13, 15):
                    i = (7, 10, 13, 15).index(j)
                    if i == 0:
                        pe.wait_ge(odd_in, 32)
                    pe.wait_ge(pool_ready, i + 1)
                    pe.matmul(ps[:, 4 + (i + 2) % 4, :], PWT[:, i, :], PP[:, i % 2, :], start=True, stop=True).then_inc(pw_ps, 1)
            for j in range(8):
                panel("owo", j, 0, YH, YL, need=(lambda k: (y_ready, 8 + k + 1)) if j == 0 else None)

            pe.wait_ge(yc_ready, 4)
            squares(LN_SQ["final"], 8, 5)
            for d in range(KD):
                pe.wait_ge(ln_aff, 8 * 8 + d + 1)
                b = (6, 7, 4, 5)[d % 4]
                wait(pe, out_sb, d - 3)
                for t in range(TT):
                    mm = pe.transpose(ps[:, b, t * P:(t + 1) * P], XT[:, d, t * P:(t + 1) * P], IDENT[:])
                mm.then_inc(out_ps, 1)

        @block.scalar
        def _(act):
            def cast(p, i=0):
                if isinstance(i, int) and p >= PANELS:
                    return
                act.wait_ge(raw_in[p % 4], 16 * (p // 4 + 1) + 16 * i)
                if not (isinstance(i, int) and p < 2):
                    act.wait_ge(pe_panel, p - 1 + 4 * i)
                act.activation(wh[:, p % 2, :], raw[:, p % 4, :], ACT.Copy).then_inc(w_hi, 1)

            def take(stage, j, dst, func=ACT.Copy, n=T, rows=slice(0, P), **kw):
                p = BASE[stage] + j
                cast(p + 2)
                act.wait_ge(pe_panel, p + 1)
                act.activation(dst, ps[rows, p % 4, 0:n], func, **kw).then_inc(taken[p % 4], 1)

            def ffn(stage, fill):
                off, f0 = 0, 22 * int(stage[3])
                at = 0
                for c, nf in enumerate(CHUNKS):
                    for a, b in zip(UP_PARTS[c], UP_PARTS[c][1:]):
                        with act.Fori(a, b) as i:
                            for f in range(2):
                                p = BASE[stage] + off + 2 * f
                                cast(p + 2, i)
                                act.wait_ge(pe_panel, p + 1 + 4 * i)
                                act.wait_ge(h_ready, f0 + f + 1 + 2 * i)
                                act.activation(SG[:, f, :], ps[:, p % 4, :], ACT.Silu).then_inc(taken[p % 4], 1)
                                cast(p + 3, i)
                        fill(at)
                        at += 1
                    off += 2 * nf
                    f0 += nf
                    with act.Fori(0, KD // 4) as i:
                        for j in range(4):
                            cast(BASE[stage] + off + j + 2, i)
                    if c < 2:
                        fill(at)
                        at += 1
                    off += KD

            def square(q, src):
                if q >= 2:
                    act.wait_ge(sq_used, q - 1)
                act.activation(SQ[:, q % 2, 0:src.shape[-1]], src, ACT.Square).then_inc(sq_ready, 1)

            def norm(stage, eps, split=True):
                no, q0, c0 = LN_NO[stage], LN_SQ[stage], LN_COL[stage]
                for d in range(KD):
                    act.wait_ge(ln_c, 8 * no + d + 1)
                    square(q0 + d, XT[:, d, :])
                act.wait_ge(sq_used, q0 + 8)
                if no == 0:
                    act.wait_ge(tr_done, 1)
                act.activation(SD[:, 0, :], ps[:, 5, :], ACT.Sqrt, bias=EPS[:, eps:eps + 1]).then_inc(sd_ready, 1)
                for d in range(KD if split else 0):
                    act.wait_ge(ln_n, 8 * no + d + 1)
                    act.activation(XH[:, d, :], XT[:, d, :], ACT.Identity, scale=COL[:, c0 + d:c0 + d + 1],
                                   bias=COL[:, 48 + c0 + d:49 + c0 + d]).then_inc(ln_hi, 1)

            def rms(stage, ready, layer=None):
                no, q0 = LN_NO[stage], LN_SQ[stage]
                for d in range(KD):
                    act.wait_ge(*ready(d))
                    square(q0 + d, XT[:, d, :])
                act.wait_ge(sq_used, q0 + 8)
                act.activation(SD[:, 0, :], ps[:, 5, :], ACT.Sqrt, bias=EPS[:, 2:3]).then_inc(sd_ready, 1)
                for d in range(KD if layer is not None else 0):
                    act.wait_ge(ln_n, 8 * no + d + 1)
                    src = (NT, NO)[layer]
                    act.activation(XH[:, d, :], src[:, d, :], ACT.Identity, scale=AG[:, layer, d, 0:1],
                                   bias=MOD[:, layer, d, 0:1]).then_inc(ln_hi, 1)

            def s5_fill(t):
                wait(act, s5_out, 64 * t)
                for b in range(2):
                    act.wait_ge(s5_t, 4 * t + b + 1)
                    act.activation(BT[:, 0, 4 * b:4 * b + 4, :], ps[:, 4 + b, :], ACT.Copy).then_inc(bt_act, 1)
                for b in range(4):
                    act.wait_ge(s5_z, 4 * t + b + 1)
                    act.activation(Z[:, 2 * b:2 * b + 2, :], ps[0:S5H, 4 + b, 0:480], ACT.Copy).then_inc(z_out, 1)

            def ffn2_fill(f):
                if f == 0:
                    act.wait_ge(zeros, 2)
                    act.wait_ge(kc_ps, 1)
                    for g in range(GROUPS):
                        n, d = slice(g * NPAD, (g + 1) * NPAD), slice(g * HD, (g + 1) * HD)
                        act.activation(KCB[d, n], ps[0:HD, 4, n], ACT.Copy)
                        act.activation(VCB[n, d], ps[n, 5, 0:HD], ACT.Copy).then_inc(kc_out, 1)

            def ffn3_fill(f):
                if f == 0:
                    act.wait_ge(cx_in, 32)
                    for m in range(MT):
                        act.activation(CXT[:, 4 * m:4 * m + 4, :].rearrange("p k c -> p (k c)"), CXN[:, m, :], ACT.Square, accum_out=CSS[:, m:m + 1]
                                       ).then_inc(cx_sd, 1)
                    act.wait_ge(cx_sd, 2)
                    act.activation(CSS[:, 2:4], CSS[:, 0:2], ACT.Sqrt, scale=1.0 / D, bias=EPS[:, 2:3]).then_inc(cx_sd, 1)
                if f == 2:
                    for k in range(KD):
                        act.wait_ge(cx_f, k + 1)
                        act.activation(CH[:, k, :], CXT[:, k, :], ACT.Copy).then_inc(cx_hi, 1)

            def softmax_exp(u, s):
                act.wait_ge(nb_ready, u + 1)
                for t in range(TT):
                    ins = act.activation(PR[:, s, POFF[t]:POFF[t] + (t + 1) * P], PR[:, s, POFF[t]:POFF[t] + (t + 1) * P], ACT.Exp,
                                         bias=NB[:, s, t:t + 1], scale=scale[0], accum_out=SM[:, s, t:t + 1])
                ins.then_inc(p_ready, 1)

            def probs_out(u, s):
                act.wait_ge(t_ps, u + 1)
                wait(act, pv_ps, u - 1)
                act.activation(PT[:, s, 0:T], ps[:, 0, :], ACT.Copy).then_inc(pt_act, 1)
                act.activation(PT[:, s, 2 * T:2 * T + 2 * P], ps[:, 2, 0:2 * P], ACT.Copy).then_inc(pt_act, 1)

            def mem_exp(u, s):
                act.wait_ge(nb_ready, u + 1)
                act.wait_ge(t_ps, u - 1)
                for t in range(TT):
                    ins = act.activation(PR[:, s, t * M:(t + 1) * M], ps[:, 4 + t // 2, (t % 2) * M:(t % 2 + 1) * M], ACT.Exp,
                                         bias=NB[:, s, t:t + 1], scale=HD ** -0.5, accum_out=SM[:, s, t:t + 1])
                ins.then_inc(p_ready, 1)

            def mem_probs_out(u, s):
                act.wait_ge(t_ps, u + 1)
                wait(act, pv_ps, u - 1)
                act.activation(PT[:, s, 0:T // 2], ps[:, 0, 0:T // 2], ACT.Copy).then_inc(pt_act, 1)
                act.activation(PT[:, s, T // 2:T], ps[:, 0, T // 2:T], ACT.Copy).then_inc(pt_act, 1)

            def mix_hi_of(mix0):
                for k in range(KD):
                    act.wait_ge(mix_ps, mix0 + k + 1)
                    act.activation(XH[:, k, :], ps[:, 4 + k % 4, :], ACT.Copy).then_inc(mix_hi, 1)

            scale = [MLA_SCALE]
            at = 0
            act.dma_start(CN1[0:48, :], A["ln_g"].rearrange("l i (k p) -> (l i k) p", p=P)).then_inc(col_in, 16)
            act.dma_start(CN1[48:96, :], A["ln_b"].rearrange("l i (k p) -> (l i k) p", p=P)).then_inc(col_in, 16)
            for name, view in VECTORS:
                v = A[name].rearrange(view, p=P)
                act.dma_start(CN2[at:at + v.shape[0], :], v).then_inc(col_in, 16)
                at += v.shape[0]
            for b in range(2):
                act.dma_start(PN[:, b, :], A["cmp_pos"].rearrange("j l d -> (j l) d")).then_inc(col_in, 16)
            cast(0)
            cast(1)
            for k2 in range(4):
                act.wait_ge(tr, k2 + 1)
                act.activation(MH[:, 2 * k2:2 * k2 + 2, :], ps[:, 4 + k2, :].rearrange("p (e m) -> p e m", e=2), ACT.Copy).then_inc(mem_hi, 1)
            for k in range(KD):
                act.wait_ge(tr, 5 + k)
                act.activation(XH[:, k, :], ps[:, 4 + k % 4, :], ACT.Copy).then_inc(x_hi, 1)
            for layer in range(2):
                for j in range(4):
                    dst = KM[:, layer, j, :] if j < 2 else MV[:, 2 * layer + j - 2, :]
                    take("mem", 4 * layer + j, dst, n=M)

            act.wait_ge(tr_done, 1)
            act.activation(CS[:].rearrange("p k e -> p e k"), COL[:, 96 + 101:96 + 117].rearrange("p (e k) -> p e k", e=2), ACT.Silu).then_inc(cs_ready, 1)
            for b, parts in enumerate((((0, 4, 1.0),), ((4, 2, 1.0), (6, 2, -1.0)), ((8, 4, -1.0),))):
                act.wait_ge(s5_tr, 2 + b)
                col = 0
                for r0, n, sign in parts:
                    ins = act.activation(CR[:].rearrange("p r g h -> p (r g h)")[:, r0 * P:(r0 + n) * P], ps[:, 5 + b, col:col + n * P], ACT.Copy, scale=sign)
                    col += n * P
                ins.then_inc(cr_out, 1)
            act.wait_ge(sin_in, 1)
            act.activation(TS5[:, 0, :], TS5[:, 2, :], ACT.Sin)
            act.activation(TS5[:, 1, :], TS5[:, 2, :], ACT.Sin, scale=0.5).then_inc(sin_out, 1)
            ffn("ffn0", s5_fill)
            norm("ffn0", 0)
            act.wait_ge(s5_out, 64 * S5T)
            for j, dst in enumerate((CQ[:, 0, :], CQ[:, 1, :], CKV[:], KR, QM[:, 0, :], QM[:, 1, :])):
                p = BASE["mla"] + j
                if j < 3:
                    act.wait_ge(pe_panel, p + 1)
                    square(LN_SQ["mla"] + j, ps[:, p % 4, :])
                take("mla", j, dst, rows=slice(0, ROPE if j == 3 else P))
            act.wait_ge(sq_used, LN_SQ["mla"] + 3)
            act.activation(SD[:, 0, :], ps[:, 4, :], ACT.Sqrt, scale=float(D // QR), bias=EPS[:, 2:3]).then_inc(sd_ready, 1)
            act.activation(SD[:, 1, :], ps[:, 5, :], ACT.Sqrt, scale=float(D // P), bias=EPS[:, 2:3]).then_inc(sd_ready, 1)
            act.wait_ge(kr_rot, 2)
            act.activation(KT[HD:QK, 0:6, :], KR2[:, 0:1, :].broadcast_to([ROPE, 6, T]), ACT.Copy).then_inc(kr_act, 1)
            for g in range(14):
                if g < 6:
                    act.wait_ge(kv_ps, g + 1)
                    act.activation(KT[0:HD, 2 * g, :], ps[0:HD, 4 + g % 4, :], ACT.Copy).then_inc(kv_act, 1)
                elif g % 2 == 0:
                    act.wait_ge(kv_ps, g + 1)
                    act.activation(V[:, (g - 6) // 2, 0:6 * HD], ps[:, 4 + g % 4, 0:6 * HD], ACT.Copy).then_inc(kv_act, 1)

            def take_q(h, s):
                act.wait_ge(q_ps, h + 1)
                if not (isinstance(h, int) and h < 2):
                    act.wait_ge(s_ps, h - 1)
                act.activation(QT[0:HD, s, :], ps[0:HD, 3, :], ACT.Copy).then_inc(q_nope, 1)

            take_q(0, 0)
            take_q(1, 1)
            softmax_exp(0, 0)

            def mla_pair(i):
                for s in range(2):
                    u = 2 * i + s
                    probs_out(u, s)
                    softmax_exp(u + 1, 1 - s)
                    take_q(u + 2, s)

            mla_pair(0)
            with act.Fori(1, HEADS // 2 - 1) as i:
                mla_pair(i)
            probs_out(10, 0)
            softmax_exp(11, 1)
            probs_out(11, 1)
            mem_exp(12, 0)
            for h in range(MEM_HEADS):
                u = 12 + h
                mem_probs_out(u, u % 2)
                if h < 3:
                    mem_exp(u + 1, 1 - u % 2)
            mix_hi_of(0)
            for j in range(8):
                cast(BASE["wo0"] + j + 2)
            norm("wo0", 1)
            ffn("ffn1", nothing)
            norm("ffn1", 0)

            for j, dst in enumerate((ZC[:, 0, :], ZC[:, 1, :], KS[:], VT[:, 0, :], KW[:], VT[:, 1, :])):
                take("kv", j, dst)
            act.wait_ge(zeros, 2)
            for n in range(4):
                act.wait_ge(hid_ps, n // 2 * 2 + 2)
                act.activation(H1[:, n // 2, n % 2, :, 0:NCMP], ps[:, 6 + n // 2, (n % 2) * 2 * NCMP:(n % 2 + 1) * 2 * NCMP].rearrange("p (g n) -> p g n", g=GROUPS),
                               ACT.Gelu_apprx_tanh, bias=COL[:, 96 + 94 + n:96 + 95 + n]).then_inc(gelu_out, 1)
            ffn("ffn2", ffn2_fill)
            norm("ffn2", 0)

            take("nsa", 0, GTT[:], ACT.Sigmoid, rows=slice(0, 36))
            for j in range(2):
                take("nsa", 1 + j, QM[:, j, :])
            for m in range(HPG):
                p = BASE["nsa"] + 3 + m
                cast(p + 2)
                act.wait_ge(pe_panel, p + 1)
                for e in range(2):
                    g, j = divmod(2 * m + e, HPG)
                    ins = act.activation(QP[g * HD:(g + 1) * HD, j, :], ps[e * HD:(e + 1) * HD, p % 4, :], ACT.Copy)
                ins.then_inc(taken[p % 4], 1)
            scale[0] = SEL_SCALE
            softmax_exp(16, 0)

            def nsa_pair(j, q, last=False):
                for k in range(4):
                    u = 16 + 4 * j + k
                    probs_out(u, k % 2)
                    if k == 1:
                        act.wait_ge(c_sub, j + 1)
                        act.activation(SC[:], SC[:], ACT.Exp, scale=SEL_SCALE).then_inc(c_exp, 1)
                    if last and k == 3:
                        mem_exp(u + 1, 0)
                    else:
                        softmax_exp(u + 1, 1 - k % 2)
                    if k == 2:
                        act.wait_ge(c_t, j + 1)
                        wait(act, c_pv, j)
                        act.activation(PTC[:], ps[0:2 * NPAD, 3, :], ACT.Copy).then_inc(c_pt, 1)

            nsa_pair(0, 0)
            nsa_pair(1, 1)
            with act.Fori(1, HPG // 2 - 1) as i:
                for q in range(2):
                    nsa_pair(2 * i + q, q)
            nsa_pair(4, 0)
            nsa_pair(5, 1, last=True)
            for h in range(MEM_HEADS):
                u = 40 + h
                mem_probs_out(u, u % 2)
                if h < 3:
                    mem_exp(u + 1, 1 - u % 2)
            mix_hi_of(8)
            for j in range(8):
                cast(BASE["wo1"] + j + 2)
            norm("wo1", 1)
            ffn("ffn3", ffn3_fill)
            norm("ffn3", 0, split=False)

            rms("even", lambda d: (ln_aff, 8 * LN_NO["ffn3"] + d + 1), 0)
            for j in range(6):
                take("even", j, UT[:, j, :, NCC:].rearrange("p t c -> p c t"))
            for j in range(2):
                take("even", 6 + j, UB[:, j, :])

            def take_z(j):
                take("even", 8 + j, ZS[:, j, :], ACT.Silu)
            take_z(0)
            take_z(1)
            for t in range(S5T):
                for b in range(4):
                    act.wait_ge(b_ps, 4 * t + b + 1)
                    g = t * GT + (b % 2) * 4
                    act.activation(H[0:S5P, b // 2, g:g + 4, :], ps[0:S5P, 4 + b, 0:4 * NC].rearrange("p (g c) -> p g c", g=4), ACT.Copy).then_inc(h_act, 1)
            for j in range(2, 8):
                take_z(j)
            for t in range(TT):
                act.wait_ge(fnet_ps, t + 1)
                act.activation(FA[:, t].rearrange("p j c -> p (j c)"), ps[:, 4 + t, :], ACT.Copy).then_inc(fnet_out, 1)
            for j in range(2):
                act.wait_ge(fnet_ps, 5 + j)
                act.activation(FB[:, j, :], ps[:, 4 + j, :], ACT.Copy).then_inc(fnet_out, 1)
            for j in range(2):
                act.wait_ge(fnet_ps, 7 + j)
                act.activation(YB[:, j, :], ps[:, 6 + j, :], ACT.Copy).then_inc(fnet_out, 1)

            def states(t):
                if t == 0:
                    act.wait_ge(scan, 3 * (NC - 1))
                wait(act, y_ps, t - 1)
                act.activation(SS[0:S5P, t % 2], H[0:S5P, :, t * GT:(t + 1) * GT, NCC - 1:NC - 1], ACT.Copy).then_inc(ss_act, 1)

            states(0)
            states(1)
            for t in range(S5T):
                act.wait_ge(y_ps, t + 1)
                act.activation(YS[:, t * GT:(t + 1) * GT, :], ps[:, 4 + t % 4, :], ACT.Copy).then_inc(y_sb, 1)
                if t + 2 < S5T:
                    states(t + 2)
            act.wait_ge(shuffle_in, 16 * (L + 1))
            for j in range(6):
                act.activation(YA[:, j, :].rearrange("p (c t) -> p t c", t=L), YT[:, j], ACT.Gelu_apprx_tanh).then_inc(ya_ready, 1)
            for j in range(6):
                act.wait_ge(ya_ready, j + 1)
                act.activation(XH[:, j, :], YA[:, j, :], ACT.Copy).then_inc(ya_hi, 1)
            for j in range(6):
                act.wait_ge(y_full, j + 1)
                take("glu", j, SIG[:, j % 2, :], ACT.Sigmoid, bias=COL[:, 96 + 72 + j:96 + 73 + j])
            for j in range(8):
                cast(BASE["ewo"] + j + 2)
            rms("odd", lambda d: taken_at("ewo", d), 1)

            act.wait_ge(odd_zero, 1)
            for j in range(4):
                take("odd", j, PU[:, j, PAD:PAD + T])

            def take_pooled(i):
                act.wait_ge(pw_ps, i + 1)
                act.activation(YO[:, i, :], ps[:, 4 + (i + 2) % 4, :], ACT.Identity, scale=COL[:, 96 + 78 + i:96 + 79 + i]).then_inc(yc_ready, 1)

            for k in range(4):
                if k >= 2:
                    act.wait_ge(*taken_at("odd", 5 + 3 * (k - 2)))
                take("odd", 4 + 3 * k, CG[:, k % 2, :])
                cast(BASE["odd"] + 4 + 3 * k + 3)
                cast(BASE["odd"] + 4 + 3 * k + 4)
                if k >= 1:
                    take_pooled(k - 1)
            take_pooled(3)
            for j in range(8):
                wait(act, y_ready, 8 + j - 1)
                take("odd", 16 + j, ZO[:, j % 2, :], ACT.Silu)
            for j in range(8):
                cast(BASE["owo"] + j + 2)
            rms("final", lambda d: taken_at("owo", d))
            for d in range(KD):
                act.wait_ge(out_ps, d + 1)
                act.activation(XO[:, :, d * P:(d + 1) * P], ps[:, (6, 7, 4, 5)[d % 4], :].rearrange("p (t c) -> p t c", t=TT), ACT.Copy).then_inc(out_sb, 1)

        @block.vector
        def _(dve):
            def rest(p, i=0):
                if isinstance(i, int) and p >= PANELS:
                    return
                dve.wait_ge(w_hi, p + 1 + 4 * i)
                dve.tensor_tensor(wl[:, p % 2, :], raw[:, p % 4, :], wh[:, p % 2, :].bitcast(F32), ALU.subtract).then_inc(w_lo, 1)

            def ffn(stage, fill):
                off = 0
                at = 0
                for c, nf in enumerate(CHUNKS):
                    for a, b in zip(UP_PARTS[c], UP_PARTS[c][1:]):
                        with dve.Fori(a, b) as i:
                            for f in range(2):
                                p = BASE[stage] + off + 2 * f
                                u = p + 1
                                rest(p + 2, i)
                                rest(p + 3, i)
                                dve.wait_ge(taken[p % 4], p // 4 + 1 + i)
                                dve.wait_ge(pe_panel, u + 1 + 4 * i)
                                k = bass.ds(2 * i + f, 1)
                                dve.tensor_tensor(HH[:, k, :], SG[:, f:f + 1, :], ps[:, u % 4:u % 4 + 1, :], ALU.mult)
                                dve.tensor_tensor(HF[:, f, :], SG[:, f, :], ps[:, u % 4, :], ALU.mult).then_inc(taken[u % 4], 1)
                                dve.wait_ge(taken[u % 4], u // 4 + 1 + i)
                                dve.tensor_tensor(HL[:, k, :], HF[:, f:f + 1, :], HH[:, k, :].bitcast(F32), ALU.subtract).then_inc(h_ready, 1)
                        fill(at)
                        at += 1
                    off += 2 * nf
                    with dve.Fori(0, KD // 4) as i:
                        for j in range(4):
                            p = BASE[stage] + off + j
                            rest(p + 2, i)
                            dve.wait_ge(pe_panel, p + 1 + 4 * i)
                            if c:
                                q = p - KD - 2 * nf
                                dve.wait_ge(taken[q % 4], q // 4 + 1 + i)
                            x = XT[:, bass.ds(4 * i + j, 1), :]
                            dve.scalar_tensor_tensor(x, x, 1.0 if c else 2 * ALPHA, ps[:, p % 4:p % 4 + 1, :], ALU.mult, ALU.add
                                                     ).then_inc(taken[p % 4], 1)
                    if c < 2:
                        fill(at)
                        at += 1
                    off += KD

            def norm(stage, split=True):
                no, c0 = LN_NO[stage], LN_COL[stage]
                dve.wait_ge(ln_mu, no + 1)
                for d in range(KD):
                    dve.tensor_tensor(XT[:, d, :], XT[:, d, :], ps[:, 4, :], ALU.subtract).then_inc(ln_c, 1)
                reciprocal(0)
                dve.wait_ge(ln_c, 8 * no + 8)

                def affine(d):
                    if not split:
                        dve.wait_ge(ln_n, 8 * no + d + 1)
                        dve.wait_ge(sct_ready, d + 1)
                        dve.scalar_tensor_tensor(XT[:, d, :], XT[:, d, :], COL[:, c0 + d:c0 + d + 1], SCT[:, d, :], ALU.mult, ALU.add).then_inc(ln_aff, 1)
                        return
                    dve.wait_ge(ln_hi, 8 * no + d + 1)
                    dve.tensor_scalar(XT[:, d, :], XT[:, d, :], COL[:, c0 + d:c0 + d + 1], COL[:, 48 + c0 + d:49 + c0 + d],
                                      ALU.mult, ALU.add).then_inc(ln_aff, 1)
                for d in range(KD):
                    dve.tensor_tensor(XT[:, d, :], XT[:, d, :], RST[:, 0, :], ALU.mult).then_inc(ln_n, 1)
                    if d >= 1:
                        affine(d - 1)
                affine(KD - 1)

            def reciprocal(j):
                rc[0] += 1
                dve.wait_ge(sd_ready, rc[0])
                dve.reciprocal(RST[:, j, :], SD[:, j, :]).then_inc(rstd_ready, 1)
                dve.wait_ge(rstd_ready, rc[0])

            def rms(stage, layer):
                no, hi = LN_NO[stage], HI_NO[stage]
                dst = (NT, NO)[layer]
                reciprocal(0)

                def affine(d):
                    dve.wait_ge(ln_hi, 8 * hi + d + 1)
                    dve.tensor_scalar(dst[:, d, :], dst[:, d, :], AG[:, layer, d, 0:1], MOD[:, layer, d, 0:1], ALU.mult, ALU.add).then_inc(ln_aff, 1)
                for d in range(KD):
                    dve.tensor_tensor(dst[:, d, :], XT[:, d, :], RST[:, 0, :], ALU.mult).then_inc(ln_n, 1)
                    if d >= 1:
                        affine(d - 1)
                affine(KD - 1)

            def modulation(layer):
                n0 = 96 + 16 + 24 * layer
                dve.wait_ge(ada_used, 12 * (layer + 1))
                dve.tensor_tensor(MOD[:, layer], ps[:, 6, 0:48].rearrange("p (m e) -> p m e", e=2),
                                  COL[:, n0:n0 + 24].rearrange("p (m o) -> p m o", o=1).broadcast_to([P, 24, 2]), ALU.add).then_inc(mod_ready, 1)
                dve.wait_ge(mod_ready, layer + 1)
                g0 = 96 + 8 * layer
                dve.scalar_tensor_tensor(AG[:, layer], MOD[:, layer, 8:16, :], 1.0, COL[:, g0:g0 + 8].rearrange("p (m o) -> p m o", o=1).broadcast_to([P, KD, 2]),
                                         ALU.add, ALU.mult)

            def gated(stage, layer):
                for j in range(8):
                    p = BASE[stage] + j
                    rest(p + 2)
                    dve.wait_ge(pe_panel, p + 1)
                    dve.scalar_tensor_tensor(XT[:, j, :], ps[:, p % 4, :], MOD[:, layer, 16 + j, 0:1], XT[:, j, :], ALU.mult, ALU.add).then_inc(taken[p % 4], 1)

            def s5_fill(t):
                wait(dve, s5_out, 64 * t)
                for b in range(2):
                    dve.wait_ge(s5_t, 4 * t + b + 3)
                    dve.tensor_copy(BT[:, 1, 4 * b:4 * b + 4, :], ps[:, 6 + b, :]).then_inc(bt_dve, 1)

            def ffn3_fill(f):
                if f == 1:
                    dve.wait_ge(cx_sd, 3)
                    dve.reciprocal(CSS[:, 0:2], CSS[:, 2:4]).then_inc(cx_n, 1)
                    dve.wait_ge(cx_n, 1)
                    for m in range(MT):
                        ins = dve.tensor_scalar(CXN[:, m, :], CXN[:, m, :], CSS[:, m:m + 1], None, ALU.mult)
                    ins.then_inc(cx_n, 1)
                if f == 2:
                    for k in range(KD):
                        if k % 2 == 0:
                            dve.wait_ge(cx_ps, k // 2 + 1)
                        dve.tensor_scalar(CXT[:, k, :], ps[:, 4 + k // 2, (k % 2) * CTX:(k % 2 + 1) * CTX], AG[:, 0, k, 1:2], MOD[:, 0, k, 1:2],
                                          ALU.mult, ALU.add).then_inc(cx_f, 1)

            def s5_parameters():
                n = [1]

                def step(ins):
                    n[0] += 1
                    ins.then_inc(s5_dve, 1)
                    dve.wait_ge(s5_dve, n[0])

                X, K, R, Q, STEP, ZR, ZI, E1, E, CM = (TS5[:, 2 + j, :] for j in range(10))
                sin, sin_half = TS5[:, 0, :], TS5[:, 1, :]
                lre, lim = PS5[:, 0, :], PS5[:, 1, :]
                two = KI5[:].bitcast(F32)

                def exponential(src, e, em1=None):
                    step(dve.tensor_scalar(X, src, -87.0, 88.0, ALU.max, ALU.min))
                    step(dve.tensor_scalar(K, X, float(1 / np.log(2.0)), MAGIC, ALU.mult, ALU.add))
                    step(dve.tensor_scalar(K, K, MAGIC, None, ALU.subtract))
                    step(dve.scalar_tensor_tensor(R, K, -LN2[0], X, ALU.mult, ALU.add))
                    step(dve.scalar_tensor_tensor(R, K, -LN2[1], R, ALU.mult, ALU.add))
                    step(dve.tensor_scalar(Q, R, 1 / 5040, None, ALU.mult))
                    for f in (720, 120, 24, 6, 2, 1):
                        step(dve.scalar_tensor_tensor(Q, Q, 1 / f, R, ALU.add, ALU.mult))
                    step(dve.tensor_scalar(K, K, 127.0, float(2 ** 23), ALU.add, ALU.mult))
                    step(dve.tensor_copy(KI5[:], K))
                    step(dve.tensor_tensor(Q, Q, two, ALU.mult))
                    step(dve.tensor_tensor(e, Q, two, ALU.add))
                    if em1 is not None:
                        step(dve.tensor_scalar(X, two, 1.0, None, ALU.subtract))
                        step(dve.tensor_tensor(em1, Q, X, ALU.add))

                exponential(PS5[:, 2, :], STEP)
                step(dve.tensor_tensor(ZI, lim, STEP, ALU.mult))
                step(dve.tensor_tensor(ZR, lre, STEP, ALU.mult))
                exponential(ZR, E, E1)
                step(dve.tensor_scalar(K, ZI, float(1 / (2 * np.pi)), MAGIC, ALU.mult, ALU.add))
                step(dve.tensor_scalar(K, K, MAGIC, None, ALU.subtract))
                step(dve.scalar_tensor_tensor(X, K, -TURN[0], ZI, ALU.mult, ALU.add))
                step(dve.scalar_tensor_tensor(X, K, -TURN[1], X, ALU.mult, ALU.add))
                step(dve.scalar_tensor_tensor(X, K, -TURN[2], X, ALU.mult, ALU.add))
                dve.tensor_scalar(X, X, -3.1415925, 3.1415925, ALU.max, ALU.min).then_inc(sin_in, 1)
                dve.wait_ge(sin_out, 1)
                step(dve.scalar_tensor_tensor(CM, sin_half, -2.0, sin_half, ALU.mult, ALU.mult))
                step(dve.tensor_tensor(Q, E, CM, ALU.mult))
                step(dve.tensor_tensor(Q, Q, E1, ALU.add))
                step(dve.tensor_tensor(R, E, sin, ALU.mult))
                step(dve.tensor_copy(PW[:, 1, 1, :], R))
                step(dve.tensor_scalar(PW[:, 0, 1, :], Q, 1.0, None, ALU.add))
                step(dve.tensor_tensor(X, lre, lre, ALU.mult))
                step(dve.tensor_tensor(K, lim, lim, ALU.mult))
                step(dve.tensor_tensor(X, X, K, ALU.add))
                step(dve.reciprocal(K, X))
                for r, (a, b, op) in enumerate(((Q, R, ALU.add), (R, Q, ALU.subtract))):
                    step(dve.tensor_tensor(X, a, lre, ALU.mult))
                    step(dve.tensor_tensor(E1, b, lim, ALU.mult))
                    step(dve.tensor_tensor(X, X, E1, op))
                    ins = dve.tensor_tensor(FB5[:, r, :], X, K, ALU.mult)
                    if r == 0:
                        step(ins)
                ins.then_inc(f_ready, 1)

            def soft_max(u, s, mask, first=False):
                dve.wait_ge(s_ps, u + 1)
                if not (isinstance(u, int) and u < 2):
                    dve.wait_ge(t_ps, u - 1)
                if not first:
                    dve.reciprocal(RS[:, 1 - s, :], SM[:, 1 - s, :]).then_inc(rs_ready, 1)
                for t, bank, col in STILES:
                    n = (t + 1) * P
                    ins = dve.tensor_tensor_reduce(PR[:, s, POFF[t]:POFF[t] + n], ps[:, bank, col:col + n], mask[:, T - n:T],
                                                   1.0, -3e38, ALU.add, ALU.max, MX[:, s, t:t + 1])
                ins.then_inc(s_sb, 1)
                dve.wait_ge(s_sb, u + 1)
                dve.tensor_scalar(NB[:, s, :], MX[:, s, :], -scale[0], None, ALU.mult).then_inc(nb_ready, 1)

            def probs_out(u, s):
                dve.wait_ge(t_ps, u + 1)
                wait(dve, pv_ps, u - 1)
                dve.tensor_copy(PT[:, s, T:2 * T], ps[:, 1, :]).then_inc(pt_dve, 1)

            def own_sums(u, s):
                dve.wait_ge(p_ready, u + 1)
                dve.reciprocal(RS[:, s, :], SM[:, s, :]).then_inc(rs_ready, 1)

            def head_out(u, s, dst):
                dve.wait_ge(rs_ready, u + 1)
                dve.wait_ge(pv_ps, u + 1)
                dve.tensor_tensor(dst, ps[:, 7, 0:TT * HD].rearrange("p (t d) -> p t d", t=TT),
                                  RS[:, s, :].rearrange("p (t o) -> p t o", o=1).broadcast_to([P, TT, HD]), ALU.mult).then_inc(o_done, 1)

            def mem_max(u, s):
                dve.wait_ge(s_ps, u + 1)
                dve.tensor_reduce(MX[:, s, 0:2], ps[:, 4, :].rearrange("p (t m) -> p t m", t=2), AX.X, ALU.max)
                dve.tensor_reduce(MX[:, s, 2:4], ps[:, 5, :].rearrange("p (t m) -> p t m", t=2), AX.X, ALU.max).then_inc(s_sb, 1)
                dve.wait_ge(s_sb, u + 1)
                dve.tensor_scalar(NB[:, s, :], MX[:, s, :], -HD ** -0.5, None, ALU.mult).then_inc(nb_ready, 1)

            def mix_lo_of(mix0):
                for k in range(KD):
                    dve.wait_ge(mix_hi, mix0 + k + 1)
                    dve.tensor_tensor(XL[:, k, :], ps[:, 4 + k % 4, :], XH[:, k, :].bitcast(F32), ALU.subtract).then_inc(x_split, 1)

            rc = [0]
            scale = [MLA_SCALE]
            dve.memset(ONES[:], 1.0 / D).then_inc(setup, 1)
            dve.memset(EPS[:, 0:1], 4e-5).then_inc(h_ready, 2)
            dve.memset(EPS[:, 1:2], 1e-5)
            dve.memset(EPS[:, 2:3], 1e-6).then_inc(setup, 1)
            rest(0)
            rest(1)
            for k2 in range(4):
                dve.wait_ge(mem_hi, k2 + 1)
                dve.tensor_tensor(ML[:, 2 * k2:2 * k2 + 2, :], ps[:, 4 + k2, :].rearrange("p (e m) -> p e m", e=2),
                                  MH[:, 2 * k2:2 * k2 + 2, :].bitcast(F32), ALU.subtract).then_inc(mem_split, 1)
            for k in range(KD):
                dve.wait_ge(x_hi, k + 1)
                dve.tensor_copy(XT[:, k, :], ps[:, 4 + k % 4, :])
                dve.tensor_tensor(XL[:, k, :], ps[:, 4 + k % 4, :], XH[:, k, :].bitcast(F32), ALU.subtract).then_inc(x_split, 1)
            dve.wait_ge(tr, 13)
            dve.tensor_copy(COL[:], ps[:, 4, 0:213])
            dve.tensor_copy(POS[:].rearrange("p j l -> p (j l)"), ps[:, 4, 256:320]).then_inc(tr_done, 1)
            for j in range(8):
                rest(BASE["mem"] + j + 2)
            for n in range(4):
                dve.wait_ge(vm_ps, n + 1)
                dve.tensor_copy(VM[:, n // 2, :, (n % 2) * P:(n % 2 + 1) * P], ps[:, 4 + n, 0:MT * P].rearrange("p (m c) -> p m c", m=MT)
                                ).then_inc(vm_ready, 1)

            dve.wait_ge(s5_tr, 1)
            dve.tensor_copy(PS5[:].rearrange("p r g -> p (r g)"), ps[:, 4, 0:3 * S5G])
            dve.tensor_copy(DT[:], ps[0:S5H, 4, 3 * S5G:4 * S5G]).then_inc(s5_dve, 1)
            dve.wait_ge(s5_dve, 1)
            s5_parameters()
            ffn("ffn0", s5_fill)
            norm("ffn0")
            dve.wait_ge(s5_out, 64 * S5T)
            for j in range(6):
                rest(BASE["mla"] + j + 2)
            reciprocal(0)
            reciprocal(1)
            for j in range(2):
                dve.wait_ge(*taken_at("mla", j))
                dve.scalar_tensor_tensor(CQ[:, j, :], CQ[:, j, :], COL[:, 96 + 98 + j:96 + 99 + j], RST[:, 0, :], ALU.mult, ALU.mult).then_inc(cq_norm, 1)
            dve.wait_ge(*taken_at("mla", 2))
            dve.scalar_tensor_tensor(CKV[:], CKV[:], COL[:, 96 + 100:96 + 101], RST[:, 1, :], ALU.mult, ALU.mult).then_inc(cq_norm, 1)
            dve.wait_ge(kr_ps, 1)
            dve.wait_ge(mla_in_s, 80)
            dve.tensor_tensor(KR2[:, 0, :], ps[ROPE:2 * ROPE, 6, :], ROT[ROPE:2 * ROPE, :], ALU.mult).then_inc(kr_rot, 1)
            dve.tensor_tensor(KR2[:, 1, :], KR, ROT[0:ROPE, :], ALU.mult).then_inc(dve_link, 1)
            dve.wait_ge(dve_link, 1)
            dve.tensor_tensor(KR2[:, 0, :], KR2[:, 0, :], KR2[:, 1, :], ALU.add).then_inc(kr_rot, 1)
            dve.wait_ge(kr_rot, 2)
            dve.tensor_copy(KT[HD:QK, 6:12, :], KR2[:, 0:1, :].broadcast_to([ROPE, 6, T])).then_inc(kr_dve, 1)
            for g in range(14):
                if g < 6:
                    dve.wait_ge(kv_ps, g + 1)
                    dve.tensor_copy(KT[0:HD, 2 * g + 1, :], ps[HD:P, 4 + g % 4, :]).then_inc(kv_dve, 1)
                elif g % 2:
                    dve.wait_ge(kv_ps, g + 1)
                    dve.tensor_copy(V[:, (g - 6) // 2, 6 * HD:], ps[:, 4 + g % 4, 0:6 * HD]).then_inc(kv_dve, 1)

            def rotate_q(h, s):
                dve.wait_ge(q_ps, h + 1)
                wait(dve, q_rope, h)
                dve.tensor_tensor(RT[HD:QK, 0, :], ps[HD:QK, 3, :], ROT[HD:QK, :], ALU.mult).then_inc(q_rot, 1)
                dve.tensor_tensor(RT[HD:QK, 1, :], ps[QK:P, 3, :], ROT[QK:P, :], ALU.mult).then_inc(q_rot, 1)
                dve.wait_ge(q_rot, 2 * h + 2)
                if not (isinstance(h, int) and h < 2):
                    dve.wait_ge(s_ps, h - 1)
                dve.tensor_tensor(QT[HD:QK, s, :], RT[HD:QK, 0, :], RT[HD:QK, 1, :], ALU.add).then_inc(q_rope, 1)

            def o_head(h):
                return O[:, :, bass.ds(h * HD, HD)]

            rotate_q(0, 0)
            rotate_q(1, 1)
            soft_max(0, 0, CAUS, first=True)

            def mla_pair(i):
                for s in range(2):
                    u = 2 * i + s
                    probs_out(u, s)
                    soft_max(u + 1, 1 - s, CAUS)
                    rotate_q(u + 2, s)
                    head_out(u, s, o_head(u))

            mla_pair(0)
            with dve.Fori(1, HEADS // 2 - 1) as i:
                mla_pair(i)
            probs_out(10, 0)
            soft_max(11, 1, CAUS)
            head_out(10, 0, o_head(10))
            probs_out(11, 1)
            mem_max(12, 0)
            own_sums(11, 1)
            head_out(11, 1, o_head(11))
            for h in range(MEM_HEADS):
                u = 12 + h
                probs_out(u, u % 2)
                if h < 3:
                    mem_max(u + 1, 1 - u % 2)
                own_sums(u, u % 2)
                head_out(u, u % 2, O[:, :, TOKW + h * HD:TOKW + (h + 1) * HD])
            mix_lo_of(0)
            for j in range(8):
                p = BASE["wo0"] + j
                rest(p + 2)
                dve.wait_ge(pe_panel, p + 1)
                dve.scalar_tensor_tensor(XT[:, j, :], XT[:, j, :], ALPHA, ps[:, p % 4, :], ALU.mult, ALU.add).then_inc(taken[p % 4], 1)
            norm("wo0")
            ffn("ffn1", nothing)
            norm("ffn1")
            modulation(0)

            for j in range(6):
                rest(BASE["kv"] + j + 2)
                if j == 2:
                    for e in range(2):
                        dve.wait_ge(*taken_at("kv", e))
                        for a in range(2):
                            for g in range(GROUPS):
                                r = slice(g * HD, (g + 1) * HD)
                                ins = dve.tensor_tensor(ZB[a * HD:(a + 1) * HD, e, :, g, 0:NCMP],
                                                        ZC[r, e, 16 * a:16 * a + 16 * NCMP].rearrange("p (n l) -> p l n", l=16),
                                                        POS[r, e, 16 * a:16 * a + 16].rearrange("p (l o) -> p l o", o=1).broadcast_to([HD, 16, NCMP]), ALU.add)
                        ins.then_inc(zb_ready, 1)
            for e, dst in enumerate((VS, VW)):
                dve.wait_ge(vt_ps, e + 1)
                dve.tensor_copy(dst[:].rearrange("p t c -> p (t c)"), ps[:, 4 + e, :]).then_inc(vt_out, 1)
            ffn("ffn2", nothing)
            norm("ffn2")
            modulation(1)

            for j in range(9):
                rest(BASE["nsa"] + j + 2)
                if j == 3:
                    dve.wait_ge(g_ps, 1)
                    for t in range(TT):
                        ins = dve.tensor_copy(G[:, :, :, t, :], ps[:, 4, t * 36:(t + 1) * 36].rearrange("p (g j b) -> p b j g", g=GROUPS, j=HPG))
                    ins.then_inc(g_out, 1)
            scale[0] = SEL_SCALE
            dve.wait_ge(cmask_in, 16)
            dve.wait_ge(bias_in[0], 32)
            soft_max(16, 0, BIAS[:, 0, 0], first=True)

            def cmp_max(j, q):
                dve.wait_ge(c_ps, j + 1)
                wait(dve, c_t, j)
                dve.tensor_tensor(SC[:].rearrange("p t g n -> p (t g n)"), ps[:, 3, 0:TT * 2 * NPAD], CB[:, q], ALU.add).then_inc(c_sc, 1)
                dve.wait_ge(c_sc, 2 * j + 1)
                dve.tensor_reduce(MC[:], SC[:], AX.X, ALU.max).then_inc(c_sc, 1)
                dve.wait_ge(c_sc, 2 * j + 2)
                dve.tensor_tensor(SC[:], SC[:], MC[:].rearrange("p t (g o) -> p t g o", o=1).broadcast_to([P, TT, GROUPS, NPAD]), ALU.subtract).then_inc(c_sub, 1)

            def cmp_probs(j):
                dve.wait_ge(c_mask, j + 1)
                dve.tensor_reduce(SMC[:], SC[:], AX.X, ALU.add).then_inc(c_sum, 1)
                dve.wait_ge(c_sum, 4 * j + 1)
                dve.tensor_scalar(SMC[:], SMC[:], 1e-30, None, ALU.max).then_inc(c_sum, 1)
                dve.wait_ge(c_sum, 4 * j + 2)
                dve.reciprocal(SMC[:], SMC[:]).then_inc(c_sum, 1)
                dve.wait_ge(c_sum, 4 * j + 3)
                dve.tensor_tensor(SMC[:], SMC[:], G[:, 0, bass.ds(j, 1)].rearrange("p o t g -> p (o t) g"), ALU.mult).then_inc(c_sum, 1)
                dve.wait_ge(c_sum, 4 * j + 4)
                dve.tensor_tensor(SC[:], SC[:], SMC[:].rearrange("p t (g o) -> p t g o", o=1).broadcast_to([P, TT, GROUPS, NPAD]), ALU.mult).then_inc(c_p, 1)

            def gated_out(u, j, k):
                s, g, br = k % 2, k % 2, k // 2
                dve.wait_ge(rs_ready, u + 1)
                dve.tensor_tensor(W4[:, s, :], RS[:, s, :], G[:, 1 + br, bass.ds(j, 1), :, g].rearrange("p o t -> p (o t)"), ALU.mult).then_inc(w4_ready, 1)
                dve.wait_ge(w4_ready, u - 15)
                dve.wait_ge(pv_ps, u + 1)
                dst = O[:, :, bass.ds(g * HPG * HD + j * HD, HD)]
                src = ps[:, 7, 0:TT * HD].rearrange("p (t d) -> p t d", t=TT)
                if br == 0:
                    dve.tensor_tensor(dst, src, W4[:, s, :].rearrange("p (t o) -> p t o", o=1).broadcast_to([P, TT, HD]), ALU.mult).then_inc(o_done, 1)
                else:
                    dve.wait_ge(o_done, u - 1)
                    for t in range(TT):
                        ins = dve.scalar_tensor_tensor(dst[:, t], src[:, t], W4[:, s, t:t + 1], dst[:, t], ALU.mult, ALU.add)
                    ins.then_inc(o_done, 1)

            def cmp_out(j):
                dve.wait_ge(c_pv, j + 1)
                dve.wait_ge(o_done, 20 + 4 * j)
                for g in range(GROUPS):
                    dst = O[:, :, bass.ds(g * HPG * HD + j * HD, HD)]
                    ins = dve.tensor_tensor(dst, dst, ps[:, 3, :].rearrange("p (t g d) -> p t g d", t=TT, g=GROUPS)[:, :, g], ALU.add)
                ins.then_inc(c_o, 1)

            def nsa_pair(j, q, slot, last=False):
                for k in range(4):
                    u = 16 + 4 * j + k
                    probs_out(u, k % 2)
                    if k == 0:
                        cmp_max(j, q)
                    if k == 2:
                        cmp_probs(j)
                    if k < 3:
                        soft_max(u + 1, 1 - k % 2, BIAS[:, q, (k + 1) % 2])
                    elif not last:
                        dve.wait_ge(bias_in[1 - q], 32 * slot)
                        soft_max(u + 1, 0, BIAS[:, 1 - q, 0])
                    else:
                        mem_max(u + 1, 0)
                        own_sums(u, k % 2)
                    gated_out(u, j, k)
                cmp_out(j)

            nsa_pair(0, 0, 1)
            nsa_pair(1, 1, 2)
            with dve.Fori(1, HPG // 2 - 1) as i:
                nsa_pair(2 * i, 0, i + 1)
                nsa_pair(2 * i + 1, 1, i + 2)
            nsa_pair(4, 0, 3)
            nsa_pair(5, 1, 0, last=True)
            for h in range(MEM_HEADS):
                u = 40 + h
                probs_out(u, u % 2)
                if h < 3:
                    mem_max(u + 1, 1 - u % 2)
                own_sums(u, u % 2)
                head_out(u, u % 2, O[:, :, TOKW + h * HD:TOKW + (h + 1) * HD])
            mix_lo_of(8)
            for j in range(8):
                p = BASE["wo1"] + j
                rest(p + 2)
                dve.wait_ge(pe_panel, p + 1)
                dve.scalar_tensor_tensor(XT[:, j, :], XT[:, j, :], ALPHA, ps[:, p % 4, :], ALU.mult, ALU.add).then_inc(taken[p % 4], 1)
            norm("wo1")
            ffn("ffn3", ffn3_fill)
            norm("ffn3", split=False)

            rms("even", 0)
            for j in range(6):
                p = BASE["even"] + j
                rest(p + 2)
                dve.wait_ge(pe_panel, p + 1)
                dve.tensor_copy(UT[:, j, :, 0:NCC].rearrange("p t c -> p c t"), ps[:, 4 + j % 2, 0:CTX].rearrange("p (c t) -> p c t", t=L)).then_inc(uc_out, 1)
            for j in range(6, 10):
                rest(BASE["even"] + j + 2)
            for t in range(S5T):
                for b in range(4):
                    dve.wait_ge(b_ps, 4 * t + b + 1)
                    g = t * GT + (b % 2) * 4
                    src = ps[S5P:P, 4 + b, 0:4 * NC].rearrange("p (g c) -> p g c", g=4)
                    dve.tensor_copy(H[S5P:P, b // 2, g:g + 4, 0:NCC], src[:, :, 0:NCC][:, :, ::-1])
                    dve.tensor_copy(H[S5P:P, b // 2, g:g + 4, NCC:], src[:, :, NCC:][:, :, ::-1]).then_inc(h_dve, 1)
            dve.wait_ge(bk_ready, 1)
            dve.wait_ge(h_act, 4 * S5T)
            dve.wait_ge(h_dve, 4 * S5T)

            def advance(k):
                before = H[:, :, :, bass.ds(k - 1, 1)].rearrange("p r g o -> p o r g").broadcast_to([P, 2, 2, S5G])
                here = H[:, :, :, bass.ds(k, 1)].rearrange("p r g o -> p r (g o)")
                wait(dve, scan, 3 * k - 3)
                dve.tensor_tensor(SCM, L8[:], before, ALU.mult).then_inc(scan, 1)
                dve.wait_ge(scan, 3 * k - 2)
                dve.tensor_tensor(SCA, SCM[:, 0], SCM[:, 1][:, ::-1], ALU.add).then_inc(scan, 1)
                dve.wait_ge(scan, 3 * k - 1)
                dve.tensor_tensor(here, here, SCA, ALU.add).then_inc(scan, 1)

            for k in range(1, 4):
                advance(k)
            with dve.Fori(1, NC // 4) as i:
                for k in range(4):
                    advance(4 * i + k)
            dve.wait_ge(scan, 3 * (NC - 1))

            def states(t):
                wait(dve, y_ps, t - 1)
                dve.tensor_copy(SS[S5P:P, t % 2], H[S5P:P, :, t * GT:(t + 1) * GT, NCC - 1:NC - 1][:, :, :, ::-1]).then_inc(ss_dve, 1)

            dve.wait_ge(fnet_ps, 8)
            for t in range(S5T):
                states(t)
            for j in range(6):
                dve.wait_ge(ya_hi, j + 1)
                dve.tensor_tensor(XL[:, j, :], YA[:, j, :], XH[:, j, :].bitcast(F32), ALU.subtract).then_inc(x_split, 1)

            for e in range(2):
                dve.wait_ge(p1_ready, e + 1)
                dve.tensor_copy(YH[:, 6 + e, :], ZS[:, 6 + e, :]).then_inc(y_full, 1)
                dve.wait_ge(y_full, e + 1)
                dve.tensor_tensor(YL[:, 6 + e, :], ZS[:, 6 + e, :], YH[:, 6 + e, :].bitcast(F32), ALU.subtract).then_inc(y_ready, 1)
            for j in range(6):
                p = BASE["glu"] + j
                rest(p + 2)
                dve.wait_ge(p1_ready, 3 + j)
                dve.wait_ge(*taken_at("glu", j))
                dve.tensor_tensor(YH[:, j, :], SIG[:, j % 2, :], ZS[:, j, :], ALU.mult)
                dve.tensor_tensor(YF[:, j % 2, :], SIG[:, j % 2, :], ZS[:, j, :], ALU.mult).then_inc(y_full, 1)
                dve.wait_ge(y_full, j + 3)
                dve.tensor_tensor(YL[:, j, :], YF[:, j % 2, :], YH[:, j, :].bitcast(F32), ALU.subtract).then_inc(y_ready, 1)
            gated("ewo", 0)
            rms("odd", 1)

            for j in range(4):
                rest(BASE["odd"] + j + 2)
            dve.wait_ge(odd_zero, 1)
            link = 0
            for k in range(4):
                p = BASE["odd"] + 4 + 3 * k
                rest(p + 2)
                rest(p + 3)
                dve.wait_ge(*taken_at("odd", 4 + 3 * k))
                dve.wait_ge(pe_panel, p + 2)
                v, cx = CV[:, k % 2, :], CX[:, k % 2, :]
                dve.tensor_tensor(v[:, 1:T + 1], CG[:, k % 2, :], ps[:, (p + 1) % 4, :], ALU.mult).then_inc(taken[(p + 1) % 4], 1)
                dve.wait_ge(*taken_at("odd", 5 + 3 * k))
                w = [COL[:, 96 + 82 + 4 * c + k:96 + 83 + 4 * c + k] for c in range(3)]
                dve.tensor_scalar(cx, v[:, 1:T + 1], w[1], None, ALU.mult).then_inc(dve_link, 1)
                dve.wait_ge(dve_link, 3 * k + 2)
                dve.scalar_tensor_tensor(cx, v[:, 0:T], w[0], cx, ALU.mult, ALU.add).then_inc(dve_link, 1)
                dve.wait_ge(dve_link, 3 * k + 3)
                dve.scalar_tensor_tensor(cx, v[:, 2:T + 2], w[2], cx, ALU.mult, ALU.add).then_inc(dve_link, 1)
                rest(p + 4)
                dve.wait_ge(dve_link, 3 * k + 4)
                dve.wait_ge(pe_panel, p + 3)
                dve.tensor_tensor(YO[:, 4 + k, :], cx, ps[:, (p + 2) % 4, :], ALU.mult).then_inc(taken[(p + 2) % 4], 1)
            for j in range(8):
                p = BASE["odd"] + 16 + j
                rest(p + 2)
                if j < 4:
                    dve.wait_ge(yc_ready, j + 1)
                else:
                    dve.wait_ge(*taken_at("odd", 6 + 3 * (j - 4)))
                dve.wait_ge(*taken_at("odd", 16 + j))
                dve.tensor_tensor(YH[:, j, :], YO[:, j, :], ZO[:, j % 2, :], ALU.mult)
                dve.tensor_tensor(YQ[:, j % 2, :], YO[:, j, :], ZO[:, j % 2, :], ALU.mult).then_inc(y_full, 1)
                dve.wait_ge(y_full, 8 + j + 1)
                dve.tensor_tensor(YL[:, j, :], YQ[:, j % 2, :], YH[:, j, :].bitcast(F32), ALU.subtract).then_inc(y_ready, 1)
            gated("owo", 1)
            reciprocal(0)
            for d in range(KD):
                dve.scalar_tensor_tensor(XT[:, d, :], XT[:, d, :], COL[:, 96 + 64 + d:96 + 65 + d], RST[:, 0, :], ALU.mult, ALU.mult).then_inc(ln_aff, 1)

        @block.gpsimd
        def _(pool):
            def norm(stage, last, split=True):
                no = LN_NO[stage]
                for d in range(KD):
                    pool.wait_ge(*taken_at(stage, last - KD + d))
                    if d == 0:
                        pool.tensor_copy(ACC[:], XT[:, 0, :]).then_inc(ln_acc, 1)
                    else:
                        pool.wait_ge(ln_acc, 8 * no + d)
                        pool.tensor_tensor(ACC[:], ACC[:], XT[:, d, :], ALU.add).then_inc(ln_acc, 1)
                for d in range(KD if split else 0):
                    pool.wait_ge(ln_aff, 8 * no + d + 1)
                    pool.tensor_tensor(XL[:, d, :], XT[:, d, :], XH[:, d, :].bitcast(F32), ALU.subtract).then_inc(x_split, 1)

            n = [0]

            def step(ins):
                n[0] += 1
                ins.then_inc(pool_link, 1)
                pool.wait_ge(pool_link, n[0])

            def product(a, b, outs, shape):
                size = int(np.prod(shape[1:]))
                t1, t2 = (t[:, 0:size] for t in (T1, T2))
                if len(shape) == 3:
                    t1, t2 = (t.rearrange("p (x y) -> p x y", x=shape[1]) for t in (t1, t2))
                if len(shape) == 4:
                    t1, t2 = (t.rearrange("p (x y z) -> p x y z", x=shape[1], y=shape[2]) for t in (t1, t2))
                for e, op in enumerate((ALU.subtract, ALU.add)):
                    pool.tensor_tensor(t1, a[0], b[e], ALU.mult)
                    step(pool.tensor_tensor(t2, a[1], b[1 - e], ALU.mult))
                    for rows, dst in outs:
                        step(pool.tensor_tensor(dst[e], t1[rows], t2[rows], op))

            FWD, BWD, ALL = slice(0, S5P), slice(S5P, P), slice(0, P)

            for r, name in enumerate(("s5_lam_re_2", "s5_lam_im_2")):
                pool.dma_start(LAMN[:, r, :].rearrange("g (d p) -> g d p", d=2), A[name][0].rearrange("d g p -> g d p")).then_inc(s5_in, 16)
            pool.dma_start(LSN, A["s5_log_step_2"][0]).then_inc(s5_in, 16)
            pool.dma_start(DN, A["s5_d_2"][0]).then_inc(s5_in, 16)
            pool.dma_start(DSEL, C["dirsel"]).then_inc(s5_in, 16)
            for r, (bn, cn) in enumerate((("s5_b_re_2", "s5_c_re_2"), ("s5_b_im_2", "s5_c_im_2"))):
                for e in range(2):
                    pool.dma_start(CN[:, r, :, e, :], A[cn][0, e].rearrange("(t g) h p -> (g h) t p", g=GT)).then_inc(s5_in, 16)
                    pool.dma_start(BN[e * S5P:(e + 1) * S5P, r], A[bn][0, e].rearrange("g p h -> p g h")).then_inc(s5_in, 16)
            pool.wait_ge(s5_in, 16 * S5_LOADS)
            step(pool.memset(PW[:, 0, 0, :], 1.0))
            step(pool.memset(PW[:, 1, 0, :], 0.0))
            pool.wait_ge(f_ready, 1)
            for k in (1, 2, 4):
                product([PW[:, r, 1:1 + k, :] for r in range(2)], [PW[:, r, k:k + 1, :].broadcast_to([P, k, S5G]) for r in range(2)],
                        [(ALL, [PW[:, r, k + 1:2 * k + 1, :] for r in range(2)])], [P, k, S5G])
            product([FB5[:, r, :].rearrange("p (g o) -> p g o", o=1).broadcast_to([P, S5G, S5H]) for r in range(2)], [BN[:, r] for r in range(2)],
                    [(ALL, [BB[:, r] for r in range(2)])], [P, S5G, S5H])

            def powers(r, rows, ks):
                return PW[rows, r, ks, :].rearrange("p k g -> p g k")
            for rows, up, down in ((FWD, slice(1, L + 1), slice(L - 1, None, -1)), (BWD, slice(L, 0, -1), slice(0, L))):
                step(pool.tensor_copy(PC[rows, 0], powers(0, rows, up)))
                step(pool.tensor_scalar(PC[rows, 1], powers(1, rows, up), -1.0, None, ALU.mult))
                for r in range(2):
                    step(pool.tensor_copy(PB[rows, r], powers(r, rows, down)))
            for r in range(2):
                step(pool.tensor_copy(L8[:, 0, r, :], PW[:, 0, L, :]))
            step(pool.tensor_copy(L8[:, 1, 0, :], PW[:, 1, L, :]))
            step(pool.tensor_scalar(L8[:, 1, 1, :], PW[:, 1, L, :], -1.0, None, ALU.mult))
            pool.wait_ge(s5_tr, 4)
            pool.wait_ge(cr_out, 3)
            step(pool.memset(SW[:], 0.0))

            def tile(t):
                gs = slice(t * GT, (t + 1) * GT)

                def over_time(x):
                    return [x[:, r, gs, :].rearrange("p g (o h) -> p g o h", o=1).broadcast_to([P, GT, L, S5H]) for r in range(2)]

                def over_channels(x):
                    return [x[:, r, gs, :].rearrange("p g (t o) -> p g t o", o=1).broadcast_to([P, GT, L, S5H]) for r in range(2)]

                def cut(x, rows, col):
                    return [x[rows, r, :, col:col + P].rearrange("p g (t h) -> p g t h", t=L) for r in range(2)]
                wait(pool, s5_z, 4 * t)
                wait(pool, s5_out, 64 * t)
                product(over_time(BB), over_channels(PB), [(ALL, cut(BK, ALL, 0))], [P, GT, L, S5H])
                product(over_time(CR), over_channels(PC), [(FWD, cut(SW, FWD, (L + 1) * S5H)), (BWD, cut(SW, BWD, 0))], [P, GT, L, S5H])
                for r in range(2):
                    ins = pool.tensor_copy(SW[:, r, :, L * S5H:(L + 1) * S5H], CR[:, r, gs, :])
                ins.then_inc(bk_ready, 1)
                step(pool.tensor_tensor(DD, IDENT[0:S5H, 0:S5H].rearrange("p (o h) -> p o h", o=1).broadcast_to([S5H, GT, S5H]),
                                        DT[:, gs].rearrange("p (g o) -> p g o", o=1).broadcast_to([S5H, GT, S5H]), ALU.mult))
                pool.wait_ge(z_out, 4 * t + 4)
                mid = Z[:, :, (L - 1) * S5H:L * S5H]
                step(pool.tensor_tensor(mid, mid, DD, ALU.add))
                for rows, col in ((FWD, (L + 1) * S5H), (BWD, 0)):
                    pool.dma_start(scratch["s5_w"][t, rows], SW[rows, :, :, col:col + P].rearrange("p r g c -> p (r g) c")).then_inc(s5_out, 16)
                pool.wait_ge(bt_act, 2 * t + 2)
                pool.wait_ge(bt_dve, 2 * t + 2)
                pool.dma_start(scratch["s5_b"][t], BT[:].rearrange("p r g c -> p (r g c)")).then_inc(s5_out, 16)
                pool.dma_start(scratch["s5_taps"][:, gs], Z[:]).then_inc(s5_out, 16)

            for t in range(S5T):
                tile(t)
            norm("ffn0", 68)
            pool.wait_ge(s5_out, 64 * S5T)
            for t in range(L):
                pool.dma_start(scratch["s5_m"][t * S5H:(t + 1) * S5H], scratch["s5_taps"][:, :, (L - 1 - t) * S5H:(L - 1 - t) * S5H + P]).then_inc(s5_out, 16)
            norm("wo0", 8)

            def load_ada(layer):
                w = A["ada_w_2"][layer].rearrange("(k p) n -> p k n", p=P)
                for n in range(12):
                    wait(pool, ada_used, 12 * layer + n - 1)
                    pool.dma_start(AW[:, n % 2], w[:, :, n * 2 * P:(n + 1) * 2 * P]).then_inc(aw_in[n % 2], 16)

            pool.wait_ge(pe_panel, BASE["ffn1"])
            for t in (H1, KCB, VCB):
                ins = pool.memset(t[:], 0.0)
                if t is not KCB:
                    ins.then_inc(zeros, 1)
            load_ada(0)
            pool.wait_ge(ada_used, 12)
            for j in range(2):
                for a in range(2):
                    pool.dma_start(W1[j][a * HD:(a + 1) * HD], A["cmp_w1"][j].rearrange("(a l d) h -> a d l h", a=2, d=HD)[a]).then_inc(w1_in, 16)
                pool.dma_start(W2[:, j], A["cmp_w2"][j].rearrange("(m p) d -> p m d", p=P)).then_inc(w1_in, 16)
            norm("ffn1", 68)
            pool.wait_ge(hid_ps, 4)
            load_ada(1)
            norm("ffn2", 68)
            pool.wait_ge(cmask_in, 16)

            def copy_q(j, q):
                pool.wait_ge(*taken_at("nsa", 6 + j // 2))
                if j >= 2:
                    pool.wait_ge(s_ps, 16 + 4 * (j - 1))
                pool.tensor_copy(QS[:, q, :], QP[:, j, :]).then_inc(qs_ready, 1)

            def mask(j):
                pool.wait_ge(c_exp, j + 1)
                pool.tensor_tensor(SC[:], SC[:], CMASK[:].rearrange("p (t o n) -> p t o n", o=1, n=NPAD).broadcast_to([P, TT, GROUPS, NPAD]), ALU.mult).then_inc(c_mask, 1)

            copy_q(0, 0)
            for j in range(HPG):
                if j + 1 < HPG:
                    copy_q(j + 1, (j + 1) % 2)
                mask(j)
            norm("wo1", 8)
            pool.wait_ge(pe_panel, BASE["ffn3"])
            pool.dma_start(CXN[:], A["ctx_2"][0].rearrange("(m p) d -> p m d", p=P)).then_inc(cx_in, 16)
            pool.dma_start(SCT[:].rearrange("p k t -> p (k t)"), C["sincos"]).then_inc(cx_in, 16)
            pool.wait_ge(cx_in, 32)
            for k in range(KD):
                pool.tensor_scalar(SCT[:, k, :], SCT[:, k, :], COL[:, 88 + k:89 + k], None, ALU.add).then_inc(sct_ready, 1)
            for k in range(KD):
                pool.wait_ge(cx_hi, k + 1)
                pool.tensor_tensor(CL[:, k, :], CXT[:, k, :], CH[:, k, :].bitcast(F32), ALU.subtract).then_inc(cx_split, 1)
            norm("ffn3", 68, split=False)

            for d in range(KD):
                pool.wait_ge(ln_aff, 8 * LN_NO["even"] + d + 1)
                pool.tensor_tensor(XL[:, d, :], NT[:, d, :], XH[:, d, :].bitcast(F32), ALU.subtract).then_inc(x_split, 1)
            u_rows = scratch["s5_u"].rearrange("(g h) t c -> t h g c", h=S5H)
            for s in range(2):
                pool.wait_ge(pe_panel, BASE["even"] + 1)
                pool.dma_start(BS[:, s].rearrange("p r g c -> p (r g c)"), scratch["s5_b"][s]).then_inc(bs_in[s], 16)
            for j in range(6):
                pool.wait_ge(*taken_at("even", j))
                pool.wait_ge(uc_out, j + 1)
                pool.dma_start(scratch["s5_u"][j * P:(j + 1) * P], UT[:, j]).then_inc(shuffle_out, 16)
            pool.wait_ge(shuffle_out, 16 * 6)
            for t in range(L):
                pool.dma_start(U[t * S5H:(t + 1) * S5H], u_rows[t]).then_inc(shuffle_in, 16)
            for t in range(2, S5T):
                pool.wait_ge(b_ps, 4 * (t - 2) + 4)
                pool.dma_start(BS[:, t % 2].rearrange("p r g c -> p (r g c)"), scratch["s5_b"][t]).then_inc(bs_in[t % 2], 16)

            def load_s5(t):
                pool.dma_start(MW[:, t % 2, 0], scratch["s5_m"][:, t * GT:(t + 1) * GT]).then_inc(mw_in[t % 2], 16)
                pool.dma_start(MW[:, t % 2, 1:3].rearrange("p r g c -> p (r g) c"), scratch["s5_w"][t]).then_inc(mw_in[t % 2], 16)
            pool.wait_ge(b_ps, 4 * S5T)
            step(pool.memset(FW[:], 0.0))
            for b in range(4):
                r = slice((b % 2) * HD, (b % 2 + 1) * HD)
                pool.dma_start(FW[r, b // 2, r], A["fnet_w_2"][0, b]).then_inc(dft_in, 16)
            pool.dma_start(DFTC[:], C["dftc"]).then_inc(dft_in, 16)
            pool.dma_start(DFTT[:].rearrange("p e t c -> p (e t c)"), C["dftt"]).then_inc(dft_in, 16)
            for p in range(BASE["even"] + 12, BASE["glu"] + 2):
                pool.wait_ge(w_hi, p + 1)
                pool.wait_ge(w_lo, p)
                pool.tensor_tensor(wl[:, p % 2, :], raw[:, p % 4, :], wh[:, p % 2, :].bitcast(F32), ALU.subtract).then_inc(w_lo, 1)
            pool.wait_ge(fnet_ps, 8)
            pool.wait_ge(s5_out, 64 * S5T + 16 * L)
            load_s5(0)
            load_s5(1)
            for j in range(2):
                pool.wait_ge(fnet_out, 7 + j)
                pool.wait_ge(*taken_at("even", 14 + j))
                pool.tensor_tensor(ZS[:, 6 + j, :], ZS[:, 6 + j, :], YB[:, j, :], ALU.mult).then_inc(p1_ready, 1)
            for t in range(2, S5T):
                pool.wait_ge(y_ps, t - 1)
                load_s5(t)
            y_rows = scratch["s5_y"].rearrange("(g h) t c -> t h g c", h=S5H)
            pool.wait_ge(y_sb, S5T)
            for t in range(L):
                pool.dma_start(y_rows[t], YS[t * S5H:(t + 1) * S5H]).then_inc(shuffle_out, 16)
            pool.wait_ge(shuffle_out, 16 * (6 + L))
            pool.dma_start(YT[:].rearrange("p j t c -> p j (t c)"), scratch["s5_y"].rearrange("(j p) t c -> p j (t c)", p=P)).then_inc(shuffle_in, 16)
            for j in range(6):
                pool.wait_ge(ya_ready, j + 1)
                pool.wait_ge(*taken_at("even", 8 + j))
                pool.tensor_tensor(ZS[:, j, :], ZS[:, j, :], YA[:, j, :], ALU.mult).then_inc(p1_ready, 1)

            pool.wait_ge(y_ready, 8)
            pool.dma_start(PINV[:].rearrange("p i t -> p (i t)"), C["poolinv"]).then_inc(odd_in, 16)
            pool.dma_start(PWT[:], A["pool_w_2"][0].rearrange("i c d -> c i d")).then_inc(odd_in, 16)
            for d in range(KD):
                pool.wait_ge(ln_aff, 8 * LN_NO["odd"] + d + 1)
                pool.tensor_tensor(XL[:, d, :], NO[:, d, :], XH[:, d, :].bitcast(F32), ALU.subtract).then_inc(x_split, 1)
            pool.wait_ge(x_split, XS["odd"] + 8)
            pool.memset(CV[:], 0.0)
            pool.memset(PU[:], 0.0).then_inc(odd_zero, 1)
            pool.wait_ge(odd_in, 32)
            for i, w in enumerate(POOL_WINDOWS):
                pool.wait_ge(*taken_at("odd", i))
                if i >= 2:
                    pool.wait_ge(pw_ps, i - 1)
                src, have, a = PU[:, i, :], 1, 0
                while have < w:
                    size = T + PAD - 2 * have + 9
                    lo = PAD - 8
                    step(pool.tensor_tensor(PS[:, a, lo:lo + size], src[:, lo:lo + size], src[:, lo + have:lo + have + size], ALU.add))
                    src, have, a = PS[:, a, :], 2 * have, 1 - a
                step(pool.tensor_tensor(PP[:, i % 2, :], src[:, PAD - w // 2:PAD - w // 2 + T], PINV[:, i, :], ALU.mult))
                pool.tensor_tensor(PP[:, i % 2, :], PP[:, i % 2, :], PU[:, i, PAD:PAD + T], ALU.subtract).then_inc(pool_ready, 1)


SCRATCH = {
    "s5_w": (S5T, P, 2 * GT, P),
    "s5_b": (S5T, P, 2 * GT * P),
    "s5_taps": (S5H, S5G, (STRIP - 2) * S5H),
    "s5_m": (P, S5G, P),
    "s5_u": (6 * P, L, NC),
    "s5_y": (6 * P, L, NCL),
}


def kernel(**inputs):
    import concourse.bacc as bacc
    from concourse.bass_utils import run_bass_kernel_spmd

    nc = bacc.Bacc("TRN2", target_bir_lowering=False, num_devices=1)
    arrays = {}

    def given(name, a):
        arrays[name] = np.ascontiguousarray(a)
        return nc.dram_tensor(name, arrays[name].shape, mybir.dt.from_np(arrays[name].dtype), kind="ExternalInput").ap()

    A = {name: given("in_" + name, a) for name, a in inputs.items()}
    C = {name: given("const_" + name, a) for name, a in constants().items()}
    out = nc.dram_tensor("out", (1, T, D), F32, kind="ExternalOutput").ap()
    scratch = {name: nc.dram_tensor(name, shape, F32, kind="Internal").ap() for name, shape in SCRATCH.items()}
    program(nc, A, C, out, scratch)
    r = run_bass_kernel_spmd(nc, [arrays], core_ids=[0])
    return r.results[0]["out"]
```

```python
from contextlib import ExitStack

import numpy as np

import concourse.bass as bass
from concourse import mybir

F32 = mybir.dt.float32
F32R = mybir.dt.float32r
I32 = mybir.dt.int32
ACT = mybir.ActivationFunctionType
ALU = mybir.AluOpType
AX = mybir.AxisListType

P = 128
D = 1024
T = 512
M = 256
KD = D // P
TT = T // P
MT = M // P
DFF = 2816
FT = DFF // P
HEADS, HD = 12, 64
MEM_HEADS = 4
TOKW = HEADS * HD
QR, ROPE = 256, 32
QK = HD + ROPE
GROUPS, HPG = 2, 6
CMP_LEN, CMP_STRIDE, CMP_HID = 32, 16, 256
NCMP = (T - CMP_LEN) // CMP_STRIDE + 1
NPAD = 32
SEL_SCALE = HD ** -0.5
MLA_SCALE = QK ** -0.5
ALPHA = (2 * 2) ** 0.25
NEG = -1e30
S5G, S5H, S5P = 48, 16, 64
L = 8
CTX = 256
NCL, NCC = T // L, CTX // L
NC = NCC + NCL
GT = 8
S5T = S5G // GT
STRIP = 2 * L + 1
FNW = 256
POOL_WINDOWS = (2, 4, 8, 16)

PAN = 8 * P
CHUNKS = (8, 8, 6)
STAGES = (("mem", 8), ("ffn0", 68), ("mla", 6), ("wo0", 8), ("ffn1", 68), ("kv", 6), ("ffn2", 68),
          ("nsa", 9), ("wo1", 8), ("ffn3", 68), ("even", 16), ("glu", 6), ("ewo", 8), ("odd", 24), ("owo", 8))
BASE = {}
_n = 0
for _name, _count in STAGES:
    BASE[_name] = _n
    _n += _count
PANELS = _n


def alibi(n):
    c = 2 ** int(np.floor(np.log2(n)))
    s = [(2.0 ** (-8.0 / c)) ** (i + 1) for i in range(c)]
    s2 = [(2.0 ** (-8.0 / (2 * c))) ** (i + 1) for i in range(2 * c)]
    return np.asarray(s + s2[0::2][: n - c], np.float32)


def constants():
    f = np.float32
    c = {}
    c["ident"] = np.eye(P, dtype=f)
    half = ROPE // 2
    freq = 10000.0 ** (-np.arange(half) / half)
    ang = np.arange(T)[None, :] * freq[:, None]
    cos = np.concatenate([np.cos(ang), np.cos(ang)])
    sin = np.concatenate([-np.sin(ang), np.sin(ang)])
    c["rope"] = np.concatenate([cos, sin, cos, sin]).astype(f)
    perm = np.zeros((ROPE, ROPE), f)
    perm[(np.arange(ROPE) + half) % ROPE, np.arange(ROPE)] = 1
    c["perm"] = perm
    dist = np.arange(P)[:, None] + (T - P) - np.arange(T)[None, :]
    c["causal"] = np.where(dist >= 0, 0, NEG).astype(f)
    slopes = alibi(HEADS).astype(np.float64)
    c["alibi"] = np.stack([np.where(dist >= 0, -m * dist / SEL_SCALE, NEG) for m in slopes]).astype(f)
    t = np.arange(T)
    start = np.arange(NCMP) * CMP_STRIDE
    ok = (start + CMP_LEN - 1)[None, :] <= t[:, None]
    okp = np.zeros((T, NPAD), bool)
    okp[:, :NCMP] = ok
    dc = np.zeros((T, NPAD))
    dc[:, :NCMP] = t[:, None] - (start + (CMP_LEN - 1) * 0.5)[None, :]
    cb = np.stack([np.where(okp, -m * dc / SEL_SCALE, NEG) for m in slopes])
    c["cmpbias"] = cb.reshape(GROUPS, HPG, TT, P, NPAD).transpose(1, 3, 2, 0, 4).reshape(HPG, P, TT * 2 * NPAD).astype(f)
    c["cmpmask"] = okp.reshape(TT, P, NPAD).transpose(1, 0, 2).reshape(P, TT * NPAD).astype(f)
    rows, grid = T // 64, 64
    rr, cc = np.meshgrid(np.arange(rows), np.arange(grid), indexing="ij")
    om = 10000.0 ** (-np.arange(D // 4) / (D // 4))
    rr, cc = rr.reshape(-1, 1), cc.reshape(-1, 1)
    pe = np.concatenate([np.sin(rr * om), np.cos(rr * om), np.sin(cc * om), np.cos(cc * om)], -1)
    c["sincos"] = pe.T.reshape(KD, P, T).transpose(1, 0, 2).reshape(P, KD * T).astype(f)
    k = np.arange(64)
    a = 2 * np.pi * np.outer(k, k) / 64
    bd = np.zeros((P, 2 * P))
    for b in range(2):
        s = slice(64 * b, 64 * b + 64)
        bd[s, 64 * b:64 * b + 64] = np.cos(a)
        bd[s, P + 64 * b:P + 64 * b + 64] = -np.sin(a)
    c["dftc"] = bd.astype(f)
    at = 2 * np.pi * (np.outer(t, t) % T) / T
    norm = 1 / np.sqrt(T * 64)
    dt = np.stack([np.cos(at), np.sin(at)]) * norm
    c["dftt"] = dt.reshape(2, TT, P, T).transpose(2, 0, 1, 3).reshape(P, 2 * TT * T).astype(f)
    inv = np.zeros((4, T))
    for i, w in enumerate(POOL_WINDOWS):
        inv[i] = 1.0 / (np.clip(t + w // 2, 0, T) - np.clip(t - w // 2, 0, T))
    c["poolinv"] = np.ascontiguousarray(np.broadcast_to(inv[None], (P, 4, T)).reshape(P, 4 * T)).astype(f)
    sel = np.zeros((2, P), f)
    sel[0, :64] = 1
    sel[1, 64:] = 1
    c["dirsel"] = sel
    return c

VECTORS = (("norm_g_2", "l (k p) -> (l k) p"), ("ada_b_2", "l (k p) -> (l k) p"), ("final_g_2", "(k p) -> k p"),
           ("s5_glu_b_2", "o (k p) -> (o k) p"), ("pool_scale_2", "o (k p) -> (o k) p"), ("conv_w_2", "o c (k p) -> (o c k) p"),
           ("cmp_b1", "j (k p) -> (j k) p"), ("mla_q_norm_g", "o (k p) -> (o k) p"), ("mla_kv_norm_g", "o (k p) -> (o k) p"),
           ("c_2", "o (k p) -> (o k) p"), ("c_ctx_2", "(k p) -> k p"))
COL_LOADS = 2 + len(VECTORS) + 2

STILES = ((3, 4, 0), (2, 5, 0), (0, 5, 3 * P), (1, 6, 0))
POFF = {3: 0, 2: 4 * P, 0: 7 * P, 1: 8 * P}
TBLOCKS = tuple((0, q * P, q, 0) for q in range(4)) + tuple((1, (q - 1) * P, q, 1) for q in range(1, 4)) + (
    (1, 3 * P, 3, 3),) + tuple((2, (q - 2) * P, q, 2) for q in range(2, 4))
PTOFF = {(q, kb): bank * T + col for bank, col, q, kb in TBLOCKS}

PAD = 16
S5_LOADS = 13
MAGIC = 1.5 * 2.0 ** 23
LN2 = (0.693359375, float(np.log(2.0) - 0.693359375))
TURN = (6.28125, float(np.float32(2 * np.pi - 6.28125)), float(2 * np.pi - 6.28125 - np.float32(2 * np.pi - 6.28125)))
ODD_COLS = tuple(range(0, 4 * P, P)) + tuple((4 + 4 * e + k) * P for k in range(4) for e in range(3)) + tuple(range(2 * D, 3 * D, P))
UP_PARTS = ((0, 4), (0, 2, 4), (0, 3))


def kv_count(g):
    if g < 6:
        return g + 1, g + 1
    return 6 + (g - 6) // 2 + 1, 6 + (g - 5) // 2




def program(nc, A, C, out, scratch):
    ctx = ExitStack()
    with ctx:
        def sb(name, shape, dt=F32):
            return ctx.enter_context(nc.sbuf_tensor(name, shape, dt))

        def sem(name):
            return ctx.enter_context(nc.semaphore(name))

        raw = sb("raw", [P, 4, PAN])
        wh = sb("wh", [P, 2, PAN], F32R)
        wl = sb("wl", [P, 2, PAN], F32R)
        XT = sb("XT", [P, KD, T])
        XH = sb("XH", [P, KD, T], F32R)
        XL = sb("XL", [P, KD, T], F32R)
        IDENT = sb("IDENT", [P, P])
        ONES = sb("ONES", [P, P])
        EPS = sb("EPS", [P, 3])
        COL = sb("COL", [P, 96 + 117])
        POS = sb("POS", [P, 2, CMP_LEN])
        ACC = sb("ACC", [P, T])
        NS = sb("NS", [P, 6, T])
        SQ, SD, RST = NS[:, 0:2, :], NS[:, 2:4, :], NS[:, 4:6, :]
        KM = sb("KM", [P, 2, 2, M])
        VM = sb("VM", [P, 2, MT, M])
        CS = sb("CS", [P, KD, 2])
        MOD = sb("MOD", [P, 2, 24, 2])
        AG = sb("AG", [P, 2, KD, 2])
        L8 = sb("L8", [P, 2, 2, S5G])
        CSS = sb("CSS", [P, 4])
        ps = ctx.enter_context(nc.psum_tensor("ps", [P, 8, T], F32))

        AS = NS[:].rearrange("p s t -> p (s t)")[:, 4 * T:].rearrange("p (s e c) -> p s e c", s=2, e=2)
        YT = VM[:].rearrange("p l m c -> p (l m c)").rearrange("p (s t c) -> p s t c", s=2, t=L)
        YB = KM[:].rearrange("p l j m -> p (l j m)").rearrange("p (j t) -> p j t", j=2)
        SCM = SQ[:, 0, 0:4 * S5G].rearrange("p (a r g) -> p a r g", a=2, r=2)
        SCA = SQ[:, 1, 0:2 * S5G].rearrange("p (r g) -> p r g", r=2)

        def phase():
            return ExitStack()

        with phase() as ph:
            def pb(name, shape, dt=F32):
                return ph.enter_context(nc.sbuf_tensor(name, shape, dt))
            XN = pb("XN", [P, TT, D])
            MN = pb("MN", [P, MT, D])
            MH = pb("MH", [P, KD, M], F32R)
            ML = pb("ML", [P, KD, M], F32R)
            MV = pb("MV", [P, 4, M])
            CN1 = pb("CN1", [96, P])
            CN2 = pb("CN2", [117, P])
            PN = pb("PN", [64, 2, HD])
        with phase() as ph:
            HH = pb("HH", [P, 8, T], F32R)
            HL = pb("HL", [P, 8, T], F32R)
            SG = pb("SG", [P, 2, T])
            HF = pb("HF", [P, 2, T])
            with ExitStack() as ph:
                Z = pb("Z", [S5H, GT, (STRIP - 2) * S5H])
                PS5 = pb("PS5", [P, 3, S5G])
                TS5 = pb("TS5", [P, 12, S5G])
                KI5 = pb("KI5", [P, S5G], I32)
                PC = pb("PC", [P, 2, S5G, L])
                PB = pb("PB", [P, 2, S5G, L])
                FB5 = pb("FB5", [P, 2, S5G])
                BB = pb("BB", [P, 2, S5G, S5H])
                CR = pb("CR", [P, 2, S5G, S5H])
                DT = pb("DT", [S5H, S5G])
                PW = RST.rearrange("p s t -> p (s t)")[:, 0:2 * (L + 1) * S5G].rearrange("p (r k g) -> p r k g", r=2, k=L + 1)
                T1 = SQ.rearrange("p s t -> p (s t)")
                T2 = SD.rearrange("p s t -> p (s t)")
                DD = ACC[0:S5H, 0:GT * S5H].rearrange("p (g h) -> p g h", g=GT)
                BK = pb("BK", [P, 2, GT, P])
                BT = pb("BT", [P, 2, GT, P])
                SW = pb("SW", [P, 2, GT, STRIP * S5H])
                flat = SW[:].rearrange("p a b c -> p (a b c)")
                BN = flat[:, 0:1536].rearrange("p (r g h) -> p r g h", r=2, g=S5G)
                CN = flat[:, 1536:3072].rearrange("p (r t d q) -> p r t d q", r=2, t=6, d=2)
                LAMN = flat[0:S5G, 3072:3328].rearrange("g (r c) -> g r c", r=2)
                LSN = flat[0:2, 3328:3328 + S5G]
                DN = flat[0:S5G, 3400:3400 + S5H]
                DSEL = flat[0:2, 3500:3500 + P]
        with phase() as ph:
            O = pb("O", [P, TT, D])
            PR = pb("PR", [P, 2, 1280])
            PT = pb("PT", [P, 2, 1280])
            MX = pb("MX", [P, 2, TT])
            NB = pb("NB", [P, 2, TT])
            SM = pb("SM", [P, 2, TT])
            RS = pb("RS", [P, 2, TT])
            QM = pb("QM", [P, 2, T])
            with ExitStack() as ph:
                ROT = pb("ROT", [P, T])
                PERM = pb("PERM", [ROPE, ROPE])
                CAUS = pb("CAUS", [P, T])
                CQ = pb("CQ", [P, 2, T])
                CKV = pb("CKV", [P, T])
                KR = ACC[0:ROPE, :]
                KT = pb("KT", [QK, HEADS, T])
                V = pb("V", [P, TT, TOKW])
                WUKV = pb("WUKV", [P, 2, HEADS, HD])
                WQ = pb("WQ", [P, 2, 2, P])
                QT = pb("QT", [QK, 2, T])
                RT = pb("RT", [QK, 2, T])
                KR2 = RT[0:ROPE]
            with ExitStack() as mid:
                def mb(name, shape, dt=F32):
                    return mid.enter_context(nc.sbuf_tensor(name, shape, dt))
                AW = mb("AW", [P, 2, KD, 2 * P])
                KS = mb("KS", [P, T])
                KW = mb("KW", [P, T])
                VS = mb("VS", [P, TT, P])
                VW = mb("VW", [P, TT, P])
                KCB = mb("KCB", [P, 2 * NPAD])
                VCB = mb("VCB", [2 * NPAD, P])
                with ExitStack() as ph:
                    ZC = pb("ZC", [P, 2, T])
                    VT = pb("VT", [P, 2, T])
                    W1 = (AW[:].rearrange("p s k c -> p (s k) c"), pb("W1", [P, CMP_LEN // 2, CMP_HID])[:])
                    ZB = pb("ZB", [P, 2, CMP_LEN // 2, GROUPS, NPAD])
                    H1 = pb("H1", [P, 2, 2, GROUPS, NPAD])
                    W2 = pb("W2", [P, 2, 2, HD])
                with ExitStack() as ph:
                    QP = pb("QP", [P, HPG, T])
                    QS = pb("QS", [P, 2, T])
                    BIAS = pb("BIAS", [P, 2, GROUPS, T])
                    CB = pb("CB", [P, 2, TT * GROUPS * NPAD])
                    CMASK = pb("CMASK", [P, TT * NPAD])
                    SC = pb("SC", [P, TT, GROUPS, NPAD])
                    MC = pb("MC", [P, TT, GROUPS])
                    SMC = pb("SMC", [P, TT, GROUPS])
                    GTT = pb("GTT", [HEADS * 3, T])
                    G = pb("G", [P, 3, HPG, TT, GROUPS])
                    PTC = pb("PTC", [2 * NPAD, T])
                    W4 = pb("W4", [P, 2, TT])
        with phase() as ph:
            U = pb("U", [P, S5G, NC])
            H = pb("H", [P, 2, S5G, NC])
            UT = H[:].rearrange("p r g c -> p (r g c)")[:, 0:6 * (CTX + T)].rearrange("p (j t c) -> p j t c", j=6, t=L)
            ZS = pb("ZS", [P, KD, T])
            with ExitStack() as late:
                def lb(name, shape, dt=F32):
                    return late.enter_context(nc.sbuf_tensor(name, shape, dt))
                UB = lb("UB", [P, 2, T])
                FB = UB
                with ExitStack() as ph:
                    BS = pb("BS", [P, 3, 2, GT, P])
                with ExitStack() as ph:
                    FA = pb("FA", [P, TT, 2, 2 * P])
                    DFTT = pb("DFTT", [P, 2, TT, T])
                    DFTC = pb("DFTC", [P, 2 * P])
                    FW = pb("FW", [P, 2, P])
            with ExitStack() as ph:
                MM = pb("MM", [P, 2, GT, P])
                WA = pb("WA", [P, 2, 2, GT, P])
                SS = pb("SS", [P, 2, 2, GT, NCL])
            WT = [WA[:, 0], WA[:, 1], MM[:], *(U[:].rearrange("p g c -> p (g c)")[:, e * 2 * GT * P:(e + 1) * 2 * GT * P].rearrange(
                "p (r g c) -> p r g c", r=2, g=GT) for e in range(2)), WA[:, 0]]
            YS = NS[:].rearrange("p s t -> p (s t)").rearrange("p (g c) -> p g c", g=S5G)
            with ExitStack() as ph:
                YH = pb("YH", [P, KD, T], F32R)
                YL = pb("YL", [P, KD, T], F32R)
        with phase() as ph:
            pb("feed_forward", [P, 20, T])
            CH = pb("CH", [P, KD, CTX], F32R)
            CL = pb("CL", [P, KD, CTX], F32R)
            SCT = pb("SCT", [P, KD, T])
            CXN = pb("CXN", [P, 2, D])
            CXT = pb("CXT", [P, KD, CTX])
            NT = SCT
        with phase() as ph:
            pb("s5_tables", [P, S5G, NC])
            YA = pb("YA", [P, 6, T])
            YF = pb("YF", [P, 2, T])
            SIG = pb("SIG", [P, 2, T])
        with phase() as ph:
            with ExitStack() as ph2:
                NO = ph2.enter_context(nc.sbuf_tensor("NO", [P, KD, T], F32))
            PU = pb("PU", [P, 4, PAD + T + PAD])
            PS = pb("PS", [P, 2, PAD + T + PAD])
            PP = pb("PP", [P, 2, T])
            YQ = pb("YQ", [P, 2, T])
            PINV = pb("PINV", [P, 4, T])
            PWT = pb("PWT", [P, 4, P])
            CG = pb("CG", [P, 2, T])
            CV = pb("CV", [P, 2, T + 2])
            CX = pb("CX", [P, 2, T])
            YO = pb("YO", [P, KD, T])
            ZO = pb("ZO", [P, 2, T])
        with phase() as ph:
            XO = pb("XO", [P, TT, D])

        raw_in = [sem(f"raw_in{s}") for s in range(4)]
        sp_in = [sem(f"sp_in{s}") for s in range(2)]
        pool_in = [sem(f"pool_in{s}") for s in range(3)]
        w_hi = sem("w_hi")
        w_lo = sem("w_lo")
        pe_panel = sem("pe_panel")
        taken = [sem(f"taken{s}") for s in range(4)]
        x_split = sem("x_split")
        x_hi = sem("x_hi")
        tr = sem("tr")
        tr_done = sem("tr_done")
        setup = sem("setup")
        ident_in = sem("ident_in")
        x_in = sem("x_in")
        mem_in = sem("mem_in")
        col_in = sem("col_in")
        mem_hi = sem("mem_hi")
        mem_split = sem("mem_split")
        vm_ps = sem("vm_ps")
        vm_ready = sem("vm_ready")
        h_ready = sem("h_ready")
        ln_acc = sem("ln_acc")
        ln_mu = sem("ln_mu")
        ln_c = sem("ln_c")
        sq_ready = sem("sq_ready")
        sq_used = sem("sq_used")
        sd_ready = sem("sd_ready")
        rstd_ready = sem("rstd_ready")
        ln_n = sem("ln_n")
        ln_hi = sem("ln_hi")
        ln_aff = sem("ln_aff")
        mla_in_s = sem("mla_in_s")
        cq_norm = sem("cq_norm")
        kr_ps = sem("kr_ps")
        kr_rot = sem("kr_rot")
        kr_act = sem("kr_act")
        kr_dve = sem("kr_dve")
        kv_ps = sem("kv_ps")
        kv_act = sem("kv_act")
        kv_dve = sem("kv_dve")
        q_ps = sem("q_ps")
        q_nope = sem("q_nope")
        q_rot = sem("q_rot")
        q_rope = sem("q_rope")
        s_ps = sem("s_ps")
        s_sb = sem("s_sb")
        nb_ready = sem("nb_ready")
        p_ready = sem("p_ready")
        t_ps = sem("t_ps")
        pt_act = sem("pt_act")
        pt_dve = sem("pt_dve")
        pv_ps = sem("pv_ps")
        rs_ready = sem("rs_ready")
        o_done = sem("o_done")
        mix_ps = sem("mix_ps")
        mix_hi = sem("mix_hi")
        dve_link = sem("dve_link")
        pool_link = sem("pool_link")
        s5_in = sem("s5_in")
        s5_tr = sem("s5_tr")
        cr_out = sem("cr_out")
        s5_dve = sem("s5_dve")
        sin_in = sem("sin_in")
        sin_out = sem("sin_out")
        f_ready = sem("f_ready")
        bk_ready = sem("bk_ready")
        s5_t = sem("s5_t")
        bt_act = sem("bt_act")
        bt_dve = sem("bt_dve")
        s5_z = sem("s5_z")
        z_out = sem("z_out")
        s5_out = sem("s5_out")
        cs_ready = sem("cs_ready")
        ada_part = sem("ada_part")
        ada_used = sem("ada_used")
        mod_ready = sem("mod_ready")
        w1_in = sem("w1_in")
        zeros = sem("zeros")
        vt_ps = sem("vt_ps")
        vt_out = sem("vt_out")
        zb_ready = sem("zb_ready")
        hid_ps = sem("hid_ps")
        gelu_out = sem("gelu_out")
        kc_ps = sem("kc_ps")
        kc_out = sem("kc_out")
        g_ps = sem("g_ps")
        g_out = sem("g_out")
        cmask_in = sem("cmask_in")
        qs_ready = sem("qs_ready")
        c_ps = sem("c_ps")
        c_sc = sem("c_sc")
        c_sub = sem("c_sub")
        c_exp = sem("c_exp")
        c_mask = sem("c_mask")
        c_sum = sem("c_sum")
        c_p = sem("c_p")
        c_t = sem("c_t")
        c_pt = sem("c_pt")
        c_pv = sem("c_pv")
        c_o = sem("c_o")
        w4_ready = sem("w4_ready")
        cx_in = sem("cx_in")
        sct_ready = sem("sct_ready")
        cx_sd = sem("cx_sd")
        cx_n = sem("cx_n")
        cx_ps = sem("cx_ps")
        cx_f = sem("cx_f")
        cx_hi = sem("cx_hi")
        cx_split = sem("cx_split")
        uc_out = sem("uc_out")
        shuffle_out = sem("shuffle_out")
        shuffle_in = sem("shuffle_in")
        b_ps = sem("b_ps")
        h_act = sem("h_act")
        h_dve = sem("h_dve")
        dft_in = sem("dft_in")
        fnet_ps = sem("fnet_ps")
        fnet_out = sem("fnet_out")
        scan = sem("scan")
        ss_act = sem("ss_act")
        ss_dve = sem("ss_dve")
        m_ps = sem("m_ps")
        w_in = sem("w_in")
        y_ps = sem("y_ps")
        y_sb = sem("y_sb")
        y_out = [sem(f"y_out{s}") for s in range(2)]
        ya_ready = sem("ya_ready")
        ya_hi = sem("ya_hi")
        p1_ready = sem("p1_ready")
        y_full = sem("y_full")
        y_ready = sem("y_ready")
        odd_in = sem("odd_in")
        odd_zero = sem("odd_zero")
        pool_ready = sem("pool_ready")
        pw_ps = sem("pw_ps")
        yc_ready = sem("yc_ready")
        out_ps = sem("out_ps")
        out_sb = sem("out_sb")
        out_done = sem("out_done")

        LN_SQ = {"ffn0": 0, "mla": 8, "wo0": 11, "ffn1": 19, "ffn2": 27, "wo1": 35, "ffn3": 43, "even": 51, "odd": 59, "final": 67}
        LN_NO = {"ffn0": 0, "wo0": 1, "ffn1": 2, "ffn2": 3, "wo1": 4, "ffn3": 5, "even": 6, "odd": 7, "final": 8}
        HI_NO = {"ffn0": 0, "wo0": 1, "ffn1": 2, "ffn2": 3, "wo1": 4, "even": 5, "odd": 6}
        XS = {"ffn0": 0, "mla": 8, "wo0": 16, "ffn1": 24, "kv": 32, "ffn2": 32, "nsa": 40, "wo1": 48, "ffn3": 56, "even": 64,
              "glu": 72, "odd": 78}
        LN_COL = {"ffn0": 0, "wo0": 8, "ffn1": 16, "ffn2": 24, "wo1": 32, "ffn3": 40}

        IN = {"q": 0, "bias": 3 * 16 * HEADS // 2, "ada": 0, "b": 16 * 12}
        IN["y"] = IN["bias"] + 32 * HPG // 2
        IN["m"] = IN["b"] + 16 * S5T // 3

        def wait(eng, s, value):
            if not (isinstance(value, int) and value <= 0):
                eng.wait_ge(s, value)

        def taken_at(stage, j, i=0):
            p = BASE[stage] + j
            return taken[p % 4], p // 4 + 1 + i

        block = ctx.enter_context(nc.Block())

        def ada_conditions(layer, n):
            return 2 if layer == 0 and n < 8 else 1

        def nothing(k):
            pass

        @block.sync
        def _(sp):
            def load(stage, j, i, src, nk=8):
                p = BASE[stage] + j
                if not (isinstance(i, int) and p + 4 * i < 4):
                    sp.wait_ge(w_lo, p - 3 + 4 * i)
                dst = raw[:, p % 4, 0:nk * P].rearrange("p (k c) -> p k c", k=nk)
                sp.dma_start(dst, src).then_inc(raw_in[p % 4], 16)

            def rows(w):
                return w.rearrange("(k p) n -> p k n", p=P)

            def plain(stage, w, cols, part=slice(None)):
                v = rows(w)
                for j, c in list(enumerate(cols))[part]:
                    load(stage, j, 0, v[:, :, c:c + P], v.shape[1])

            def ffn(stage, layer, half):
                gu, down = rows(A["ffn_w_gu"][layer, half]), rows(A["ffn_w_down"][layer, half])
                off, f0 = 0, 0
                for nf in CHUNKS:
                    with sp.Fori(0, nf // 2) as i:
                        for j in range(4):
                            c = (j % 2) * DFF + (f0 + j // 2) * P
                            load(stage, off + j, i, gu[:, :, bass.ds(i * (2 * P) + c, P)])
                    off += 2 * nf
                    with sp.Fori(0, KD // 4) as i:
                        for j in range(4):
                            load(stage, off + j, i, down[:, f0:f0 + nf, bass.ds(i * (4 * P) + j * P, P)], nf)
                    off += KD
                    f0 += nf

            sp.dma_start(IDENT[:], C["ident"]).then_inc(ident_in, 16)
            sp.dma_start(MN[:], A["mem"][0].rearrange("(m p) d -> p m d", p=P)).then_inc(mem_in, 16)
            sp.dma_start(XN[:], A["x"][0].rearrange("(t p) d -> p t d", p=P)).then_inc(x_in, 16)
            for layer in range(2):
                v = rows(A["w_mem_kv"][layer])
                for j in range(4):
                    load("mem", 4 * layer + j, 0, v[:, :, j * P:(j + 1) * P])
            ffn("ffn0", 0, 0)
            plain("mla", A["mla_w_in"][0], (0, P, QR, QR + P, QR + P + ROPE, QR + 2 * P + ROPE))
            plain("wo0", A["w_out"][0], range(0, D, P), slice(0, 4))
            sp.wait_ge(pe_panel, BASE["mla"])
            for e in range(2):
                sp.dma_start(WUKV[:, e], A["mla_w_ukv"][0].rearrange("p (h e c) -> p e h c", e=2, c=HD)[:, e]).then_inc(mla_in_s, 16)
            sp.dma_start(ROT[:], C["rope"]).then_inc(mla_in_s, 16)
            sp.dma_start(PERM[:], C["perm"]).then_inc(mla_in_s, 16)
            sp.dma_start(CAUS[:], C["causal"]).then_inc(mla_in_s, 16)
            wuq = A["mla_w_uq"][0].rearrange("(k p) (h c) -> p k h c", p=P, c=QK)

            def load_q(i, s):
                w = wuq[:, :, bass.ds(2 * i + s, 1), :].rearrange("p k o c -> p k (o c)")
                half = HD + ROPE // 2
                if not isinstance(i, int):
                    sp.wait_ge(q_ps, 2 * i + s - 1)
                sp.dma_start(WQ[:, s, :, 0:QK], w).then_inc(sp_in[s], 16)
                sp.dma_start(WQ[:, s, :, QK:QK + ROPE // 2], w[:, :, half:QK]).then_inc(sp_in[s], 16)
                sp.dma_start(WQ[:, s, :, QK + ROPE // 2:P], w[:, :, HD:half]).then_inc(sp_in[s], 16)
            for s in range(2):
                load_q(0, s)
            with sp.Fori(1, HEADS // 2) as i:
                for s in range(2):
                    load_q(i, s)
            plain("wo0", A["w_out"][0], range(0, D, P), slice(4, 8))
            ffn("ffn1", 0, 1)
            plain("kv", A["nsa_w_kv"], range(0, 6 * P, P))
            ffn("ffn2", 1, 0)
            nsa = A["nsa_w_in"][0]
            plain("nsa", nsa, (TOKW, TOKW + 3 * HEADS, TOKW + 3 * HEADS + P) + tuple(range(0, TOKW, P)))
            alibi_pairs = C["alibi"].rearrange("(g j) p t -> j p g t", g=GROUPS)
            sp.wait_ge(pe_panel, BASE["nsa"])
            sp.dma_start(CMASK[:], C["cmpmask"]).then_inc(cmask_in, 16)

            def load_bias(j, s):
                bias = alibi_pairs[bass.ds(j, 1)].rearrange("o p g t -> p (o g) t")
                cmp_bias = C["cmpbias"][bass.ds(j, 1)].rearrange("o p n -> p (o n)")
                if not isinstance(j, int):
                    sp.wait_ge(s_sb, 4 * j + 12)
                    sp.wait_ge(c_sc, 2 * j - 3)
                sp.dma_start(BIAS[:, s], bias).then_inc(sp_in[s], 16)
                sp.dma_start(CB[:, s], cmp_bias).then_inc(sp_in[s], 16)
            for s in range(2):
                load_bias(s, s)
            plain("wo1", A["w_out"][1], range(0, D, P), slice(0, 4))
            with sp.Fori(1, HPG // 2) as i:
                for s in range(2):
                    load_bias(2 * i + s, s)
            plain("wo1", A["w_out"][1], range(0, D, P), slice(4, 8))
            ffn("ffn3", 1, 1)
            plain("even", A["even_w_in_2"][0], range(0, 2 * D, P))
            glu = A["s5_glu_w_2"][0]
            plain("glu", glu, range(0, 6 * P, P), slice(0, 4))
            y_rows = scratch["s5_y"].rearrange("(g h) t c -> t h g c", h=S5H)
            y_chunks = scratch["s5_y"].rearrange("(j p) t c -> j p (t c)", p=P)
            for t in range(S5T + 1):
                if t < S5T:
                    sp.wait_ge(y_sb, t + 1)
                    for e in range(L):
                        sp.dma_start(y_rows[e][:, t * GT:(t + 1) * GT], YS[e * S5H:(e + 1) * S5H, t * GT:(t + 1) * GT]).then_inc(y_out[t % 2], 16)
                if t > 0:
                    sp.wait_ge(y_out[(t - 1) % 2], 16 * L * ((t - 1) // 2 + 1))
                    wait(sp, ya_ready, t - 2)
                    sp.dma_start(YT[:, (t - 1) % 2].rearrange("p t c -> p (t c)"), y_chunks[t - 1]).then_inc(sp_in[(t - 1) % 2], 16)
            plain("glu", glu, range(0, 6 * P, P), slice(4, 6))
            plain("ewo", A["even_w_out_2"][0], range(0, D, P))
            plain("odd", A["odd_w_in_2"][0], ODD_COLS)
            plain("owo", A["odd_w_out_2"][0], range(0, D, P))
            rows_out = out[0].rearrange("(t p) d -> p t d", p=P)
            for half in range(2):
                sp.wait_ge(out_sb, 4 * half + 4)
                sp.dma_start(rows_out[:, :, half * T:(half + 1) * T], XO[:, :, half * T:(half + 1) * T]).then_inc(out_done, 16)
            sp.wait_ge(out_done, 32)

        @block.tensor
        def _(pe):
            def panel(stage, j, i, hi, lo, nk=8, n=T, need=None):
                p = BASE[stage] + j
                pe.wait_ge(w_lo, p + 1 + 4 * i)
                if not (isinstance(i, int) and p + 4 * i < 4):
                    pe.wait_ge(taken[p % 4], p // 4 + i)
                for k in range(nk):
                    if need is not None:
                        pe.wait_ge(*need(k))
                    for a, (w, x) in enumerate(((wh, hi), (wl, hi), (wh, lo))):
                        mm = pe.matmul(ps[:, p % 4, 0:n], w[:, p % 2, k * P:(k + 1) * P], x[:, k, 0:n],
                                       start=(k == 0 and a == 0), stop=(k == nk - 1 and a == 2))
                mm.then_inc(pe_panel, 1)

            def pair(stage, hi, lo, need, nk=8, n=T):
                p, behind = BASE[stage], 3
                pe.wait_ge(w_lo, p + 2)
                for e in range(2):
                    if p + e >= 4:
                        pe.wait_ge(taken[(p + e) % 4], (p + e) // 4)
                for k in range(nk + behind):
                    for e, c in ((0, k), (1, k - behind)):
                        if not 0 <= c < nk:
                            continue
                        if e == 0:
                            pe.wait_ge(*need(c))
                        for a, (w, x) in enumerate(((wh, hi), (wl, hi), (wh, lo))):
                            mm = pe.matmul(ps[:, (p + e) % 4, 0:n], w[:, (p + e) % 2, c * P:(c + 1) * P], x[:, c, 0:n],
                                           start=(c == 0 and a == 0), stop=(c == nk - 1 and a == 2))
                        if c == nk - 1:
                            mm.then_inc(pe_panel, 1)

            def panels(stage, count, need, hi=XH, lo=XL, nk=8, after=None):
                pair(stage, hi, lo, need, nk)
                for j in range(2, count):
                    panel(stage, j, 0, hi, lo, nk)
                    if after is not None:
                        after(j)

            def split_at(stage):
                return lambda k: (x_split, XS[stage] + k + 1)

            def ffn(stage, fill):
                no = int(stage[3])
                off, f0 = 0, 22 * no
                at = 0
                for c, nf in enumerate(CHUNKS):
                    for a, b in zip(UP_PARTS[c], UP_PARTS[c][1:]):
                        if c == 0:
                            pair(stage, XH, XL, split_at(stage))
                            for j in (2, 3):
                                panel(stage, j, 0, XH, XL)
                            a = 1
                        with pe.Fori(a, b) as i:
                            for j in range(4):
                                panel(stage, off + j, i, XH, XL)
                        fill(at)
                        at += 1
                    off += 2 * nf
                    need = lambda k: (h_ready, f0 + k + 3)
                    with pe.Fori(0, KD // 4) as i:
                        for j in range(4):
                            panel(stage, off + j, i, HH, HL, nf, need=need if j == 0 else None)
                    if c < 2:
                        fill(at)
                        at += 1
                    off += KD
                    f0 += nf

            def norm(stage):
                no, q0 = LN_NO[stage], LN_SQ[stage]
                pe.wait_ge(ln_acc, 8 * no + 8)
                pe.matmul(ps[:, 4, :], ONES[:], ACC[:], start=True, stop=True).then_inc(ln_mu, 1)
                squares(q0, 8, 5)

            def square(q0, d, count, bank):
                pe.wait_ge(sq_ready, q0 + d + 1)
                pe.matmul(ps[:, bank, :], ONES[:], SQ[:, (q0 + d) % 2, :], start=d == 0, stop=d == count - 1).then_inc(sq_used, 1)

            def squares(q0, count, bank):
                for d in range(count):
                    square(q0, d, count, bank)

            def probs_t(u, s):
                pe.wait_ge(p_ready, u + 1)
                wait(pe, pt_act, 2 * u)
                wait(pe, pt_dve, u)
                for bank, col, q, kb in TBLOCKS:
                    mm = pe.transpose(ps[:, bank, col:col + P], PR[:, s, POFF[q] + kb * P:POFF[q] + (kb + 1) * P], IDENT[:])
                mm.then_inc(t_ps, 1)

            def pv(u, s, vals):
                pe.wait_ge(pt_act, 2 * u + 2)
                pe.wait_ge(pt_dve, u + 1)
                wait(pe, o_done, u)
                for q in range(TT):
                    for kb in range(q + 1):
                        mm = pe.matmul(ps[:, 7, q * HD:(q + 1) * HD], PT[:, s, PTOFF[q, kb]:PTOFF[q, kb] + P],
                                       vals(kb), start=kb == 0, stop=kb == q)
                mm.then_inc(pv_ps, 1)

            def scores(u, q, keys):
                wait(pe, s_sb, u)
                for t, bank, col in STILES:
                    n = (t + 1) * P
                    mm = pe.matmul(ps[:, bank, col:col + n], q(t), keys(n), start=True, stop=True)
                mm.then_inc(s_ps, 1)

            def mem_scores(u, h, first):
                r = slice((h % 2) * HD, (h % 2) * HD + HD)
                pe.wait_ge(p_ready, u) if not first else wait(pe, s_sb, u)
                for t in range(TT):
                    mm = pe.matmul(ps[:, 4 + t // 2, (t % 2) * M:(t % 2 + 1) * M], QM[r, h // 2, t * P:(t + 1) * P],
                                   KM[r, mem_layer[0], h // 2, :], start=True, stop=True)
                mm.then_inc(s_ps, 1)

            def mem_probs_t(u, s):
                pe.wait_ge(p_ready, u + 1)
                wait(pe, pt_act, 2 * u)
                wait(pe, pt_dve, u)
                for m in range(MT):
                    for t in range(TT):
                        mm = pe.transpose(ps[:, m, t * P:(t + 1) * P], PR[:, s, t * M + m * P:t * M + (m + 1) * P], IDENT[:])
                mm.then_inc(t_ps, 1)

            def mem_pv(u, s, h):
                pe.wait_ge(pt_act, 2 * u + 2)
                pe.wait_ge(pt_dve, u + 1)
                wait(pe, o_done, u)
                for t in range(TT):
                    for m in range(MT):
                        mm = pe.matmul(ps[:, 7, t * HD:(t + 1) * HD], PT[:, s, m * T + t * P:m * T + (t + 1) * P],
                                       VM[:, mem_layer[0], m, h * HD:(h + 1) * HD], start=m == 0, stop=m == MT - 1)
                mm.then_inc(pv_ps, 1)

            def mix_t(base, mix0):
                for k in range(KD):
                    pe.wait_ge(x_split, base + k - 3 if k > 3 else base)
                    for t in range(TT):
                        mm = pe.transpose(ps[:, 4 + k % 4, t * P:(t + 1) * P], O[:, t, k * P:(k + 1) * P], IDENT[:])
                    mm.then_inc(mix_ps, 1)

            def s5_fill(t):
                pe.wait_ge(bk_ready, t + 1)
                wait(pe, z_out, 4 * t)
                for b in range(4):
                    for g in range(4):
                        mm = pe.transpose(ps[:, 4 + b, g * P:(g + 1) * P], BK[:, b // 2, (b % 2) * 4 + g, :], IDENT[:])
                    mm.then_inc(s5_t, 1)
                for b in range(4):
                    if b < 2:
                        pe.wait_ge(bt_act, 2 * t + b + 1)
                    else:
                        pe.wait_ge(bt_dve, 2 * t + b - 1)
                    for e in range(2):
                        g = 2 * b + e
                        for r in range(2):
                            mm = pe.matmul(ps[0:S5H, 4 + b, e * 240:(e + 1) * 240], BB[:, r, t * GT + g, :],
                                           SW[:, r, g, S5H:(STRIP - 1) * S5H], start=r == 0, stop=r == 1)
                    mm.then_inc(s5_z, 1)

            def ada_fill(layer, f):
                if layer == 1 and f == 0:
                    pe.wait_ge(mod_ready, 1)
                for n in (2 * f, 2 * f + 1):
                    pe.wait_ge(ada_part, 12 * layer + n + 1)
                    for c in range(2):
                        for e in range(ada_conditions(layer, n)):
                            m = 2 * n + c
                            mm = pe.matmul(ps[:, 6, 2 * m + e:2 * m + e + 1], AS[:, n % 2, e, c * P:(c + 1) * P], ONES[:, 0:1], start=True, stop=True)
                    mm.then_inc(ada_used, 1)

            def ffn2_fill(f):
                ada_fill(1, f)
                if f == 0:
                    pe.wait_ge(gelu_out, 4)
                    pe.wait_ge(vt_out, 2)
                    for m in range(2):
                        pe.matmul(ps[0:HD, 4, 0:2 * NPAD], W2[:, 0, m, :], H1[:, 0, m].rearrange("p g n -> p (g n)"), start=m == 0, stop=m == 1)
                    for m in range(2):
                        mm = pe.matmul(ps[0:2 * NPAD, 5, 0:HD], H1[:, 1, m].rearrange("p g n -> p (g n)"), W2[:, 1, m, :], start=m == 0, stop=m == 1)
                    mm.then_inc(kc_ps, 1)

            def ffn3_fill(f):
                if f == 2:
                    pe.wait_ge(cx_n, 2)
                    for k2 in range(4):
                        for e in range(2):
                            for m in range(MT):
                                k = 2 * k2 + e
                                mm = pe.transpose(ps[:, 4 + k2, e * CTX + m * P:e * CTX + (m + 1) * P], CXN[:, m, k * P:(k + 1) * P], IDENT[:])
                        mm.then_inc(cx_ps, 1)

            mem_layer = [0]

            pe.wait_ge(ident_in, 16)
            pe.wait_ge(mem_in, 16)
            for k2 in range(4):
                for e in range(2):
                    for m in range(MT):
                        k = 2 * k2 + e
                        mm = pe.transpose(ps[:, 4 + k2, e * M + m * P:e * M + (m + 1) * P], MN[:, m, k * P:(k + 1) * P], IDENT[:])
                mm.then_inc(tr, 1)
            pe.wait_ge(x_in, 16)
            for k in range(KD):
                if k < 4:
                    pe.wait_ge(mem_split, k + 1)
                else:
                    pe.wait_ge(x_split, k - 3)
                for t in range(TT):
                    mm = pe.transpose(ps[:, 4 + k % 4, t * P:(t + 1) * P], XN[:, t, k * P:(k + 1) * P], IDENT[:])
                mm.then_inc(tr, 1)
            pe.wait_ge(col_in, 16 * COL_LOADS)
            pe.wait_ge(x_split, 5)
            pe.transpose(ps[:, 4, 0:96], CN1[:], IDENT[0:96, 0:96])
            pe.transpose(ps[:, 4, 96:96 + 117], CN2[:], IDENT[0:117, 0:117])
            pe.transpose(ps[:, 4, 256:256 + 64], PN[:].rearrange("a b c -> a (b c)"), IDENT[0:64, 0:64]).then_inc(tr, 1)

            for j in range(8):
                panel("mem", j, 0, MH, ML, n=M, need=(lambda k: (mem_split, k // 2 + 1)) if j == 0 else None)
            for layer in range(2):
                for j in range(2):
                    pe.wait_ge(*taken_at("mem", 4 * layer + 2 + j))
                    if layer == 0 and j == 0:
                        pe.wait_ge(tr_done, 1)
                        pe.wait_ge(x_split, 8)
                    for m in range(MT):
                        mm = pe.transpose(ps[:, 4 + 2 * layer + j, m * P:(m + 1) * P], MV[:, 2 * layer + j, m * P:(m + 1) * P], IDENT[:])
                    mm.then_inc(vm_ps, 1)

            pe.wait_ge(setup, 2)
            pe.wait_ge(s5_in, 16 * S5_LOADS)
            pe.wait_ge(vm_ready, 4)
            for r in range(2):
                pe.transpose(ps[:, 4, r * S5G:(r + 1) * S5G], LAMN[:, r, :], IDENT[0:S5G, 0:S5G])
            pe.matmul(ps[:, 4, 2 * S5G:3 * S5G], DSEL, LSN, start=True, stop=True)
            pe.transpose(ps[0:S5H, 4, 3 * S5G:4 * S5G], DN, IDENT[0:S5G, 0:S5G]).then_inc(s5_tr, 1)
            for n in range(12):
                mm = pe.transpose(ps[:, 5 + n // 4, (n % 4) * P:(n % 4 + 1) * P], CN[:, n // 6, n % 6].rearrange("p d q -> p (d q)"), IDENT[:])
                if n % 4 == 3:
                    mm.then_inc(s5_tr, 1)
            ffn("ffn0", s5_fill)
            pe.wait_ge(z_out, 4 * S5T)
            norm("ffn0")
            def mla_squares(j):
                if j == 2:
                    squares(LN_SQ["mla"], 2, 4)

            panels("mla", 6, split_at("mla"), after=mla_squares)
            squares(LN_SQ["mla"] + 2, 1, 5)
            pe.wait_ge(mla_in_s, 80)
            pe.wait_ge(*taken_at("mla", 3))
            pe.wait_ge(vm_ready, 4)
            pe.matmul(ps[ROPE:2 * ROPE, 6, :], PERM[:], KR, start=True, stop=True).then_inc(kr_ps, 1)
            pe.wait_ge(cq_norm, 3)
            pe.wait_ge(kr_rot, 1)
            for g in range(14):
                if g < 6:
                    lhs, rhs, n = WUKV[:, 0, 2 * g:2 * g + 2, :].rearrange("p h c -> p (h c)"), CKV[:], T
                else:
                    t, half = (g - 6) // 2, g % 2
                    lhs, rhs, n = CKV[:, t * P:(t + 1) * P], WUKV[:, 1, 6 * half:6 * half + 6, :], 6 * HD
                if g >= 4:
                    pe.wait_ge(kv_act, kv_count(g - 4)[0])
                    pe.wait_ge(kv_dve, kv_count(g - 4)[1])
                pe.matmul(ps[:, 4 + g % 4, 0:n], lhs, rhs, start=True, stop=True).then_inc(kv_ps, 1)

            def project_q(h, s, turn):
                pe.wait_ge(sp_in[s], 48 * turn + 48)
                wait(pe, q_nope, h)
                wait(pe, q_rot, 2 * h)
                for k in range(2):
                    mm = pe.matmul(ps[:, 3, :], WQ[:, s, k, :], CQ[:, k, :], start=k == 0, stop=k == 1)
                mm.then_inc(q_ps, 1)

            def mla_scores(h, s):
                pe.wait_ge(q_nope, h + 1)
                pe.wait_ge(q_rope, h + 1)
                scores(h, lambda t: QT[:, s, t * P:(t + 1) * P],
                       lambda n: KT[:, bass.ds(h, 1), 0:n].rearrange("p o n -> p (o n)"))

            def mla_pv(h, s):
                pv(h, s, lambda kb: V[:, kb, bass.ds(h * HD, HD)])

            pe.wait_ge(kv_act, kv_count(13)[0])
            pe.wait_ge(kv_dve, kv_count(13)[1])
            pe.wait_ge(kr_act, 1)
            pe.wait_ge(kr_dve, 1)
            pe.wait_ge(*taken_at("mla", 5))
            pe.wait_ge(*taken_at("mla", 2))
            project_q(0, 0, 0)
            project_q(1, 1, 0)
            mla_scores(0, 0)
            project_q(2, 0, 1)
            mla_scores(1, 1)

            def mla_unit(u, s, turn=None, begin=False):
                probs_t(u, s)
                if turn is not None:
                    project_q(u + 3, 1 - s, turn)
                if not begin:
                    mla_pv(u - 1, 1 - s)
                mla_scores(u + 2, s)

            mla_unit(0, 0, 1, begin=True)
            mla_unit(1, 1, 2)
            with pe.Fori(1, HEADS // 2 - 2) as i:
                mla_unit(2 * i, 0, i + 1)
                mla_unit(2 * i + 1, 1, i + 2)
            mla_unit(8, 0, 5)
            mla_unit(9, 1)
            for h in range(2):
                u = 10 + h
                probs_t(u, h)
                mla_pv(u - 1, 1 - h)
                mem_scores(u + 2, h, h == 0)
            for h in range(MEM_HEADS):
                u = 12 + h
                mem_probs_t(u, u % 2)
                if h == 0:
                    mla_pv(11, 1)
                else:
                    mem_pv(u - 1, 1 - u % 2, h - 1)
                if h < 2:
                    mem_scores(u + 2, h + 2, False)
            mem_pv(15, 1, 3)
            pe.wait_ge(o_done, 16)
            mix_t(XS["wo0"], 0)
            panels("wo0", 8, split_at("wo0"))
            norm("wo0")
            ffn("ffn1", lambda f: ada_fill(0, f))
            norm("ffn1")

            panels("kv", 6, split_at("kv"))
            for e in range(2):
                pe.wait_ge(*taken_at("kv", 3 + 2 * e))
                for t in range(TT):
                    mm = pe.transpose(ps[:, 4 + e, t * P:(t + 1) * P], VT[:, e, t * P:(t + 1) * P], IDENT[:])
                mm.then_inc(vt_ps, 1)
            pe.wait_ge(w1_in, 96)
            pe.wait_ge(mod_ready, 1)
            for j in range(2):
                pe.wait_ge(zb_ready, j + 1)
                for m in range(2):
                    for l in range(CMP_LEN // 2):
                        mm = pe.matmul(ps[:, 6 + j, m * 2 * NCMP:(m + 1) * 2 * NCMP], W1[j][:, l, m * P:(m + 1) * P], ZB[:, j, l, :, 0:NCMP],
                                       start=l == 0, stop=l == CMP_LEN // 2 - 1)
                    mm.then_inc(hid_ps, 1)

            ffn("ffn2", ffn2_fill)
            pe.wait_ge(kc_out, 2)
            norm("ffn2")
            def gates_t(j):
                if j == 2:
                    pe.wait_ge(*taken_at("nsa", 0))
                    for t in range(TT):
                        mm = pe.transpose(ps[:, 4, t * 36:(t + 1) * 36], GTT[:, t * P:(t + 1) * P], IDENT[0:36, 0:36])
                    mm.then_inc(g_ps, 1)

            panels("nsa", 9, split_at("nsa"), after=gates_t)

            def nsa_scores(u, k, q):
                r = slice((k % 2) * HD, (k % 2) * HD + HD)
                keys = (KS, KW)[k // 2]
                scores(u, lambda t: QS[r, q, t * P:(t + 1) * P], lambda n: keys[r, 0:n])

            def nsa_pv(u, k):
                vals = (VS, VW)[k // 2]
                pv(u, k % 2, lambda kb: vals[:, kb, (k % 2) * HD:(k % 2 + 1) * HD])

            def cmp_scores(j, q):
                wait(pe, c_o, j)
                for t in range(TT):
                    mm = pe.matmul(ps[:, 3, t * 2 * NPAD:(t + 1) * 2 * NPAD], QS[:, q, t * P:(t + 1) * P], KCB[:], start=True, stop=True)
                mm.then_inc(c_ps, 1)

            def cmp_t(j):
                pe.wait_ge(c_p, j + 1)
                for t in range(TT):
                    mm = pe.transpose(ps[0:2 * NPAD, 3, t * P:(t + 1) * P], SC[:, t].rearrange("p g n -> p (g n)"), IDENT[:])
                mm.then_inc(c_t, 1)

            def cmp_pv(j):
                pe.wait_ge(c_pt, j + 1)
                for t in range(TT):
                    mm = pe.matmul(ps[:, 3, t * P:(t + 1) * P], PTC[:, t * P:(t + 1) * P], VCB[:], start=True, stop=True)
                mm.then_inc(c_pv, 1)

            for j in range(5, 9):
                pe.wait_ge(*taken_at("nsa", j))
            pe.wait_ge(g_out, 1)
            pe.wait_ge(qs_ready, 1)
            nsa_scores(16, 0, 0)
            nsa_scores(17, 1, 0)

            def nsa_pair(j, q, last=False):
                for k in range(4):
                    u = 16 + 4 * j + k
                    begin = isinstance(j, int) and j == 0 and k == 0
                    probs_t(u, k % 2)
                    if not begin:
                        nsa_pv(u - 1, (k - 1) % 4)
                    if k == 0 and not begin:
                        cmp_pv(j - 1)
                    if k == 1:
                        cmp_scores(j, q)
                    if k < 2:
                        nsa_scores(u + 2, k + 2, q)
                    elif not last:
                        if k == 2:
                            pe.wait_ge(qs_ready, j + 2)
                        nsa_scores(u + 2, k - 2, 1 - q)
                    else:
                        mem_scores(u + 2, k - 2, k == 2)
                    if k == 3:
                        cmp_t(j)

            nsa_pair(0, 0)
            nsa_pair(1, 1)
            with pe.Fori(1, HPG // 2 - 1) as i:
                for q in range(2):
                    nsa_pair(2 * i + q, q)
            mem_layer[0] = 1
            nsa_pair(4, 0)
            nsa_pair(5, 1, last=True)
            for h in range(MEM_HEADS):
                u = 40 + h
                mem_probs_t(u, u % 2)
                if h == 0:
                    nsa_pv(39, 3)
                    cmp_pv(HPG - 1)
                else:
                    mem_pv(u - 1, 1 - u % 2, h - 1)
                if h < 2:
                    mem_scores(u + 2, h + 2, False)
            mem_pv(43, 1, 3)
            pe.wait_ge(o_done, 44)
            pe.wait_ge(c_o, HPG)
            mix_t(XS["wo1"], 8)
            panels("wo1", 8, split_at("wo1"))
            norm("wo1")
            ffn("ffn3", ffn3_fill)
            pe.wait_ge(cx_f, 8)
            norm("ffn3")

            squares(LN_SQ["even"], 8, 5)
            for j in range(6):
                p = BASE["even"] + j
                pe.wait_ge(w_lo, p + 1)
                wait(pe, uc_out, j - 1)
                pe.wait_ge(*taken_at("even", j - 4))
                for k in range(KD):
                    if j == 0:
                        pe.wait_ge(x_split, XS["even"] + k + 1)
                        pe.wait_ge(cx_split, k + 1)
                    for a, (w, x, c) in enumerate(((wh, XH, CH), (wl, XH, CH), (wh, XL, CL))):
                        lhs = w[:, p % 2, k * P:(k + 1) * P]
                        first, last = k == 0 and a == 0, k == KD - 1 and a == 2
                        pe.matmul(ps[:, 4 + j % 2, 0:CTX], lhs, c[:, k, :], start=first, stop=last)
                        mm = pe.matmul(ps[:, p % 4, :], lhs, x[:, k, :], start=first, stop=last)
                mm.then_inc(pe_panel, 1)
            for j in range(6, 10):
                panel("even", j, 0, XH, XL)
            pe.wait_ge(shuffle_in, 16 * L)
            for t in range(S5T):
                pe.wait_ge(pool_in[t % 3], (IN["b"] if t % 3 < 2 else 0) + 16 * (t // 3 + 1))
                for b in range(4):
                    if t == 0 and b < 2:
                        pe.wait_ge(uc_out, 6)
                    wait(pe, h_act, 4 * (t - 1) + b + 1)
                    wait(pe, h_dve, 4 * (t - 1) + b + 1)
                    for g in range(4):
                        e = (b % 2) * 4 + g
                        mm = pe.matmul(ps[:, 4 + b, g * NC:(g + 1) * NC], BS[:, t % 3, b // 2, e, :], U[:, t * GT + e, :], start=True, stop=True)
                    mm.then_inc(b_ps, 1)
            for j in range(10, 16):
                panel("even", j, 0, XH, XL)
            for j in range(2):
                pe.wait_ge(*taken_at("even", 6 + j))
            pe.wait_ge(dft_in, 16 * 6)
            for t in range(TT):
                pe.wait_ge(h_act, 4 * (S5T - 1) + t + 1)
                pe.wait_ge(h_dve, 4 * (S5T - 1) + t + 1)
                for j in range(2):
                    mm = pe.matmul(ps[:, 4 + t, j * 2 * P:(j + 1) * 2 * P], UB[:, j, t * P:(t + 1) * P], DFTC[:], start=True, stop=True)
                mm.then_inc(fnet_ps, 1)
            for j in range(2):
                pe.wait_ge(fnet_out, 4)
                for t in range(TT):
                    for e in range(2):
                        mm = pe.matmul(ps[:, 4 + j, :], FA[:, t, j, e * P:(e + 1) * P], DFTT[:, e, t, :],
                                       start=t == 0 and e == 0, stop=t == TT - 1 and e == 1)
                mm.then_inc(fnet_ps, 1)
            for j in range(2):
                pe.wait_ge(fnet_out, 5 + j)
                pe.matmul(ps[:, 6 + j, :], FW[:, j, :], FB[:, j, :], start=True, stop=True).then_inc(fnet_ps, 1)
            for j in range(12, 16):
                pe.wait_ge(*taken_at("even", j))
            for t in range(S5T):
                pe.wait_ge(pool_in[t % 2], IN["m"] + 16 * (t // 2 + 1))
                if t >= 4:
                    pe.wait_ge(fnet_out, t + 1)
                for g in range(GT):
                    mm = pe.matmul(ps[:, t, g * NCL:(g + 1) * NCL], MM[:, t % 2, g, :], U[:, t * GT + g, NCC:], start=g == 0, stop=False)
                mm.then_inc(m_ps, 1)
            for t in range(S5T):
                pe.wait_ge(w_in, 16 * (5 if t < 5 else 6))
                pe.wait_ge(ss_act, t + 1)
                pe.wait_ge(ss_dve, t + 1)
                for g in range(GT):
                    for r in range(2):
                        mm = pe.matmul(ps[:, t, g * NCL:(g + 1) * NCL], WT[t][:, r, g, :], SS[:, t % 2, r, g, :], start=False, stop=g == GT - 1 and r == 1)
                mm.then_inc(y_ps, 1)
            panels("glu", 6, split_at("glu"), nk=6)

            def squares_behind(stage):
                return lambda j: square(LN_SQ[stage], j - 2, 8, 5)

            panels("ewo", 8, lambda k: (y_ready, k + 3 if k < 6 else k - 5), YH, YL, after=squares_behind("odd"))
            for d in (6, 7):
                square(LN_SQ["odd"], d, 8, 5)

            def pooled(j):
                if j in (7, 10, 13, 15):
                    i = (7, 10, 13, 15).index(j)
                    if i == 0:
                        pe.wait_ge(odd_in, 32)
                    pe.wait_ge(pool_ready, i + 1)
                    pe.matmul(ps[:, 4 + (i + 2) % 4, :], PWT[:, i, :], PP[:, i % 2, :], start=True, stop=True).then_inc(pw_ps, 1)

            panels("odd", 24, split_at("odd"), after=pooled)
            pe.wait_ge(yc_ready, 4)
            panels("owo", 8, lambda k: (y_ready, 8 + k + 1), YH, YL, after=squares_behind("final"))

            for d in (6, 7):
                square(LN_SQ["final"], d, 8, 5)
            for d in range(KD):
                pe.wait_ge(ln_aff, 8 * 8 + d + 1)
                b = (6, 7, 4, 5)[d % 4]
                wait(pe, out_sb, d - 3)
                for t in range(TT):
                    mm = pe.transpose(ps[:, b, t * P:(t + 1) * P], XT[:, d, t * P:(t + 1) * P], IDENT[:])
                mm.then_inc(out_ps, 1)

        @block.scalar
        def _(act):
            def cast(p, i=0):
                if isinstance(i, int) and p >= PANELS:
                    return
                act.wait_ge(raw_in[p % 4], 16 * (p // 4 + 1) + 16 * i)
                if not (isinstance(i, int) and p < 2):
                    act.wait_ge(pe_panel, p - 1 + 4 * i)
                act.activation(wh[:, p % 2, :], raw[:, p % 4, :], ACT.Copy).then_inc(w_hi, 1)

            def take(stage, j, dst, func=ACT.Copy, n=T, rows=slice(0, P), **kw):
                p = BASE[stage] + j
                cast(p + 2)
                act.wait_ge(pe_panel, p + 1)
                act.activation(dst, ps[rows, p % 4, 0:n], func, **kw).then_inc(taken[p % 4], 1)

            def ffn(stage, fill):
                off, f0 = 0, 22 * int(stage[3])
                at = 0
                for c, nf in enumerate(CHUNKS):
                    for a, b in zip(UP_PARTS[c], UP_PARTS[c][1:]):
                        with act.Fori(a, b) as i:
                            for f in range(2):
                                p = BASE[stage] + off + 2 * f
                                cast(p + 2, i)
                                act.wait_ge(pe_panel, p + 1 + 4 * i)
                                act.wait_ge(h_ready, f0 + f + 1 + 2 * i)
                                act.activation(SG[:, f, :], ps[:, p % 4, :], ACT.Silu).then_inc(taken[p % 4], 1)
                                cast(p + 3, i)
                        fill(at)
                        at += 1
                    off += 2 * nf
                    f0 += nf
                    with act.Fori(0, KD // 4) as i:
                        for j in range(4):
                            cast(BASE[stage] + off + j + 2, i)
                    if c < 2:
                        fill(at)
                        at += 1
                    off += KD

            def square(q, src):
                if q >= 2:
                    act.wait_ge(sq_used, q - 1)
                act.activation(SQ[:, q % 2, 0:src.shape[-1]], src, ACT.Square).then_inc(sq_ready, 1)

            def norm(stage, eps, split=True):
                no, q0, c0 = LN_NO[stage], LN_SQ[stage], LN_COL[stage]
                for d in range(KD):
                    act.wait_ge(ln_c, 8 * no + d + 1)
                    square(q0 + d, XT[:, d, :])
                act.wait_ge(sq_used, q0 + 8)
                if no == 0:
                    act.wait_ge(tr_done, 1)
                act.activation(SD[:, 0, :], ps[:, 5, :], ACT.Sqrt, bias=EPS[:, eps:eps + 1]).then_inc(sd_ready, 1)
                for d in range(KD if split else 0):
                    act.wait_ge(ln_n, 8 * no + d + 1)
                    act.activation(XH[:, d, :], XT[:, d, :], ACT.Identity, scale=COL[:, c0 + d:c0 + d + 1],
                                   bias=COL[:, 48 + c0 + d:49 + c0 + d]).then_inc(ln_hi, 1)

            def rms(stage, ready, layer=None, wout=None):
                no, q0 = LN_NO[stage], LN_SQ[stage]
                for d in range(KD):
                    if wout is not None:
                        for j in (0, 1) if d == 0 else (d + 1,):
                            if j < 8:
                                cast(BASE[wout] + j + 2)
                    act.wait_ge(*ready(d))
                    square(q0 + d, XT[:, d, :])
                act.wait_ge(sq_used, q0 + 8)
                act.activation(SD[:, 0, :], ps[:, 5, :], ACT.Sqrt, bias=EPS[:, 2:3]).then_inc(sd_ready, 1)
                for d in range(KD if layer is not None else 0):
                    act.wait_ge(ln_n, 8 * no + d + 1)
                    src = (NT, NO)[layer]
                    act.activation(XH[:, d, :], src[:, d, :], ACT.Identity, scale=AG[:, layer, d, 0:1],
                                   bias=MOD[:, layer, d, 0:1]).then_inc(ln_hi, 1)

            def s5_fill(t):
                wait(act, s5_out, 64 * t)
                for b in range(2):
                    act.wait_ge(s5_t, 4 * t + b + 1)
                    act.activation(BT[:, 0, 4 * b:4 * b + 4, :], ps[:, 4 + b, :], ACT.Copy).then_inc(bt_act, 1)
                for b in range(4):
                    act.wait_ge(s5_z, 4 * t + b + 1)
                    act.activation(Z[:, 2 * b:2 * b + 2, :], ps[0:S5H, 4 + b, 0:480], ACT.Copy).then_inc(z_out, 1)

            def ffn2_fill(f):
                if f == 0:
                    act.wait_ge(zeros, 2)
                    act.wait_ge(kc_ps, 1)
                    for g in range(GROUPS):
                        n, d = slice(g * NPAD, (g + 1) * NPAD), slice(g * HD, (g + 1) * HD)
                        act.activation(KCB[d, n], ps[0:HD, 4, n], ACT.Copy)
                        act.activation(VCB[n, d], ps[n, 5, 0:HD], ACT.Copy).then_inc(kc_out, 1)

            def ffn3_fill(f):
                if f == 0:
                    act.wait_ge(cx_in, 32)
                    for m in range(MT):
                        act.activation(CXT[:, 4 * m:4 * m + 4, :].rearrange("p k c -> p (k c)"), CXN[:, m, :], ACT.Square, accum_out=CSS[:, m:m + 1]
                                       ).then_inc(cx_sd, 1)
                    act.wait_ge(cx_sd, 2)
                    act.activation(CSS[:, 2:4], CSS[:, 0:2], ACT.Sqrt, scale=1.0 / D, bias=EPS[:, 2:3]).then_inc(cx_sd, 1)
                if f == 2:
                    for k in range(KD):
                        act.wait_ge(cx_f, k + 1)
                        act.activation(CH[:, k, :], CXT[:, k, :], ACT.Copy).then_inc(cx_hi, 1)

            def softmax_exp(u, s):
                act.wait_ge(nb_ready, u + 1)
                for t in range(TT):
                    ins = act.activation(PR[:, s, POFF[t]:POFF[t] + (t + 1) * P], PR[:, s, POFF[t]:POFF[t] + (t + 1) * P], ACT.Exp,
                                         bias=NB[:, s, t:t + 1], scale=scale[0], accum_out=SM[:, s, t:t + 1])
                ins.then_inc(p_ready, 1)

            def probs_out(u, s):
                act.wait_ge(t_ps, u + 1)
                wait(act, pv_ps, u - 1)
                act.activation(PT[:, s, 0:T], ps[:, 0, :], ACT.Copy).then_inc(pt_act, 1)
                act.activation(PT[:, s, 2 * T:2 * T + 2 * P], ps[:, 2, 0:2 * P], ACT.Copy).then_inc(pt_act, 1)

            def mem_exp(u, s):
                act.wait_ge(nb_ready, u + 1)
                act.wait_ge(t_ps, u - 1)
                for t in range(TT):
                    ins = act.activation(PR[:, s, t * M:(t + 1) * M], ps[:, 4 + t // 2, (t % 2) * M:(t % 2 + 1) * M], ACT.Exp,
                                         bias=NB[:, s, t:t + 1], scale=HD ** -0.5, accum_out=SM[:, s, t:t + 1])
                ins.then_inc(p_ready, 1)

            def mem_probs_out(u, s):
                act.wait_ge(t_ps, u + 1)
                wait(act, pv_ps, u - 1)
                act.activation(PT[:, s, 0:T // 2], ps[:, 0, 0:T // 2], ACT.Copy).then_inc(pt_act, 1)
                act.activation(PT[:, s, T // 2:T], ps[:, 0, T // 2:T], ACT.Copy).then_inc(pt_act, 1)

            def mix_hi_of(mix0):
                for k in range(KD):
                    act.wait_ge(mix_ps, mix0 + k + 1)
                    act.activation(XH[:, k, :], ps[:, 4 + k % 4, :], ACT.Copy).then_inc(mix_hi, 1)

            scale = [MLA_SCALE]
            at = 0
            act.dma_start(CN1[0:48, :], A["ln_g"].rearrange("l i (k p) -> (l i k) p", p=P)).then_inc(col_in, 16)
            act.dma_start(CN1[48:96, :], A["ln_b"].rearrange("l i (k p) -> (l i k) p", p=P)).then_inc(col_in, 16)
            for name, view in VECTORS:
                v = A[name].rearrange(view, p=P)
                act.dma_start(CN2[at:at + v.shape[0], :], v).then_inc(col_in, 16)
                at += v.shape[0]
            for b in range(2):
                act.dma_start(PN[:, b, :], A["cmp_pos"].rearrange("j l d -> (j l) d")).then_inc(col_in, 16)
            cast(0)
            cast(1)
            for k2 in range(4):
                act.wait_ge(tr, k2 + 1)
                act.activation(MH[:, 2 * k2:2 * k2 + 2, :], ps[:, 4 + k2, :].rearrange("p (e m) -> p e m", e=2), ACT.Copy).then_inc(mem_hi, 1)
            for k in range(KD):
                act.wait_ge(tr, 5 + k)
                act.activation(XH[:, k, :], ps[:, 4 + k % 4, :], ACT.Copy).then_inc(x_hi, 1)
            for layer in range(2):
                for j in range(4):
                    dst = KM[:, layer, j, :] if j < 2 else MV[:, 2 * layer + j - 2, :]
                    take("mem", 4 * layer + j, dst, n=M)

            act.wait_ge(tr_done, 1)
            act.activation(CS[:].rearrange("p k e -> p e k"), COL[:, 96 + 101:96 + 117].rearrange("p (e k) -> p e k", e=2), ACT.Silu).then_inc(cs_ready, 1)
            for b, parts in enumerate((((0, 4, 1.0),), ((4, 2, 1.0), (6, 2, -1.0)), ((8, 4, -1.0),))):
                act.wait_ge(s5_tr, 2 + b)
                col = 0
                for r0, n, sign in parts:
                    ins = act.activation(CR[:].rearrange("p r g h -> p (r g h)")[:, r0 * P:(r0 + n) * P], ps[:, 5 + b, col:col + n * P], ACT.Copy, scale=sign)
                    col += n * P
                ins.then_inc(cr_out, 1)
            act.wait_ge(sin_in, 1)
            act.activation(TS5[:, 0, :], TS5[:, 2, :], ACT.Sin)
            act.activation(TS5[:, 1, :], TS5[:, 2, :], ACT.Sin, scale=0.5).then_inc(sin_out, 1)
            ffn("ffn0", s5_fill)
            norm("ffn0", 0)
            act.wait_ge(s5_out, 64 * S5T)
            for j, dst in enumerate((CQ[:, 0, :], CQ[:, 1, :], CKV[:], KR, QM[:, 0, :], QM[:, 1, :])):
                p = BASE["mla"] + j
                if j < 3:
                    act.wait_ge(pe_panel, p + 1)
                    square(LN_SQ["mla"] + j, ps[:, p % 4, :])
                take("mla", j, dst, rows=slice(0, ROPE if j == 3 else P))
            act.wait_ge(sq_used, LN_SQ["mla"] + 3)
            act.activation(SD[:, 0, :], ps[:, 4, :], ACT.Sqrt, scale=float(D // QR), bias=EPS[:, 2:3]).then_inc(sd_ready, 1)
            act.activation(SD[:, 1, :], ps[:, 5, :], ACT.Sqrt, scale=float(D // P), bias=EPS[:, 2:3]).then_inc(sd_ready, 1)
            act.wait_ge(kr_rot, 2)
            act.activation(KT[HD:QK, 0:6, :], KR2[:, 0:1, :].broadcast_to([ROPE, 6, T]), ACT.Copy).then_inc(kr_act, 1)
            for g in range(14):
                if g < 6:
                    act.wait_ge(kv_ps, g + 1)
                    act.activation(KT[0:HD, 2 * g, :], ps[0:HD, 4 + g % 4, :], ACT.Copy).then_inc(kv_act, 1)
                elif g % 2 == 0:
                    act.wait_ge(kv_ps, g + 1)
                    act.activation(V[:, (g - 6) // 2, 0:6 * HD], ps[:, 4 + g % 4, 0:6 * HD], ACT.Copy).then_inc(kv_act, 1)

            def take_q(h, s):
                act.wait_ge(q_ps, h + 1)
                if not (isinstance(h, int) and h < 2):
                    act.wait_ge(s_ps, h - 1)
                act.activation(QT[0:HD, s, :], ps[0:HD, 3, :], ACT.Copy).then_inc(q_nope, 1)

            for h in range(3):
                take_q(h, h % 2)
            for h in range(2):
                softmax_exp(h, h)

            def mla_unit(u, s, project=True):
                probs_out(u, s)
                if project:
                    take_q(u + 3, 1 - s)
                softmax_exp(u + 2, s)

            mla_unit(0, 0)
            mla_unit(1, 1)
            with act.Fori(1, HEADS // 2 - 2) as i:
                for s in range(2):
                    mla_unit(2 * i + s, s)
            mla_unit(8, 0)
            mla_unit(9, 1, project=False)
            for h in range(2):
                probs_out(10 + h, h)
                mem_exp(12 + h, h)
            for h in range(MEM_HEADS):
                u = 12 + h
                mem_probs_out(u, u % 2)
                if h < 2:
                    mem_exp(u + 2, u % 2)
            mix_hi_of(0)
            for j in range(8):
                cast(BASE["wo0"] + j + 2)
            norm("wo0", 1)
            ffn("ffn1", nothing)
            norm("ffn1", 0)

            for j, dst in enumerate((ZC[:, 0, :], ZC[:, 1, :], KS[:], VT[:, 0, :], KW[:], VT[:, 1, :])):
                take("kv", j, dst)
            act.wait_ge(zeros, 2)
            for n in range(4):
                act.wait_ge(hid_ps, n // 2 * 2 + 2)
                act.activation(H1[:, n // 2, n % 2, :, 0:NCMP], ps[:, 6 + n // 2, (n % 2) * 2 * NCMP:(n % 2 + 1) * 2 * NCMP].rearrange("p (g n) -> p g n", g=GROUPS),
                               ACT.Gelu_apprx_tanh, bias=COL[:, 96 + 94 + n:96 + 95 + n]).then_inc(gelu_out, 1)
            ffn("ffn2", ffn2_fill)
            norm("ffn2", 0)

            take("nsa", 0, GTT[:], ACT.Sigmoid, rows=slice(0, 36))
            for j in range(2):
                take("nsa", 1 + j, QM[:, j, :])
            for m in range(HPG):
                p = BASE["nsa"] + 3 + m
                cast(p + 2)
                act.wait_ge(pe_panel, p + 1)
                for e in range(2):
                    g, j = divmod(2 * m + e, HPG)
                    ins = act.activation(QP[g * HD:(g + 1) * HD, j, :], ps[e * HD:(e + 1) * HD, p % 4, :], ACT.Copy)
                ins.then_inc(taken[p % 4], 1)
            scale[0] = SEL_SCALE
            softmax_exp(16, 0)
            softmax_exp(17, 1)

            def nsa_pair(j, q, last=False):
                for k in range(4):
                    u = 16 + 4 * j + k
                    probs_out(u, k % 2)
                    if k == 2:
                        act.wait_ge(c_sub, j + 1)
                        act.activation(SC[:], SC[:], ACT.Exp, scale=SEL_SCALE).then_inc(c_exp, 1)
                    if last and k >= 2:
                        mem_exp(u + 2, k % 2)
                    else:
                        softmax_exp(u + 2, k % 2)
                    if k == 3:
                        act.wait_ge(c_t, j + 1)
                        wait(act, c_pv, j)
                        act.activation(PTC[:], ps[0:2 * NPAD, 3, :], ACT.Copy).then_inc(c_pt, 1)

            nsa_pair(0, 0)
            nsa_pair(1, 1)
            with act.Fori(1, HPG // 2 - 1) as i:
                for q in range(2):
                    nsa_pair(2 * i + q, q)
            nsa_pair(4, 0)
            nsa_pair(5, 1, last=True)
            for h in range(MEM_HEADS):
                u = 40 + h
                mem_probs_out(u, u % 2)
                if h < 2:
                    mem_exp(u + 2, u % 2)
            mix_hi_of(8)
            for j in range(8):
                cast(BASE["wo1"] + j + 2)
            norm("wo1", 1)
            ffn("ffn3", ffn3_fill)
            norm("ffn3", 0, split=False)

            rms("even", lambda d: (ln_aff, 8 * LN_NO["ffn3"] + d + 1), 0)
            for j in range(6):
                take("even", j, UT[:, j, :, NCC:].rearrange("p t c -> p c t"))
            for j in range(2):
                take("even", 6 + j, UB[:, j, :])

            def take_z(j):
                take("even", 8 + j, ZS[:, j, :], ACT.Silu)
            take_z(0)
            take_z(1)
            for t in range(S5T):
                for b in range(4):
                    act.wait_ge(b_ps, 4 * t + b + 1)
                    g = t * GT + (b % 2) * 4
                    act.activation(H[0:S5P, b // 2, g:g + 4, :], ps[0:S5P, 4 + b, 0:4 * NC].rearrange("p (g c) -> p g c", g=4), ACT.Copy).then_inc(h_act, 1)
            for j in range(2, 8):
                take_z(j)
            for t in range(TT):
                act.wait_ge(fnet_ps, t + 1)
                act.activation(FA[:, t].rearrange("p j c -> p (j c)"), ps[:, 4 + t, :], ACT.Copy).then_inc(fnet_out, 1)
            for j in range(2):
                act.wait_ge(fnet_ps, 5 + j)
                act.activation(FB[:, j, :], ps[:, 4 + j, :], ACT.Copy).then_inc(fnet_out, 1)
            for j in range(2):
                act.wait_ge(fnet_ps, 7 + j)
                act.activation(YB[:, j, :], ps[:, 6 + j, :], ACT.Copy).then_inc(fnet_out, 1)

            def states(t):
                if t == 0:
                    act.wait_ge(scan, 3 * (NC - 1))
                wait(act, y_ps, t - 1)
                act.activation(SS[0:S5P, t % 2], H[0:S5P, :, t * GT:(t + 1) * GT, NCC - 1:NC - 1], ACT.Copy).then_inc(ss_act, 1)

            states(0)
            states(1)
            for t in range(S5T):
                act.wait_ge(y_ps, t + 1)
                act.activation(YS[:, t * GT:(t + 1) * GT, :], ps[:, t, :], ACT.Copy).then_inc(y_sb, 1)
                if t + 2 < S5T:
                    states(t + 2)
            for j in range(6):
                act.wait_ge(sp_in[j % 2], IN["y"] + 16 * (j // 2 + 1))
                act.activation(YA[:, j, :].rearrange("p (c t) -> p t c", t=L), YT[:, j % 2], ACT.Gelu_apprx_tanh).then_inc(ya_ready, 1)
            for j in range(6):
                act.wait_ge(ya_ready, j + 1)
                act.activation(XH[:, j, :], YA[:, j, :], ACT.Copy).then_inc(ya_hi, 1)
            for j in range(6):
                act.wait_ge(y_full, j + 1)
                take("glu", j, SIG[:, j % 2, :], ACT.Sigmoid, bias=COL[:, 96 + 72 + j:96 + 73 + j])
            rms("odd", lambda d: taken_at("ewo", d), 1, "ewo")

            act.wait_ge(odd_zero, 1)
            for j in range(4):
                take("odd", j, PU[:, j, PAD:PAD + T])

            def take_pooled(i):
                act.wait_ge(pw_ps, i + 1)
                act.activation(YO[:, i, :], ps[:, 4 + (i + 2) % 4, :], ACT.Identity, scale=COL[:, 96 + 78 + i:96 + 79 + i]).then_inc(yc_ready, 1)

            for k in range(4):
                if k >= 2:
                    act.wait_ge(*taken_at("odd", 5 + 3 * (k - 2)))
                take("odd", 4 + 3 * k, CG[:, k % 2, :])
                cast(BASE["odd"] + 4 + 3 * k + 3)
                cast(BASE["odd"] + 4 + 3 * k + 4)
                if k >= 1:
                    take_pooled(k - 1)
            take_pooled(3)
            for j in range(8):
                wait(act, y_ready, 8 + j - 1)
                take("odd", 16 + j, ZO[:, j % 2, :], ACT.Silu)
            rms("final", lambda d: taken_at("owo", d), wout="owo")
            for d in range(KD):
                act.wait_ge(out_ps, d + 1)
                act.activation(XO[:, :, d * P:(d + 1) * P], ps[:, (6, 7, 4, 5)[d % 4], :].rearrange("p (t c) -> p t c", t=TT), ACT.Copy).then_inc(out_sb, 1)

        @block.vector
        def _(dve):
            def rest(p, i=0):
                if isinstance(i, int) and p >= PANELS:
                    return
                dve.wait_ge(w_hi, p + 1 + 4 * i)
                dve.tensor_tensor(wl[:, p % 2, :], raw[:, p % 4, :], wh[:, p % 2, :].bitcast(F32), ALU.subtract).then_inc(w_lo, 1)

            def ffn(stage, fill):
                off = 0
                at = 0
                for c, nf in enumerate(CHUNKS):
                    for a, b in zip(UP_PARTS[c], UP_PARTS[c][1:]):
                        with dve.Fori(a, b) as i:
                            for f in range(2):
                                p = BASE[stage] + off + 2 * f
                                u = p + 1
                                rest(p + 2, i)
                                rest(p + 3, i)
                                dve.wait_ge(taken[p % 4], p // 4 + 1 + i)
                                dve.wait_ge(pe_panel, u + 1 + 4 * i)
                                k = bass.ds(2 * i + f, 1)
                                dve.tensor_tensor(HH[:, k, :], SG[:, f:f + 1, :], ps[:, u % 4:u % 4 + 1, :], ALU.mult)
                                dve.tensor_tensor(HF[:, f, :], SG[:, f, :], ps[:, u % 4, :], ALU.mult).then_inc(taken[u % 4], 1)
                                dve.wait_ge(taken[u % 4], u // 4 + 1 + i)
                                dve.tensor_tensor(HL[:, k, :], HF[:, f:f + 1, :], HH[:, k, :].bitcast(F32), ALU.subtract).then_inc(h_ready, 1)
                        fill(at)
                        at += 1
                    off += 2 * nf
                    with dve.Fori(0, KD // 4) as i:
                        for j in range(4):
                            p = BASE[stage] + off + j
                            rest(p + 2, i)
                            dve.wait_ge(pe_panel, p + 1 + 4 * i)
                            if c:
                                q = p - KD - 2 * nf
                                dve.wait_ge(taken[q % 4], q // 4 + 1 + i)
                            x = XT[:, bass.ds(4 * i + j, 1), :]
                            dve.scalar_tensor_tensor(x, x, 1.0 if c else 2 * ALPHA, ps[:, p % 4:p % 4 + 1, :], ALU.mult, ALU.add
                                                     ).then_inc(taken[p % 4], 1)
                    if c < 2:
                        fill(at)
                        at += 1
                    off += KD

            def norm(stage, split=True):
                no, c0 = LN_NO[stage], LN_COL[stage]
                dve.wait_ge(ln_mu, no + 1)
                for d in range(KD):
                    dve.tensor_tensor(XT[:, d, :], XT[:, d, :], ps[:, 4, :], ALU.subtract).then_inc(ln_c, 1)
                reciprocal(0)
                dve.wait_ge(ln_c, 8 * no + 8)

                def affine(d):
                    if not split:
                        dve.wait_ge(ln_n, 8 * no + d + 1)
                        dve.wait_ge(sct_ready, d + 1)
                        dve.scalar_tensor_tensor(XT[:, d, :], XT[:, d, :], COL[:, c0 + d:c0 + d + 1], SCT[:, d, :], ALU.mult, ALU.add).then_inc(ln_aff, 1)
                        return
                    dve.wait_ge(ln_hi, 8 * no + d + 1)
                    dve.tensor_scalar(XT[:, d, :], XT[:, d, :], COL[:, c0 + d:c0 + d + 1], COL[:, 48 + c0 + d:49 + c0 + d],
                                      ALU.mult, ALU.add).then_inc(ln_aff, 1)
                for d in range(KD):
                    dve.tensor_tensor(XT[:, d, :], XT[:, d, :], RST[:, 0, :], ALU.mult).then_inc(ln_n, 1)
                    if d >= 1:
                        affine(d - 1)
                affine(KD - 1)

            def reciprocal(j):
                rc[0] += 1
                dve.wait_ge(sd_ready, rc[0])
                dve.reciprocal(RST[:, j, :], SD[:, j, :]).then_inc(rstd_ready, 1)
                dve.wait_ge(rstd_ready, rc[0])

            def rms(stage, layer):
                no, hi = LN_NO[stage], HI_NO[stage]
                dst = (NT, NO)[layer]
                reciprocal(0)

                def affine(d):
                    dve.wait_ge(ln_hi, 8 * hi + d + 1)
                    dve.tensor_scalar(dst[:, d, :], dst[:, d, :], AG[:, layer, d, 0:1], MOD[:, layer, d, 0:1], ALU.mult, ALU.add).then_inc(ln_aff, 1)
                for d in range(KD):
                    dve.tensor_tensor(dst[:, d, :], XT[:, d, :], RST[:, 0, :], ALU.mult).then_inc(ln_n, 1)
                    if d >= 1:
                        affine(d - 1)
                affine(KD - 1)

            def modulation(layer):
                n0 = 96 + 16 + 24 * layer
                dve.wait_ge(ada_used, 12 * (layer + 1))
                g0 = 96 + 8 * layer
                parts = ps[:, 6, 0:48].rearrange("p (m e) -> p m e", e=2)
                for e, count in ((1, 16), (0, 24))[layer:]:
                    ins = dve.scalar_tensor_tensor(MOD[:, layer, 0:count, e], parts[:, 0:count, e], float(D), COL[:, n0:n0 + count], ALU.mult, ALU.add)
                ins.then_inc(mod_ready, 1)
                dve.wait_ge(mod_ready, layer + 1)
                for e in range(2 - layer):
                    dve.scalar_tensor_tensor(AG[:, layer, :, e], MOD[:, layer, 8:16, e], 1.0, COL[:, g0:g0 + 8], ALU.add, ALU.mult)

            def gated(stage, layer):
                for j in range(8):
                    p = BASE[stage] + j
                    rest(p + 2)
                    dve.wait_ge(pe_panel, p + 1)
                    dve.scalar_tensor_tensor(XT[:, j, :], ps[:, p % 4, :], MOD[:, layer, 16 + j, 0:1], XT[:, j, :], ALU.mult, ALU.add).then_inc(taken[p % 4], 1)

            def s5_fill(t):
                wait(dve, s5_out, 64 * t)
                for b in range(2):
                    dve.wait_ge(s5_t, 4 * t + b + 3)
                    dve.tensor_copy(BT[:, 1, 4 * b:4 * b + 4, :], ps[:, 6 + b, :]).then_inc(bt_dve, 1)

            def ffn3_fill(f):
                if f == 1:
                    dve.wait_ge(cx_sd, 3)
                    dve.reciprocal(CSS[:, 0:2], CSS[:, 2:4]).then_inc(cx_n, 1)
                    dve.wait_ge(cx_n, 1)
                    for m in range(MT):
                        ins = dve.tensor_scalar(CXN[:, m, :], CXN[:, m, :], CSS[:, m:m + 1], None, ALU.mult)
                    ins.then_inc(cx_n, 1)
                if f == 2:
                    for k in range(KD):
                        if k % 2 == 0:
                            dve.wait_ge(cx_ps, k // 2 + 1)
                        dve.tensor_scalar(CXT[:, k, :], ps[:, 4 + k // 2, (k % 2) * CTX:(k % 2 + 1) * CTX], AG[:, 0, k, 1:2], MOD[:, 0, k, 1:2],
                                          ALU.mult, ALU.add).then_inc(cx_f, 1)

            def s5_parameters():
                n = [1]

                def step(ins):
                    n[0] += 1
                    ins.then_inc(s5_dve, 1)
                    dve.wait_ge(s5_dve, n[0])

                X, K, R, Q, STEP, ZR, ZI, E1, E, CM = (TS5[:, 2 + j, :] for j in range(10))
                sin, sin_half = TS5[:, 0, :], TS5[:, 1, :]
                lre, lim = PS5[:, 0, :], PS5[:, 1, :]
                two = KI5[:].bitcast(F32)

                def exponential(src, e, em1=None):
                    step(dve.tensor_scalar(X, src, -87.0, 88.0, ALU.max, ALU.min))
                    step(dve.tensor_scalar(K, X, float(1 / np.log(2.0)), MAGIC, ALU.mult, ALU.add))
                    step(dve.tensor_scalar(K, K, MAGIC, None, ALU.subtract))
                    step(dve.scalar_tensor_tensor(R, K, -LN2[0], X, ALU.mult, ALU.add))
                    step(dve.scalar_tensor_tensor(R, K, -LN2[1], R, ALU.mult, ALU.add))
                    step(dve.tensor_scalar(Q, R, 1 / 5040, None, ALU.mult))
                    for f in (720, 120, 24, 6, 2, 1):
                        step(dve.scalar_tensor_tensor(Q, Q, 1 / f, R, ALU.add, ALU.mult))
                    step(dve.tensor_scalar(K, K, 127.0, float(2 ** 23), ALU.add, ALU.mult))
                    step(dve.tensor_copy(KI5[:], K))
                    step(dve.tensor_tensor(Q, Q, two, ALU.mult))
                    step(dve.tensor_tensor(e, Q, two, ALU.add))
                    if em1 is not None:
                        step(dve.tensor_scalar(X, two, 1.0, None, ALU.subtract))
                        step(dve.tensor_tensor(em1, Q, X, ALU.add))

                exponential(PS5[:, 2, :], STEP)
                step(dve.tensor_tensor(ZI, lim, STEP, ALU.mult))
                step(dve.tensor_tensor(ZR, lre, STEP, ALU.mult))
                exponential(ZR, E, E1)
                step(dve.tensor_scalar(K, ZI, float(1 / (2 * np.pi)), MAGIC, ALU.mult, ALU.add))
                step(dve.tensor_scalar(K, K, MAGIC, None, ALU.subtract))
                step(dve.scalar_tensor_tensor(X, K, -TURN[0], ZI, ALU.mult, ALU.add))
                step(dve.scalar_tensor_tensor(X, K, -TURN[1], X, ALU.mult, ALU.add))
                step(dve.scalar_tensor_tensor(X, K, -TURN[2], X, ALU.mult, ALU.add))
                dve.tensor_scalar(X, X, -3.1415925, 3.1415925, ALU.max, ALU.min).then_inc(sin_in, 1)
                dve.wait_ge(sin_out, 1)
                step(dve.scalar_tensor_tensor(CM, sin_half, -2.0, sin_half, ALU.mult, ALU.mult))
                step(dve.tensor_tensor(Q, E, CM, ALU.mult))
                step(dve.tensor_tensor(Q, Q, E1, ALU.add))
                step(dve.tensor_tensor(R, E, sin, ALU.mult))
                step(dve.tensor_copy(PW[:, 1, 1, :], R))
                step(dve.tensor_scalar(PW[:, 0, 1, :], Q, 1.0, None, ALU.add))
                step(dve.tensor_tensor(X, lre, lre, ALU.mult))
                step(dve.tensor_tensor(K, lim, lim, ALU.mult))
                step(dve.tensor_tensor(X, X, K, ALU.add))
                step(dve.reciprocal(K, X))
                for r, (a, b, op) in enumerate(((Q, R, ALU.add), (R, Q, ALU.subtract))):
                    step(dve.tensor_tensor(X, a, lre, ALU.mult))
                    step(dve.tensor_tensor(E1, b, lim, ALU.mult))
                    step(dve.tensor_tensor(X, X, E1, op))
                    ins = dve.tensor_tensor(FB5[:, r, :], X, K, ALU.mult)
                    if r == 0:
                        step(ins)
                ins.then_inc(f_ready, 1)

            def soft_max(u, s, mask, first=False):
                dve.wait_ge(s_ps, u + 1)
                if not (isinstance(u, int) and u < 2):
                    dve.wait_ge(t_ps, u - 1)
                if not first:
                    dve.reciprocal(RS[:, s, :], SM[:, s, :]).then_inc(rs_ready, 1)
                for t, bank, col in STILES:
                    n = (t + 1) * P
                    ins = dve.tensor_tensor_reduce(PR[:, s, POFF[t]:POFF[t] + n], ps[:, bank, col:col + n], mask[:, T - n:T],
                                                   1.0, -3e38, ALU.add, ALU.max, MX[:, s, t:t + 1])
                ins.then_inc(s_sb, 1)
                dve.wait_ge(s_sb, u + 1)
                dve.tensor_scalar(NB[:, s, :], MX[:, s, :], -scale[0], None, ALU.mult).then_inc(nb_ready, 1)

            def probs_out(u, s):
                dve.wait_ge(t_ps, u + 1)
                wait(dve, pv_ps, u - 1)
                dve.tensor_copy(PT[:, s, T:2 * T], ps[:, 1, :]).then_inc(pt_dve, 1)

            def own_sums(u, s):
                dve.wait_ge(p_ready, u + 1)
                dve.reciprocal(RS[:, s, :], SM[:, s, :]).then_inc(rs_ready, 1)

            def head_out(u, s, dst):
                dve.wait_ge(rs_ready, u + 1)
                dve.wait_ge(pv_ps, u + 1)
                dve.tensor_tensor(dst, ps[:, 7, 0:TT * HD].rearrange("p (t d) -> p t d", t=TT),
                                  RS[:, s, :].rearrange("p (t o) -> p t o", o=1).broadcast_to([P, TT, HD]), ALU.mult).then_inc(o_done, 1)

            def mem_max(u, s):
                dve.wait_ge(s_ps, u + 1)
                dve.tensor_reduce(MX[:, s, 0:2], ps[:, 4, :].rearrange("p (t m) -> p t m", t=2), AX.X, ALU.max)
                dve.tensor_reduce(MX[:, s, 2:4], ps[:, 5, :].rearrange("p (t m) -> p t m", t=2), AX.X, ALU.max).then_inc(s_sb, 1)
                dve.wait_ge(s_sb, u + 1)
                dve.tensor_scalar(NB[:, s, :], MX[:, s, :], -HD ** -0.5, None, ALU.mult).then_inc(nb_ready, 1)

            def mix_lo_of(mix0):
                for k in range(KD):
                    dve.wait_ge(mix_hi, mix0 + k + 1)
                    dve.tensor_tensor(XL[:, k, :], ps[:, 4 + k % 4, :], XH[:, k, :].bitcast(F32), ALU.subtract).then_inc(x_split, 1)

            rc = [0]
            scale = [MLA_SCALE]
            dve.memset(ONES[:], 1.0 / D).then_inc(setup, 1)
            dve.memset(EPS[:, 0:1], 4e-5).then_inc(h_ready, 2)
            dve.memset(EPS[:, 1:2], 1e-5)
            dve.memset(EPS[:, 2:3], 1e-6).then_inc(setup, 1)
            rest(0)
            rest(1)
            for k2 in range(4):
                dve.wait_ge(mem_hi, k2 + 1)
                dve.tensor_tensor(ML[:, 2 * k2:2 * k2 + 2, :], ps[:, 4 + k2, :].rearrange("p (e m) -> p e m", e=2),
                                  MH[:, 2 * k2:2 * k2 + 2, :].bitcast(F32), ALU.subtract).then_inc(mem_split, 1)
            for k in range(KD):
                dve.wait_ge(x_hi, k + 1)
                dve.tensor_copy(XT[:, k, :], ps[:, 4 + k % 4, :])
                dve.tensor_tensor(XL[:, k, :], ps[:, 4 + k % 4, :], XH[:, k, :].bitcast(F32), ALU.subtract).then_inc(x_split, 1)
            dve.wait_ge(tr, 13)
            dve.tensor_copy(COL[:], ps[:, 4, 0:213])
            dve.tensor_copy(POS[:].rearrange("p j l -> p (j l)"), ps[:, 4, 256:320]).then_inc(tr_done, 1)
            for j in range(8):
                rest(BASE["mem"] + j + 2)
            for n in range(4):
                dve.wait_ge(vm_ps, n + 1)
                dve.tensor_copy(VM[:, n // 2, :, (n % 2) * P:(n % 2 + 1) * P], ps[:, 4 + n, 0:MT * P].rearrange("p (m c) -> p m c", m=MT)
                                ).then_inc(vm_ready, 1)

            dve.wait_ge(s5_tr, 1)
            dve.tensor_copy(PS5[:].rearrange("p r g -> p (r g)"), ps[:, 4, 0:3 * S5G])
            dve.tensor_copy(DT[:], ps[0:S5H, 4, 3 * S5G:4 * S5G]).then_inc(s5_dve, 1)
            dve.wait_ge(s5_dve, 1)
            s5_parameters()
            ffn("ffn0", s5_fill)
            norm("ffn0")
            dve.wait_ge(s5_out, 64 * S5T)
            for j in range(6):
                rest(BASE["mla"] + j + 2)
            reciprocal(0)
            reciprocal(1)
            for j in range(2):
                dve.wait_ge(*taken_at("mla", j))
                dve.scalar_tensor_tensor(CQ[:, j, :], CQ[:, j, :], COL[:, 96 + 98 + j:96 + 99 + j], RST[:, 0, :], ALU.mult, ALU.mult).then_inc(cq_norm, 1)
            dve.wait_ge(*taken_at("mla", 2))
            dve.scalar_tensor_tensor(CKV[:], CKV[:], COL[:, 96 + 100:96 + 101], RST[:, 1, :], ALU.mult, ALU.mult).then_inc(cq_norm, 1)
            dve.wait_ge(kr_ps, 1)
            dve.wait_ge(mla_in_s, 80)
            dve.tensor_tensor(KR2[:, 0, :], ps[ROPE:2 * ROPE, 6, :], ROT[ROPE:2 * ROPE, :], ALU.mult).then_inc(kr_rot, 1)
            dve.tensor_tensor(KR2[:, 1, :], KR, ROT[0:ROPE, :], ALU.mult).then_inc(dve_link, 1)
            dve.wait_ge(dve_link, 1)
            dve.tensor_tensor(KR2[:, 0, :], KR2[:, 0, :], KR2[:, 1, :], ALU.add).then_inc(kr_rot, 1)
            dve.wait_ge(kr_rot, 2)
            dve.tensor_copy(KT[HD:QK, 6:12, :], KR2[:, 0:1, :].broadcast_to([ROPE, 6, T])).then_inc(kr_dve, 1)
            for g in range(14):
                if g < 6:
                    dve.wait_ge(kv_ps, g + 1)
                    dve.tensor_copy(KT[0:HD, 2 * g + 1, :], ps[HD:P, 4 + g % 4, :]).then_inc(kv_dve, 1)
                elif g % 2:
                    dve.wait_ge(kv_ps, g + 1)
                    dve.tensor_copy(V[:, (g - 6) // 2, 6 * HD:], ps[:, 4 + g % 4, 0:6 * HD]).then_inc(kv_dve, 1)

            def rotate_q(h, s):
                dve.wait_ge(q_ps, h + 1)
                wait(dve, q_rope, h)
                dve.tensor_tensor(RT[HD:QK, 0, :], ps[HD:QK, 3, :], ROT[HD:QK, :], ALU.mult).then_inc(q_rot, 1)
                dve.tensor_tensor(RT[HD:QK, 1, :], ps[QK:P, 3, :], ROT[QK:P, :], ALU.mult).then_inc(q_rot, 1)
                dve.wait_ge(q_rot, 2 * h + 2)
                if not (isinstance(h, int) and h < 2):
                    dve.wait_ge(s_ps, h - 1)
                dve.tensor_tensor(QT[HD:QK, s, :], RT[HD:QK, 0, :], RT[HD:QK, 1, :], ALU.add).then_inc(q_rope, 1)

            def o_head(h):
                return O[:, :, bass.ds(h * HD, HD)]

            for h in range(3):
                rotate_q(h, h % 2)
            for h in range(2):
                soft_max(h, h, CAUS, first=True)

            def mla_unit(u, s, project=True, begin=False):
                probs_out(u, s)
                if project:
                    rotate_q(u + 3, 1 - s)
                if not begin:
                    head_out(u - 1, 1 - s, o_head(u - 1))
                soft_max(u + 2, s, CAUS)

            mla_unit(0, 0, begin=True)
            mla_unit(1, 1)
            with dve.Fori(1, HEADS // 2 - 2) as i:
                for s in range(2):
                    mla_unit(2 * i + s, s)
            mla_unit(8, 0)
            mla_unit(9, 1, project=False)

            def mem_out(u, h):
                head_out(u, u % 2, O[:, :, TOKW + h * HD:TOKW + (h + 1) * HD])

            for h in range(2):
                u = 10 + h
                probs_out(u, h)
                head_out(u - 1, 1 - h, o_head(u - 1))
                own_sums(u, h)
                mem_max(u + 2, h)
            for h in range(MEM_HEADS):
                u = 12 + h
                probs_out(u, u % 2)
                if h == 0:
                    head_out(11, 1, o_head(11))
                else:
                    mem_out(u - 1, h - 1)
                own_sums(u, u % 2)
                if h < 2:
                    mem_max(u + 2, u % 2)
            mem_out(15, 3)
            mix_lo_of(0)
            for j in range(8):
                p = BASE["wo0"] + j
                rest(p + 2)
                dve.wait_ge(pe_panel, p + 1)
                dve.scalar_tensor_tensor(XT[:, j, :], XT[:, j, :], ALPHA, ps[:, p % 4, :], ALU.mult, ALU.add).then_inc(taken[p % 4], 1)
            norm("wo0")
            ffn("ffn1", nothing)
            norm("ffn1")
            modulation(0)

            for j in range(6):
                rest(BASE["kv"] + j + 2)
                if j == 2:
                    for e in range(2):
                        dve.wait_ge(*taken_at("kv", e))
                        for a in range(2):
                            for g in range(GROUPS):
                                r = slice(g * HD, (g + 1) * HD)
                                ins = dve.tensor_tensor(ZB[a * HD:(a + 1) * HD, e, :, g, 0:NCMP],
                                                        ZC[r, e, 16 * a:16 * a + 16 * NCMP].rearrange("p (n l) -> p l n", l=16),
                                                        POS[r, e, 16 * a:16 * a + 16].rearrange("p (l o) -> p l o", o=1).broadcast_to([HD, 16, NCMP]), ALU.add)
                        ins.then_inc(zb_ready, 1)
            for e, dst in enumerate((VS, VW)):
                dve.wait_ge(vt_ps, e + 1)
                dve.tensor_copy(dst[:].rearrange("p t c -> p (t c)"), ps[:, 4 + e, :]).then_inc(vt_out, 1)
            ffn("ffn2", nothing)
            norm("ffn2")
            modulation(1)

            for j in range(9):
                rest(BASE["nsa"] + j + 2)
                if j == 3:
                    dve.wait_ge(g_ps, 1)
                    for t in range(TT):
                        ins = dve.tensor_copy(G[:, :, :, t, :], ps[:, 4, t * 36:(t + 1) * 36].rearrange("p (g j b) -> p b j g", g=GROUPS, j=HPG))
                    ins.then_inc(g_out, 1)
            scale[0] = SEL_SCALE
            dve.wait_ge(cmask_in, 16)
            dve.wait_ge(sp_in[0], IN["bias"] + 32)
            for g in range(GROUPS):
                soft_max(16 + g, g, BIAS[:, 0, g], first=True)

            def cmp_max(j, q):
                dve.wait_ge(c_ps, j + 1)
                wait(dve, c_t, j)
                dve.tensor_tensor(SC[:].rearrange("p t g n -> p (t g n)"), ps[:, 3, 0:TT * 2 * NPAD], CB[:, q], ALU.add).then_inc(c_sc, 1)
                dve.wait_ge(c_sc, 2 * j + 1)
                dve.tensor_reduce(MC[:], SC[:], AX.X, ALU.max).then_inc(c_sc, 1)
                dve.wait_ge(c_sc, 2 * j + 2)
                dve.tensor_tensor(SC[:], SC[:], MC[:].rearrange("p t (g o) -> p t g o", o=1).broadcast_to([P, TT, GROUPS, NPAD]), ALU.subtract).then_inc(c_sub, 1)

            def cmp_probs(j):
                dve.wait_ge(c_mask, j + 1)
                dve.tensor_reduce(SMC[:], SC[:], AX.X, ALU.add).then_inc(c_sum, 1)
                dve.wait_ge(c_sum, 4 * j + 1)
                dve.tensor_scalar(SMC[:], SMC[:], 1e-30, None, ALU.max).then_inc(c_sum, 1)
                dve.wait_ge(c_sum, 4 * j + 2)
                dve.reciprocal(SMC[:], SMC[:]).then_inc(c_sum, 1)
                dve.wait_ge(c_sum, 4 * j + 3)
                dve.tensor_tensor(SMC[:], SMC[:], G[:, 0, bass.ds(j, 1)].rearrange("p o t g -> p (o t) g"), ALU.mult).then_inc(c_sum, 1)
                dve.wait_ge(c_sum, 4 * j + 4)
                dve.tensor_tensor(SC[:], SC[:], SMC[:].rearrange("p t (g o) -> p t g o", o=1).broadcast_to([P, TT, GROUPS, NPAD]), ALU.mult).then_inc(c_p, 1)

            def gated_out(u, j, k):
                s, g, br = k % 2, k % 2, k // 2
                dve.wait_ge(rs_ready, u + 1)
                dve.tensor_tensor(W4[:, s, :], RS[:, s, :], G[:, 1 + br, bass.ds(j, 1), :, g].rearrange("p o t -> p (o t)"), ALU.mult).then_inc(w4_ready, 1)
                dve.wait_ge(w4_ready, u - 15)
                dve.wait_ge(pv_ps, u + 1)
                dst = O[:, :, bass.ds(g * HPG * HD + j * HD, HD)]
                src = ps[:, 7, 0:TT * HD].rearrange("p (t d) -> p t d", t=TT)
                if br == 0:
                    dve.tensor_tensor(dst, src, W4[:, s, :].rearrange("p (t o) -> p t o", o=1).broadcast_to([P, TT, HD]), ALU.mult).then_inc(o_done, 1)
                else:
                    dve.wait_ge(o_done, u - 1)
                    for t in range(TT):
                        ins = dve.scalar_tensor_tensor(dst[:, t], src[:, t], W4[:, s, t:t + 1], dst[:, t], ALU.mult, ALU.add)
                    ins.then_inc(o_done, 1)

            def cmp_out(j):
                dve.wait_ge(c_pv, j + 1)
                dve.wait_ge(o_done, 20 + 4 * j)
                for g in range(GROUPS):
                    dst = O[:, :, bass.ds(g * HPG * HD + j * HD, HD)]
                    ins = dve.tensor_tensor(dst, dst, ps[:, 3, :].rearrange("p (t g d) -> p t g d", t=TT, g=GROUPS)[:, :, g], ALU.add)
                ins.then_inc(c_o, 1)

            def nsa_pair(j, q, slot, last=False):
                for k in range(4):
                    u = 16 + 4 * j + k
                    begin = isinstance(j, int) and j == 0 and k == 0
                    probs_out(u, k % 2)
                    if k > 0:
                        gated_out(u - 1, j, k - 1)
                    elif not begin:
                        gated_out(u - 1, j - 1, 3)
                        cmp_out(j - 1)
                    if k == 1:
                        cmp_max(j, q)
                    if k == 3:
                        cmp_probs(j)
                    if k < 2:
                        soft_max(u + 2, k % 2, BIAS[:, q, k % 2])
                    elif not last:
                        if k == 2:
                            dve.wait_ge(sp_in[1 - q], 32 * slot + IN["bias"])
                        soft_max(u + 2, k % 2, BIAS[:, 1 - q, k % 2])
                    else:
                        own_sums(u, k % 2)
                        mem_max(u + 2, k % 2)

            nsa_pair(0, 0, 1)
            nsa_pair(1, 1, 2)
            with dve.Fori(1, HPG // 2 - 1) as i:
                nsa_pair(2 * i, 0, i + 1)
                nsa_pair(2 * i + 1, 1, i + 2)
            nsa_pair(4, 0, 3)
            nsa_pair(5, 1, 0, last=True)
            for h in range(MEM_HEADS):
                u = 40 + h
                probs_out(u, u % 2)
                if h == 0:
                    gated_out(39, 5, 3)
                    cmp_out(HPG - 1)
                else:
                    mem_out(u - 1, h - 1)
                own_sums(u, u % 2)
                if h < 2:
                    mem_max(u + 2, u % 2)
            mem_out(43, 3)
            mix_lo_of(8)
            for j in range(8):
                p = BASE["wo1"] + j
                rest(p + 2)
                dve.wait_ge(pe_panel, p + 1)
                dve.scalar_tensor_tensor(XT[:, j, :], XT[:, j, :], ALPHA, ps[:, p % 4, :], ALU.mult, ALU.add).then_inc(taken[p % 4], 1)
            norm("wo1")
            ffn("ffn3", ffn3_fill)
            norm("ffn3", split=False)

            rms("even", 0)
            for j in range(6):
                p = BASE["even"] + j
                rest(p + 2)
                dve.wait_ge(pe_panel, p + 1)
                dve.tensor_copy(UT[:, j, :, 0:NCC].rearrange("p t c -> p c t"), ps[:, 4 + j % 2, 0:CTX].rearrange("p (c t) -> p c t", t=L)).then_inc(uc_out, 1)
            for j in range(6, 10):
                rest(BASE["even"] + j + 2)
            for t in range(S5T):
                for b in range(4):
                    dve.wait_ge(b_ps, 4 * t + b + 1)
                    g = t * GT + (b % 2) * 4
                    src = ps[S5P:P, 4 + b, 0:4 * NC].rearrange("p (g c) -> p g c", g=4)
                    dve.tensor_copy(H[S5P:P, b // 2, g:g + 4, 0:NCC], src[:, :, 0:NCC][:, :, ::-1])
                    dve.tensor_copy(H[S5P:P, b // 2, g:g + 4, NCC:], src[:, :, NCC:][:, :, ::-1]).then_inc(h_dve, 1)
            dve.wait_ge(bk_ready, 1)
            dve.wait_ge(h_act, 4 * S5T)
            dve.wait_ge(h_dve, 4 * S5T)

            def advance(k):
                before = H[:, :, :, bass.ds(k - 1, 1)].rearrange("p r g o -> p o r g").broadcast_to([P, 2, 2, S5G])
                here = H[:, :, :, bass.ds(k, 1)].rearrange("p r g o -> p r (g o)")
                wait(dve, scan, 3 * k - 3)
                dve.tensor_tensor(SCM, L8[:], before, ALU.mult).then_inc(scan, 1)
                dve.wait_ge(scan, 3 * k - 2)
                dve.tensor_tensor(SCA, SCM[:, 0], SCM[:, 1][:, ::-1], ALU.add).then_inc(scan, 1)
                dve.wait_ge(scan, 3 * k - 1)
                dve.tensor_tensor(here, here, SCA, ALU.add).then_inc(scan, 1)

            for k in range(1, 4):
                advance(k)
            with dve.Fori(1, NC // 4) as i:
                for k in range(4):
                    advance(4 * i + k)
            dve.wait_ge(scan, 3 * (NC - 1))

            def states(t):
                wait(dve, y_ps, t - 1)
                dve.tensor_copy(SS[S5P:P, t % 2], H[S5P:P, :, t * GT:(t + 1) * GT, NCC - 1:NC - 1][:, :, :, ::-1]).then_inc(ss_dve, 1)

            dve.wait_ge(fnet_ps, 8)
            for t in range(S5T):
                states(t)
            for j in range(6):
                dve.wait_ge(ya_hi, j + 1)
                dve.tensor_tensor(XL[:, j, :], YA[:, j, :], XH[:, j, :].bitcast(F32), ALU.subtract).then_inc(x_split, 1)

            for e in range(2):
                dve.wait_ge(p1_ready, e + 1)
                dve.tensor_copy(YH[:, 6 + e, :], ZS[:, 6 + e, :]).then_inc(y_full, 1)
                dve.wait_ge(y_full, e + 1)
                dve.tensor_tensor(YL[:, 6 + e, :], ZS[:, 6 + e, :], YH[:, 6 + e, :].bitcast(F32), ALU.subtract).then_inc(y_ready, 1)
            for j in range(6):
                p = BASE["glu"] + j
                rest(p + 2)
                dve.wait_ge(p1_ready, 3 + j)
                dve.wait_ge(*taken_at("glu", j))
                dve.tensor_tensor(YH[:, j, :], SIG[:, j % 2, :], ZS[:, j, :], ALU.mult)
                dve.tensor_tensor(YF[:, j % 2, :], SIG[:, j % 2, :], ZS[:, j, :], ALU.mult).then_inc(y_full, 1)
                dve.wait_ge(y_full, j + 3)
                dve.tensor_tensor(YL[:, j, :], YF[:, j % 2, :], YH[:, j, :].bitcast(F32), ALU.subtract).then_inc(y_ready, 1)
            gated("ewo", 0)
            rms("odd", 1)

            for j in range(4):
                rest(BASE["odd"] + j + 2)
            dve.wait_ge(odd_zero, 1)
            link = 0
            for k in range(4):
                p = BASE["odd"] + 4 + 3 * k
                rest(p + 2)
                rest(p + 3)
                dve.wait_ge(*taken_at("odd", 4 + 3 * k))
                dve.wait_ge(pe_panel, p + 2)
                v, cx = CV[:, k % 2, :], CX[:, k % 2, :]
                dve.tensor_tensor(v[:, 1:T + 1], CG[:, k % 2, :], ps[:, (p + 1) % 4, :], ALU.mult).then_inc(taken[(p + 1) % 4], 1)
                dve.wait_ge(*taken_at("odd", 5 + 3 * k))
                w = [COL[:, 96 + 82 + 4 * c + k:96 + 83 + 4 * c + k] for c in range(3)]
                dve.tensor_scalar(cx, v[:, 1:T + 1], w[1], None, ALU.mult).then_inc(dve_link, 1)
                dve.wait_ge(dve_link, 3 * k + 2)
                dve.scalar_tensor_tensor(cx, v[:, 0:T], w[0], cx, ALU.mult, ALU.add).then_inc(dve_link, 1)
                dve.wait_ge(dve_link, 3 * k + 3)
                dve.scalar_tensor_tensor(cx, v[:, 2:T + 2], w[2], cx, ALU.mult, ALU.add).then_inc(dve_link, 1)
                rest(p + 4)
                dve.wait_ge(dve_link, 3 * k + 4)
                dve.wait_ge(pe_panel, p + 3)
                dve.tensor_tensor(YO[:, 4 + k, :], cx, ps[:, (p + 2) % 4, :], ALU.mult).then_inc(taken[(p + 2) % 4], 1)
            for j in range(8):
                p = BASE["odd"] + 16 + j
                rest(p + 2)
                if j < 4:
                    dve.wait_ge(yc_ready, j + 1)
                else:
                    dve.wait_ge(*taken_at("odd", 6 + 3 * (j - 4)))
                dve.wait_ge(*taken_at("odd", 16 + j))
                dve.tensor_tensor(YH[:, j, :], YO[:, j, :], ZO[:, j % 2, :], ALU.mult)
                dve.tensor_tensor(YQ[:, j % 2, :], YO[:, j, :], ZO[:, j % 2, :], ALU.mult).then_inc(y_full, 1)
                dve.wait_ge(y_full, 8 + j + 1)
                dve.tensor_tensor(YL[:, j, :], YQ[:, j % 2, :], YH[:, j, :].bitcast(F32), ALU.subtract).then_inc(y_ready, 1)
            gated("owo", 1)
            reciprocal(0)
            for d in range(KD):
                dve.scalar_tensor_tensor(XT[:, d, :], XT[:, d, :], COL[:, 96 + 64 + d:96 + 65 + d], RST[:, 0, :], ALU.mult, ALU.mult).then_inc(ln_aff, 1)

        @block.gpsimd
        def _(pool):
            def norm(stage, last, split=True):
                no = LN_NO[stage]
                for d in range(KD):
                    pool.wait_ge(*taken_at(stage, last - KD + d))
                    if d == 0:
                        pool.tensor_copy(ACC[:], XT[:, 0, :]).then_inc(ln_acc, 1)
                    else:
                        pool.wait_ge(ln_acc, 8 * no + d)
                        pool.tensor_tensor(ACC[:], ACC[:], XT[:, d, :], ALU.add).then_inc(ln_acc, 1)
                for d in range(KD if split else 0):
                    pool.wait_ge(ln_aff, 8 * no + d + 1)
                    pool.tensor_tensor(XL[:, d, :], XT[:, d, :], XH[:, d, :].bitcast(F32), ALU.subtract).then_inc(x_split, 1)

            n = [0]

            def step(ins):
                n[0] += 1
                ins.then_inc(pool_link, 1)
                pool.wait_ge(pool_link, n[0])

            def product(a, b, outs, shape):
                size = int(np.prod(shape[1:]))
                t1, t2 = (t[:, 0:size] for t in (T1, T2))
                if len(shape) == 3:
                    t1, t2 = (t.rearrange("p (x y) -> p x y", x=shape[1]) for t in (t1, t2))
                if len(shape) == 4:
                    t1, t2 = (t.rearrange("p (x y z) -> p x y z", x=shape[1], y=shape[2]) for t in (t1, t2))
                for e, op in enumerate((ALU.subtract, ALU.add)):
                    pool.tensor_tensor(t1, a[0], b[e], ALU.mult)
                    step(pool.tensor_tensor(t2, a[1], b[1 - e], ALU.mult))
                    for rows, dst in outs:
                        step(pool.tensor_tensor(dst[e], t1[rows], t2[rows], op))

            FWD, BWD, ALL = slice(0, S5P), slice(S5P, P), slice(0, P)

            for r, name in enumerate(("s5_lam_re_2", "s5_lam_im_2")):
                pool.dma_start(LAMN[:, r, :].rearrange("g (d p) -> g d p", d=2), A[name][0].rearrange("d g p -> g d p")).then_inc(s5_in, 16)
            pool.dma_start(LSN, A["s5_log_step_2"][0]).then_inc(s5_in, 16)
            pool.dma_start(DN, A["s5_d_2"][0]).then_inc(s5_in, 16)
            pool.dma_start(DSEL, C["dirsel"]).then_inc(s5_in, 16)
            for r, (bn, cn) in enumerate((("s5_b_re_2", "s5_c_re_2"), ("s5_b_im_2", "s5_c_im_2"))):
                for e in range(2):
                    pool.dma_start(CN[:, r, :, e, :], A[cn][0, e].rearrange("(t g) h p -> (g h) t p", g=GT)).then_inc(s5_in, 16)
                    pool.dma_start(BN[e * S5P:(e + 1) * S5P, r], A[bn][0, e].rearrange("g p h -> p g h")).then_inc(s5_in, 16)
            pool.wait_ge(s5_in, 16 * S5_LOADS)
            step(pool.memset(PW[:, 0, 0, :], 1.0))
            step(pool.memset(PW[:, 1, 0, :], 0.0))
            pool.wait_ge(f_ready, 1)
            for k in (1, 2, 4):
                product([PW[:, r, 1:1 + k, :] for r in range(2)], [PW[:, r, k:k + 1, :].broadcast_to([P, k, S5G]) for r in range(2)],
                        [(ALL, [PW[:, r, k + 1:2 * k + 1, :] for r in range(2)])], [P, k, S5G])
            product([FB5[:, r, :].rearrange("p (g o) -> p g o", o=1).broadcast_to([P, S5G, S5H]) for r in range(2)], [BN[:, r] for r in range(2)],
                    [(ALL, [BB[:, r] for r in range(2)])], [P, S5G, S5H])

            def powers(r, rows, ks):
                return PW[rows, r, ks, :].rearrange("p k g -> p g k")
            for rows, up, down in ((FWD, slice(1, L + 1), slice(L - 1, None, -1)), (BWD, slice(L, 0, -1), slice(0, L))):
                step(pool.tensor_copy(PC[rows, 0], powers(0, rows, up)))
                step(pool.tensor_scalar(PC[rows, 1], powers(1, rows, up), -1.0, None, ALU.mult))
                for r in range(2):
                    step(pool.tensor_copy(PB[rows, r], powers(r, rows, down)))
            for r in range(2):
                step(pool.tensor_copy(L8[:, 0, r, :], PW[:, 0, L, :]))
            step(pool.tensor_copy(L8[:, 1, 0, :], PW[:, 1, L, :]))
            step(pool.tensor_scalar(L8[:, 1, 1, :], PW[:, 1, L, :], -1.0, None, ALU.mult))
            pool.wait_ge(s5_tr, 4)
            pool.wait_ge(cr_out, 3)
            step(pool.memset(SW[:], 0.0))

            def tile(t):
                gs = slice(t * GT, (t + 1) * GT)

                def over_time(x):
                    return [x[:, r, gs, :].rearrange("p g (o h) -> p g o h", o=1).broadcast_to([P, GT, L, S5H]) for r in range(2)]

                def over_channels(x):
                    return [x[:, r, gs, :].rearrange("p g (t o) -> p g t o", o=1).broadcast_to([P, GT, L, S5H]) for r in range(2)]

                def cut(x, rows, col):
                    return [x[rows, r, :, col:col + P].rearrange("p g (t h) -> p g t h", t=L) for r in range(2)]
                wait(pool, s5_z, 4 * t)
                wait(pool, s5_out, 64 * t)
                product(over_time(BB), over_channels(PB), [(ALL, cut(BK, ALL, 0))], [P, GT, L, S5H])
                product(over_time(CR), over_channels(PC), [(FWD, cut(SW, FWD, (L + 1) * S5H)), (BWD, cut(SW, BWD, 0))], [P, GT, L, S5H])
                for r in range(2):
                    ins = pool.tensor_copy(SW[:, r, :, L * S5H:(L + 1) * S5H], CR[:, r, gs, :])
                ins.then_inc(bk_ready, 1)
                step(pool.tensor_tensor(DD, IDENT[0:S5H, 0:S5H].rearrange("p (o h) -> p o h", o=1).broadcast_to([S5H, GT, S5H]),
                                        DT[:, gs].rearrange("p (g o) -> p g o", o=1).broadcast_to([S5H, GT, S5H]), ALU.mult))
                pool.wait_ge(z_out, 4 * t + 4)
                mid = Z[:, :, (L - 1) * S5H:L * S5H]
                step(pool.tensor_tensor(mid, mid, DD, ALU.add))
                for rows, col in ((FWD, (L + 1) * S5H), (BWD, 0)):
                    pool.dma_start(scratch["s5_w"][t, rows], SW[rows, :, :, col:col + P].rearrange("p r g c -> p (r g) c")).then_inc(s5_out, 16)
                pool.wait_ge(bt_act, 2 * t + 2)
                pool.wait_ge(bt_dve, 2 * t + 2)
                pool.dma_start(scratch["s5_b"][t], BT[:].rearrange("p r g c -> p (r g c)")).then_inc(s5_out, 16)
                pool.dma_start(scratch["s5_taps"][:, gs], Z[:]).then_inc(s5_out, 16)

            for t in range(S5T):
                tile(t)
            norm("ffn0", 68)
            pool.wait_ge(s5_out, 64 * S5T)
            for t in range(L):
                pool.dma_start(scratch["s5_m"][t * S5H:(t + 1) * S5H], scratch["s5_taps"][:, :, (L - 1 - t) * S5H:(L - 1 - t) * S5H + P]).then_inc(s5_out, 16)
            norm("wo0", 8)

            def load_ada(layer):
                w = A["ada_w_2"][layer].rearrange("(k p) n -> p k n", p=P)
                prod = NS[:].rearrange("p s t -> p (s t)")[:, 0:KD * 2 * P].rearrange("p (k c) -> p k c", k=KD)

                def load(n):
                    pool.dma_start(AW[:, n % 2], w[:, :, n * 2 * P:(n + 1) * 2 * P]).then_inc(pool_in[n % 2], 16)
                load(0)
                load(1)
                for n in range(12):
                    pool.wait_ge(pool_in[n % 2], IN["ada"] + 16 * (6 * layer + n // 2 + 1))
                    wait(pool, ada_used, 12 * layer + n - 1)
                    for e in range(ada_conditions(layer, n)):
                        step(pool.tensor_tensor(prod, AW[:, n % 2], CS[:, :, e:e + 1].broadcast_to([P, KD, 2 * P]), ALU.mult))
                        step(pool.tensor_tensor(prod[:, 0:4], prod[:, 0:4], prod[:, 4:8], ALU.add))
                        step(pool.tensor_tensor(prod[:, 0:2], prod[:, 0:2], prod[:, 2:4], ALU.add))
                        ins = pool.tensor_tensor(AS[:, n % 2, e], prod[:, 0], prod[:, 1], ALU.add)
                        if e < ada_conditions(layer, n) - 1:
                            step(ins)
                    ins.then_inc(ada_part, 1)
                    pool.wait_ge(ada_part, 12 * layer + n + 1)
                    if n + 2 < 12:
                        load(n + 2)

            pool.wait_ge(pe_panel, BASE["ffn1"])
            for t in (H1, KCB, VCB):
                ins = pool.memset(t[:], 0.0)
                if t is not KCB:
                    ins.then_inc(zeros, 1)
            pool.wait_ge(cs_ready, 1)
            load_ada(0)
            for j in range(2):
                for a in range(2):
                    pool.dma_start(W1[j][a * HD:(a + 1) * HD], A["cmp_w1"][j].rearrange("(a l d) h -> a d l h", a=2, d=HD)[a]).then_inc(w1_in, 16)
                pool.dma_start(W2[:, j], A["cmp_w2"][j].rearrange("(m p) d -> p m d", p=P)).then_inc(w1_in, 16)
            norm("ffn1", 68)
            pool.wait_ge(hid_ps, 4)
            load_ada(1)
            norm("ffn2", 68)
            pool.wait_ge(cmask_in, 16)

            def copy_q(j, q):
                pool.wait_ge(*taken_at("nsa", 6 + j // 2))
                if j >= 2:
                    pool.wait_ge(s_ps, 16 + 4 * (j - 1))
                pool.tensor_copy(QS[:, q, :], QP[:, j, :]).then_inc(qs_ready, 1)

            def mask(j):
                pool.wait_ge(c_exp, j + 1)
                pool.tensor_tensor(SC[:], SC[:], CMASK[:].rearrange("p (t o n) -> p t o n", o=1, n=NPAD).broadcast_to([P, TT, GROUPS, NPAD]), ALU.mult).then_inc(c_mask, 1)

            copy_q(0, 0)
            for j in range(HPG):
                if j + 1 < HPG:
                    copy_q(j + 1, (j + 1) % 2)
                mask(j)
            norm("wo1", 8)
            pool.wait_ge(pe_panel, BASE["ffn3"])
            pool.dma_start(CXN[:], A["ctx_2"][0].rearrange("(m p) d -> p m d", p=P)).then_inc(cx_in, 16)
            pool.dma_start(SCT[:].rearrange("p k t -> p (k t)"), C["sincos"]).then_inc(cx_in, 16)
            pool.wait_ge(cx_in, 32)
            for k in range(KD):
                pool.tensor_scalar(SCT[:, k, :], SCT[:, k, :], COL[:, 88 + k:89 + k], None, ALU.add).then_inc(sct_ready, 1)
            for k in range(KD):
                pool.wait_ge(cx_hi, k + 1)
                pool.tensor_tensor(CL[:, k, :], CXT[:, k, :], CH[:, k, :].bitcast(F32), ALU.subtract).then_inc(cx_split, 1)
            norm("ffn3", 68, split=False)

            for d in range(KD):
                pool.wait_ge(ln_aff, 8 * LN_NO["even"] + d + 1)
                pool.tensor_tensor(XL[:, d, :], NT[:, d, :], XH[:, d, :].bitcast(F32), ALU.subtract).then_inc(x_split, 1)
            u_rows = scratch["s5_u"].rearrange("(g h) t c -> t h g c", h=S5H)
            for s in range(3):
                pool.wait_ge(pe_panel, BASE["even"] + 1)
                pool.dma_start(BS[:, s].rearrange("p r g c -> p (r g c)"), scratch["s5_b"][s]).then_inc(pool_in[s], 16)
            for j in range(6):
                pool.wait_ge(*taken_at("even", j))
                pool.wait_ge(uc_out, j + 1)
                pool.dma_start(scratch["s5_u"][j * P:(j + 1) * P], UT[:, j]).then_inc(shuffle_out, 16)
            pool.wait_ge(shuffle_out, 16 * 6)
            for t in range(L):
                pool.dma_start(U[t * S5H:(t + 1) * S5H], u_rows[t]).then_inc(shuffle_in, 16)
            for t in range(3, S5T):
                pool.wait_ge(b_ps, 4 * (t - 3) + 4)
                pool.dma_start(BS[:, t % 3].rearrange("p r g c -> p (r g c)"), scratch["s5_b"][t]).then_inc(pool_in[t % 3], 16)

            pool.wait_ge(b_ps, 4 * S5T)
            step(pool.memset(FW[:], 0.0))
            for b in range(4):
                r = slice((b % 2) * HD, (b % 2 + 1) * HD)
                pool.dma_start(FW[r, b // 2, r], A["fnet_w_2"][0, b]).then_inc(dft_in, 16)
            pool.dma_start(DFTC[:], C["dftc"]).then_inc(dft_in, 16)
            pool.dma_start(DFTT[:].rearrange("p e t c -> p (e t c)"), C["dftt"]).then_inc(dft_in, 16)
            for p in range(BASE["even"] + 12, BASE["glu"] + 2):
                pool.wait_ge(w_hi, p + 1)
                pool.wait_ge(w_lo, p)
                pool.tensor_tensor(wl[:, p % 2, :], raw[:, p % 4, :], wh[:, p % 2, :].bitcast(F32), ALU.subtract).then_inc(w_lo, 1)
            pool.wait_ge(fnet_ps, 8)
            pool.wait_ge(s5_out, 64 * S5T + 16 * L)
            for t in range(S5T):
                wait(pool, m_ps, t - 1)
                pool.dma_start(MM[:, t % 2], scratch["s5_m"][:, t * GT:(t + 1) * GT]).then_inc(pool_in[t % 2], 16)

            def load_w(t):
                pool.dma_start(WT[t].rearrange("p r g c -> p (r g c)"), scratch["s5_w"][t].rearrange("p g c -> p (g c)")).then_inc(w_in, 16)
            load_w(0)
            load_w(1)
            pool.wait_ge(m_ps, S5T)
            for t in range(2, 5):
                load_w(t)
            pool.wait_ge(y_ps, 1)
            load_w(5)
            for j in range(2):
                pool.wait_ge(fnet_out, 7 + j)
                pool.wait_ge(*taken_at("even", 14 + j))
                pool.tensor_tensor(ZS[:, 6 + j, :], ZS[:, 6 + j, :], YB[:, j, :], ALU.mult).then_inc(p1_ready, 1)
            for j in range(6):
                pool.wait_ge(ya_ready, j + 1)
                pool.wait_ge(*taken_at("even", 8 + j))
                pool.tensor_tensor(ZS[:, j, :], ZS[:, j, :], YA[:, j, :], ALU.mult).then_inc(p1_ready, 1)

            pool.wait_ge(y_ready, 8)
            pool.dma_start(PINV[:].rearrange("p i t -> p (i t)"), C["poolinv"]).then_inc(odd_in, 16)
            pool.dma_start(PWT[:], A["pool_w_2"][0].rearrange("i c d -> c i d")).then_inc(odd_in, 16)
            for d in range(KD):
                pool.wait_ge(ln_aff, 8 * LN_NO["odd"] + d + 1)
                pool.tensor_tensor(XL[:, d, :], NO[:, d, :], XH[:, d, :].bitcast(F32), ALU.subtract).then_inc(x_split, 1)
            pool.wait_ge(x_split, XS["odd"] + 8)
            pool.memset(CV[:], 0.0)
            pool.memset(PU[:], 0.0).then_inc(odd_zero, 1)
            pool.wait_ge(odd_in, 32)
            for i, w in enumerate(POOL_WINDOWS):
                pool.wait_ge(*taken_at("odd", i))
                if i >= 2:
                    pool.wait_ge(pw_ps, i - 1)
                src, have, a = PU[:, i, :], 1, 0
                while have < w:
                    size = T + PAD - 2 * have + 9
                    lo = PAD - 8
                    step(pool.tensor_tensor(PS[:, a, lo:lo + size], src[:, lo:lo + size], src[:, lo + have:lo + have + size], ALU.add))
                    src, have, a = PS[:, a, :], 2 * have, 1 - a
                step(pool.tensor_tensor(PP[:, i % 2, :], src[:, PAD - w // 2:PAD - w // 2 + T], PINV[:, i, :], ALU.mult))
                pool.tensor_tensor(PP[:, i % 2, :], PP[:, i % 2, :], PU[:, i, PAD:PAD + T], ALU.subtract).then_inc(pool_ready, 1)


SCRATCH = {
    "s5_w": (S5T, P, 2 * GT, P),
    "s5_b": (S5T, P, 2 * GT * P),
    "s5_taps": (S5H, S5G, (STRIP - 2) * S5H),
    "s5_m": (P, S5G, P),
    "s5_u": (6 * P, L, NC),
    "s5_y": (6 * P, L, NCL),
}


def kernel(**inputs):
    import concourse.bacc as bacc
    from concourse.bass_utils import run_bass_kernel_spmd

    nc = bacc.Bacc("TRN2", target_bir_lowering=False, num_devices=1)
    arrays = {}

    def given(name, a):
        arrays[name] = np.ascontiguousarray(a)
        return nc.dram_tensor(name, arrays[name].shape, mybir.dt.from_np(arrays[name].dtype), kind="ExternalInput").ap()

    A = {name: given("in_" + name, a) for name, a in inputs.items()}
    C = {name: given("const_" + name, a) for name, a in constants().items()}
    out = nc.dram_tensor("out", (1, T, D), F32, kind="ExternalOutput").ap()
    scratch = {name: nc.dram_tensor(name, shape, F32, kind="Internal").ap() for name, shape in SCRATCH.items()}
    program(nc, A, C, out, scratch)
    r = run_bass_kernel_spmd(nc, [arrays], core_ids=[0])
    return r.results[0]["out"]
```

```python
from contextlib import ExitStack

import numpy as np

import concourse.bass as bass
from concourse import mybir

F32 = mybir.dt.float32
F32R = mybir.dt.float32r
I32 = mybir.dt.int32
ACT = mybir.ActivationFunctionType
ALU = mybir.AluOpType
AX = mybir.AxisListType

P = 128
D = 1024
T = 512
M = 256
KD = D // P
TT = T // P
MT = M // P
DFF = 2816
FT = DFF // P
HEADS, HD = 12, 64
MEM_HEADS = 4
TOKW = HEADS * HD
QR, ROPE = 256, 32
QK = HD + ROPE
GROUPS, HPG = 2, 6
CMP_LEN, CMP_STRIDE, CMP_HID = 32, 16, 256
NCMP = (T - CMP_LEN) // CMP_STRIDE + 1
NPAD = 32
SEL_SCALE = HD ** -0.5
MLA_SCALE = QK ** -0.5
ALPHA = (2 * 2) ** 0.25
NEG = -1e30
S5G, S5H, S5P = 48, 16, 64
L = 8
CTX = 256
NCL, NCC = T // L, CTX // L
NC = NCC + NCL
GT = 8
S5T = S5G // GT
STRIP = 2 * L + 1
FNW = 256
POOL_WINDOWS = (2, 4, 8, 16)

PAN = 8 * P
CHUNKS = (8, 8, 6)
STAGES = (("mem", 8), ("ffn0", 68), ("mla", 6), ("wo0", 8), ("ffn1", 68), ("kv", 6), ("ffn2", 68),
          ("nsa", 9), ("wo1", 8), ("ctx", 6), ("ffn3", 68), ("even", 16), ("glu", 6), ("ewo", 8), ("odd", 24), ("owo", 8))
COUNT = dict(STAGES)
BASE = {}
_n = 0
for _name, _count in STAGES:
    BASE[_name] = _n
    _n += _count
PANELS = _n


def alibi(n):
    c = 2 ** int(np.floor(np.log2(n)))
    s = [(2.0 ** (-8.0 / c)) ** (i + 1) for i in range(c)]
    s2 = [(2.0 ** (-8.0 / (2 * c))) ** (i + 1) for i in range(2 * c)]
    return np.asarray(s + s2[0::2][: n - c], np.float32)


def constants():
    f = np.float32
    c = {}
    c["ident"] = np.eye(P, dtype=f)
    half = ROPE // 2
    freq = 10000.0 ** (-np.arange(half) / half)
    ang = np.arange(T)[None, :] * freq[:, None]
    cos = np.concatenate([np.cos(ang), np.cos(ang)])
    sin = np.concatenate([-np.sin(ang), np.sin(ang)])
    c["rope"] = np.concatenate([cos, sin, cos, sin]).astype(f)
    perm = np.zeros((ROPE, ROPE), f)
    perm[(np.arange(ROPE) + half) % ROPE, np.arange(ROPE)] = 1
    c["perm"] = perm
    dist = np.arange(P)[:, None] + (T - P) - np.arange(T)[None, :]
    c["causal"] = np.where(dist >= 0, 0, NEG).astype(f)
    slopes = alibi(HEADS).astype(np.float64)
    c["alibi"] = np.stack([np.where(dist >= 0, -m * dist / SEL_SCALE, NEG) for m in slopes]).astype(f)
    t = np.arange(T)
    start = np.arange(NCMP) * CMP_STRIDE
    ok = (start + CMP_LEN - 1)[None, :] <= t[:, None]
    okp = np.zeros((T, NPAD), bool)
    okp[:, :NCMP] = ok
    dc = np.zeros((T, NPAD))
    dc[:, :NCMP] = t[:, None] - (start + (CMP_LEN - 1) * 0.5)[None, :]
    cb = np.stack([np.where(okp, -m * dc / SEL_SCALE, NEG) for m in slopes])
    c["cmpbias"] = cb.reshape(GROUPS, HPG, TT, P, NPAD).transpose(1, 3, 2, 0, 4).reshape(HPG, P, TT * 2 * NPAD).astype(f)
    c["cmpmask"] = okp.reshape(TT, P, NPAD).transpose(1, 0, 2).reshape(P, TT * NPAD).astype(f)
    rows, grid = T // 64, 64
    rr, cc = np.meshgrid(np.arange(rows), np.arange(grid), indexing="ij")
    om = 10000.0 ** (-np.arange(D // 4) / (D // 4))
    rr, cc = rr.reshape(-1, 1), cc.reshape(-1, 1)
    pe = np.concatenate([np.sin(rr * om), np.cos(rr * om), np.sin(cc * om), np.cos(cc * om)], -1)
    c["sincos"] = pe.T.reshape(KD, P, T).transpose(1, 0, 2).reshape(P, KD * T).astype(f)
    k = np.arange(64)
    a = 2 * np.pi * np.outer(k, k) / 64
    bd = np.zeros((P, 2 * P))
    for b in range(2):
        s = slice(64 * b, 64 * b + 64)
        bd[s, 64 * b:64 * b + 64] = np.cos(a)
        bd[s, P + 64 * b:P + 64 * b + 64] = -np.sin(a)
    c["dftc"] = bd.astype(f)
    at = 2 * np.pi * (np.outer(t, t) % T) / T
    norm = 1 / np.sqrt(T * 64)
    dt = np.stack([np.cos(at), np.sin(at)]) * norm
    c["dftt"] = dt.reshape(2, TT, P, T).transpose(2, 0, 1, 3).reshape(P, 2 * TT * T).astype(f)
    inv = np.zeros((4, T))
    for i, w in enumerate(POOL_WINDOWS):
        inv[i] = 1.0 / (np.clip(t + w // 2, 0, T) - np.clip(t - w // 2, 0, T))
    c["poolinv"] = np.ascontiguousarray(np.broadcast_to(inv[None], (P, 4, T)).reshape(P, 4 * T)).astype(f)
    sel = np.zeros((2, P), f)
    sel[0, :64] = 1
    sel[1, 64:] = 1
    c["dirsel"] = sel
    return c

VECTORS = (("norm_g_2", "l (k p) -> (l k) p"), ("ada_b_2", "l (k p) -> (l k) p"), ("final_g_2", "(k p) -> k p"),
           ("s5_glu_b_2", "o (k p) -> (o k) p"), ("pool_scale_2", "o (k p) -> (o k) p"), ("conv_w_2", "o c (k p) -> (o c k) p"),
           ("cmp_b1", "j (k p) -> (j k) p"), ("mla_q_norm_g", "o (k p) -> (o k) p"), ("mla_kv_norm_g", "o (k p) -> (o k) p"),
           ("c_2", "o (k p) -> (o k) p"), ("c_ctx_2", "(k p) -> k p"))
COL_LOADS = 2 + len(VECTORS) + 2

STILES = ((3, 4, 0), (2, 5, 0), (0, 5, 3 * P), (1, 6, 0))
POFF = {3: 0, 2: 4 * P, 0: 7 * P, 1: 8 * P}
TBLOCKS = tuple((0, q * P, q, 0) for q in range(4)) + tuple((1, (q - 1) * P, q, 1) for q in range(1, 4)) + (
    (1, 3 * P, 3, 3),) + tuple((2, (q - 2) * P, q, 2) for q in range(2, 4))
PTOFF = {(q, kb): bank * T + col for bank, col, q, kb in TBLOCKS}

PAD = 16
S5_LOADS = 13
MAGIC = 1.5 * 2.0 ** 23
LN2 = (0.693359375, float(np.log(2.0) - 0.693359375))
TURN = (6.28125, float(np.float32(2 * np.pi - 6.28125)), float(2 * np.pi - 6.28125 - np.float32(2 * np.pi - 6.28125)))
ODD_COLS = tuple(range(0, 4 * P, P)) + tuple((4 + 4 * e + k) * P for k in range(4) for e in range(3)) + tuple(range(2 * D, 3 * D, P))
UP_PARTS = ((0, 4), (0, 2, 4), (0, 3))


def kv_count(g):
    if g < 6:
        return g + 1, g + 1
    return 6 + (g - 6) // 2 + 1, 6 + (g - 5) // 2




def program(nc, A, C, out, scratch):
    ctx = ExitStack()
    with ctx:
        def sb(name, shape, dt=F32):
            return ctx.enter_context(nc.sbuf_tensor(name, shape, dt))

        def sem(name):
            return ctx.enter_context(nc.semaphore(name))

        raw = sb("raw", [P, 4, PAN])
        wh = sb("wh", [P, 2, PAN], F32R)
        wl = sb("wl", [P, 2, PAN], F32R)
        XT = sb("XT", [P, KD, T])
        XH = sb("XH", [P, KD, T], F32R)
        XL = sb("XL", [P, KD, T], F32R)
        IDENT = sb("IDENT", [P, P])
        ONES = sb("ONES", [P, P])
        EPS = sb("EPS", [P, 3])
        COL = sb("COL", [P, 96 + 117])
        POS = sb("POS", [P, 2, CMP_LEN])
        ACC = sb("ACC", [P, T])
        NS = sb("NS", [P, 6, T])
        SQ, SD, RST = NS[:, 0:2, :], NS[:, 2:4, :], NS[:, 4:6, :]
        KM = sb("KM", [P, 2, 2, M])
        VM = sb("VM", [P, 2, MT, M])
        CS = sb("CS", [P, KD, 2])
        MOD = sb("MOD", [P, 2, 24, 2])
        AG = sb("AG", [P, 2, KD, 2])
        L8 = sb("L8", [P, 2, 2, S5G])
        CSS = sb("CSS", [P, 4])
        ps = ctx.enter_context(nc.psum_tensor("ps", [P, 8, T], F32))

        AS = NS[:].rearrange("p s t -> p (s t)")[:, 4 * T:].rearrange("p (s e c) -> p s e c", s=2, e=2)
        YT = VM[:].rearrange("p l m c -> p (l m c)").rearrange("p (s t c) -> p s t c", s=2, t=L)
        YB = KM[:].rearrange("p l j m -> p (l j m)").rearrange("p (j t) -> p j t", j=2)
        SCM = SQ[:, 0, 0:4 * S5G].rearrange("p (a r g) -> p a r g", a=2, r=2)
        SCA = SQ[:, 1, 0:2 * S5G].rearrange("p (r g) -> p r g", r=2)

        def phase():
            return ExitStack()

        with phase() as ph:
            def pb(name, shape, dt=F32):
                return ph.enter_context(nc.sbuf_tensor(name, shape, dt))
            XN = pb("XN", [P, TT, D])
            MN = pb("MN", [P, MT, D])
            MH = pb("MH", [P, KD, M], F32R)
            ML = pb("ML", [P, KD, M], F32R)
            MV = pb("MV", [P, 4, M])
            CN1 = pb("CN1", [96, P])
            CN2 = pb("CN2", [117, P])
            PN = pb("PN", [64, 2, HD])
        with phase() as ph:
            HH = pb("HH", [P, 8, T], F32R)
            HL = pb("HL", [P, 8, T], F32R)
            SG = pb("SG", [P, 2, T])
            HF = pb("HF", [P, 2, T])
            with ExitStack() as ph:
                Z = pb("Z", [S5H, GT, (STRIP - 2) * S5H])
                PS5 = pb("PS5", [P, 3, S5G])
                TS5 = pb("TS5", [P, 12, S5G])
                KI5 = pb("KI5", [P, S5G], I32)
                PC = pb("PC", [P, 2, S5G, L])
                PB = pb("PB", [P, 2, S5G, L])
                FB5 = pb("FB5", [P, 2, S5G])
                BB = pb("BB", [P, 2, S5G, S5H])
                CR = pb("CR", [P, 2, S5G, S5H])
                DT = pb("DT", [S5H, S5G])
                PW = RST.rearrange("p s t -> p (s t)")[:, 0:2 * (L + 1) * S5G].rearrange("p (r k g) -> p r k g", r=2, k=L + 1)
                T1 = SQ.rearrange("p s t -> p (s t)")
                T2 = SD.rearrange("p s t -> p (s t)")
                DD = ACC[0:S5H, 0:GT * S5H].rearrange("p (g h) -> p g h", g=GT)
                BK = pb("BK", [P, 2, GT, P])
                BT = pb("BT", [P, 2, GT, P])
                SW = pb("SW", [P, 2, GT, STRIP * S5H])
                flat = SW[:].rearrange("p a b c -> p (a b c)")
                BN = flat[:, 0:1536].rearrange("p (r g h) -> p r g h", r=2, g=S5G)
                CN = flat[:, 1536:3072].rearrange("p (r t d q) -> p r t d q", r=2, t=6, d=2)
                LAMN = flat[0:S5G, 3072:3328].rearrange("g (r c) -> g r c", r=2)
                LSN = flat[0:2, 3328:3328 + S5G]
                DN = flat[0:S5G, 3400:3400 + S5H]
                DSEL = flat[0:2, 3500:3500 + P]
        with phase() as ph:
            O = pb("O", [P, TT, D])
            PR = pb("PR", [P, 2, 1280])
            PT = pb("PT", [P, 2, 1280])
            MX = pb("MX", [P, 2, TT])
            NB = pb("NB", [P, 2, TT])
            SM = pb("SM", [P, 2, TT])
            RS = pb("RS", [P, 2, TT])
            QM = pb("QM", [P, 2, T])
            with ExitStack() as ph:
                ROT = pb("ROT", [P, T])
                PERM = pb("PERM", [ROPE, ROPE])
                CAUS = pb("CAUS", [P, T])
                CQ = pb("CQ", [P, 2, T])
                CKV = pb("CKV", [P, T])
                KR = ACC[0:ROPE, :]
                KT = pb("KT", [QK, HEADS, T])
                V = pb("V", [P, TT, TOKW])
                WUKV = pb("WUKV", [P, 2, HEADS, HD])
                WQ = pb("WQ", [P, 2, 2, P])
                QT = pb("QT", [QK, 2, T])
                RT = pb("RT", [QK, 2, T])
                KR2 = RT[0:ROPE]
            with ExitStack() as mid:
                def mb(name, shape, dt=F32):
                    return mid.enter_context(nc.sbuf_tensor(name, shape, dt))
                with ExitStack() as ph:
                    AW = pb("AW", [P, 2, KD, 2 * P])
                KX = mb("KX", [P, 2, GROUPS, 2, T], F32R)
                KS = mb("KS", [P, T])
                KW = mb("KW", [P, T])
                VS = mb("VS", [P, TT, P])
                VW = mb("VW", [P, TT, P])
                KCB = mb("KCB", [P, 2 * NPAD])
                VCB = mb("VCB", [2 * NPAD, P])
                with ExitStack() as ph:
                    ZC = pb("ZC", [P, 2, T])
                    VT = pb("VT", [P, 2, T])
                    W1 = (AW[:].rearrange("p s k c -> p (s k) c"), pb("W1", [P, CMP_LEN // 2, CMP_HID])[:])
                    ZB = pb("ZB", [P, 2, CMP_LEN // 2, GROUPS, NPAD])
                    H1 = pb("H1", [P, 2, 2, GROUPS, NPAD])
                    W2 = pb("W2", [P, 2, 2, HD])
                with ExitStack() as ph:
                    QP = pb("QP", [P, HPG, T])
                    QS = pb("QS", [P, 2, GROUPS, T], F32R)
                    BIAS = pb("BIAS", [P, 2, GROUPS, T])
                    CB = pb("CB", [P, 2, TT * GROUPS * NPAD])
                    CMASK = pb("CMASK", [P, TT * NPAD])
                    SC = pb("SC", [P, TT, GROUPS, NPAD])
                    MC = pb("MC", [P, TT, GROUPS])
                    SMC = pb("SMC", [P, TT, GROUPS])
                    GTT = pb("GTT", [HEADS * 3, T])
                    G = pb("G", [P, 3, HPG, TT, GROUPS])
                    PTC = pb("PTC", [2 * NPAD, T])
                    W4 = pb("W4", [P, 2, TT])
        with phase() as ph:
            U = pb("U", [P, S5G, NCL])
            H = pb("H", [P, 2, S5G, NCL + 1])
            UT = H[:].rearrange("p r g c -> p (r g c)")[:, 0:6 * T].rearrange("p (j t c) -> p j t c", j=6, t=L)
            ZS = pb("ZS", [P, KD, T])
            with ExitStack() as late:
                def lb(name, shape, dt=F32):
                    return late.enter_context(nc.sbuf_tensor(name, shape, dt))
                UB = lb("UB", [P, 2, T])
                FB = UB
                with ExitStack() as ph:
                    FA = pb("FA", [P, TT, 2, 2 * P])
                    DFTT = pb("DFTT", [P, 2, TT, T])
                    DFTC = pb("DFTC", [P, 2 * P])
                    FW = pb("FW", [P, 2, P])
            with ExitStack() as ph:
                WB = pb("WB", [P, 2, GT, P])
                WA = pb("WA", [P, 2, 2, GT, P])
                SS = pb("SS", [P, 2, 2, GT, NCL])
                MM = pb("MM", [P, 2, GT, P])
            WT = [WA[:, 0], WA[:, 1], WB[:], MM[:], U[:].rearrange("p g c -> p (g c)")[:, 0:2 * GT * P].rearrange("p (r g c) -> p r g c", r=2, g=GT),
                  WA[:, 0]]
            YS = NS[:].rearrange("p s t -> p (s t)").rearrange("p (g c) -> p g c", g=S5G)
            with ExitStack() as ph:
                pb("odd_results", [P, 6, T])
                YH = pb("YH", [P, KD, T], F32R)
                YL = pb("YL", [P, KD, T], F32R)
        with phase() as ph:
            pb("feed_forward", [P, 20, T])
            SCT = pb("SCT", [P, KD, T])
            NT = SCT
            with ExitStack() as ph:
                CH = pb("CH", [P, KD, CTX], F32R)
                CL = pb("CL", [P, KD, CTX], F32R)
                CXN = pb("CXN", [P, 2, D])
                CXT = pb("CXT", [P, KD, CTX])
                UTC = pb("UTC", [P, 6, L, NCC])
            with ExitStack() as ph:
                UC = pb("UC", [P, S5G, NCC])
                HC = pb("HC", [P, 2, S5G, NCC + 1])
                BS = pb("BS", [P, 3, 2, GT, P])
        with phase() as ph:
            pb("s5_tables", [P, S5G, NCL])
            YA = pb("YA", [P, 6, T])
            YF = pb("YF", [P, 2, T])
            SIG = pb("SIG", [P, 2, T])
        with phase() as ph:
            with ExitStack() as ph2:
                NO = ph2.enter_context(nc.sbuf_tensor("NO", [P, KD, T], F32))
            PU = pb("PU", [P, 4, PAD + T + PAD])
            PS = pb("PS", [P, 2, PAD + T + PAD])
            PP = pb("PP", [P, 2, T])
            YQ = pb("YQ", [P, 2, T])
            PINV = pb("PINV", [P, 4, T])
            PWT = pb("PWT", [P, 4, P])
            CG = pb("CG", [P, 2, T])
            CV = pb("CV", [P, 2, T + 2])
            CX = pb("CX", [P, 2, T])
            YO = pb("YO", [P, KD, T])
            ZO = pb("ZO", [P, 2, T])
        with phase() as ph:
            XO = pb("XO", [P, TT, D])

        raw_in = [sem(f"raw_in{s}") for s in range(4)]
        sp_in = [sem(f"sp_in{s}") for s in range(2)]
        pool_in = [sem(f"pool_in{s}") for s in range(3)]
        w_hi = sem("w_hi")
        w_lo = sem("w_lo")
        pe_panel = sem("pe_panel")
        taken = [sem(f"taken{s}") for s in range(4)]
        x_split = sem("x_split")
        x_dve = sem("x_dve")
        x_hi = sem("x_hi")
        tr = sem("tr")
        tr_done = sem("tr_done")
        setup = sem("setup")
        ident_in = sem("ident_in")
        x_in = sem("x_in")
        mem_in = sem("mem_in")
        col_in = sem("col_in")
        mem_hi = sem("mem_hi")
        mem_split = sem("mem_split")
        vm_ps = sem("vm_ps")
        vm_ready = sem("vm_ready")
        h_ready = sem("h_ready")
        ln_acc = sem("ln_acc")
        ln_mu = sem("ln_mu")
        ln_c = sem("ln_c")
        sq_ready = sem("sq_ready")
        sq_used = sem("sq_used")
        sd_ready = sem("sd_ready")
        rstd_ready = sem("rstd_ready")
        ln_n = sem("ln_n")
        ln_hi = sem("ln_hi")
        ln_aff = sem("ln_aff")
        mla_in_s = sem("mla_in_s")
        cq_norm = sem("cq_norm")
        kr_ps = sem("kr_ps")
        kr_rot = sem("kr_rot")
        kr_act = sem("kr_act")
        kr_dve = sem("kr_dve")
        kv_ps = sem("kv_ps")
        kv_act = sem("kv_act")
        kv_dve = sem("kv_dve")
        q_ps = sem("q_ps")
        q_nope = sem("q_nope")
        q_rot = sem("q_rot")
        q_rope = sem("q_rope")
        s_ps = sem("s_ps")
        s_sb = sem("s_sb")
        nb_ready = sem("nb_ready")
        p_ready = sem("p_ready")
        t_ps = sem("t_ps")
        pt_act = sem("pt_act")
        pt_dve = sem("pt_dve")
        pv_ps = sem("pv_ps")
        rs_ready = sem("rs_ready")
        o_done = sem("o_done")
        mix_ps = sem("mix_ps")
        mix_hi = sem("mix_hi")
        dve_link = sem("dve_link")
        pool_link = sem("pool_link")
        s5_in = sem("s5_in")
        s5_tr = sem("s5_tr")
        cr_out = sem("cr_out")
        s5_dve = sem("s5_dve")
        sin_in = sem("sin_in")
        sin_out = sem("sin_out")
        f_ready = sem("f_ready")
        bk_ready = sem("bk_ready")
        s5_t = sem("s5_t")
        bt_act = sem("bt_act")
        bt_dve = sem("bt_dve")
        s5_z = sem("s5_z")
        z_out = sem("z_out")
        s5_out = sem("s5_out")
        cs_ready = sem("cs_ready")
        ada_part = sem("ada_part")
        ada_used = sem("ada_used")
        mod_ready = sem("mod_ready")
        w1_in = sem("w1_in")
        zeros = sem("zeros")
        vt_ps = sem("vt_ps")
        vt_out = sem("vt_out")
        zb_ready = sem("zb_ready")
        hid_ps = sem("hid_ps")
        gelu_out = sem("gelu_out")
        kc_ps = sem("kc_ps")
        kc_out = sem("kc_out")
        g_ps = sem("g_ps")
        g_out = sem("g_out")
        cmask_in = sem("cmask_in")
        qs_hi = sem("qs_hi")
        qs_ready = sem("qs_ready")
        kx_hi = sem("kx_hi")
        kx_ready = sem("kx_ready")
        c_sc = sem("c_sc")
        c_sub = sem("c_sub")
        c_exp = sem("c_exp")
        c_mask = sem("c_mask")
        c_sum = sem("c_sum")
        c_p = sem("c_p")
        c_t = sem("c_t")
        c_pt = sem("c_pt")
        c_pv = sem("c_pv")
        c_o = sem("c_o")
        w4_ready = sem("w4_ready")
        cx_in = sem("cx_in")
        sct_ready = sem("sct_ready")
        cx_sd = sem("cx_sd")
        cx_n = sem("cx_n")
        cx_ps = sem("cx_ps")
        cx_f = sem("cx_f")
        cx_hi = sem("cx_hi")
        cx_split = sem("cx_split")
        shuffle_out = sem("shuffle_out")
        shuffle_in = sem("shuffle_in")
        b_ps = sem("b_ps")
        h_act = sem("h_act")
        h_dve = sem("h_dve")
        dft_in = sem("dft_in")
        fnet_ps = sem("fnet_ps")
        fnet_out = sem("fnet_out")
        scan = sem("scan")
        ss_act = sem("ss_act")
        ss_dve = sem("ss_dve")
        m_ps = sem("m_ps")
        w_in = sem("w_in")
        y_ps = sem("y_ps")
        y_sb = sem("y_sb")
        y_out = [sem(f"y_out{s}") for s in range(2)]
        ya_ready = sem("ya_ready")
        ya_hi = sem("ya_hi")
        p1_ready = sem("p1_ready")
        y_full = sem("y_full")
        y_ready = sem("y_ready")
        odd_in = sem("odd_in")
        odd_zero = sem("odd_zero")
        pool_ready = sem("pool_ready")
        pw_ps = sem("pw_ps")
        yc_ready = sem("yc_ready")
        out_ps = sem("out_ps")
        out_sb = sem("out_sb")
        out_done = sem("out_done")

        LN_SQ = {"ffn0": 0, "mla": 8, "wo0": 11, "ffn1": 19, "ffn2": 27, "wo1": 35, "ffn3": 43, "even": 51, "odd": 59, "final": 67}
        LN_NO = {"ffn0": 0, "wo0": 1, "ffn1": 2, "ffn2": 3, "wo1": 4, "ffn3": 5, "even": 6, "odd": 7, "final": 8}
        HI_NO = {"ffn0": 0, "wo0": 1, "ffn1": 2, "ffn2": 3, "wo1": 4, "even": 5, "odd": 6}
        XS = {"ffn0": 0, "mla": 8, "wo0": 14, "ffn1": 22, "kv": 28, "ffn2": 28, "nsa": 34, "wo1": 40, "ffn3": 48, "even": 54,
              "glu": 60, "odd": 66}
        XD = {"mla": 0, "ffn1": 2, "kv": 4, "ffn2": 4, "nsa": 6, "ffn3": 8, "even": 10, "odd": 12}
        BY_DVE = (3, 7)
        LN_COL = {"ffn0": 0, "wo0": 8, "ffn1": 16, "ffn2": 24, "wo1": 32, "ffn3": 40}

        IN = {"q": 0, "bias": 3 * 16 * HEADS // 2, "ada": 0, "b": 16 * 12}
        IN["y"] = IN["bias"] + 32 * HPG // 2
        IN["m"] = IN["b"] + 2 * 16 * S5T // 3

        def wait(eng, s, value):
            if not (isinstance(value, int) and value <= 0):
                eng.wait_ge(s, value)

        def taken_at(stage, j, i=0):
            p = BASE[stage] + j
            return taken[p % 4], p // 4 + 1 + i

        block = ctx.enter_context(nc.Block())

        def ada_conditions(layer, n):
            return 2 if layer == 0 and n < 8 else 1

        def nothing(k):
            pass

        @block.sync
        def _(sp):
            def load(stage, j, i, src, nk=8):
                p = BASE[stage] + j
                if not (isinstance(i, int) and p + 4 * i < 4):
                    sp.wait_ge(w_lo, p - 3 + 4 * i)
                dst = raw[:, p % 4, 0:nk * P].rearrange("p (k c) -> p k c", k=nk)
                sp.dma_start(dst, src).then_inc(raw_in[p % 4], 16)

            def rows(w):
                return w.rearrange("(k p) n -> p k n", p=P)

            def plain(stage, w, cols, part=slice(None)):
                v = rows(w)
                for j, c in list(enumerate(cols))[part]:
                    load(stage, j, 0, v[:, :, c:c + P], v.shape[1])

            def ffn(stage, layer, half):
                gu, down = rows(A["ffn_w_gu"][layer, half]), rows(A["ffn_w_down"][layer, half])
                off, f0 = 0, 0
                for nf in CHUNKS:
                    with sp.Fori(0, nf // 2) as i:
                        for j in range(4):
                            c = (j % 2) * DFF + (f0 + j // 2) * P
                            load(stage, off + j, i, gu[:, :, bass.ds(i * (2 * P) + c, P)])
                    off += 2 * nf
                    with sp.Fori(0, KD // 4) as i:
                        for j in range(4):
                            load(stage, off + j, i, down[:, f0:f0 + nf, bass.ds(i * (4 * P) + j * P, P)], nf)
                    off += KD
                    f0 += nf

            sp.dma_start(IDENT[:], C["ident"]).then_inc(ident_in, 16)
            sp.dma_start(MN[:], A["mem"][0].rearrange("(m p) d -> p m d", p=P)).then_inc(mem_in, 16)
            vectors = [(CN1[0:48, :], A["ln_g"].rearrange("l i (k p) -> (l i k) p", p=P)),
                       (CN1[48:96, :], A["ln_b"].rearrange("l i (k p) -> (l i k) p", p=P))]
            vectors += [(PN[:, b, :], A["cmp_pos"].rearrange("j l d -> (j l) d")) for b in range(2)]
            at = 0
            for name, view in VECTORS:
                v = A[name].rearrange(view, p=P)
                vectors.append((CN2[at:at + v.shape[0], :], v))
                at += v.shape[0]
            for j in range(8):
                if j == 2:
                    sp.dma_start(XN[:], A["x"][0].rearrange("(t p) d -> p t d", p=P)).then_inc(x_in, 16)
                load("mem", j, 0, rows(A["w_mem_kv"][j // 4])[:, :, (j % 4) * P:(j % 4 + 1) * P])
                if j == 3:
                    for dst, src in vectors:
                        sp.dma_start(dst, src).then_inc(col_in, 16)
            ffn("ffn0", 0, 0)
            plain("mla", A["mla_w_in"][0], (0, P, QR, QR + P, QR + P + ROPE, QR + 2 * P + ROPE))
            sp.wait_ge(pe_panel, BASE["mla"])
            sp.wait_ge(s5_out, 64 * S5T)
            for e in range(2):
                sp.dma_start(WUKV[:, e], A["mla_w_ukv"][0].rearrange("p (h e c) -> p e h c", e=2, c=HD)[:, e]).then_inc(mla_in_s, 16)
            sp.dma_start(ROT[:], C["rope"]).then_inc(mla_in_s, 16)
            sp.dma_start(PERM[:], C["perm"]).then_inc(mla_in_s, 16)
            sp.dma_start(CAUS[:], C["causal"]).then_inc(mla_in_s, 16)
            plain("wo0", A["w_out"][0], range(0, D, P), slice(0, 4))
            wuq = A["mla_w_uq"][0].rearrange("(k p) (h c) -> p k h c", p=P, c=QK)

            def load_q(i, s):
                w = wuq[:, :, bass.ds(2 * i + s, 1), :].rearrange("p k o c -> p k (o c)")
                half = HD + ROPE // 2
                if not isinstance(i, int):
                    sp.wait_ge(q_ps, 2 * i + s - 1)
                sp.dma_start(WQ[:, s, :, 0:QK], w).then_inc(sp_in[s], 16)
                sp.dma_start(WQ[:, s, :, QK:QK + ROPE // 2], w[:, :, half:QK]).then_inc(sp_in[s], 16)
                sp.dma_start(WQ[:, s, :, QK + ROPE // 2:P], w[:, :, HD:half]).then_inc(sp_in[s], 16)
            for s in range(2):
                load_q(0, s)
            with sp.Fori(1, HEADS // 2) as i:
                for s in range(2):
                    load_q(i, s)
            plain("wo0", A["w_out"][0], range(0, D, P), slice(4, 8))
            ffn("ffn1", 0, 1)
            plain("kv", A["nsa_w_kv"], range(0, 6 * P, P))
            ffn("ffn2", 1, 0)
            nsa = A["nsa_w_in"][0]
            plain("nsa", nsa, (TOKW, TOKW + 3 * HEADS, TOKW + 3 * HEADS + P) + tuple(range(0, TOKW, P)))
            alibi_pairs = C["alibi"].rearrange("(g j) p t -> j p g t", g=GROUPS)
            sp.wait_ge(pe_panel, BASE["nsa"])
            sp.dma_start(CMASK[:], C["cmpmask"]).then_inc(cmask_in, 16)

            def load_bias(j, s):
                bias = alibi_pairs[bass.ds(j, 1)].rearrange("o p g t -> p (o g) t")
                cmp_bias = C["cmpbias"][bass.ds(j, 1)].rearrange("o p n -> p (o n)")
                if not isinstance(j, int):
                    sp.wait_ge(s_sb, 4 * j + 12)
                    sp.wait_ge(c_sc, 2 * j - 3)
                sp.dma_start(BIAS[:, s], bias).then_inc(sp_in[s], 16)
                sp.dma_start(CB[:, s], cmp_bias).then_inc(sp_in[s], 16)
            for s in range(2):
                load_bias(s, s)
            plain("wo1", A["w_out"][1], range(0, D, P), slice(0, 4))
            with sp.Fori(1, HPG // 2) as i:
                for s in range(2):
                    load_bias(2 * i + s, s)
            plain("wo1", A["w_out"][1], range(0, D, P), slice(4, 8))
            plain("ctx", A["even_w_in_2"][0], range(0, 6 * P, P))
            ffn("ffn3", 1, 1)
            plain("even", A["even_w_in_2"][0], range(0, 2 * D, P))
            glu = A["s5_glu_w_2"][0]
            plain("glu", glu, range(0, 6 * P, P), slice(0, 4))
            y_rows = scratch["s5_y"].rearrange("(g h) t c -> t h g c", h=S5H)
            y_chunks = scratch["s5_y"].rearrange("(j p) t c -> j p (t c)", p=P)
            for t in range(S5T + 1):
                if t < S5T:
                    sp.wait_ge(y_sb, t + 1)
                    for e in range(L):
                        sp.dma_start(y_rows[e][:, t * GT:(t + 1) * GT], YS[e * S5H:(e + 1) * S5H, t * GT:(t + 1) * GT]).then_inc(y_out[t % 2], 16)
                if t > 0:
                    sp.wait_ge(y_out[(t - 1) % 2], 16 * L * ((t - 1) // 2 + 1))
                    wait(sp, ya_ready, t - 2)
                    sp.dma_start(YT[:, (t - 1) % 2].rearrange("p t c -> p (t c)"), y_chunks[t - 1]).then_inc(sp_in[(t - 1) % 2], 16)
            plain("glu", glu, range(0, 6 * P, P), slice(4, 6))
            plain("ewo", A["even_w_out_2"][0], range(0, D, P))
            plain("odd", A["odd_w_in_2"][0], ODD_COLS)
            plain("owo", A["odd_w_out_2"][0], range(0, D, P))
            rows_out = out[0].rearrange("(t p) d -> p t d", p=P)
            for half in range(2):
                sp.wait_ge(out_sb, 4 * half + 4)
                sp.dma_start(rows_out[:, :, half * T:(half + 1) * T], XO[:, :, half * T:(half + 1) * T]).then_inc(out_done, 16)
            sp.wait_ge(out_done, 32)

        @block.tensor
        def _(pe):
            def panel(stage, j, i, hi, lo, nk=8, n=T, need=None):
                p = BASE[stage] + j
                pe.wait_ge(w_lo, p + 1 + 4 * i)
                if not (isinstance(i, int) and p + 4 * i < 4):
                    pe.wait_ge(taken[p % 4], p // 4 + i)
                for k in range(nk):
                    if need is not None:
                        pe.wait_ge(*need(k))
                    for a, (w, x) in enumerate(((wh, hi), (wl, hi), (wh, lo))):
                        mm = pe.matmul(ps[:, p % 4, 0:n], w[:, p % 2, k * P:(k + 1) * P], x[:, k, 0:n],
                                       start=(k == 0 and a == 0), stop=(k == nk - 1 and a == 2))
                mm.then_inc(pe_panel, 1)

            def pair(stage, hi, lo, need, nk=8, n=T):
                p, behind = BASE[stage], 3
                pe.wait_ge(w_lo, p + 2)
                for e in range(2):
                    if p + e >= 4:
                        pe.wait_ge(taken[(p + e) % 4], (p + e) // 4)
                for k in range(nk + behind):
                    for e, c in ((0, k), (1, k - behind)):
                        if not 0 <= c < nk:
                            continue
                        for a, (w, x) in enumerate(((wh, hi), (wl, hi), (wh, lo))):
                            if e == 0 and a != 1:
                                pe.wait_ge(*need(c)[a // 2])
                            mm = pe.matmul(ps[:, (p + e) % 4, 0:n], w[:, (p + e) % 2, c * P:(c + 1) * P], x[:, c, 0:n],
                                           start=(c == 0 and a == 0), stop=(c == nk - 1 and a == 2))
                        if c == nk - 1:
                            mm.then_inc(pe_panel, 1)

            def panels(stage, count, need, hi=XH, lo=XL, nk=8, after=None):
                pair(stage, hi, lo, need, nk)
                for j in range(2, count):
                    panel(stage, j, 0, hi, lo, nk)
                    if after is not None:
                        after(j)

            def split_at(stage):
                no = {"mla": "ffn0", "ffn1": "wo0", "kv": "ffn1", "nsa": "ffn2", "ffn3": "wo1", "odd": "odd"}.get(stage)

                def all_of(k):
                    if stage in XD and k in BY_DVE:
                        return x_dve, XD[stage] + BY_DVE.index(k) + 1
                    return x_split, XS[stage] + k + 1 - (sum(e < k for e in BY_DVE) if stage in XD else 0)
                return lambda k: (all_of(k) if no is None else (ln_hi, 8 * HI_NO[no] + k + 1), all_of(k))

            def ffn(stage, fill):
                no = int(stage[3])
                off, f0 = 0, 22 * no
                at = 0
                for c, nf in enumerate(CHUNKS):
                    for a, b in zip(UP_PARTS[c], UP_PARTS[c][1:]):
                        if c == 0:
                            pair(stage, XH, XL, split_at(stage))
                            for j in (2, 3):
                                panel(stage, j, 0, XH, XL)
                            a = 1
                        with pe.Fori(a, b) as i:
                            for j in range(4):
                                panel(stage, off + j, i, XH, XL)
                        fill(at)
                        at += 1
                    off += 2 * nf
                    need = lambda k: (h_ready, f0 + k + 3)
                    with pe.Fori(0, KD // 4) as i:
                        for j in range(4):
                            panel(stage, off + j, i, HH, HL, nf, need=need if j == 0 else None)
                    if c < 2:
                        fill(at)
                        at += 1
                    off += KD
                    f0 += nf

            def norm(stage, beside=nothing):
                no, q0 = LN_NO[stage], LN_SQ[stage]
                beside(0)
                pe.wait_ge(ln_acc, 7 * no + 7)
                pe.matmul(ps[:, 4, :], ONES[:], ACC[:], start=True, stop=False)
                pe.wait_ge(*taken_at(stage, COUNT[stage] - 1))
                pe.matmul(ps[:, 4, :], ONES[:], XT[:, KD - 1, :], start=False, stop=True).then_inc(ln_mu, 1)
                beside(1)
                squares(q0, 8, 5)
                beside(2)

            def square(q0, d, count, bank):
                pe.wait_ge(sq_ready, q0 + d + 1)
                pe.matmul(ps[:, bank, :], ONES[:], SQ[:, (q0 + d) % 2, :], start=d == 0, stop=d == count - 1).then_inc(sq_used, 1)

            def squares(q0, count, bank):
                for d in range(count):
                    square(q0, d, count, bank)

            def probs_t(u, s):
                pe.wait_ge(p_ready, u + 1)
                wait(pe, pt_act, 2 * u)
                wait(pe, pt_dve, u)
                for bank, col, q, kb in TBLOCKS:
                    mm = pe.transpose(ps[:, bank, col:col + P], PR[:, s, POFF[q] + kb * P:POFF[q] + (kb + 1) * P], IDENT[:])
                mm.then_inc(t_ps, 1)

            def pv(u, s, vals):
                pe.wait_ge(pt_act, 2 * u + 2)
                pe.wait_ge(pt_dve, u + 1)
                wait(pe, o_done, u)
                for q in range(TT):
                    for kb in range(q + 1):
                        mm = pe.matmul(ps[:, 7, q * HD:(q + 1) * HD], PT[:, s, PTOFF[q, kb]:PTOFF[q, kb] + P],
                                       vals(kb), start=kb == 0, stop=kb == q)
                mm.then_inc(pv_ps, 1)

            def scores(u, q, keys):
                wait(pe, s_sb, u)
                for t, bank, col in STILES:
                    n = (t + 1) * P
                    mm = pe.matmul(ps[:, bank, col:col + n], q(t), keys(n), start=True, stop=True)
                mm.then_inc(s_ps, 1)

            def mem_scores(u, h, first):
                r = slice((h % 2) * HD, (h % 2) * HD + HD)
                pe.wait_ge(p_ready, u) if not first else wait(pe, s_sb, u)
                for t in range(TT):
                    mm = pe.matmul(ps[:, 4 + t // 2, (t % 2) * M:(t % 2 + 1) * M], QM[r, h // 2, t * P:(t + 1) * P],
                                   KM[r, mem_layer[0], h // 2, :], start=True, stop=True)
                mm.then_inc(s_ps, 1)

            def mem_probs_t(u, s):
                pe.wait_ge(p_ready, u + 1)
                wait(pe, pt_act, 2 * u)
                wait(pe, pt_dve, u)
                for m in range(MT):
                    for t in range(TT):
                        mm = pe.transpose(ps[:, m, t * P:(t + 1) * P], PR[:, s, t * M + m * P:t * M + (m + 1) * P], IDENT[:])
                mm.then_inc(t_ps, 1)

            def mem_pv(u, s, h):
                pe.wait_ge(pt_act, 2 * u + 2)
                pe.wait_ge(pt_dve, u + 1)
                wait(pe, o_done, u)
                for t in range(TT):
                    for m in range(MT):
                        mm = pe.matmul(ps[:, 7, t * HD:(t + 1) * HD], PT[:, s, m * T + t * P:m * T + (t + 1) * P],
                                       VM[:, mem_layer[0], m, h * HD:(h + 1) * HD], start=m == 0, stop=m == MT - 1)
                mm.then_inc(pv_ps, 1)

            def mix_t(base, mix0):
                for k in range(KD):
                    pe.wait_ge(x_split, base + k - 3 if k > 3 else base)
                    for t in range(TT):
                        mm = pe.transpose(ps[:, 4 + k % 4, t * P:(t + 1) * P], O[:, t, k * P:(k + 1) * P], IDENT[:])
                    mm.then_inc(mix_ps, 1)

            def s5_fill(t):
                pe.wait_ge(bk_ready, t + 1)
                wait(pe, z_out, 4 * t)
                for b in range(4):
                    for g in range(4):
                        mm = pe.transpose(ps[:, 4 + b, g * P:(g + 1) * P], BK[:, b // 2, (b % 2) * 4 + g, :], IDENT[:])
                    mm.then_inc(s5_t, 1)
                for b in range(4):
                    if b < 2:
                        pe.wait_ge(bt_act, 2 * t + b + 1)
                    else:
                        pe.wait_ge(bt_dve, 2 * t + b - 1)
                    for e in range(2):
                        g = 2 * b + e
                        for r in range(2):
                            mm = pe.matmul(ps[0:S5H, 4 + b, e * 240:(e + 1) * 240], BB[:, r, t * GT + g, :],
                                           SW[:, r, g, S5H:(STRIP - 1) * S5H], start=r == 0, stop=r == 1)
                    mm.then_inc(s5_z, 1)

            def ada_fill(layer, f):
                if layer == 1 and f == 0:
                    pe.wait_ge(mod_ready, 1)
                for n in (2 * f, 2 * f + 1):
                    pe.wait_ge(ada_part, 12 * layer + n + 1)
                    for c in range(2):
                        for e in range(ada_conditions(layer, n)):
                            m = 2 * n + c
                            mm = pe.matmul(ps[:, 6, 2 * m + e:2 * m + e + 1], AS[:, n % 2, e, c * P:(c + 1) * P], ONES[:, 0:1], start=True, stop=True)
                    mm.then_inc(ada_used, 1)

            def ffn2_fill(f):
                ada_fill(1, f)
                if f == 0:
                    pe.wait_ge(gelu_out, 4)
                    pe.wait_ge(vt_out, 2)
                    for m in range(2):
                        pe.matmul(ps[0:HD, 4, 0:2 * NPAD], W2[:, 0, m, :], H1[:, 0, m].rearrange("p g n -> p (g n)"), start=m == 0, stop=m == 1)
                    for m in range(2):
                        mm = pe.matmul(ps[0:2 * NPAD, 5, 0:HD], H1[:, 1, m].rearrange("p g n -> p (g n)"), W2[:, 1, m, :], start=m == 0, stop=m == 1)
                    mm.then_inc(kc_ps, 1)

            def context_t(j):
                if j == 2:
                    pe.wait_ge(cx_n, 2)
                    for k2 in range(4):
                        for e in range(2):
                            for m in range(MT):
                                k = 2 * k2 + e
                                mm = pe.transpose(ps[:, 4 + k2, e * CTX + m * P:e * CTX + (m + 1) * P], CXN[:, m, k * P:(k + 1) * P], IDENT[:])
                        mm.then_inc(cx_ps, 1)

            def context_in(k):
                for j in ((0,), (1,), (2, 3, 4, 5))[k]:
                    panel("ctx", j, 0, CH, CL, n=CTX, need=(lambda k: (cx_split, k + 1)) if j == 0 else None)

            def b_slot(t):
                return pool_in[t % 3], (IN["b"] if t % 3 < 2 else 0) + 16 * (t // 3 + 1)

            def context_b(t):
                pe.wait_ge(*b_slot(t))
                if t == 0:
                    pe.wait_ge(shuffle_in, 16 * L)
                    pe.wait_ge(cx_f, 8)
                wait(pe, h_act, t - 1)
                wait(pe, h_dve, t - 1)
                for r in range(2):
                    for g in range(GT):
                        mm = pe.matmul(ps[:, 6 + t % 2, (r * GT + g) * NCC:(r * GT + g + 1) * NCC], BS[:, t % 3, r, g, :], UC[:, t * GT + g, :],
                                       start=True, stop=True)
                mm.then_inc(b_ps, 1)

            def context_b_beside(k):
                for t in ((), (0,), (1, 2))[k]:
                    context_b(t)

            mem_layer = [0]

            pe.wait_ge(ident_in, 16)
            pe.wait_ge(mem_in, 16)
            for k2 in range(4):
                for e in range(2):
                    for m in range(MT):
                        k = 2 * k2 + e
                        mm = pe.transpose(ps[:, 4 + k2, e * M + m * P:e * M + (m + 1) * P], MN[:, m, k * P:(k + 1) * P], IDENT[:])
                mm.then_inc(tr, 1)
            for k in range(KD):
                panel("mem", k, 0, MH, ML, n=M, need=(lambda c: (mem_split, c // 2 + 1)) if k == 0 else None)
                if k == 0:
                    pe.wait_ge(x_in, 16)
                if k < 4:
                    pe.wait_ge(mem_split, k + 1)
                else:
                    pe.wait_ge(x_split, k - 3)
                for t in range(TT):
                    mm = pe.transpose(ps[:, 4 + k % 4, t * P:(t + 1) * P], XN[:, t, k * P:(k + 1) * P], IDENT[:])
                mm.then_inc(tr, 1)
            pe.wait_ge(col_in, 16 * COL_LOADS)
            pe.wait_ge(x_split, 5)
            pe.transpose(ps[:, 4, 0:96], CN1[:], IDENT[0:96, 0:96])
            pe.transpose(ps[:, 4, 96:96 + 117], CN2[:], IDENT[0:117, 0:117])
            pe.transpose(ps[:, 4, 256:256 + 64], PN[:].rearrange("a b c -> a (b c)"), IDENT[0:64, 0:64]).then_inc(tr, 1)

            for layer in range(2):
                for j in range(2):
                    pe.wait_ge(*taken_at("mem", 4 * layer + 2 + j))
                    if layer == 0 and j == 0:
                        pe.wait_ge(tr_done, 1)
                        pe.wait_ge(x_split, 8)
                    for m in range(MT):
                        mm = pe.transpose(ps[:, 4 + 2 * layer + j, m * P:(m + 1) * P], MV[:, 2 * layer + j, m * P:(m + 1) * P], IDENT[:])
                    mm.then_inc(vm_ps, 1)

            pe.wait_ge(setup, 2)
            pe.wait_ge(s5_in, 16 * S5_LOADS)
            pe.wait_ge(vm_ready, 4)
            for r in range(2):
                pe.transpose(ps[:, 4, r * S5G:(r + 1) * S5G], LAMN[:, r, :], IDENT[0:S5G, 0:S5G])
            pe.matmul(ps[:, 4, 2 * S5G:3 * S5G], DSEL, LSN, start=True, stop=True)
            pe.transpose(ps[0:S5H, 4, 3 * S5G:4 * S5G], DN, IDENT[0:S5G, 0:S5G]).then_inc(s5_tr, 1)
            for n in range(12):
                mm = pe.transpose(ps[:, 5 + n // 4, (n % 4) * P:(n % 4 + 1) * P], CN[:, n // 6, n % 6].rearrange("p d q -> p (d q)"), IDENT[:])
                if n % 4 == 3:
                    mm.then_inc(s5_tr, 1)
            ffn("ffn0", s5_fill)
            pe.wait_ge(z_out, 4 * S5T)
            norm("ffn0")
            def mla_squares(j):
                if j == 2:
                    squares(LN_SQ["mla"], 2, 4)
                if j == 3:
                    squares(LN_SQ["mla"] + 2, 1, 5)
                if j == 4:
                    pe.wait_ge(mla_in_s, 80)
                    pe.wait_ge(*taken_at("mla", 3))
                    pe.wait_ge(vm_ready, 4)
                    pe.matmul(ps[ROPE:2 * ROPE, 6, :], PERM[:], KR, start=True, stop=True).then_inc(kr_ps, 1)

            panels("mla", 6, split_at("mla"), after=mla_squares)
            def project_q(h, s, turn):
                pe.wait_ge(sp_in[s], 48 * turn + 48)
                wait(pe, q_nope, h)
                wait(pe, q_rot, 2 * h)
                for k in range(2):
                    mm = pe.matmul(ps[:, 3, :], WQ[:, s, k, :], CQ[:, k, :], start=k == 0, stop=k == 1)
                mm.then_inc(q_ps, 1)

            pe.wait_ge(cq_norm, 2)
            pe.wait_ge(*taken_at("mla", 3))
            project_q(0, 0, 0)
            pe.wait_ge(cq_norm, 3)
            pe.wait_ge(kr_rot, 1)
            for g in range(14):
                if g < 6:
                    lhs, rhs, n = WUKV[:, 0, 2 * g:2 * g + 2, :].rearrange("p h c -> p (h c)"), CKV[:], T
                else:
                    t, half = (g - 6) // 2, g % 2
                    lhs, rhs, n = CKV[:, t * P:(t + 1) * P], WUKV[:, 1, 6 * half:6 * half + 6, :], 6 * HD
                if g >= 4:
                    pe.wait_ge(kv_act, kv_count(g - 4)[0])
                    pe.wait_ge(kv_dve, kv_count(g - 4)[1])
                pe.matmul(ps[:, 4 + g % 4, 0:n], lhs, rhs, start=True, stop=True).then_inc(kv_ps, 1)
                if g == 5:
                    project_q(1, 1, 0)

            def mla_scores(h, s):
                pe.wait_ge(q_nope, h + 1)
                pe.wait_ge(q_rope, h + 1)
                scores(h, lambda t: QT[:, s, t * P:(t + 1) * P],
                       lambda n: KT[:, bass.ds(h, 1), 0:n].rearrange("p o n -> p (o n)"))

            def mla_pv(h, s):
                pv(h, s, lambda kb: V[:, kb, bass.ds(h * HD, HD)])

            pe.wait_ge(kv_act, kv_count(13)[0])
            pe.wait_ge(kv_dve, kv_count(13)[1])
            pe.wait_ge(kr_act, 1)
            pe.wait_ge(kr_dve, 1)
            pe.wait_ge(*taken_at("mla", 5))
            pe.wait_ge(*taken_at("mla", 2))
            mla_scores(0, 0)
            project_q(2, 0, 1)
            mla_scores(1, 1)

            def mla_unit(u, s, turn=None, begin=False):
                probs_t(u, s)
                if turn is not None:
                    project_q(u + 3, 1 - s, turn)
                if not begin:
                    mla_pv(u - 1, 1 - s)
                mla_scores(u + 2, s)

            mla_unit(0, 0, 1, begin=True)
            mla_unit(1, 1, 2)
            with pe.Fori(1, HEADS // 2 - 2) as i:
                mla_unit(2 * i, 0, i + 1)
                mla_unit(2 * i + 1, 1, i + 2)
            mla_unit(8, 0, 5)
            mla_unit(9, 1)
            for h in range(2):
                u = 10 + h
                probs_t(u, h)
                mla_pv(u - 1, 1 - h)
                mem_scores(u + 2, h, h == 0)
            for h in range(MEM_HEADS):
                u = 12 + h
                mem_probs_t(u, u % 2)
                if h == 0:
                    mla_pv(11, 1)
                else:
                    mem_pv(u - 1, 1 - u % 2, h - 1)
                if h < 2:
                    mem_scores(u + 2, h + 2, False)
            mem_pv(15, 1, 3)
            pe.wait_ge(o_done, 16)
            mix_t(XS["wo0"], 0)
            panels("wo0", 8, split_at("wo0"))
            norm("wo0")
            ffn("ffn1", lambda f: ada_fill(0, f))
            norm("ffn1")

            panels("kv", 6, split_at("kv"))
            for e in range(2):
                pe.wait_ge(*taken_at("kv", 3 + 2 * e))
                for t in range(TT):
                    mm = pe.transpose(ps[:, 4 + e, t * P:(t + 1) * P], VT[:, e, t * P:(t + 1) * P], IDENT[:])
                mm.then_inc(vt_ps, 1)
            pe.wait_ge(w1_in, 96)
            pe.wait_ge(mod_ready, 1)
            for j in range(2):
                pe.wait_ge(zb_ready, j + 1)
                for m in range(2):
                    for l in range(CMP_LEN // 2):
                        mm = pe.matmul(ps[:, 6 + j, m * 2 * NCMP:(m + 1) * 2 * NCMP], W1[j][:, l, m * P:(m + 1) * P], ZB[:, j, l, :, 0:NCMP],
                                       start=l == 0, stop=l == CMP_LEN // 2 - 1)
                    mm.then_inc(hid_ps, 1)

            ffn("ffn2", ffn2_fill)
            pe.wait_ge(kc_out, 2)
            norm("ffn2")
            def gates_t(j):
                if j == 2:
                    pe.wait_ge(*taken_at("nsa", 0))
                    for t in range(TT):
                        mm = pe.transpose(ps[:, 4, t * 36:(t + 1) * 36], GTT[:, t * P:(t + 1) * P], IDENT[0:36, 0:36])
                    mm.then_inc(g_ps, 1)

            panels("nsa", 9, split_at("nsa"), after=gates_t)

            def nsa_scores(u, k, q):
                wait(pe, s_sb, u)
                for t, bank, col in STILES:
                    n = (t + 1) * P
                    for e in range(2):
                        mm = pe.matmul(ps[:, bank, col:col + n], QS[:, q, k % 2, t * P:(t + 1) * P], KX[:, k // 2, k % 2, e, 0:n], start=e == 0, stop=e == 1)
                mm.then_inc(s_ps, 1)

            def nsa_pv(u, k):
                vals = (VS, VW)[k // 2]
                pv(u, k % 2, lambda kb: vals[:, kb, (k % 2) * HD:(k % 2 + 1) * HD])

            def cmp_scores(u, j):
                wait(pe, s_sb, u)
                for t in range(TT):
                    pe.matmul(ps[:, 6, (4 + t) * 2 * NPAD:(5 + t) * 2 * NPAD], QP[:, bass.ds(j, 1), t * P:(t + 1) * P].rearrange("p o t -> p (o t)"), KCB[:], start=True, stop=True)

            def cmp_t(j):
                pe.wait_ge(c_p, j + 1)
                wait(pe, c_o, j)
                for t in range(TT):
                    mm = pe.transpose(ps[0:2 * NPAD, 3, t * P:(t + 1) * P], SC[:, t].rearrange("p g n -> p (g n)"), IDENT[:])
                mm.then_inc(c_t, 1)

            def cmp_pv(j):
                pe.wait_ge(c_pt, j + 1)
                for t in range(TT):
                    mm = pe.matmul(ps[:, 3, t * P:(t + 1) * P], PTC[:, t * P:(t + 1) * P], VCB[:], start=True, stop=True)
                mm.then_inc(c_pv, 1)

            for j in range(5, 9):
                pe.wait_ge(*taken_at("nsa", j))
            pe.wait_ge(g_out, 1)
            pe.wait_ge(kx_ready, 4)
            pe.wait_ge(qs_ready, 2)
            nsa_scores(16, 0, 0)
            nsa_scores(17, 1, 0)
            pe.wait_ge(kx_ready, 8)

            def nsa_pair(j, q, last=False):
                for k in range(4):
                    u = 16 + 4 * j + k
                    first = isinstance(j, int) and j == 0
                    probs_t(u, k % 2)
                    if k > 0 or not first:
                        nsa_pv(u - 1, (k - 1) % 4)
                    if k == 1:
                        cmp_scores(u + 2, j)
                    if k < 2:
                        nsa_scores(u + 2, k + 2, q)
                    elif not last:
                        if k == 2:
                            pe.wait_ge(qs_ready, 2 * j + 4)
                        nsa_scores(u + 2, k - 2, 1 - q)
                    else:
                        mem_scores(u + 2, k - 2, k == 2)
                    if k == 0 and not first:
                        cmp_t(j - 1)
                    if k == 1 and not first:
                        cmp_pv(j - 1)

            nsa_pair(0, 0)
            nsa_pair(1, 1)
            with pe.Fori(1, HPG // 2 - 1) as i:
                for q in range(2):
                    nsa_pair(2 * i + q, q)
            mem_layer[0] = 1
            nsa_pair(4, 0)
            nsa_pair(5, 1, last=True)
            for h in range(MEM_HEADS):
                u = 40 + h
                mem_probs_t(u, u % 2)
                if h == 0:
                    nsa_pv(39, 3)
                else:
                    mem_pv(u - 1, 1 - u % 2, h - 1)
                if h < 2:
                    mem_scores(u + 2, h + 2, False)
                if h == 0:
                    cmp_t(HPG - 1)
                if h == 1:
                    cmp_pv(HPG - 1)
            mem_pv(43, 1, 3)
            pe.wait_ge(o_done, 44)
            pe.wait_ge(c_o, HPG)
            mix_t(XS["wo1"], 8)
            panels("wo1", 8, split_at("wo1"), after=context_t)
            norm("wo1", context_in)
            ffn("ffn3", nothing)
            norm("ffn3", context_b_beside)

            squares(LN_SQ["even"], 8, 5)
            for t in range(3, S5T):
                context_b(t)
            panels("even", 10, split_at("even"))
            pe.wait_ge(shuffle_in, 2 * 16 * L)
            for t in range(S5T):
                pe.wait_ge(*b_slot(S5T + t))
                for b in range(4):
                    pe.wait_ge(h_act, S5T + (4 * (t - 1) + b + 1 if t > 0 else 0))
                    pe.wait_ge(h_dve, S5T + (4 * (t - 1) + b + 1 if t > 0 else 0))
                    for g in range(4):
                        e = (b % 2) * 4 + g
                        mm = pe.matmul(ps[:, 4 + b, g * NCL:(g + 1) * NCL], BS[:, t % 3, b // 2, e, :], U[:, t * GT + e, :], start=True, stop=True)
                    mm.then_inc(b_ps, 1)
            for j in range(10, 16):
                panel("even", j, 0, XH, XL)
            for j in range(2):
                pe.wait_ge(*taken_at("even", 6 + j))
            pe.wait_ge(dft_in, 16 * 6)
            for t in range(TT):
                pe.wait_ge(h_act, S5T + 4 * (S5T - 1) + t + 1)
                pe.wait_ge(h_dve, S5T + 4 * (S5T - 1) + t + 1)
                for j in range(2):
                    mm = pe.matmul(ps[:, 4 + t, j * 2 * P:(j + 1) * 2 * P], UB[:, j, t * P:(t + 1) * P], DFTC[:], start=True, stop=True)
                mm.then_inc(fnet_ps, 1)
            for j in range(2):
                pe.wait_ge(fnet_out, 4)
                for t in range(TT):
                    for e in range(2):
                        mm = pe.matmul(ps[:, 4 + j, :], FA[:, t, j, e * P:(e + 1) * P], DFTT[:, e, t, :],
                                       start=t == 0 and e == 0, stop=t == TT - 1 and e == 1)
                mm.then_inc(fnet_ps, 1)
            for j in range(2):
                pe.wait_ge(fnet_out, 5 + j)
                pe.matmul(ps[:, 6 + j, :], FW[:, j, :], FB[:, j, :], start=True, stop=True).then_inc(fnet_ps, 1)
            for j in range(12, 16):
                pe.wait_ge(*taken_at("even", j))
            for t in range(S5T):
                pe.wait_ge(pool_in[t % 2], IN["m"] + 16 * (t // 2 + 1))
                if t >= 4:
                    pe.wait_ge(fnet_out, t + 1)
                for g in range(GT):
                    mm = pe.matmul(ps[:, t, g * NCL:(g + 1) * NCL], MM[:, t % 2, g, :], U[:, t * GT + g, :], start=g == 0, stop=False)
                mm.then_inc(m_ps, 1)
            for t in range(S5T):
                if t < 3:
                    pe.wait_ge(pool_in[2], 16 * (4 + 3))
                else:
                    pe.wait_ge(w_in, 16 * (2 if t < 5 else 3))
                pe.wait_ge(ss_act, t + 1)
                pe.wait_ge(ss_dve, t + 1)
                for g in range(GT):
                    for r in range(2):
                        mm = pe.matmul(ps[:, t, g * NCL:(g + 1) * NCL], WT[t][:, r, g, :], SS[:, t % 2, r, g, :], start=False, stop=g == GT - 1 and r == 1)
                mm.then_inc(y_ps, 1)
            panels("glu", 6, split_at("glu"), nk=6)

            def squares_behind(stage):
                return lambda j: square(LN_SQ[stage], j - 2, 8, 5)

            panels("ewo", 8, lambda k: 2 * ((y_ready, k + 3 if k < 6 else k - 5),), YH, YL, after=squares_behind("odd"))
            for d in (6, 7):
                square(LN_SQ["odd"], d, 8, 5)

            def pooled(j):
                if j in (7, 10, 13, 15):
                    i = (7, 10, 13, 15).index(j)
                    if i == 0:
                        pe.wait_ge(odd_in, 32)
                    pe.wait_ge(pool_ready, i + 1)
                    pe.matmul(ps[:, 4 + (i + 2) % 4, :], PWT[:, i, :], PP[:, i % 2, :], start=True, stop=True).then_inc(pw_ps, 1)

            panels("odd", 24, split_at("odd"), after=pooled)
            pe.wait_ge(yc_ready, 4)
            panels("owo", 8, lambda k: 2 * ((y_ready, 8 + k + 1),), YH, YL, after=squares_behind("final"))

            for d in (6, 7):
                square(LN_SQ["final"], d, 8, 5)
            for d in range(KD):
                pe.wait_ge(ln_aff, 8 * 8 + d + 1)
                b = (6, 7, 4, 5)[d % 4]
                wait(pe, out_sb, d - 3)
                for t in range(TT):
                    mm = pe.transpose(ps[:, b, t * P:(t + 1) * P], XT[:, d, t * P:(t + 1) * P], IDENT[:])
                mm.then_inc(out_ps, 1)

        @block.scalar
        def _(act):
            def cast(p, i=0):
                if isinstance(i, int) and p >= PANELS:
                    return
                act.wait_ge(raw_in[p % 4], 16 * (p // 4 + 1) + 16 * i)
                if not (isinstance(i, int) and p < 2):
                    act.wait_ge(pe_panel, p - 1 + 4 * i)
                act.activation(wh[:, p % 2, :], raw[:, p % 4, :], ACT.Copy).then_inc(w_hi, 1)

            def take(stage, j, dst, func=ACT.Copy, n=T, rows=slice(0, P), **kw):
                p = BASE[stage] + j
                cast(p + 2)
                act.wait_ge(pe_panel, p + 1)
                act.activation(dst, ps[rows, p % 4, 0:n], func, **kw).then_inc(taken[p % 4], 1)

            def ffn(stage, fill):
                off, f0 = 0, 22 * int(stage[3])
                at = 0
                for c, nf in enumerate(CHUNKS):
                    for a, b in zip(UP_PARTS[c], UP_PARTS[c][1:]):
                        with act.Fori(a, b) as i:
                            for f in range(2):
                                p = BASE[stage] + off + 2 * f
                                cast(p + 2, i)
                                act.wait_ge(pe_panel, p + 1 + 4 * i)
                                act.wait_ge(h_ready, f0 + f + 1 + 2 * i)
                                act.activation(SG[:, f, :], ps[:, p % 4, :], ACT.Silu).then_inc(taken[p % 4], 1)
                                cast(p + 3, i)
                        fill(at)
                        at += 1
                    off += 2 * nf
                    f0 += nf
                    with act.Fori(0, KD // 4) as i:
                        for j in range(4):
                            cast(BASE[stage] + off + j + 2, i)
                    if c < 2:
                        fill(at)
                        at += 1
                    off += KD

            def square(q, src):
                if q >= 2:
                    act.wait_ge(sq_used, q - 1)
                act.activation(SQ[:, q % 2, 0:src.shape[-1]], src, ACT.Square).then_inc(sq_ready, 1)

            def norm(stage, eps, split=True, beside=nothing):
                no, q0, c0 = LN_NO[stage], LN_SQ[stage], LN_COL[stage]
                beside("start")
                for d in range(KD):
                    act.wait_ge(ln_c, 8 * no + d + 1)
                    square(q0 + d, XT[:, d, :])
                    beside(("square", d))
                act.wait_ge(sq_used, q0 + 8)
                if no == 0:
                    act.wait_ge(tr_done, 1)
                act.activation(SD[:, 0, :], ps[:, 5, :], ACT.Sqrt, bias=EPS[:, eps:eps + 1]).then_inc(sd_ready, 1)
                beside("root")
                for d in range(KD if split else 0):
                    act.wait_ge(ln_n, 8 * no + d + 1)
                    act.activation(XH[:, d, :], XT[:, d, :], ACT.Identity, scale=COL[:, c0 + d:c0 + d + 1],
                                   bias=COL[:, 48 + c0 + d:49 + c0 + d]).then_inc(ln_hi, 1)
                    beside(("hi", d))

            def rms(stage, ready, layer=None, wout=None, beside=nothing):
                no, q0 = LN_NO[stage], LN_SQ[stage]
                for d in range(KD):
                    if wout is not None:
                        for j in (0, 1) if d == 0 else (d + 1,):
                            if j < 8:
                                cast(BASE[wout] + j + 2)
                    act.wait_ge(*ready(d))
                    square(q0 + d, XT[:, d, :])
                    beside(("square", d))
                act.wait_ge(sq_used, q0 + 8)
                act.activation(SD[:, 0, :], ps[:, 5, :], ACT.Sqrt, bias=EPS[:, 2:3]).then_inc(sd_ready, 1)
                beside("root")
                for d in range(KD if layer is not None else 0):
                    act.wait_ge(ln_n, 8 * no + d + 1)
                    src = (NT, NO)[layer]
                    act.activation(XH[:, d, :], src[:, d, :], ACT.Identity, scale=AG[:, layer, d, 0:1],
                                   bias=MOD[:, layer, d, 0:1]).then_inc(ln_hi, 1)
                    beside(("hi", d))

            def s5_fill(t):
                wait(act, s5_out, 64 * t)
                for b in range(2):
                    act.wait_ge(s5_t, 4 * t + b + 1)
                    act.activation(BT[:, 0, 4 * b:4 * b + 4, :], ps[:, 4 + b, :], ACT.Copy).then_inc(bt_act, 1)
                for b in range(4):
                    act.wait_ge(s5_z, 4 * t + b + 1)
                    act.activation(Z[:, 2 * b:2 * b + 2, :], ps[0:S5H, 4 + b, 0:480], ACT.Copy).then_inc(z_out, 1)

            def ffn2_fill(f):
                if f == 0:
                    act.wait_ge(zeros, 2)
                    act.wait_ge(kc_ps, 1)
                    for g in range(GROUPS):
                        n, d = slice(g * NPAD, (g + 1) * NPAD), slice(g * HD, (g + 1) * HD)
                        act.activation(KCB[d, n], ps[0:HD, 4, n], ACT.Copy)
                        act.activation(VCB[n, d], ps[n, 5, 0:HD], ACT.Copy).then_inc(kc_out, 1)

            def context(step):
                if step == 0:
                    act.wait_ge(cx_in, 32)
                    for m in range(MT):
                        act.activation(CXT[:, 4 * m:4 * m + 4, :].rearrange("p k c -> p (k c)"), CXN[:, m, :], ACT.Square, accum_out=CSS[:, m:m + 1]
                                       ).then_inc(cx_sd, 1)
                    act.wait_ge(cx_sd, 2)
                    act.activation(CSS[:, 2:4], CSS[:, 0:2], ACT.Sqrt, scale=1.0 / D, bias=EPS[:, 2:3]).then_inc(cx_sd, 1)
                if step == 2:
                    for k in range(KD):
                        act.wait_ge(cx_f, k + 1)
                        act.activation(CH[:, k, :], CXT[:, k, :], ACT.Copy).then_inc(cx_hi, 1)

            def context_in(at):
                def result(j):
                    p = BASE["ctx"] + j
                    act.wait_ge(pe_panel, p + 1)
                    act.activation(UTC[:, j].rearrange("p t c -> p c t"), ps[:, p % 4, 0:CTX].rearrange("p (c t) -> p c t", t=L), ACT.Copy
                                   ).then_inc(taken[p % 4], 1)
                for p in {"start": (2,), ("square", 1): (3,), "root": (4, 5), ("hi", 2): (6,), ("hi", 5): (7,)}.get(at, ()):
                    cast(BASE["ctx"] + p)
                for j in {"root": (0, 1, 2, 3), ("hi", 2): (4,), ("hi", 5): (5,)}.get(at, ()):
                    result(j)

            def context_states(t):
                act.wait_ge(b_ps, t + 1)
                act.activation(HC[0:S5P, :, t * GT:(t + 1) * GT, 1:], ps[0:S5P, 6 + t % 2, :].rearrange("p (r g c) -> p r g c", r=2, g=GT), ACT.Copy
                               ).then_inc(h_act, 1)

            def context_states_beside(at):
                for t in {"root": (0, 1)}.get(at, ()):
                    context_states(t)

            def context_states_beside_even(at):
                for t in {("square", 3): (2,), "root": (3,), ("hi", 3): (4,), ("hi", 7): (5,)}.get(at, ()):
                    context_states(t)

            def softmax_exp(u, s):
                act.wait_ge(nb_ready, u + 1)
                for t in range(TT):
                    ins = act.activation(PR[:, s, POFF[t]:POFF[t] + (t + 1) * P], PR[:, s, POFF[t]:POFF[t] + (t + 1) * P], ACT.Exp,
                                         bias=NB[:, s, t:t + 1], scale=scale[0], accum_out=SM[:, s, t:t + 1])
                ins.then_inc(p_ready, 1)

            def probs_out(u, s):
                act.wait_ge(t_ps, u + 1)
                wait(act, pv_ps, u - 1)
                act.activation(PT[:, s, 0:T], ps[:, 0, :], ACT.Copy).then_inc(pt_act, 1)
                act.activation(PT[:, s, 2 * T:2 * T + 2 * P], ps[:, 2, 0:2 * P], ACT.Copy).then_inc(pt_act, 1)

            def mem_exp(u, s):
                act.wait_ge(nb_ready, u + 1)
                act.wait_ge(t_ps, u - 1)
                for t in range(TT):
                    ins = act.activation(PR[:, s, t * M:(t + 1) * M], ps[:, 4 + t // 2, (t % 2) * M:(t % 2 + 1) * M], ACT.Exp,
                                         bias=NB[:, s, t:t + 1], scale=HD ** -0.5, accum_out=SM[:, s, t:t + 1])
                ins.then_inc(p_ready, 1)

            def mem_probs_out(u, s):
                act.wait_ge(t_ps, u + 1)
                wait(act, pv_ps, u - 1)
                act.activation(PT[:, s, 0:T // 2], ps[:, 0, 0:T // 2], ACT.Copy).then_inc(pt_act, 1)
                act.activation(PT[:, s, T // 2:T], ps[:, 0, T // 2:T], ACT.Copy).then_inc(pt_act, 1)

            def mix_hi_of(mix0):
                for k in range(KD):
                    act.wait_ge(mix_ps, mix0 + k + 1)
                    act.activation(XH[:, k, :], ps[:, 4 + k % 4, :], ACT.Copy).then_inc(mix_hi, 1)

            scale = [MLA_SCALE]
            cast(0)
            cast(1)
            for k2 in range(4):
                act.wait_ge(tr, k2 + 1)
                act.activation(MH[:, 2 * k2:2 * k2 + 2, :], ps[:, 4 + k2, :].rearrange("p (e m) -> p e m", e=2), ACT.Copy).then_inc(mem_hi, 1)
            for layer in range(2):
                for j in range(4):
                    k = 4 * layer + j
                    take("mem", k, KM[:, layer, j, :] if j < 2 else MV[:, 2 * layer + j - 2, :], n=M)
                    act.wait_ge(tr, 5 + k)
                    act.activation(XH[:, k, :], ps[:, 4 + k % 4, :], ACT.Copy).then_inc(x_hi, 1)

            act.wait_ge(tr_done, 1)
            act.activation(CS[:].rearrange("p k e -> p e k"), COL[:, 96 + 101:96 + 117].rearrange("p (e k) -> p e k", e=2), ACT.Silu).then_inc(cs_ready, 1)
            for b, parts in enumerate((((0, 4, 1.0),), ((4, 2, 1.0), (6, 2, -1.0)), ((8, 4, -1.0),))):
                act.wait_ge(s5_tr, 2 + b)
                col = 0
                for r0, n, sign in parts:
                    ins = act.activation(CR[:].rearrange("p r g h -> p (r g h)")[:, r0 * P:(r0 + n) * P], ps[:, 5 + b, col:col + n * P], ACT.Copy, scale=sign)
                    col += n * P
                ins.then_inc(cr_out, 1)
            act.wait_ge(sin_in, 1)
            act.activation(TS5[:, 0, :], TS5[:, 2, :], ACT.Sin)
            act.activation(TS5[:, 1, :], TS5[:, 2, :], ACT.Sin, scale=0.5).then_inc(sin_out, 1)
            ffn("ffn0", s5_fill)
            norm("ffn0", 0)
            act.wait_ge(s5_out, 64 * S5T)
            for j, dst in enumerate((CQ[:, 0, :], CQ[:, 1, :], CKV[:], KR, QM[:, 0, :], QM[:, 1, :])):
                p = BASE["mla"] + j
                if j < 3:
                    act.wait_ge(pe_panel, p + 1)
                    square(LN_SQ["mla"] + j, ps[:, p % 4, :])
                take("mla", j, dst, rows=slice(0, ROPE if j == 3 else P))
                if j in (3, 4):
                    act.wait_ge(sq_used, LN_SQ["mla"] + j - 1)
                    act.activation(SD[:, j - 3, :], ps[:, j + 1, :], ACT.Sqrt, scale=float(D // (QR if j == 3 else P)), bias=EPS[:, 2:3]).then_inc(sd_ready, 1)
            def take_q(h, s):
                act.wait_ge(q_ps, h + 1)
                if not (isinstance(h, int) and h < 2):
                    act.wait_ge(s_ps, h - 1)
                act.activation(QT[0:HD, s, :], ps[0:HD, 3, :], ACT.Copy).then_inc(q_nope, 1)

            take_q(0, 0)
            for g in range(14):
                if g < 6:
                    act.wait_ge(kv_ps, g + 1)
                    act.activation(KT[0:HD, 2 * g, :], ps[0:HD, 4 + g % 4, :], ACT.Copy).then_inc(kv_act, 1)
                    if g == 5:
                        take_q(1, 1)
                        act.wait_ge(kr_rot, 2)
                        act.activation(KT[HD:QK, 0:6, :], KR2[:, 0:1, :].broadcast_to([ROPE, 6, T]), ACT.Copy).then_inc(kr_act, 1)
                elif g % 2 == 0:
                    act.wait_ge(kv_ps, g + 1)
                    act.activation(V[:, (g - 6) // 2, 0:6 * HD], ps[:, 4 + g % 4, 0:6 * HD], ACT.Copy).then_inc(kv_act, 1)

            take_q(2, 0)
            for h in range(2):
                softmax_exp(h, h)

            def mla_unit(u, s, project=True):
                probs_out(u, s)
                if project:
                    take_q(u + 3, 1 - s)
                softmax_exp(u + 2, s)

            mla_unit(0, 0)
            mla_unit(1, 1)
            with act.Fori(1, HEADS // 2 - 2) as i:
                for s in range(2):
                    mla_unit(2 * i + s, s)
            mla_unit(8, 0)
            mla_unit(9, 1, project=False)
            for h in range(2):
                probs_out(10 + h, h)
                mem_exp(12 + h, h)
            for h in range(MEM_HEADS):
                u = 12 + h
                mem_probs_out(u, u % 2)
                if h < 2:
                    mem_exp(u + 2, u % 2)
            mix_hi_of(0)
            for j in range(8):
                cast(BASE["wo0"] + j + 2)
            norm("wo0", 1)
            ffn("ffn1", nothing)
            norm("ffn1", 0)

            for j, dst in enumerate((ZC[:, 0, :], ZC[:, 1, :], KS[:], VT[:, 0, :], KW[:], VT[:, 1, :])):
                take("kv", j, dst)
            act.wait_ge(zeros, 2)
            for n in range(4):
                act.wait_ge(hid_ps, n // 2 * 2 + 2)
                act.activation(H1[:, n // 2, n % 2, :, 0:NCMP], ps[:, 6 + n // 2, (n % 2) * 2 * NCMP:(n % 2 + 1) * 2 * NCMP].rearrange("p (g n) -> p g n", g=GROUPS),
                               ACT.Gelu_apprx_tanh, bias=COL[:, 96 + 94 + n:96 + 95 + n]).then_inc(gelu_out, 1)
            ffn("ffn2", ffn2_fill)
            norm("ffn2", 0)

            take("nsa", 0, GTT[:], ACT.Sigmoid, rows=slice(0, 36))
            for j in range(2):
                take("nsa", 1 + j, QM[:, j, :])
            def split_q(j, q):
                for g in range(GROUPS):
                    r = slice(g * HD, (g + 1) * HD)
                    act.activation(QS[r, q, g, :], QP[r, bass.ds(j, 1), :].rearrange("p o t -> p (o t)"), ACT.Copy).then_inc(qs_hi, 1)

            for m in range(HPG):
                p = BASE["nsa"] + 3 + m
                cast(p + 2)
                act.wait_ge(pe_panel, p + 1)
                for e in range(2):
                    g, j = divmod(2 * m + e, HPG)
                    ins = act.activation(QP[g * HD:(g + 1) * HD, j, :], ps[e * HD:(e + 1) * HD, p % 4, :], ACT.Copy)
                ins.then_inc(taken[p % 4], 1)
                if m == 3:
                    act.wait_ge(*taken_at("nsa", 6))
                    split_q(0, 0)
                if m < 4:
                    br, g = divmod(m, GROUPS)
                    act.wait_ge(mod_ready, 2)
                    for half in range(2):
                        act.activation(KX[half * HD:(half + 1) * HD, br, g, 0, :], (KS, KW)[br][g * HD:(g + 1) * HD, :], ACT.Copy).then_inc(kx_hi, 1)

            scale[0] = SEL_SCALE
            softmax_exp(16, 0)
            softmax_exp(17, 1)

            def cmp_probs_out(j):
                act.wait_ge(c_t, j + 1)
                wait(act, c_pv, j)
                act.activation(PTC[:], ps[0:2 * NPAD, 3, :], ACT.Copy).then_inc(c_pt, 1)

            def nsa_pair(j, q, last=False):
                for k in range(4):
                    u = 16 + 4 * j + k
                    probs_out(u, k % 2)
                    if k == 0 and not last:
                        act.wait_ge(s_ps, 16 + 4 * j)
                        split_q(j + 1, 1 - q)
                    if k == 1 and not (isinstance(j, int) and j == 0):
                        cmp_probs_out(j - 1)
                    if k == 2:
                        act.wait_ge(c_sub, j + 1)
                        act.activation(SC[:], SC[:], ACT.Exp, scale=SEL_SCALE).then_inc(c_exp, 1)
                    if last and k >= 2:
                        mem_exp(u + 2, k % 2)
                    else:
                        softmax_exp(u + 2, k % 2)

            nsa_pair(0, 0)
            nsa_pair(1, 1)
            with act.Fori(1, HPG // 2 - 1) as i:
                for q in range(2):
                    nsa_pair(2 * i + q, q)
            nsa_pair(4, 0)
            nsa_pair(5, 1, last=True)
            for h in range(MEM_HEADS):
                u = 40 + h
                mem_probs_out(u, u % 2)
                if h == 1:
                    cmp_probs_out(HPG - 1)
                if h < 2:
                    mem_exp(u + 2, u % 2)
            mix_hi_of(8)
            for j in range(8):
                cast(BASE["wo1"] + j + 2)
                context(j)
            norm("wo1", 1, beside=context_in)
            ffn("ffn3", nothing)
            norm("ffn3", 0, split=False, beside=context_states_beside)

            rms("even", lambda d: (ln_aff, 8 * LN_NO["ffn3"] + d + 1), 0, beside=context_states_beside_even)
            for j in range(6):
                take("even", j, UT[:, j].rearrange("p t c -> p c t"))
            for j in range(2):
                take("even", 6 + j, UB[:, j, :])

            def take_z(j):
                take("even", 8 + j, ZS[:, j, :], ACT.Silu)
            take_z(0)
            take_z(1)
            for t in range(S5T):
                for b in range(4):
                    act.wait_ge(b_ps, S5T + 4 * t + b + 1)
                    if t == 0 and b == 0:
                        act.wait_ge(shuffle_out, 2 * 16 * 6)
                    g = t * GT + (b % 2) * 4
                    act.activation(H[0:S5P, b // 2, g:g + 4, 1:], ps[0:S5P, 4 + b, 0:4 * NCL].rearrange("p (g c) -> p g c", g=4), ACT.Copy).then_inc(h_act, 1)
            for j in range(2, 8):
                take_z(j)
            for t in range(TT):
                act.wait_ge(fnet_ps, t + 1)
                act.activation(FA[:, t].rearrange("p j c -> p (j c)"), ps[:, 4 + t, :], ACT.Copy).then_inc(fnet_out, 1)
            for j in range(2):
                act.wait_ge(fnet_ps, 5 + j)
                act.activation(FB[:, j, :], ps[:, 4 + j, :], ACT.Copy).then_inc(fnet_out, 1)
            for j in range(2):
                act.wait_ge(fnet_ps, 7 + j)
                act.activation(YB[:, j, :], ps[:, 6 + j, :], ACT.Copy).then_inc(fnet_out, 1)

            def states(t):
                if t == 0:
                    act.wait_ge(scan, 3 * NC + 2)
                wait(act, y_ps, t - 1)
                act.activation(SS[0:S5P, t % 2], H[0:S5P, :, t * GT:(t + 1) * GT, 0:NCL], ACT.Copy).then_inc(ss_act, 1)

            def gelu(j):
                act.wait_ge(sp_in[j % 2], IN["y"] + 16 * (j // 2 + 1))
                act.activation(YA[:, j, :].rearrange("p (c t) -> p t c", t=L), YT[:, j % 2], ACT.Gelu_apprx_tanh).then_inc(ya_ready, 1)
                act.wait_ge(ya_ready, j + 1)
                act.activation(XH[:, j, :], YA[:, j, :], ACT.Copy).then_inc(ya_hi, 1)

            states(0)
            states(1)
            for t in range(S5T):
                act.wait_ge(y_ps, t + 1)
                act.activation(YS[:, t * GT:(t + 1) * GT, :], ps[:, t, :], ACT.Copy).then_inc(y_sb, 1)
                if t + 2 < S5T:
                    states(t + 2)
                if t >= 2:
                    gelu(t - 2)
            for j in range(4, 6):
                gelu(j)
            for j in range(6):
                act.wait_ge(y_full, j + 1)
                take("glu", j, SIG[:, j % 2, :], ACT.Sigmoid, bias=COL[:, 96 + 72 + j:96 + 73 + j])
            rms("odd", lambda d: taken_at("ewo", d), 1, "ewo")

            act.wait_ge(odd_zero, 1)
            for j in range(4):
                take("odd", j, PU[:, j, PAD:PAD + T])

            def take_pooled(i):
                act.wait_ge(pw_ps, i + 1)
                act.activation(YO[:, i, :], ps[:, 4 + (i + 2) % 4, :], ACT.Identity, scale=COL[:, 96 + 78 + i:96 + 79 + i]).then_inc(yc_ready, 1)

            for k in range(4):
                if k >= 2:
                    act.wait_ge(*taken_at("odd", 5 + 3 * (k - 2)))
                take("odd", 4 + 3 * k, CG[:, k % 2, :])
                cast(BASE["odd"] + 4 + 3 * k + 3)
                cast(BASE["odd"] + 4 + 3 * k + 4)
                if k >= 1:
                    take_pooled(k - 1)
            take_pooled(3)
            for j in range(8):
                wait(act, y_ready, 8 + j - 1)
                take("odd", 16 + j, ZO[:, j % 2, :], ACT.Silu)
            rms("final", lambda d: taken_at("owo", d), wout="owo")
            for d in range(KD):
                act.wait_ge(out_ps, d + 1)
                act.activation(XO[:, :, d * P:(d + 1) * P], ps[:, (6, 7, 4, 5)[d % 4], :].rearrange("p (t c) -> p t c", t=TT), ACT.Copy).then_inc(out_sb, 1)

        @block.vector
        def _(dve):
            def rest(p, i=0):
                if isinstance(i, int) and p >= PANELS:
                    return
                dve.wait_ge(w_hi, p + 1 + 4 * i)
                dve.tensor_tensor(wl[:, p % 2, :], raw[:, p % 4, :], wh[:, p % 2, :].bitcast(F32), ALU.subtract).then_inc(w_lo, 1)

            def ffn(stage, fill):
                off = 0
                at = 0
                for c, nf in enumerate(CHUNKS):
                    for a, b in zip(UP_PARTS[c], UP_PARTS[c][1:]):
                        with dve.Fori(a, b) as i:
                            for f in range(2):
                                p = BASE[stage] + off + 2 * f
                                u = p + 1
                                rest(p + 2, i)
                                rest(p + 3, i)
                                dve.wait_ge(taken[p % 4], p // 4 + 1 + i)
                                dve.wait_ge(pe_panel, u + 1 + 4 * i)
                                k = bass.ds(2 * i + f, 1)
                                dve.tensor_tensor(HH[:, k, :], SG[:, f:f + 1, :], ps[:, u % 4:u % 4 + 1, :], ALU.mult)
                                dve.tensor_tensor(HF[:, f, :], SG[:, f, :], ps[:, u % 4, :], ALU.mult).then_inc(taken[u % 4], 1)
                                dve.wait_ge(taken[u % 4], u // 4 + 1 + i)
                                dve.tensor_tensor(HL[:, k, :], HF[:, f:f + 1, :], HH[:, k, :].bitcast(F32), ALU.subtract).then_inc(h_ready, 1)
                        fill(at)
                        at += 1
                    off += 2 * nf
                    with dve.Fori(0, KD // 4) as i:
                        for j in range(4):
                            p = BASE[stage] + off + j
                            rest(p + 2, i)
                            dve.wait_ge(pe_panel, p + 1 + 4 * i)
                            if c:
                                q = p - KD - 2 * nf
                                dve.wait_ge(taken[q % 4], q // 4 + 1 + i)
                            x = XT[:, bass.ds(4 * i + j, 1), :]
                            dve.scalar_tensor_tensor(x, x, 1.0 if c else 2 * ALPHA, ps[:, p % 4:p % 4 + 1, :], ALU.mult, ALU.add
                                                     ).then_inc(taken[p % 4], 1)
                    if c < 2:
                        fill(at)
                        at += 1
                    off += KD

            def norm(stage, split=True, beside=nothing):
                no, c0 = LN_NO[stage], LN_COL[stage]
                dve.wait_ge(ln_mu, no + 1)
                for d in range(KD):
                    dve.tensor_tensor(XT[:, d, :], XT[:, d, :], ps[:, 4, :], ALU.subtract).then_inc(ln_c, 1)
                beside("centred")
                reciprocal(0)
                dve.wait_ge(ln_c, 8 * no + 8)

                def affine(d):
                    if not split:
                        dve.wait_ge(ln_n, 8 * no + d + 1)
                        dve.wait_ge(sct_ready, d + 1)
                        dve.scalar_tensor_tensor(XT[:, d, :], XT[:, d, :], COL[:, c0 + d:c0 + d + 1], SCT[:, d, :], ALU.mult, ALU.add).then_inc(ln_aff, 1)
                        return
                    dve.wait_ge(ln_hi, 8 * no + d + 1)
                    dve.tensor_scalar(XT[:, d, :], XT[:, d, :], COL[:, c0 + d:c0 + d + 1], COL[:, 48 + c0 + d:49 + c0 + d],
                                      ALU.mult, ALU.add).then_inc(ln_aff, 1)
                for d in range(KD + 2):
                    if d < KD:
                        dve.tensor_tensor(XT[:, d, :], XT[:, d, :], RST[:, 0, :], ALU.mult).then_inc(ln_n, 1)
                    if 1 <= d <= KD:
                        affine(d - 1)
                    if split and d - 2 in BY_DVE:
                        low_part(XT, no, d - 2)
                    beside(d)

            def low_part(src, no, d):
                dve.wait_ge(ln_aff, 8 * no + d + 1)
                dve.tensor_tensor(XL[:, d, :], src[:, d, :], XH[:, d, :].bitcast(F32), ALU.subtract).then_inc(x_dve, 1)

            def reciprocal(j):
                rc[0] += 1
                dve.wait_ge(sd_ready, rc[0])
                dve.reciprocal(RST[:, j, :], SD[:, j, :]).then_inc(rstd_ready, 1)
                dve.wait_ge(rstd_ready, rc[0])

            def rms(stage, layer, beside=nothing):
                no, hi = LN_NO[stage], HI_NO[stage]
                dst = (NT, NO)[layer]
                reciprocal(0)
                beside("root")

                def affine(d):
                    dve.wait_ge(ln_hi, 8 * hi + d + 1)
                    dve.tensor_scalar(dst[:, d, :], dst[:, d, :], AG[:, layer, d, 0:1], MOD[:, layer, d, 0:1], ALU.mult, ALU.add).then_inc(ln_aff, 1)
                for d in range(KD + 2):
                    if d < KD:
                        dve.tensor_tensor(dst[:, d, :], XT[:, d, :], RST[:, 0, :], ALU.mult).then_inc(ln_n, 1)
                    if 1 <= d <= KD:
                        affine(d - 1)
                    if d - 2 in BY_DVE:
                        low_part(dst, no, d - 2)
                    beside(d)

            def modulation(layer):
                n0 = 96 + 16 + 24 * layer
                dve.wait_ge(ada_used, 12 * (layer + 1))
                g0 = 96 + 8 * layer
                parts = ps[:, 6, 0:48].rearrange("p (m e) -> p m e", e=2)
                for e, count in ((1, 16), (0, 24))[layer:]:
                    ins = dve.scalar_tensor_tensor(MOD[:, layer, 0:count, e], parts[:, 0:count, e], float(D), COL[:, n0:n0 + count], ALU.mult, ALU.add)
                ins.then_inc(mod_ready, 1)
                dve.wait_ge(mod_ready, layer + 1)
                for e in range(2 - layer):
                    dve.scalar_tensor_tensor(AG[:, layer, :, e], MOD[:, layer, 8:16, e], 1.0, COL[:, g0:g0 + 8], ALU.add, ALU.mult)

            def gated(stage, layer):
                for j in range(8):
                    p = BASE[stage] + j
                    rest(p + 2)
                    dve.wait_ge(pe_panel, p + 1)
                    dve.scalar_tensor_tensor(XT[:, j, :], ps[:, p % 4, :], MOD[:, layer, 16 + j, 0:1], XT[:, j, :], ALU.mult, ALU.add).then_inc(taken[p % 4], 1)

            def s5_fill(t):
                wait(dve, s5_out, 64 * t)
                for b in range(2):
                    dve.wait_ge(s5_t, 4 * t + b + 3)
                    dve.tensor_copy(BT[:, 1, 4 * b:4 * b + 4, :], ps[:, 6 + b, :]).then_inc(bt_dve, 1)

            def context(step):
                if step == 0:
                    dve.wait_ge(cx_sd, 3)
                    dve.reciprocal(CSS[:, 0:2], CSS[:, 2:4]).then_inc(cx_n, 1)
                    dve.wait_ge(cx_n, 1)
                    for m in range(MT):
                        ins = dve.tensor_scalar(CXN[:, m, :], CXN[:, m, :], CSS[:, m:m + 1], None, ALU.mult)
                    ins.then_inc(cx_n, 1)
                if step == 2:
                    for k in range(KD):
                        if k % 2 == 0:
                            dve.wait_ge(cx_ps, k // 2 + 1)
                        dve.tensor_scalar(CXT[:, k, :], ps[:, 4 + k // 2, (k % 2) * CTX:(k % 2 + 1) * CTX], AG[:, 0, k, 1:2], MOD[:, 0, k, 1:2],
                                          ALU.mult, ALU.add).then_inc(cx_f, 1)

            def context_in(at):
                for p in {4: (0,), 6: (1,)}.get(at, ()):
                    dve.wait_ge(w_lo, BASE["ffn3"] + p)
                    rest(BASE["ffn3"] + p)

            def context_states(t):
                dve.wait_ge(b_ps, t + 1)
                if t == 0:
                    dve.memset(HC[:, :, :, 0:1], 0.0).then_inc(scan, 1)
                src = ps[S5P:P, 6 + t % 2, :].rearrange("p (r g c) -> p r g c", r=2, g=GT)
                dve.tensor_copy(HC[S5P:P, :, t * GT:(t + 1) * GT, 1:], src[:, :, :, ::-1]).then_inc(h_dve, 1)

            def context_states_beside(at):
                for t in {"centred": (0,), 9: (1, 2)}.get(at, ()):
                    context_states(t)

            def context_states_beside_even(at):
                for t in {"root": (3,), 3: (4,), 9: (5,)}.get(at, ()):
                    context_states(t)

            def s5_parameters():
                n = [1]

                def step(ins):
                    n[0] += 1
                    ins.then_inc(s5_dve, 1)
                    dve.wait_ge(s5_dve, n[0])

                X, K, R, Q, STEP, ZR, ZI, E1, E, CM = (TS5[:, 2 + j, :] for j in range(10))
                sin, sin_half = TS5[:, 0, :], TS5[:, 1, :]
                lre, lim = PS5[:, 0, :], PS5[:, 1, :]
                two = KI5[:].bitcast(F32)

                def exponential(src, e, em1=None):
                    step(dve.tensor_scalar(X, src, -87.0, 88.0, ALU.max, ALU.min))
                    step(dve.tensor_scalar(K, X, float(1 / np.log(2.0)), MAGIC, ALU.mult, ALU.add))
                    step(dve.tensor_scalar(K, K, MAGIC, None, ALU.subtract))
                    step(dve.scalar_tensor_tensor(R, K, -LN2[0], X, ALU.mult, ALU.add))
                    step(dve.scalar_tensor_tensor(R, K, -LN2[1], R, ALU.mult, ALU.add))
                    step(dve.tensor_scalar(Q, R, 1 / 5040, None, ALU.mult))
                    for f in (720, 120, 24, 6, 2, 1):
                        step(dve.scalar_tensor_tensor(Q, Q, 1 / f, R, ALU.add, ALU.mult))
                    step(dve.tensor_scalar(K, K, 127.0, float(2 ** 23), ALU.add, ALU.mult))
                    step(dve.tensor_copy(KI5[:], K))
                    step(dve.tensor_tensor(Q, Q, two, ALU.mult))
                    step(dve.tensor_tensor(e, Q, two, ALU.add))
                    if em1 is not None:
                        step(dve.tensor_scalar(X, two, 1.0, None, ALU.subtract))
                        step(dve.tensor_tensor(em1, Q, X, ALU.add))

                exponential(PS5[:, 2, :], STEP)
                step(dve.tensor_tensor(ZI, lim, STEP, ALU.mult))
                step(dve.tensor_tensor(ZR, lre, STEP, ALU.mult))
                exponential(ZR, E, E1)
                step(dve.tensor_scalar(K, ZI, float(1 / (2 * np.pi)), MAGIC, ALU.mult, ALU.add))
                step(dve.tensor_scalar(K, K, MAGIC, None, ALU.subtract))
                step(dve.scalar_tensor_tensor(X, K, -TURN[0], ZI, ALU.mult, ALU.add))
                step(dve.scalar_tensor_tensor(X, K, -TURN[1], X, ALU.mult, ALU.add))
                step(dve.scalar_tensor_tensor(X, K, -TURN[2], X, ALU.mult, ALU.add))
                dve.tensor_scalar(X, X, -3.1415925, 3.1415925, ALU.max, ALU.min).then_inc(sin_in, 1)
                dve.wait_ge(sin_out, 1)
                step(dve.scalar_tensor_tensor(CM, sin_half, -2.0, sin_half, ALU.mult, ALU.mult))
                step(dve.tensor_tensor(Q, E, CM, ALU.mult))
                step(dve.tensor_tensor(Q, Q, E1, ALU.add))
                step(dve.tensor_tensor(R, E, sin, ALU.mult))
                step(dve.tensor_copy(PW[:, 1, 1, :], R))
                step(dve.tensor_scalar(PW[:, 0, 1, :], Q, 1.0, None, ALU.add))
                step(dve.tensor_tensor(X, lre, lre, ALU.mult))
                step(dve.tensor_tensor(K, lim, lim, ALU.mult))
                step(dve.tensor_tensor(X, X, K, ALU.add))
                step(dve.reciprocal(K, X))
                for r, (a, b, op) in enumerate(((Q, R, ALU.add), (R, Q, ALU.subtract))):
                    step(dve.tensor_tensor(X, a, lre, ALU.mult))
                    step(dve.tensor_tensor(E1, b, lim, ALU.mult))
                    step(dve.tensor_tensor(X, X, E1, op))
                    ins = dve.tensor_tensor(FB5[:, r, :], X, K, ALU.mult)
                    if r == 0:
                        step(ins)
                ins.then_inc(f_ready, 1)

            def soft_max(u, s, mask, first=False):
                dve.wait_ge(s_ps, u + 1)
                if not (isinstance(u, int) and u < 2):
                    dve.wait_ge(t_ps, u - 1)
                if not first:
                    dve.reciprocal(RS[:, s, :], SM[:, s, :]).then_inc(rs_ready, 1)
                for t, bank, col in STILES:
                    n = (t + 1) * P
                    ins = dve.tensor_tensor_reduce(PR[:, s, POFF[t]:POFF[t] + n], ps[:, bank, col:col + n], mask[:, T - n:T],
                                                   1.0, -3e38, ALU.add, ALU.max, MX[:, s, t:t + 1])
                ins.then_inc(s_sb, 1)
                dve.wait_ge(s_sb, u + 1)
                dve.tensor_scalar(NB[:, s, :], MX[:, s, :], -scale[0], None, ALU.mult).then_inc(nb_ready, 1)

            def probs_out(u, s):
                dve.wait_ge(t_ps, u + 1)
                wait(dve, pv_ps, u - 1)
                dve.tensor_copy(PT[:, s, T:2 * T], ps[:, 1, :]).then_inc(pt_dve, 1)

            def own_sums(u, s):
                dve.wait_ge(p_ready, u + 1)
                dve.reciprocal(RS[:, s, :], SM[:, s, :]).then_inc(rs_ready, 1)

            def head_out(u, s, dst):
                dve.wait_ge(rs_ready, u + 1)
                dve.wait_ge(pv_ps, u + 1)
                dve.tensor_tensor(dst, ps[:, 7, 0:TT * HD].rearrange("p (t d) -> p t d", t=TT),
                                  RS[:, s, :].rearrange("p (t o) -> p t o", o=1).broadcast_to([P, TT, HD]), ALU.mult).then_inc(o_done, 1)

            def mem_max(u, s):
                dve.wait_ge(s_ps, u + 1)
                dve.tensor_reduce(MX[:, s, 0:2], ps[:, 4, :].rearrange("p (t m) -> p t m", t=2), AX.X, ALU.max)
                dve.tensor_reduce(MX[:, s, 2:4], ps[:, 5, :].rearrange("p (t m) -> p t m", t=2), AX.X, ALU.max).then_inc(s_sb, 1)
                dve.wait_ge(s_sb, u + 1)
                dve.tensor_scalar(NB[:, s, :], MX[:, s, :], -HD ** -0.5, None, ALU.mult).then_inc(nb_ready, 1)

            def mix_lo_of(mix0):
                for k in range(KD):
                    dve.wait_ge(mix_hi, mix0 + k + 1)
                    dve.tensor_tensor(XL[:, k, :], ps[:, 4 + k % 4, :], XH[:, k, :].bitcast(F32), ALU.subtract).then_inc(x_split, 1)

            rc = [0]
            scale = [MLA_SCALE]
            dve.memset(ONES[:], 1.0 / D).then_inc(setup, 1)
            dve.memset(EPS[:, 0:1], 4e-5).then_inc(h_ready, 2)
            dve.memset(EPS[:, 1:2], 1e-5)
            dve.memset(EPS[:, 2:3], 1e-6).then_inc(setup, 1)
            rest(0)
            rest(1)
            for k2 in range(4):
                dve.wait_ge(mem_hi, k2 + 1)
                dve.tensor_tensor(ML[:, 2 * k2:2 * k2 + 2, :], ps[:, 4 + k2, :].rearrange("p (e m) -> p e m", e=2),
                                  MH[:, 2 * k2:2 * k2 + 2, :].bitcast(F32), ALU.subtract).then_inc(mem_split, 1)
            for k in range(KD):
                rest(BASE["mem"] + k + 2)
                dve.wait_ge(x_hi, k + 1)
                dve.tensor_copy(XT[:, k, :], ps[:, 4 + k % 4, :])
                dve.tensor_tensor(XL[:, k, :], ps[:, 4 + k % 4, :], XH[:, k, :].bitcast(F32), ALU.subtract).then_inc(x_split, 1)
            dve.wait_ge(tr, 13)
            dve.tensor_copy(COL[:], ps[:, 4, 0:213])
            dve.tensor_copy(POS[:].rearrange("p j l -> p (j l)"), ps[:, 4, 256:320]).then_inc(tr_done, 1)
            for n in range(4):
                dve.wait_ge(vm_ps, n + 1)
                dve.tensor_copy(VM[:, n // 2, :, (n % 2) * P:(n % 2 + 1) * P], ps[:, 4 + n, 0:MT * P].rearrange("p (m c) -> p m c", m=MT)
                                ).then_inc(vm_ready, 1)

            dve.wait_ge(s5_tr, 1)
            dve.tensor_copy(PS5[:].rearrange("p r g -> p (r g)"), ps[:, 4, 0:3 * S5G])
            dve.tensor_copy(DT[:], ps[0:S5H, 4, 3 * S5G:4 * S5G]).then_inc(s5_dve, 1)
            dve.wait_ge(s5_dve, 1)
            s5_parameters()
            ffn("ffn0", s5_fill)
            norm("ffn0")
            dve.wait_ge(s5_out, 64 * S5T)
            for j in range(6):
                rest(BASE["mla"] + j + 2)
                if j == 3:
                    reciprocal(0)
                    for e in range(2):
                        dve.wait_ge(*taken_at("mla", e))
                        dve.scalar_tensor_tensor(CQ[:, e, :], CQ[:, e, :], COL[:, 96 + 98 + e:96 + 99 + e], RST[:, 0, :], ALU.mult, ALU.mult).then_inc(cq_norm, 1)
                if j == 4:
                    reciprocal(1)
                    dve.wait_ge(*taken_at("mla", 2))
                    dve.scalar_tensor_tensor(CKV[:], CKV[:], COL[:, 96 + 100:96 + 101], RST[:, 1, :], ALU.mult, ALU.mult).then_inc(cq_norm, 1)
            def rotate_q(h, s):
                dve.wait_ge(q_ps, h + 1)
                wait(dve, q_rope, h)
                dve.tensor_tensor(RT[HD:QK, 0, :], ps[HD:QK, 3, :], ROT[HD:QK, :], ALU.mult).then_inc(q_rot, 1)
                dve.tensor_tensor(RT[HD:QK, 1, :], ps[QK:P, 3, :], ROT[QK:P, :], ALU.mult).then_inc(q_rot, 1)
                dve.wait_ge(q_rot, 2 * h + 2)
                if not (isinstance(h, int) and h < 2):
                    dve.wait_ge(s_ps, h - 1)
                dve.tensor_tensor(QT[HD:QK, s, :], RT[HD:QK, 0, :], RT[HD:QK, 1, :], ALU.add).then_inc(q_rope, 1)

            dve.wait_ge(kr_ps, 1)
            dve.wait_ge(mla_in_s, 80)
            dve.tensor_tensor(KR2[:, 0, :], ps[ROPE:2 * ROPE, 6, :], ROT[ROPE:2 * ROPE, :], ALU.mult).then_inc(kr_rot, 1)
            dve.tensor_tensor(KR2[:, 1, :], KR, ROT[0:ROPE, :], ALU.mult).then_inc(dve_link, 1)
            dve.wait_ge(dve_link, 1)
            dve.tensor_tensor(KR2[:, 0, :], KR2[:, 0, :], KR2[:, 1, :], ALU.add).then_inc(kr_rot, 1)
            rotate_q(0, 0)
            for g in range(14):
                if g < 6:
                    dve.wait_ge(kv_ps, g + 1)
                    dve.tensor_copy(KT[0:HD, 2 * g + 1, :], ps[HD:P, 4 + g % 4, :]).then_inc(kv_dve, 1)
                    if g == 5:
                        rotate_q(1, 1)
                        dve.wait_ge(kr_rot, 2)
                        dve.tensor_copy(KT[HD:QK, 6:12, :], KR2[:, 0:1, :].broadcast_to([ROPE, 6, T])).then_inc(kr_dve, 1)
                elif g % 2:
                    dve.wait_ge(kv_ps, g + 1)
                    dve.tensor_copy(V[:, (g - 6) // 2, 6 * HD:], ps[:, 4 + g % 4, 0:6 * HD]).then_inc(kv_dve, 1)

            def o_head(h):
                return O[:, :, bass.ds(h * HD, HD)]

            rotate_q(2, 0)
            for h in range(2):
                soft_max(h, h, CAUS, first=True)

            def mla_unit(u, s, project=True, begin=False):
                probs_out(u, s)
                if project:
                    rotate_q(u + 3, 1 - s)
                if not begin:
                    head_out(u - 1, 1 - s, o_head(u - 1))
                soft_max(u + 2, s, CAUS)

            mla_unit(0, 0, begin=True)
            mla_unit(1, 1)
            with dve.Fori(1, HEADS // 2 - 2) as i:
                for s in range(2):
                    mla_unit(2 * i + s, s)
            mla_unit(8, 0)
            mla_unit(9, 1, project=False)

            def mem_out(u, h):
                head_out(u, u % 2, O[:, :, TOKW + h * HD:TOKW + (h + 1) * HD])

            for h in range(2):
                u = 10 + h
                probs_out(u, h)
                head_out(u - 1, 1 - h, o_head(u - 1))
                own_sums(u, h)
                mem_max(u + 2, h)
            for h in range(MEM_HEADS):
                u = 12 + h
                probs_out(u, u % 2)
                if h == 0:
                    head_out(11, 1, o_head(11))
                else:
                    mem_out(u - 1, h - 1)
                own_sums(u, u % 2)
                if h < 2:
                    mem_max(u + 2, u % 2)
            mem_out(15, 3)
            mix_lo_of(0)
            for j in range(8):
                p = BASE["wo0"] + j
                rest(p + 2)
                dve.wait_ge(pe_panel, p + 1)
                dve.scalar_tensor_tensor(XT[:, j, :], XT[:, j, :], ALPHA, ps[:, p % 4, :], ALU.mult, ALU.add).then_inc(taken[p % 4], 1)
            norm("wo0")
            ffn("ffn1", nothing)
            norm("ffn1")
            modulation(0)

            for j in range(6):
                rest(BASE["kv"] + j + 2)
                if j == 2:
                    for e in range(2):
                        dve.wait_ge(*taken_at("kv", e))
                        for a in range(2):
                            for g in range(GROUPS):
                                r = slice(g * HD, (g + 1) * HD)
                                ins = dve.tensor_tensor(ZB[a * HD:(a + 1) * HD, e, :, g, 0:NCMP],
                                                        ZC[r, e, 16 * a:16 * a + 16 * NCMP].rearrange("p (n l) -> p l n", l=16),
                                                        POS[r, e, 16 * a:16 * a + 16].rearrange("p (l o) -> p l o", o=1).broadcast_to([HD, 16, NCMP]), ALU.add)
                        ins.then_inc(zb_ready, 1)
            for e, dst in enumerate((VS, VW)):
                dve.wait_ge(vt_ps, e + 1)
                dve.tensor_copy(dst[:].rearrange("p t c -> p (t c)"), ps[:, 4 + e, :]).then_inc(vt_out, 1)
            ffn("ffn2", nothing)
            norm("ffn2")
            modulation(1)

            for j in range(9):
                rest(BASE["nsa"] + j + 2)
                if 4 <= j < 8:
                    br, g = divmod(j - 4, GROUPS)
                    dve.wait_ge(kx_hi, 2 * (j - 3))
                    r = slice(g * HD, (g + 1) * HD)
                    for half in range(2):
                        dve.tensor_tensor(KX[half * HD:(half + 1) * HD, br, g, 1, :], (KS, KW)[br][r], KX[r, br, g, 0, :].bitcast(F32), ALU.subtract
                                          ).then_inc(kx_ready, 1)
                if j == 3:
                    dve.wait_ge(g_ps, 1)
                    for t in range(TT):
                        ins = dve.tensor_copy(G[:, :, :, t, :], ps[:, 4, t * 36:(t + 1) * 36].rearrange("p (g j b) -> p b j g", g=GROUPS, j=HPG))
                    ins.then_inc(g_out, 1)
            scale[0] = SEL_SCALE
            dve.wait_ge(cmask_in, 16)
            dve.wait_ge(sp_in[0], IN["bias"] + 32)
            for g in range(GROUPS):
                soft_max(16 + g, g, BIAS[:, 0, g], first=True)

            def cmp_take(u, j, q):
                dve.wait_ge(s_ps, u + 1)
                wait(dve, c_t, j)
                dve.tensor_tensor(SC[:].rearrange("p t g n -> p (t g n)"), ps[:, 6, TT * 2 * NPAD:], CB[:, q], ALU.add).then_inc(c_sc, 1)

            def cmp_max(j):
                dve.wait_ge(c_sc, 2 * j + 1)
                dve.tensor_reduce(MC[:], SC[:], AX.X, ALU.max).then_inc(c_sc, 1)
                dve.wait_ge(c_sc, 2 * j + 2)
                dve.tensor_tensor(SC[:], SC[:], MC[:].rearrange("p t (g o) -> p t g o", o=1).broadcast_to([P, TT, GROUPS, NPAD]), ALU.subtract).then_inc(c_sub, 1)

            def cmp_probs(j):
                dve.wait_ge(c_mask, j + 1)
                dve.tensor_reduce(SMC[:], SC[:], AX.X, ALU.add).then_inc(c_sum, 1)
                dve.wait_ge(c_sum, 4 * j + 1)
                dve.tensor_scalar(SMC[:], SMC[:], 1e-30, None, ALU.max).then_inc(c_sum, 1)
                dve.wait_ge(c_sum, 4 * j + 2)
                dve.reciprocal(SMC[:], SMC[:]).then_inc(c_sum, 1)
                dve.wait_ge(c_sum, 4 * j + 3)
                dve.tensor_tensor(SMC[:], SMC[:], G[:, 0, bass.ds(j, 1)].rearrange("p o t g -> p (o t) g"), ALU.mult).then_inc(c_sum, 1)
                dve.wait_ge(c_sum, 4 * j + 4)
                dve.tensor_tensor(SC[:], SC[:], SMC[:].rearrange("p t (g o) -> p t g o", o=1).broadcast_to([P, TT, GROUPS, NPAD]), ALU.mult).then_inc(c_p, 1)

            def gated_out(u, j, k):
                s, g, br = k % 2, k % 2, k // 2
                dve.wait_ge(rs_ready, u + 1)
                dve.tensor_tensor(W4[:, s, :], RS[:, s, :], G[:, 1 + br, bass.ds(j, 1), :, g].rearrange("p o t -> p (o t)"), ALU.mult).then_inc(w4_ready, 1)
                dve.wait_ge(w4_ready, u - 15)
                dve.wait_ge(pv_ps, u + 1)
                dst = O[:, :, bass.ds(g * HPG * HD + j * HD, HD)]
                src = ps[:, 7, 0:TT * HD].rearrange("p (t d) -> p t d", t=TT)
                if br == 0:
                    dve.tensor_tensor(dst, src, W4[:, s, :].rearrange("p (t o) -> p t o", o=1).broadcast_to([P, TT, HD]), ALU.mult).then_inc(o_done, 1)
                else:
                    dve.wait_ge(o_done, u - 1)
                    for t in range(TT):
                        ins = dve.scalar_tensor_tensor(dst[:, t], src[:, t], W4[:, s, t:t + 1], dst[:, t], ALU.mult, ALU.add)
                    ins.then_inc(o_done, 1)

            def cmp_out(j):
                dve.wait_ge(c_pv, j + 1)
                dve.wait_ge(o_done, 20 + 4 * j)
                for g in range(GROUPS):
                    dst = O[:, :, bass.ds(g * HPG * HD + j * HD, HD)]
                    ins = dve.tensor_tensor(dst, dst, ps[:, 3, :].rearrange("p (t g d) -> p t g d", t=TT, g=GROUPS)[:, :, g], ALU.add)
                ins.then_inc(c_o, 1)

            def nsa_pair(j, q, slot, last=False):
                for k in range(4):
                    u = 16 + 4 * j + k
                    begin = isinstance(j, int) and j == 0 and k == 0
                    probs_out(u, k % 2)
                    if k > 0:
                        gated_out(u - 1, j, k - 1)
                    elif not begin:
                        gated_out(u - 1, j - 1, 3)
                    if k == 1:
                        cmp_take(u + 2, j, q)
                    if k < 2:
                        soft_max(u + 2, k % 2, BIAS[:, q, k % 2])
                    elif not last:
                        if k == 2:
                            dve.wait_ge(sp_in[1 - q], 32 * slot + IN["bias"])
                        soft_max(u + 2, k % 2, BIAS[:, 1 - q, k % 2])
                    else:
                        own_sums(u, k % 2)
                        mem_max(u + 2, k % 2)
                    if k == 1:
                        if not (isinstance(j, int) and j == 0):
                            cmp_out(j - 1)
                        cmp_max(j)
                    if k == 3:
                        cmp_probs(j)

            nsa_pair(0, 0, 1)
            nsa_pair(1, 1, 2)
            with dve.Fori(1, HPG // 2 - 1) as i:
                nsa_pair(2 * i, 0, i + 1)
                nsa_pair(2 * i + 1, 1, i + 2)
            nsa_pair(4, 0, 3)
            nsa_pair(5, 1, 0, last=True)
            for h in range(MEM_HEADS):
                u = 40 + h
                probs_out(u, u % 2)
                if h == 0:
                    gated_out(39, 5, 3)
                else:
                    mem_out(u - 1, h - 1)
                own_sums(u, u % 2)
                if h < 2:
                    mem_max(u + 2, u % 2)
                if h == 1:
                    cmp_out(HPG - 1)
            mem_out(43, 3)
            mix_lo_of(8)
            for j in range(8):
                p = BASE["wo1"] + j
                rest(p + 2)
                dve.wait_ge(pe_panel, p + 1)
                dve.scalar_tensor_tensor(XT[:, j, :], XT[:, j, :], ALPHA, ps[:, p % 4, :], ALU.mult, ALU.add).then_inc(taken[p % 4], 1)
                context(j)
            norm("wo1", beside=context_in)
            ffn("ffn3", nothing)
            norm("ffn3", split=False, beside=context_states_beside)

            rms("even", 0, beside=context_states_beside_even)

            def advance(states, k, before_first):
                before = states[:, :, :, bass.ds(k - 1, 1)].rearrange("p r g o -> p o r g").broadcast_to([P, 2, 2, S5G])
                here = states[:, :, :, bass.ds(k, 1)].rearrange("p r g o -> p r (g o)")
                n = before_first + 3 * k - 3
                dve.wait_ge(scan, n)
                dve.tensor_tensor(SCM, L8[:], before, ALU.mult).then_inc(scan, 1)
                dve.wait_ge(scan, n + 1)
                dve.tensor_tensor(SCA, SCM[:, 0], SCM[:, 1][:, ::-1], ALU.add).then_inc(scan, 1)
                dve.wait_ge(scan, n + 2)
                dve.tensor_tensor(here, here, SCA, ALU.add).then_inc(scan, 1)

            dve.wait_ge(bk_ready, 1)
            dve.wait_ge(h_act, S5T)
            dve.wait_ge(h_dve, S5T)
            with dve.Fori(0, 2) as i:
                for j in range(4):
                    rest(BASE["even"] + j + 2, i)
                    for k in range(3):
                        advance(HC, 12 * i + 3 * j + k + 1, 1)
            for j in range(2):
                rest(BASE["even"] + 10 + j)
                for k in range(4):
                    advance(HC, 24 + 4 * j + k + 1, 1)
            dve.wait_ge(scan, 3 * NCC + 1)
            dve.wait_ge(shuffle_out, 2 * 16 * 6)
            dve.tensor_copy(H[:, :, :, 0:1], HC[:, :, :, NCC:]).then_inc(scan, 1)
            for t in range(S5T):
                for b in range(4):
                    dve.wait_ge(b_ps, S5T + 4 * t + b + 1)
                    g = t * GT + (b % 2) * 4
                    src = ps[S5P:P, 4 + b, 0:4 * NCL].rearrange("p (g c) -> p g c", g=4)
                    dve.tensor_copy(H[S5P:P, b // 2, g:g + 4, 1:], src[:, :, ::-1]).then_inc(h_dve, 1)
            dve.wait_ge(h_act, 5 * S5T)
            dve.wait_ge(h_dve, 5 * S5T)
            with dve.Fori(0, NCL // 4) as i:
                for k in range(4):
                    advance(H, 4 * i + k + 1, 3 * NCC + 2)
            dve.wait_ge(scan, 3 * NC + 2)

            def states(t):
                wait(dve, y_ps, t - 1)
                dve.tensor_copy(SS[S5P:P, t % 2], H[S5P:P, :, t * GT:(t + 1) * GT, 0:NCL][:, :, :, ::-1]).then_inc(ss_dve, 1)

            dve.wait_ge(fnet_ps, 8)
            for t in range(S5T):
                states(t)
            for j in range(6):
                dve.wait_ge(ya_hi, j + 1)
                dve.tensor_tensor(XL[:, j, :], YA[:, j, :], XH[:, j, :].bitcast(F32), ALU.subtract).then_inc(x_split, 1)

            for e in range(2):
                dve.wait_ge(p1_ready, e + 1)
                dve.tensor_copy(YH[:, 6 + e, :], ZS[:, 6 + e, :]).then_inc(y_full, 1)
                dve.wait_ge(y_full, e + 1)
                dve.tensor_tensor(YL[:, 6 + e, :], ZS[:, 6 + e, :], YH[:, 6 + e, :].bitcast(F32), ALU.subtract).then_inc(y_ready, 1)
            for j in range(6):
                p = BASE["glu"] + j
                rest(p + 2)
                dve.wait_ge(p1_ready, 3 + j)
                dve.wait_ge(*taken_at("glu", j))
                dve.tensor_tensor(YH[:, j, :], SIG[:, j % 2, :], ZS[:, j, :], ALU.mult)
                dve.tensor_tensor(YF[:, j % 2, :], SIG[:, j % 2, :], ZS[:, j, :], ALU.mult).then_inc(y_full, 1)
                dve.wait_ge(y_full, j + 3)
                dve.tensor_tensor(YL[:, j, :], YF[:, j % 2, :], YH[:, j, :].bitcast(F32), ALU.subtract).then_inc(y_ready, 1)
            gated("ewo", 0)
            rms("odd", 1)

            for j in range(4):
                rest(BASE["odd"] + j + 2)
            dve.wait_ge(odd_zero, 1)
            link = 0
            for k in range(4):
                p = BASE["odd"] + 4 + 3 * k
                rest(p + 2)
                rest(p + 3)
                dve.wait_ge(*taken_at("odd", 4 + 3 * k))
                dve.wait_ge(pe_panel, p + 2)
                v, cx = CV[:, k % 2, :], CX[:, k % 2, :]
                dve.tensor_tensor(v[:, 1:T + 1], CG[:, k % 2, :], ps[:, (p + 1) % 4, :], ALU.mult).then_inc(taken[(p + 1) % 4], 1)
                dve.wait_ge(*taken_at("odd", 5 + 3 * k))
                w = [COL[:, 96 + 82 + 4 * c + k:96 + 83 + 4 * c + k] for c in range(3)]
                dve.tensor_scalar(cx, v[:, 1:T + 1], w[1], None, ALU.mult).then_inc(dve_link, 1)
                dve.wait_ge(dve_link, 3 * k + 2)
                dve.scalar_tensor_tensor(cx, v[:, 0:T], w[0], cx, ALU.mult, ALU.add).then_inc(dve_link, 1)
                dve.wait_ge(dve_link, 3 * k + 3)
                dve.scalar_tensor_tensor(cx, v[:, 2:T + 2], w[2], cx, ALU.mult, ALU.add).then_inc(dve_link, 1)
                rest(p + 4)
                dve.wait_ge(dve_link, 3 * k + 4)
                dve.wait_ge(pe_panel, p + 3)
                dve.tensor_tensor(YO[:, 4 + k, :], cx, ps[:, (p + 2) % 4, :], ALU.mult).then_inc(taken[(p + 2) % 4], 1)
            for j in range(8):
                p = BASE["odd"] + 16 + j
                rest(p + 2)
                if j < 4:
                    dve.wait_ge(yc_ready, j + 1)
                else:
                    dve.wait_ge(*taken_at("odd", 6 + 3 * (j - 4)))
                dve.wait_ge(*taken_at("odd", 16 + j))
                dve.tensor_tensor(YH[:, j, :], YO[:, j, :], ZO[:, j % 2, :], ALU.mult)
                dve.tensor_tensor(YQ[:, j % 2, :], YO[:, j, :], ZO[:, j % 2, :], ALU.mult).then_inc(y_full, 1)
                dve.wait_ge(y_full, 8 + j + 1)
                dve.tensor_tensor(YL[:, j, :], YQ[:, j % 2, :], YH[:, j, :].bitcast(F32), ALU.subtract).then_inc(y_ready, 1)
            gated("owo", 1)
            reciprocal(0)
            for d in range(KD):
                dve.scalar_tensor_tensor(XT[:, d, :], XT[:, d, :], COL[:, 96 + 64 + d:96 + 65 + d], RST[:, 0, :], ALU.mult, ALU.mult).then_inc(ln_aff, 1)

        @block.gpsimd
        def _(pool):
            def norm(stage, last, split=True, beside=None):
                no = LN_NO[stage]
                for d in range(KD - 1):
                    pool.wait_ge(*taken_at(stage, last - KD + d))
                    if d == 0:
                        pool.tensor_copy(ACC[:], XT[:, 0, :]).then_inc(ln_acc, 1)
                    else:
                        pool.wait_ge(ln_acc, 7 * no + d)
                        pool.tensor_tensor(ACC[:], ACC[:], XT[:, d, :], ALU.add).then_inc(ln_acc, 1)
                if beside is not None:
                    beside()
                for d in range(KD if split else 0):
                    if d in BY_DVE:
                        continue
                    pool.wait_ge(ln_aff, 8 * no + d + 1)
                    pool.tensor_tensor(XL[:, d, :], XT[:, d, :], XH[:, d, :].bitcast(F32), ALU.subtract).then_inc(x_split, 1)

            n = [0]

            def step(ins):
                n[0] += 1
                ins.then_inc(pool_link, 1)
                pool.wait_ge(pool_link, n[0])

            def product(a, b, outs, shape):
                size = int(np.prod(shape[1:]))
                t1, t2 = (t[:, 0:size] for t in (T1, T2))
                if len(shape) == 3:
                    t1, t2 = (t.rearrange("p (x y) -> p x y", x=shape[1]) for t in (t1, t2))
                if len(shape) == 4:
                    t1, t2 = (t.rearrange("p (x y z) -> p x y z", x=shape[1], y=shape[2]) for t in (t1, t2))
                for e, op in enumerate((ALU.subtract, ALU.add)):
                    pool.tensor_tensor(t1, a[0], b[e], ALU.mult)
                    step(pool.tensor_tensor(t2, a[1], b[1 - e], ALU.mult))
                    for rows, dst in outs:
                        step(pool.tensor_tensor(dst[e], t1[rows], t2[rows], op))

            FWD, BWD, ALL = slice(0, S5P), slice(S5P, P), slice(0, P)

            for r, name in enumerate(("s5_lam_re_2", "s5_lam_im_2")):
                pool.dma_start(LAMN[:, r, :].rearrange("g (d p) -> g d p", d=2), A[name][0].rearrange("d g p -> g d p")).then_inc(s5_in, 16)
            pool.dma_start(LSN, A["s5_log_step_2"][0]).then_inc(s5_in, 16)
            pool.dma_start(DN, A["s5_d_2"][0]).then_inc(s5_in, 16)
            pool.dma_start(DSEL, C["dirsel"]).then_inc(s5_in, 16)
            for r, (bn, cn) in enumerate((("s5_b_re_2", "s5_c_re_2"), ("s5_b_im_2", "s5_c_im_2"))):
                for e in range(2):
                    pool.dma_start(CN[:, r, :, e, :], A[cn][0, e].rearrange("(t g) h p -> (g h) t p", g=GT)).then_inc(s5_in, 16)
                    pool.dma_start(BN[e * S5P:(e + 1) * S5P, r], A[bn][0, e].rearrange("g p h -> p g h")).then_inc(s5_in, 16)
            pool.wait_ge(s5_in, 16 * S5_LOADS)
            step(pool.memset(PW[:, 0, 0, :], 1.0))
            step(pool.memset(PW[:, 1, 0, :], 0.0))
            pool.wait_ge(f_ready, 1)
            for k in (1, 2, 4):
                product([PW[:, r, 1:1 + k, :] for r in range(2)], [PW[:, r, k:k + 1, :].broadcast_to([P, k, S5G]) for r in range(2)],
                        [(ALL, [PW[:, r, k + 1:2 * k + 1, :] for r in range(2)])], [P, k, S5G])
            product([FB5[:, r, :].rearrange("p (g o) -> p g o", o=1).broadcast_to([P, S5G, S5H]) for r in range(2)], [BN[:, r] for r in range(2)],
                    [(ALL, [BB[:, r] for r in range(2)])], [P, S5G, S5H])

            def powers(r, rows, ks):
                return PW[rows, r, ks, :].rearrange("p k g -> p g k")
            for rows, up, down in ((FWD, slice(1, L + 1), slice(L - 1, None, -1)), (BWD, slice(L, 0, -1), slice(0, L))):
                step(pool.tensor_copy(PC[rows, 0], powers(0, rows, up)))
                step(pool.tensor_scalar(PC[rows, 1], powers(1, rows, up), -1.0, None, ALU.mult))
                for r in range(2):
                    step(pool.tensor_copy(PB[rows, r], powers(r, rows, down)))
            for r in range(2):
                step(pool.tensor_copy(L8[:, 0, r, :], PW[:, 0, L, :]))
            step(pool.tensor_copy(L8[:, 1, 0, :], PW[:, 1, L, :]))
            step(pool.tensor_scalar(L8[:, 1, 1, :], PW[:, 1, L, :], -1.0, None, ALU.mult))
            pool.wait_ge(s5_tr, 4)
            pool.wait_ge(cr_out, 3)
            step(pool.memset(SW[:], 0.0))

            def tile(t):
                gs = slice(t * GT, (t + 1) * GT)

                def over_time(x):
                    return [x[:, r, gs, :].rearrange("p g (o h) -> p g o h", o=1).broadcast_to([P, GT, L, S5H]) for r in range(2)]

                def over_channels(x):
                    return [x[:, r, gs, :].rearrange("p g (t o) -> p g t o", o=1).broadcast_to([P, GT, L, S5H]) for r in range(2)]

                def cut(x, rows, col):
                    return [x[rows, r, :, col:col + P].rearrange("p g (t h) -> p g t h", t=L) for r in range(2)]
                wait(pool, s5_z, 4 * t)
                wait(pool, s5_out, 64 * t)
                product(over_time(BB), over_channels(PB), [(ALL, cut(BK, ALL, 0))], [P, GT, L, S5H])
                product(over_time(CR), over_channels(PC), [(FWD, cut(SW, FWD, (L + 1) * S5H)), (BWD, cut(SW, BWD, 0))], [P, GT, L, S5H])
                for r in range(2):
                    ins = pool.tensor_copy(SW[:, r, :, L * S5H:(L + 1) * S5H], CR[:, r, gs, :])
                ins.then_inc(bk_ready, 1)
                step(pool.tensor_tensor(DD, IDENT[0:S5H, 0:S5H].rearrange("p (o h) -> p o h", o=1).broadcast_to([S5H, GT, S5H]),
                                        DT[:, gs].rearrange("p (g o) -> p g o", o=1).broadcast_to([S5H, GT, S5H]), ALU.mult))
                pool.wait_ge(z_out, 4 * t + 4)
                mid = Z[:, :, (L - 1) * S5H:L * S5H]
                step(pool.tensor_tensor(mid, mid, DD, ALU.add))
                for rows, col in ((FWD, (L + 1) * S5H), (BWD, 0)):
                    pool.dma_start(scratch["s5_w"][t, rows], SW[rows, :, :, col:col + P].rearrange("p r g c -> p (r g) c")).then_inc(s5_out, 16)
                pool.wait_ge(bt_act, 2 * t + 2)
                pool.wait_ge(bt_dve, 2 * t + 2)
                pool.dma_start(scratch["s5_b"][t], BT[:].rearrange("p r g c -> p (r g c)")).then_inc(s5_out, 16)
                pool.dma_start(scratch["s5_taps"][:, gs], Z[:]).then_inc(s5_out, 16)

            for t in range(S5T):
                tile(t)
            norm("ffn0", 68)
            pool.wait_ge(s5_out, 64 * S5T)
            for t in range(L):
                pool.dma_start(scratch["s5_m"][t * S5H:(t + 1) * S5H], scratch["s5_taps"][:, :, (L - 1 - t) * S5H:(L - 1 - t) * S5H + P]).then_inc(s5_out, 16)
            norm("wo0", 8)

            def load_ada(layer):
                w = A["ada_w_2"][layer].rearrange("(k p) n -> p k n", p=P)
                prod = NS[:].rearrange("p s t -> p (s t)")[:, 0:KD * 2 * P].rearrange("p (k c) -> p k c", k=KD)

                def load(n):
                    pool.dma_start(AW[:, n % 2], w[:, :, n * 2 * P:(n + 1) * 2 * P]).then_inc(pool_in[n % 2], 16)
                load(0)
                load(1)
                for n in range(12):
                    pool.wait_ge(pool_in[n % 2], IN["ada"] + 16 * (6 * layer + n // 2 + 1))
                    wait(pool, ada_used, 12 * layer + n - 1)
                    for e in range(ada_conditions(layer, n)):
                        step(pool.tensor_tensor(prod, AW[:, n % 2], CS[:, :, e:e + 1].broadcast_to([P, KD, 2 * P]), ALU.mult))
                        step(pool.tensor_tensor(prod[:, 0:4], prod[:, 0:4], prod[:, 4:8], ALU.add))
                        step(pool.tensor_tensor(prod[:, 0:2], prod[:, 0:2], prod[:, 2:4], ALU.add))
                        ins = pool.tensor_tensor(AS[:, n % 2, e], prod[:, 0], prod[:, 1], ALU.add)
                        if e < ada_conditions(layer, n) - 1:
                            step(ins)
                    ins.then_inc(ada_part, 1)
                    pool.wait_ge(ada_part, 12 * layer + n + 1)
                    if n + 2 < 12:
                        load(n + 2)

            pool.wait_ge(pe_panel, BASE["ffn1"])
            for t in (H1, KCB, VCB):
                ins = pool.memset(t[:], 0.0)
                if t is not KCB:
                    ins.then_inc(zeros, 1)
            pool.wait_ge(cs_ready, 1)
            load_ada(0)
            for j in range(2):
                for a in range(2):
                    pool.dma_start(W1[j][a * HD:(a + 1) * HD], A["cmp_w1"][j].rearrange("(a l d) h -> a d l h", a=2, d=HD)[a]).then_inc(w1_in, 16)
                pool.dma_start(W2[:, j], A["cmp_w2"][j].rearrange("(m p) d -> p m d", p=P)).then_inc(w1_in, 16)
            norm("ffn1", 68)
            pool.wait_ge(hid_ps, 4)
            load_ada(1)
            norm("ffn2", 68)
            pool.wait_ge(cmask_in, 16)

            def rest_of_q(j, q):
                for g in range(GROUPS):
                    r, other = slice(g * HD, (g + 1) * HD), slice((1 - g) * HD, (2 - g) * HD)
                    pool.wait_ge(qs_hi, 2 * j + g + 1)
                    pool.tensor_tensor(QS[other, q, g, :], QP[r, j, :], QS[r, q, g, :].bitcast(F32), ALU.subtract).then_inc(qs_ready, 1)
                    pool.wait_ge(qs_ready, 2 * j + g + 1)

            def mask(j):
                pool.wait_ge(c_exp, j + 1)
                pool.tensor_tensor(SC[:], SC[:], CMASK[:].rearrange("p (t o n) -> p t o n", o=1, n=NPAD).broadcast_to([P, TT, GROUPS, NPAD]), ALU.mult).then_inc(c_mask, 1)

            pool.wait_ge(x_split, XS["nsa"] + 6)
            rest_of_q(0, 0)
            for j in range(HPG):
                if j + 1 < HPG:
                    wait(pool, c_mask, j)
                    rest_of_q(j + 1, (j + 1) % 2)
                mask(j)
            pool.wait_ge(mix_ps, 16)
            pool.dma_start(CXN[:], A["ctx_2"][0].rearrange("(m p) d -> p m d", p=P)).then_inc(cx_in, 16)
            pool.dma_start(SCT[:].rearrange("p k t -> p (k t)"), C["sincos"]).then_inc(cx_in, 16)
            for k in range(KD):
                pool.wait_ge(cx_hi, k + 1)
                pool.tensor_tensor(CL[:, k, :], CXT[:, k, :], CH[:, k, :].bitcast(F32), ALU.subtract).then_inc(cx_split, 1)

            def rests(p0, p1):
                for p in range(p0, p1):
                    pool.wait_ge(w_hi, p + 1)
                    pool.wait_ge(w_lo, p)
                    pool.tensor_tensor(wl[:, p % 2, :], raw[:, p % 4, :], wh[:, p % 2, :].bitcast(F32), ALU.subtract).then_inc(w_lo, 1)

            norm("wo1", 8, beside=lambda: rests(BASE["ctx"] + 2, BASE["ctx"] + 6))
            u_rows = scratch["s5_u"].rearrange("(g h) t c -> t h g c", h=S5H)

            def load_b(t):
                pool.dma_start(BS[:, t % 3].rearrange("p r g c -> p (r g c)"), scratch["s5_b"][t % S5T]).then_inc(pool_in[t % 3], 16)
            for j in range(6):
                pool.wait_ge(*taken_at("ctx", j))
                pool.dma_start(scratch["s5_u"][j * P:(j + 1) * P, :, 0:NCC], UTC[:, j]).then_inc(shuffle_out, 16)
            pool.wait_ge(shuffle_out, 16 * 6)
            pool.wait_ge(pe_panel, BASE["ffn3"])
            for t in range(L):
                pool.dma_start(UC[t * S5H:(t + 1) * S5H], u_rows[t][:, :, 0:NCC]).then_inc(shuffle_in, 16)
            for t in range(3):
                load_b(t)
            pool.wait_ge(cx_in, 32)
            for k in range(KD):
                pool.tensor_scalar(SCT[:, k, :], SCT[:, k, :], COL[:, 88 + k:89 + k], None, ALU.add).then_inc(sct_ready, 1)
            norm("ffn3", 68, split=False)
            for t in range(3, S5T):
                pool.wait_ge(b_ps, t - 2)
                load_b(t)

            for d in range(KD):
                if d in BY_DVE:
                    continue
                pool.wait_ge(ln_aff, 8 * LN_NO["even"] + d + 1)
                pool.tensor_tensor(XL[:, d, :], NT[:, d, :], XH[:, d, :].bitcast(F32), ALU.subtract).then_inc(x_split, 1)
            for t in range(3):
                pool.wait_ge(b_ps, t + 4)
                load_b(S5T + t)
            for j in range(6):
                pool.wait_ge(*taken_at("even", j))
                pool.dma_start(scratch["s5_u"][j * P:(j + 1) * P, :, NCC:], UT[:, j]).then_inc(shuffle_out, 16)
            pool.wait_ge(shuffle_out, 2 * 16 * 6)
            for t in range(L):
                pool.dma_start(U[t * S5H:(t + 1) * S5H], u_rows[t][:, :, NCC:]).then_inc(shuffle_in, 16)
            for t in range(3, S5T):
                pool.wait_ge(b_ps, S5T + 4 * (t - 3) + 4)
                load_b(S5T + t)

            pool.wait_ge(b_ps, 5 * S5T)
            pool.wait_ge(scan, 3 * NCC + 2)
            step(pool.memset(FW[:], 0.0))
            for b in range(4):
                r = slice((b % 2) * HD, (b % 2 + 1) * HD)
                pool.dma_start(FW[r, b // 2, r], A["fnet_w_2"][0, b]).then_inc(dft_in, 16)
            pool.dma_start(DFTC[:], C["dftc"]).then_inc(dft_in, 16)
            pool.dma_start(DFTT[:].rearrange("p e t c -> p (e t c)"), C["dftt"]).then_inc(dft_in, 16)
            rests(BASE["even"] + 12, BASE["glu"] + 2)
            def load_w(t):
                pool.dma_start(WT[t].rearrange("p r g c -> p (r g c)"), scratch["s5_w"][t].rearrange("p g c -> p (g c)")
                               ).then_inc(pool_in[2] if t < 3 else w_in, 16)
            pool.wait_ge(s5_out, 64 * S5T + 16 * L)
            for t in range(S5T):
                wait(pool, m_ps, t - 1)
                pool.dma_start(MM[:, t % 2], scratch["s5_m"][:, t * GT:(t + 1) * GT]).then_inc(pool_in[t % 2], 16)
                if t == 1:
                    pool.wait_ge(fnet_ps, 8)
                if 1 <= t < 4:
                    load_w(t - 1)
            pool.wait_ge(m_ps, S5T)
            for t in (3, 4):
                load_w(t)
            pool.wait_ge(y_ps, 1)
            pool.wait_ge(w_in, 32)
            load_w(5)
            for j in range(2):
                pool.wait_ge(fnet_out, 7 + j)
                pool.wait_ge(*taken_at("even", 14 + j))
                pool.tensor_tensor(ZS[:, 6 + j, :], ZS[:, 6 + j, :], YB[:, j, :], ALU.mult).then_inc(p1_ready, 1)
            for j in range(6):
                pool.wait_ge(ya_ready, j + 1)
                pool.wait_ge(*taken_at("even", 8 + j))
                pool.tensor_tensor(ZS[:, j, :], ZS[:, j, :], YA[:, j, :], ALU.mult).then_inc(p1_ready, 1)

            pool.wait_ge(y_ready, 8)
            pool.dma_start(PINV[:].rearrange("p i t -> p (i t)"), C["poolinv"]).then_inc(odd_in, 16)
            pool.dma_start(PWT[:], A["pool_w_2"][0].rearrange("i c d -> c i d")).then_inc(odd_in, 16)
            for d in range(KD):
                if d in BY_DVE:
                    continue
                pool.wait_ge(ln_aff, 8 * LN_NO["odd"] + d + 1)
                pool.tensor_tensor(XL[:, d, :], NO[:, d, :], XH[:, d, :].bitcast(F32), ALU.subtract).then_inc(x_split, 1)
            pool.wait_ge(x_split, XS["odd"] + 6)
            pool.wait_ge(x_dve, XD["odd"] + 2)
            pool.memset(CV[:], 0.0)
            pool.memset(PU[:], 0.0).then_inc(odd_zero, 1)
            pool.wait_ge(odd_in, 32)
            for i, w in enumerate(POOL_WINDOWS):
                pool.wait_ge(*taken_at("odd", i))
                if i >= 2:
                    pool.wait_ge(pw_ps, i - 1)
                src, have, a = PU[:, i, :], 1, 0
                while have < w:
                    size = T + PAD - 2 * have + 9
                    lo = PAD - 8
                    step(pool.tensor_tensor(PS[:, a, lo:lo + size], src[:, lo:lo + size], src[:, lo + have:lo + have + size], ALU.add))
                    src, have, a = PS[:, a, :], 2 * have, 1 - a
                step(pool.tensor_tensor(PP[:, i % 2, :], src[:, PAD - w // 2:PAD - w // 2 + T], PINV[:, i, :], ALU.mult))
                pool.tensor_tensor(PP[:, i % 2, :], PP[:, i % 2, :], PU[:, i, PAD:PAD + T], ALU.subtract).then_inc(pool_ready, 1)


SCRATCH = {
    "s5_w": (S5T, P, 2 * GT, P),
    "s5_b": (S5T, P, 2 * GT * P),
    "s5_taps": (S5H, S5G, (STRIP - 2) * S5H),
    "s5_m": (P, S5G, P),
    "s5_u": (6 * P, L, NC),
    "s5_y": (6 * P, L, NCL),
}


def kernel(**inputs):
    import concourse.bacc as bacc
    from concourse.bass_utils import run_bass_kernel_spmd

    nc = bacc.Bacc("TRN2", target_bir_lowering=False, num_devices=1)
    arrays = {}

    def given(name, a):
        arrays[name] = np.ascontiguousarray(a)
        return nc.dram_tensor(name, arrays[name].shape, mybir.dt.from_np(arrays[name].dtype), kind="ExternalInput").ap()

    A = {name: given("in_" + name, a) for name, a in inputs.items()}
    C = {name: given("const_" + name, a) for name, a in constants().items()}
    out = nc.dram_tensor("out", (1, T, D), F32, kind="ExternalOutput").ap()
    scratch = {name: nc.dram_tensor(name, shape, F32, kind="Internal").ap() for name, shape in SCRATCH.items()}
    program(nc, A, C, out, scratch)
    r = run_bass_kernel_spmd(nc, [arrays], core_ids=[0])
    return r.results[0]["out"]
```
